# Optimizing a Trainium2 kernel written in Bass

```python
import math
import jax
import jax.numpy as jnp
from jax import lax
import numpy as np

D_MODEL = 1024
BATCH = 1
SEQ = 1024
DEPTH = 1
DEC_BATCH = 8
DEC_SEQ = 8
PAST_LEN = 4096
PAGE_SIZE = 128

N_HEADS = 8
HEAD_DIM = 64
KV_HEADS = 2
HPG = N_HEADS // KV_HEADS
ATT_W = N_HEADS * HEAD_DIM
L_CMP = 32
S_CMP = 16
L_SLC = 64
N_SEL = 16
WINDOW = 512
CMP_HID = 64
Q_BLOCK = 64
ROPE_THETA = 10000.0
N_KV_SLOTS = 4
SSM_HEADS = 8
SSM_HEAD_DIM = 64
D_INNER = SSM_HEADS * SSM_HEAD_DIM
SSM_GROUPS = 2
D_STATE = 64
CONV_W = 4
CONV_DIM = D_INNER + 2 * SSM_GROUPS * D_STATE
SSM_CHUNK = 128
N_EXPERT_GROUPS = 4
EXPERTS_PER_GROUP = 8
N_EXPERTS = N_EXPERT_GROUPS * EXPERTS_PER_GROUP
TOP_K = 2
D_EXPERT = 512
MOE_BLOCK = 128
PLE_DIM = 256
EPS = 1e-6
SPLIT_SIZES = (ATT_W, 6 * KV_HEADS * HEAD_DIM, 3 * N_HEADS, D_INNER, CONV_DIM, SSM_HEADS)
D_IN_PROJ = ATT_W + 6 * KV_HEADS * HEAD_DIM + 3 * N_HEADS + D_INNER + CONV_DIM + SSM_HEADS

kernel_name = 'hymba_nsa_ssd_hmoe_decode_step'

def rmsnorm(x, g):
    xf = x.astype(jnp.float32)
    y = xf * lax.rsqrt(jnp.mean(xf * xf, axis=-1, keepdims=True) + EPS)
    return (y * g.astype(jnp.float32)).astype(x.dtype)

def rope(x, pos):
    half = HEAD_DIM // 2
    inv = ROPE_THETA ** (-jnp.arange(half, dtype=jnp.float32) / half)
    ang = pos.astype(jnp.float32)[:, None] * inv[None, :]
    cos, sin = jnp.cos(ang)[:, None, :], jnp.sin(ang)[:, None, :]
    xf = x.astype(jnp.float32)
    x1, x2 = xf[..., :half], xf[..., half:]
    return jnp.concatenate([x1 * cos - x2 * sin, x2 * cos + x1 * sin], axis=-1).astype(x.dtype)

def masked_softmax(s, mask):
    s = jnp.where(mask, s, -1e30)
    e = jnp.exp(s - jnp.max(s, axis=-1, keepdims=True)) * mask
    return e / jnp.maximum(jnp.sum(e, axis=-1, keepdims=True), 1e-30)

def compress(rows, pe, w1, w2):
    bt, t_kv = rows.shape[:2]
    n_seg = t_kv // S_CMP
    n_cmp = (t_kv - L_CMP) // S_CMP + 1
    seg = rows[:, :n_seg * S_CMP].reshape(bt, n_seg, S_CMP, KV_HEADS, HEAD_DIM)
    w1r = w1.reshape(L_CMP, HEAD_DIM, CMP_HID)
    hid = jnp.einsum('ld,ldf->f', pe, w1r, preferred_element_type=jnp.float32)
    for r in range(L_CMP // S_CMP):
        part = jnp.einsum('bnsgd,sdf->bngf', seg, w1r[r * S_CMP:(r + 1) * S_CMP], preferred_element_type=jnp.float32)
        hid = hid + part[:, r:r + n_cmp]
    return jnp.einsum('bngf,fd->bngd', jax.nn.silu(hid).astype(rows.dtype), w2)

def cover_matrix(n_cmp, n_slc):
    c0 = jnp.arange(n_cmp)[:, None] * S_CMP
    s0 = jnp.arange(n_slc)[None, :] * L_SLC
    shared = jnp.minimum(c0 + L_CMP, s0 + L_SLC) - jnp.maximum(c0, s0)
    return jnp.maximum(shared, 0).astype(jnp.float32) / L_CMP

def nsa_attention(q, kv_all, win_all, q_off, cmp_pe, cmp_w1, cmp_w2):
    bt, lq = q.shape[:2]
    t_kv = kv_all.shape[1]
    scale = HEAD_DIM ** -0.5
    q_rot = rope(q, q_off + jnp.arange(lq))
    kc = compress(kv_all[:, :, 0], cmp_pe[0], cmp_w1[0], cmp_w2[0])
    vc = compress(kv_all[:, :, 1], cmp_pe[1], cmp_w1[1], cmp_w2[1])
    n_cmp = kc.shape[1]
    n_slc = -(-t_kv // L_SLC)

    def to_blocks(r):
        r = jnp.pad(r, ((0, 0), (0, n_slc * L_SLC - t_kv), (0, 0), (0, 0)))
        return r.reshape(bt, n_slc, L_SLC, KV_HEADS, HEAD_DIM).transpose(0, 3, 1, 2, 4)

    ks, vs = to_blocks(kv_all[:, :, 2]), to_blocks(kv_all[:, :, 3])
    kw, vw = win_all[:, :, 0], win_all[:, :, 1]
    cover = cover_matrix(n_cmp, n_slc)
    cmp_end = jnp.arange(n_cmp) * S_CMP + (L_CMP - 1)
    blk = jnp.arange(n_slc)
    k_sel = min(N_SEL, n_slc)
    qb = math.gcd(lq, Q_BLOCK)
    n_qb = lq // qb
    qa = jnp.arange(qb)
    band = jnp.arange(qb + WINDOW)
    bi = jnp.arange(bt)[:, None, None, None]
    gi = jnp.arange(KV_HEADS)[None, :, None, None]

    def one_block(args):
        i, qp, qr = args
        pos = q_off + i * qb + qa
        s1 = jnp.einsum('bqghd,bngd->bghqn', qp, kc, preferred_element_type=jnp.float32) * scale
        p1 = masked_softmax(s1, cmp_end[None, :] <= pos[:, None])
        o_c = jnp.einsum('bghqn,bngd->bqghd', p1.astype(vc.dtype), vc)
        imp = jnp.einsum('bghqn,nj->bgqj', p1, cover)
        cur = pos // L_SLC
        vis = blk[None, :] <= cur[:, None]
        forced = vis & ((blk[None, :] == 0) | (blk[None, :] >= cur[:, None] - 1))
        score = jnp.where(forced, 1e9, jnp.where(vis, imp, -1.0))
        top_s, idx = lax.top_k(score, k_sel)
        kg = ks[bi, gi, idx].reshape(bt, KV_HEADS, qb, k_sel * L_SLC, HEAD_DIM)
        vg = vs[bi, gi, idx].reshape(bt, KV_HEADS, qb, k_sel * L_SLC, HEAD_DIM)
        kpos = idx[..., None] * L_SLC + jnp.arange(L_SLC)
        ok = ((top_s > -0.5)[..., None] & (kpos <= pos[None, None, :, None, None])).reshape(bt, KV_HEADS, qb, k_sel * L_SLC)
        s2 = jnp.einsum('bqghd,bgqmd->bghqm', qr, kg, preferred_element_type=jnp.float32) * scale
        p2 = masked_softmax(s2, ok[:, :, None])
        o_s = jnp.einsum('bghqm,bgqmd->bqghd', p2.astype(vg.dtype), vg)
        kwb = lax.dynamic_slice_in_dim(kw, i * qb, qb + WINDOW, axis=1)
        vwb = lax.dynamic_slice_in_dim(vw, i * qb, qb + WINDOW, axis=1)
        kpos_w = q_off - WINDOW + i * qb + band
        m3 = (band[None, :] > qa[:, None]) & (band[None, :] <= qa[:, None] + WINDOW) & (kpos_w >= 0)[None, :]
        s3 = jnp.einsum('bqghd,bkgd->bghqk', qr, kwb, preferred_element_type=jnp.float32) * scale
        p3 = masked_softmax(s3, m3)
        o_w = jnp.einsum('bghqk,bkgd->bqghd', p3.astype(vwb.dtype), vwb)
        return o_c, o_s, o_w

    def split_q(t):
        return jnp.moveaxis(t.reshape(bt, n_qb, qb, KV_HEADS, HPG, HEAD_DIM), 1, 0)

    def merge(o):
        return jnp.moveaxis(o, 0, 1).reshape(bt, lq, N_HEADS, HEAD_DIM)

    oc, os_, ow = lax.map(one_block, (jnp.arange(n_qb), split_q(q), split_q(q_rot)))
    return merge(oc), merge(os_), merge(ow)

def ssd_scan(x, a, b, c, s0, cl):
    bt, L, H, P = x.shape
    nc = L // cl
    x = x.reshape(bt, nc, cl, H, P)
    b = b.reshape(bt, nc, cl, H, -1)
    c = c.reshape(bt, nc, cl, H, -1)
    acum = jnp.cumsum(a.reshape(bt, nc, cl, H).transpose(0, 3, 1, 2), axis=-1)
    causal = jnp.tril(jnp.ones((cl, cl), dtype=bool))
    decay = jnp.exp(jnp.where(causal, acum[..., :, None] - acum[..., None, :], -jnp.inf))
    cb = jnp.einsum('bclhn,bcshn->bhcls', c, b) * decay
    y_diag = jnp.einsum('bhcls,bcshp->bclhp', cb, x)
    w_end = jnp.exp(acum[..., -1:] - acum)
    chunk_states = jnp.einsum('bclhn,bhcl,bclhp->bchpn', b, w_end, x)
    chunk_decay = jnp.exp(acum[..., -1])

    def step(s, inp):
        st, dec = inp
        return s * dec[..., None, None] + st, s

    s_final, s_in = lax.scan(step, s0, (jnp.moveaxis(chunk_states, 1, 0), jnp.moveaxis(chunk_decay, 2, 0)))
    y_off = jnp.einsum('bclhn,cbhpn,bhcl->bclhp', c, s_in, jnp.exp(acum))
    return (y_diag + y_off).reshape(bt, L, H, P), s_final

def token_mixers(a, q_off, kv_past, win_buf, ssm0, conv0, win_keep, w):
    bt, L, _ = a.shape
    cuts = [int(v) for v in np.cumsum(SPLIT_SIZES)[:-1]]
    q, kvs, gl, z, xbc, dt = jnp.split(a @ w['w_in'], cuts, axis=-1)
    pos = q_off + jnp.arange(L)
    q = rmsnorm(q.reshape(bt, L, N_HEADS, HEAD_DIM), w['q_norm'])
    kvs = kvs.reshape(bt, L, 6, KV_HEADS, HEAD_DIM)
    k_c = rmsnorm(kvs[:, :, 0], w['k_norm'][0])
    k_s = rope(rmsnorm(kvs[:, :, 2], w['k_norm'][1]), pos)
    k_w = rope(rmsnorm(kvs[:, :, 4], w['k_norm'][2]), pos)
    kv_new = jnp.stack([k_c, kvs[:, :, 1], k_s, kvs[:, :, 3]], axis=2)
    win_new = jnp.stack([k_w, kvs[:, :, 5]], axis=2)
    kv_all = jnp.concatenate([kv_past, kv_new], axis=1)
    win_cat = jnp.concatenate([win_buf, win_new], axis=1)
    win_all = jnp.pad(win_cat, ((0, 0), (WINDOW - win_buf.shape[1], 0), (0, 0), (0, 0), (0, 0)))
    o_c, o_s, o_w = nsa_attention(q, kv_all, win_all, q_off, w['cmp_pe'], w['cmp_w1'], w['cmp_w2'])
    g = jax.nn.sigmoid(gl.astype(jnp.float32)).reshape(bt, L, N_HEADS, 3, 1)
    attn = (g[:, :, :, 0] * o_c + g[:, :, :, 1] * o_s + g[:, :, :, 2] * o_w).astype(a.dtype).reshape(bt, L, ATT_W)
    xbc_all = jnp.concatenate([conv0, xbc], axis=1)
    conv = w['conv_b'] + xbc_all[:, 0:L] * w['conv_w'][0]
    for j in range(1, CONV_W):
        conv = conv + xbc_all[:, j:j + L] * w['conv_w'][j]
    conv_new = xbc_all[:, xbc_all.shape[1] - (CONV_W - 1):]
    xs, b_in, c_in = jnp.split(jax.nn.silu(conv), [D_INNER, D_INNER + SSM_GROUPS * D_STATE], axis=-1)
    rep = SSM_HEADS // SSM_GROUPS
    xs = xs.reshape(bt, L, SSM_HEADS, SSM_HEAD_DIM).astype(jnp.float32)
    b_h = jnp.repeat(b_in.reshape(bt, L, SSM_GROUPS, D_STATE), rep, axis=2).astype(jnp.float32)
    c_h = jnp.repeat(c_in.reshape(bt, L, SSM_GROUPS, D_STATE), rep, axis=2).astype(jnp.float32)
    dt = jax.nn.softplus(dt.astype(jnp.float32) + w['dt_bias'].astype(jnp.float32))
    a_h = -jnp.exp(w['a_log'].astype(jnp.float32))
    y, ssm_new = ssd_scan(xs * dt[..., None], a_h * dt, b_h, c_h, ssm0.astype(jnp.float32), math.gcd(L, SSM_CHUNK))
    y = y + w['ssm_d'].astype(jnp.float32)[:, None] * xs
    gated = y.reshape(bt, L, D_INNER) * jax.nn.silu(z.astype(jnp.float32))
    ssd_out = rmsnorm(gated, w['ssm_norm']).astype(a.dtype)
    mix = jnp.concatenate([attn, ssd_out], axis=-1) @ w['w_out']
    return mix, kv_new, win_cat[:, win_cat.shape[1] - win_keep:], ssm_new.astype(ssm0.dtype), conv_new

def hier_moe(f, w_rg, b_rg, w_re, b_re, w_gate, w_up, w_down):
    bt, L, d = f.shape
    xf = f.reshape(bt * L, d)
    n_tok = xf.shape[0]
    pg = jax.nn.softmax(jnp.dot(xf, w_rg, preferred_element_type=jnp.float32) + b_rg.astype(jnp.float32), axis=-1)
    g_sel = jnp.argmax(pg, axis=-1)
    g_w = jnp.max(pg, axis=-1)
    el = (jnp.dot(xf, w_re, preferred_element_type=jnp.float32) + b_re.astype(jnp.float32)).reshape(n_tok, N_EXPERT_GROUPS, EXPERTS_PER_GROUP)
    el = el[jnp.arange(n_tok), g_sel]
    top_p, top_i = lax.top_k(jax.nn.softmax(el, axis=-1), TOP_K)
    wts = (g_w[:, None] * top_p / jnp.sum(top_p, axis=-1, keepdims=True)).reshape(-1)
    eid = (g_sel[:, None] * EXPERTS_PER_GROUP + top_i).reshape(-1)
    n_asg = eid.shape[0]
    order = jnp.argsort(eid)
    e_sorted = eid[order]
    tok = order // TOP_K
    sizes = jnp.bincount(eid, length=N_EXPERTS)
    start = jnp.cumsum(sizes) - sizes
    padded = (sizes + MOE_BLOCK - 1) // MOE_BLOCK * MOE_BLOCK
    pend = jnp.cumsum(padded)
    dest = (pend - padded)[e_sorted] + jnp.arange(n_asg) - start[e_sorted]
    n_blk = -(-n_asg // MOE_BLOCK) + N_EXPERTS
    xpad = jnp.zeros((n_blk * MOE_BLOCK, d), xf.dtype).at[dest].set(xf[tok])
    blk_e = jnp.minimum(jnp.searchsorted(pend, jnp.arange(n_blk) * MOE_BLOCK, side='right'), N_EXPERTS - 1)

    def expert_block(args):
        xb, e = args
        hb = jax.nn.silu(xb @ w_gate[e]) * (xb @ w_up[e])
        return hb @ w_down[e]

    ypad = lax.map(expert_block, (xpad.reshape(n_blk, MOE_BLOCK, d), blk_e)).reshape(n_blk * MOE_BLOCK, d)
    y = ypad[dest] * wts[order][:, None].astype(xf.dtype)
    return jnp.zeros_like(xf).at[tok].add(y).reshape(bt, L, d)

def decoder_layer(x, p, q_off, kv_past, win_buf, ssm0, conv0, win_keep, w):
    mix, kv_new, win_new, ssm_new, conv_new = token_mixers(rmsnorm(x, w['attn_norm']), q_off, kv_past, win_buf, ssm0, conv0, win_keep, w)
    h = x + mix
    h = h + hier_moe(rmsnorm(h, w['ffn_norm']), w['w_rg'], w['b_rg'], w['w_re'], w['b_re'], w['w_gate'], w['w_up'], w['w_down'])
    h = h + jax.nn.sigmoid(h @ w['w_ple_gate']) * rmsnorm(p @ w['w_ple_proj'], w['ple_norm'])
    return h, kv_new, win_new, ssm_new, conv_new

def setup_inputs(seed: int = 0) -> dict:
    key = jax.random.key(seed)
    keys = iter(list(jax.random.split(key, 48)))

    def nrm(shape, scale=1.0):
        return scale * jax.random.normal(next(keys), shape, jnp.float32)

    def gain(shape):
        return 1.0 + 0.1 * jax.random.normal(next(keys), shape, jnp.float32)

    n_pages = PAST_LEN // PAGE_SIZE
    n_used = DEC_BATCH * n_pages
    n_pool = n_used + n_used // 4
    wbuf = min(WINDOW, PAST_LEN)
    inp = {}
    inp['x_prompt'] = nrm((BATCH, SEQ, D_MODEL))
    inp['x_sample'] = nrm((DEC_BATCH, DEC_SEQ, D_MODEL))
    inp['cache_kv'] = nrm((DEPTH, n_pool, PAGE_SIZE, N_KV_SLOTS, KV_HEADS, HEAD_DIM))
    inp['cache_win'] = nrm((DEPTH, DEC_BATCH, wbuf, 2, KV_HEADS, HEAD_DIM))
    inp['state_ssm'] = nrm((DEPTH, DEC_BATCH, SSM_HEADS, SSM_HEAD_DIM, D_STATE), 0.5)
    inp['state_conv'] = nrm((DEPTH, DEC_BATCH, CONV_W - 1, CONV_DIM))
    inp['page_table'] = jax.random.permutation(next(keys), n_pool)[:n_used].reshape(DEC_BATCH, n_pages).astype(jnp.int32)
    inp['p_prompt'] = nrm((DEPTH, BATCH, SEQ, PLE_DIM))
    inp['p_sample'] = nrm((DEPTH, DEC_BATCH, DEC_SEQ, PLE_DIM))
    inp['w_in'] = nrm((DEPTH, D_MODEL, D_IN_PROJ), D_MODEL ** -0.5)
    inp['w_out'] = nrm((DEPTH, ATT_W + D_INNER, D_MODEL), (ATT_W + D_INNER) ** -0.5)
    inp['q_norm'] = gain((DEPTH, HEAD_DIM))
    inp['k_norm'] = gain((DEPTH, 3, HEAD_DIM))
    inp['cmp_pe'] = nrm((DEPTH, 2, L_CMP, HEAD_DIM), 0.1)
    inp['cmp_w1'] = nrm((DEPTH, 2, L_CMP * HEAD_DIM, CMP_HID), (L_CMP * HEAD_DIM) ** -0.5)
    inp['cmp_w2'] = nrm((DEPTH, 2, CMP_HID, HEAD_DIM), CMP_HID ** -0.5)
    inp['conv_w'] = nrm((DEPTH, CONV_W, CONV_DIM), CONV_W ** -0.5)
    inp['conv_b'] = nrm((DEPTH, CONV_DIM), 0.1)
    dt0 = jnp.exp(jax.random.uniform(next(keys), (DEPTH, SSM_HEADS), jnp.float32, math.log(1e-3), math.log(1e-1)))
    inp['dt_bias'] = dt0 + jnp.log(-jnp.expm1(-dt0))
    inp['a_log'] = jnp.log(jax.random.uniform(next(keys), (DEPTH, SSM_HEADS), jnp.float32, 1.0, 16.0))
    inp['ssm_d'] = gain((DEPTH, SSM_HEADS))
    inp['ssm_norm'] = gain((DEPTH, D_INNER))
    inp['attn_norm'] = gain((DEPTH, D_MODEL))
    inp['ffn_norm'] = gain((DEPTH, D_MODEL))
    inp['w_rg'] = nrm((DEPTH, D_MODEL, N_EXPERT_GROUPS), D_MODEL ** -0.5)
    inp['b_rg'] = nrm((DEPTH, N_EXPERT_GROUPS), 0.01)
    inp['w_re'] = nrm((DEPTH, D_MODEL, N_EXPERTS), D_MODEL ** -0.5)
    inp['b_re'] = nrm((DEPTH, N_EXPERTS), 0.01)
    inp['w_gate'] = nrm((DEPTH, N_EXPERTS, D_MODEL, D_EXPERT), D_MODEL ** -0.5)
    inp['w_up'] = nrm((DEPTH, N_EXPERTS, D_MODEL, D_EXPERT), D_MODEL ** -0.5)
    inp['w_down'] = nrm((DEPTH, N_EXPERTS, D_EXPERT, D_MODEL), D_EXPERT ** -0.5)
    inp['w_ple_proj'] = nrm((DEPTH, PLE_DIM, D_MODEL), PLE_DIM ** -0.5)
    inp['ple_norm'] = gain((DEPTH, D_MODEL))
    inp['w_ple_gate'] = nrm((DEPTH, D_MODEL, D_MODEL), D_MODEL ** -0.5)
    return inp

def reference(x_prompt, x_sample, cache_kv, cache_win, state_ssm, state_conv, page_table, p_prompt, p_sample,
              w_in, w_out, q_norm, k_norm, cmp_pe, cmp_w1, cmp_w2, conv_w, conv_b, dt_bias, a_log, ssm_d, ssm_norm,
              attn_norm, ffn_norm, w_rg, b_rg, w_re, b_re, w_gate, w_up, w_down, w_ple_proj, ple_norm, w_ple_gate):
    hp, hs = x_prompt, x_sample
    bp = x_prompt.shape[0]
    kv_p, kv_s, win_p, win_s, ssm_p, ssm_s, conv_p, conv_s = [], [], [], [], [], [], [], []
    for l in range(DEPTH):
        w = dict(w_in=w_in[l], w_out=w_out[l], q_norm=q_norm[l], k_norm=k_norm[l], cmp_pe=cmp_pe[l],
                 cmp_w1=cmp_w1[l], cmp_w2=cmp_w2[l], conv_w=conv_w[l], conv_b=conv_b[l], dt_bias=dt_bias[l],
                 a_log=a_log[l], ssm_d=ssm_d[l], ssm_norm=ssm_norm[l], attn_norm=attn_norm[l],
                 ffn_norm=ffn_norm[l], w_rg=w_rg[l], b_rg=b_rg[l], w_re=w_re[l], b_re=b_re[l],
                 w_gate=w_gate[l], w_up=w_up[l], w_down=w_down[l], w_ple_proj=w_ple_proj[l],
                 ple_norm=ple_norm[l], w_ple_gate=w_ple_gate[l])
        hp, kvn, winn, ssmn, convn = decoder_layer(
            hp, p_prompt[l], 0,
            jnp.zeros((bp, 0, N_KV_SLOTS, KV_HEADS, HEAD_DIM), hp.dtype),
            jnp.zeros((bp, 0, 2, KV_HEADS, HEAD_DIM), hp.dtype),
            jnp.zeros((bp, SSM_HEADS, SSM_HEAD_DIM, D_STATE), hp.dtype),
            jnp.zeros((bp, CONV_W - 1, CONV_DIM), hp.dtype),
            min(WINDOW, hp.shape[1]), w)
        kv_p.append(kvn); win_p.append(winn); ssm_p.append(ssmn); conv_p.append(convn)
        pool = cache_kv[l]
        kv_past = pool[page_table].reshape(page_table.shape[0], page_table.shape[1] * PAGE_SIZE, N_KV_SLOTS, KV_HEADS, HEAD_DIM)
        hs, kvn, winn, ssmn, convn = decoder_layer(
            hs, p_sample[l], PAST_LEN, kv_past, cache_win[l], state_ssm[l], state_conv[l], cache_win.shape[2], w)
        kv_s.append(kvn); win_s.append(winn); ssm_s.append(ssmn); conv_s.append(convn)
    return (hp, hs, jnp.stack(kv_p), jnp.stack(kv_s), jnp.stack(win_p), jnp.stack(win_s), jnp.stack(ssm_p), jnp.stack(ssm_s), jnp.stack(conv_p), jnp.stack(conv_s))


_drawn_inputs = setup_inputs


def setup_inputs(seed=0):
    import zlib

    import numpy as np

    out = dict(_drawn_inputs(seed))
    spreads = {}
    factors = {'q_norm': 4.27, 'b_rg': 2.88, 'b_re': 11.463}
    for name, (base, spread) in spreads.items():
        noise = np.random.default_rng([zlib.crc32(name.encode()), seed]).standard_normal(out[name].shape)
        drawn = base * np.exp(spread * noise) if base else spread * noise
        out[name] = jnp.asarray(drawn.astype(out[name].dtype))
    for name, factor in factors.items():
        out[name] = (out[name] * factor).astype(out[name].dtype)
    return out
```

```python
from contextlib import ExitStack

import numpy as np

import concourse.bass as bass
from concourse import mybir

ALU = mybir.AluOpType
ACT = mybir.ActivationFunctionType
F32 = mybir.dt.float32
I32 = mybir.dt.int32
U32 = mybir.dt.uint32
AX = mybir.AxisListType.X
P = 128

D_MODEL, SEQ, DEC_BATCH, DEC_SEQ, PAST, PAGE = 1024, 1024, 8, 8, 4096, 128
HEADS, HD, KVH = 8, 64, 2
HPG = HEADS // KVH
ATT_W = HEADS * HD
L_CMP, S_CMP, L_SLC, N_SEL, WINDOW = 32, 16, 64, 16, 512
SH, SN, D_INNER = 8, 64, 512
CONV_DIM, CONV_W = 768, 4
NG, EPG, NE = 4, 8, 32
D_EXP = 512
PLE = 256
EPS = 1e-6
KC = D_MODEL // P
NT = SEQ // P
TILES = NT + 1
TOK = TILES * P
N_SMP = DEC_BATCH * DEC_SEQ
N_PAGES = PAST // PAGE
N_CMP_P = (SEQ - L_CMP) // S_CMP + 1
N_SEG_S = PAST // S_CMP
N_CMP_S = (PAST + DEC_SEQ - L_CMP) // S_CMP + 1
N_SLC_S = -(-(PAST + DEC_SEQ) // L_SLC)
SCALE = HD ** -0.5
NEG = -1e30
C_KV, C_GL, C_Z, C_XBC, C_DT, C_END = 512, 1280, 1304, 1816, 2584, 2592
QKV = 20 * HD
MAIN_BLOCKS = NE
OVER_BLOCKS = 2 * (SEQ + N_SMP) // P - 1
DUMP = (MAIN_BLOCKS + OVER_BLOCKS) * P
SLOTS = DUMP + 2 * P


class Chain:

    def __init__(self, eng, sem, per=0, i=None):
        self.eng, self.sem, self.per, self.i, self.k = eng, sem, per, i, 0

    def __call__(self, ins, passed=None):
        self.k += 1
        ins.then_inc(self.sem, 1)
        base = self.k if self.i is None else self.i * self.per + self.k
        self.eng.wait_ge(self.sem, base)
        if passed is not None:
            self.eng.sem_inc(passed, 1)

    def close(self):
        assert self.k == self.per, (self.k, self.per)


def hold(eng, sem, value, passed):
    eng.wait_ge(sem, value)
    eng.sem_inc(passed, 1)


class Phase(ExitStack):

    def __init__(self, nc, name):
        super().__init__()
        self.nc, self.name, self.own = nc, name, []
        self.passed = self.sem("passed")
        self.callback(self.release)

    def release(self):
        self.nc.clear_and_free_semaphores(self.own)
        self.nc.all_engine_barrier()

    def sb(self, name, shape, dt=F32):
        return self.enter_context(self.nc.sbuf_tensor(f"{self.name}_{name}", shape, dt))

    def ps(self, name, shape):
        return self.enter_context(self.nc.psum_tensor(f"{self.name}_{name}", shape, F32))

    def sem(self, name):
        self.own.append(self.nc.alloc_semaphore(name=f"{self.name}_{name}"))
        return self.own[-1]


def project_phase(nc, d):
    with Phase(nc, "proj") as ph:
        w = ph.sb("w", [P, KC, C_END])
        x = ph.sb("x", [P, KC, P])
        sq = ph.sb("sq", [P, KC, P])
        a = ph.sb("a", [P, KC, P])
        lnv = ph.sb("lnv", [P, P])
        rinv = ph.sb("rinv", [P, P])
        gain = ph.sb("gain", [P, KC])
        qkv = ph.sb("qkv", [P, QKV])
        qkv_sq = ph.sb("qkv_sq", [P, QKV])
        qrot = ph.sb("qrot", [P, ATT_W])
        krot = ph.sb("krot", [P, 2, 2, HD])
        tmp = ph.sb("tmp", [P, HEADS, HD // 2])
        ss = ph.sb("ss", [P, 20])
        hr = ph.sb("hr", [P, 20])
        hgain = ph.sb("hgain", [P, 4, HD])
        trig = ph.sb("trig", [P, 2, HD // 2])
        gdt = ph.sb("gdt", [P, 32])
        z = ph.sb("z", [P, D_INNER])
        xbc = ph.sb("xbc", [P, 6, P])
        turned = ph.sb("turned", [P, 12, P])
        ones = ph.sb("ones", [P, P])
        ident = ph.sb("ident", [P, P])
        eps = ph.sb("eps", [P, 1])
        p_q, p_kv, p_kw = ph.ps("p_q", [P, 512]), ph.ps("p_kv", [P, 512]), ph.ps("p_kw", [P, 512])
        p_z, p_x0, p_x1 = ph.ps("p_z", [P, 512]), ph.ps("p_x0", [P, 3, P]), ph.ps("p_x1", [P, 3, P])
        p_ss = ph.ps("p_ss", [P, 512])

        const_ready, w_ready = ph.sem("const_ready"), ph.sem("w_ready")
        x_ready, x_free = ph.sem("x_ready"), ph.sem("x_free")
        trig_ready, trig_free = ph.sem("trig_ready"), ph.sem("trig_free")
        sq_ready, ss_ready, ln_ready, rinv_ready = ph.sem("sq_ready"), ph.sem("ss_ready"), ph.sem("ln_ready"), ph.sem("rinv_ready")
        a_ready, proj_ready = ph.sem("a_ready"), ph.sem("proj_ready")
        qkv_ready, z_ready, banks_free = ph.sem("qkv_ready"), ph.sem("z_ready"), ph.sem("banks_free")
        hss_ready, hln_ready, hr_ready, rot_ready = ph.sem("hss_ready"), ph.sem("hln_ready"), ph.sem("hr_ready"), ph.sem("rot_ready")
        turn_ready, turned_ready = ph.sem("turn_ready"), ph.sem("turned_ready")
        stored, a_free, dve_step = ph.sem("stored"), ph.sem("a_free"), ph.sem("dve_step")
        STORES = 8

        block = ph.enter_context(nc.Block())

        @block.sync
        def _(sp):
            sp.sem_inc(x_free, 1)
            sp.sem_inc(trig_free, 1)
            sp.sem_inc(a_free, 1)
            sp.sem_inc(banks_free, 1)
            sp.dma_start(ident[:], d["ident"]).then_inc(const_ready, 16)
            sp.dma_start(gain[:], d["attn_norm"]).then_inc(const_ready, 16)
            sp.dma_start(hgain[:], d["head_gain"]).then_inc(const_ready, 16)
            for k in range(KC):
                sp.dma_start(w[:, k, :], d["w_in"][:, k, :]).then_inc(w_ready, 16)
            with sp.Fori(0, TILES) as t:
                sp.wait_ge(x_free, t + 1)
                sp.dma_start(x[:], d["xT"][bass.ds(t, 1)].rearrange("o p c n -> (o p) c n")).then_inc(x_ready, 16)
                sp.wait_ge(trig_free, t + 1)
                sp.dma_start(trig[:], d["trig"][bass.ds(t, 1)].rearrange("o p c n -> (o p) c n")).then_inc(trig_ready, 16)

        @block.gpsimd
        def _(pool):
            with pool.Fori(0, TILES) as t:
                tok = bass.ds(t * P, P)
                hold(pool, z_ready, t * 3 + 3, ph.passed)
                pool.dma_start(d["z"][tok, :], z[:]).then_inc(stored, 16)
                pool.dma_start(d["gdt"][tok, :], gdt[:]).then_inc(stored, 16)
                pool.dma_start(d["xbc"][:, :, tok], xbc[:]).then_inc(stored, 16)
                hold(pool, rot_ready, t + 1, ph.passed)
                pool.dma_start(d["kv_out"][tok, 0:256], qkv[:, 512:768]).then_inc(stored, 16)
                pool.dma_start(d["kv_out"][tok, 256:384], krot[:, 0]).then_inc(stored, 16)
                pool.dma_start(d["kv_out"][tok, 384:512], qkv[:, 896:1024]).then_inc(stored, 16)
                pool.dma_start(d["win_new"][tok, 0:128], krot[:, 1]).then_inc(stored, 16)
                pool.dma_start(d["win_new"][tok, 128:256], qkv[:, 1152:1280]).then_inc(stored, 16)
                hold(pool, turned_ready, t * 3 + 3, ph.passed)
                pool.dma_start(d["turned"][:, :, tok], turned[:]).then_inc(stored, 16)
            pool.wait_ge(stored, TILES * 9 * 16)

        @block.scalar
        def _(act):
            act.wait_ge(const_ready, 49)
            with act.Fori(0, TILES) as t:
                act.wait_ge(x_ready, t * 16 + 16)
                nc.scalar.activation(sq[:], x[:], ACT.Square).then_inc(sq_ready, 1)
                act.wait_ge(ss_ready, t + 1)
                nc.scalar.activation(lnv[:], p_ss[:, 0:P], ACT.Ln, bias=eps[:], scale=1.0 / D_MODEL).then_inc(ln_ready, 1)
                act.wait_ge(ln_ready, t + 1)
                nc.scalar.activation(rinv[:], lnv[:], ACT.Exp, scale=-0.5).then_inc(rinv_ready, 1)
                act.wait_ge(proj_ready, t * 5 + 3)
                act.wait_ge(banks_free, t + 1)
                nc.scalar.activation(qkv[:, 0:512], p_q[:], ACT.Copy)
                nc.scalar.activation(qkv[:, 512:1024], p_kv[:], ACT.Copy)
                nc.scalar.activation(qkv[:, 1024:1280], p_kw[:, 0:256], ACT.Copy)
                nc.scalar.activation(gdt[:], p_kw[:, 256:288], ACT.Copy).then_inc(qkv_ready, 1)
                act.wait_ge(hss_ready, t + 1)
                nc.scalar.activation(ss[:], ss[:], ACT.Ln, bias=eps[:], scale=1.0 / HD).then_inc(hln_ready, 1)
                act.wait_ge(hln_ready, t + 1)
                nc.scalar.activation(hr[:], ss[:], ACT.Exp, scale=-0.5).then_inc(hr_ready, 1)
                act.wait_ge(turn_ready, t * 3 + 2)
                nc.scalar.activation(turned[:, 4:8, :], p_kv[:].rearrange("p (a b) -> p a b", a=4), ACT.Copy).then_inc(turned_ready, 1)

        @block.vector
        def _(dve):
            nc.vector.memset(ones[:], 1.0)
            nc.vector.memset(eps[:], EPS).then_inc(const_ready, 1)
            dve.wait_ge(const_ready, 49)
            with dve.Fori(0, TILES) as t:
                link = Chain(dve, dve_step, 21, t)
                dve.wait_ge(rinv_ready, t + 1)
                dve.wait_ge(a_free, t + 1)
                link(nc.vector.tensor_tensor(a[:], x[:], rinv[:].unsqueeze(1).broadcast_to([P, KC, P]), ALU.mult))
                dve.sem_inc(x_free, 1)
                nc.vector.tensor_tensor(a[:], a[:], gain[:].unsqueeze(2).broadcast_to([P, KC, P]), ALU.mult).then_inc(a_ready, 1)
                dve.wait_ge(proj_ready, t * 5 + 5)
                dve.wait_ge(banks_free, t + 1)
                nc.vector.tensor_copy(z[:], p_z[:]).then_inc(z_ready, 1)
                nc.vector.tensor_copy(xbc[:, 0:3, :], p_x0[:]).then_inc(z_ready, 1)
                dve.wait_ge(qkv_ready, t + 1)
                nc.vector.tensor_copy(xbc[:, 3:6, :], p_x1[:]).then_inc(z_ready, 1)
                link(nc.vector.tensor_tensor(qkv_sq[:], qkv[:], qkv[:], ALU.mult))
                nc.vector.reduce_sum(ss[:], qkv_sq[:].rearrange("p (h e) -> p h e", e=HD), AX).then_inc(hss_ready, 1)
                dve.wait_ge(hr_ready, t + 1)
                q3 = qkv[:, 0:512].rearrange("p (h e) -> p h e", e=HD)
                link(nc.vector.tensor_tensor(q3, q3, hr[:, 0:8].unsqueeze(2).broadcast_to([P, 8, HD]), ALU.mult))
                link(nc.vector.tensor_tensor(q3, q3, hgain[:, 0:1, :].broadcast_to([P, 8, HD]), ALU.mult))
                for b in range(3):
                    k3 = qkv[:, 512 + 256 * b:640 + 256 * b].rearrange("p (h e) -> p h e", e=HD)
                    link(nc.vector.tensor_tensor(k3, k3, hr[:, 8 + 4 * b:10 + 4 * b].unsqueeze(2).broadcast_to([P, 2, HD]), ALU.mult))
                    link(nc.vector.tensor_tensor(k3, k3, hgain[:, 1 + b:2 + b, :].broadcast_to([P, 2, HD]), ALU.mult))
                dve.wait_ge(trig_ready, t * 16 + 16)
                sets = [(q3, qrot[:].rearrange("p (h e) -> p h e", e=HD), 8)]
                sets += [(qkv[:, 768 + 256 * b:896 + 256 * b].rearrange("p (h e) -> p h e", e=HD), krot[:, b], 2) for b in range(2)]
                H2 = HD // 2
                for src, dst, n in sets:
                    cos = trig[:, 0:1, :].broadcast_to([P, n, H2])
                    sin = trig[:, 1:2, :].broadcast_to([P, n, H2])
                    x1, x2, t2 = src[:, :, 0:H2], src[:, :, H2:HD], tmp[:, 0:n, :]
                    nc.vector.tensor_tensor(dst[:, :, 0:H2], x1, cos, ALU.mult)
                    link(nc.vector.tensor_tensor(t2, x2, sin, ALU.mult))
                    link(nc.vector.tensor_tensor(dst[:, :, 0:H2], dst[:, :, 0:H2], t2, ALU.subtract))
                    nc.vector.tensor_tensor(dst[:, :, H2:HD], x2, cos, ALU.mult)
                    link(nc.vector.tensor_tensor(t2, x1, sin, ALU.mult))
                    last = nc.vector.tensor_tensor(dst[:, :, H2:HD], dst[:, :, H2:HD], t2, ALU.add)
                    if n == 2 and dst is not sets[1][1]:
                        last.then_inc(rot_ready, 1)
                    else:
                        link(last)
                dve.wait_ge(turn_ready, t * 3 + 3)
                nc.vector.tensor_copy(turned[:, 0:4, :], p_q[:].rearrange("p (a b) -> p a b", a=4)).then_inc(turned_ready, 1)
                nc.vector.tensor_copy(turned[:, 8:12, :], p_kw[:].rearrange("p (a b) -> p a b", a=4)).then_inc(turned_ready, 1)
                dve.sem_inc(trig_free, 1)
                dve.wait_ge(turned_ready, t * 3 + 3)
                dve.wait_ge(stored, t * 144 + 144)
                dve.sem_inc(banks_free, 1)
                link.close()

        @block.tensor
        def _(pe):
            pe.wait_ge(const_ready, 49)
            pe.wait_ge(w_ready, 16 * KC)
            with pe.Fori(0, TILES) as t:
                pe.wait_ge(sq_ready, t + 1)
                for k in range(KC):
                    mm = nc.tensor.matmul(p_ss[:, 0:P], ones[:], sq[:, k, :], start=(k == 0), stop=(k == KC - 1))
                mm.then_inc(ss_ready, 1)
                pe.wait_ge(a_ready, t + 1)
                pe.wait_ge(banks_free, t + 1)
                for dst, c0, c1 in ((p_q[:], 0, 512), (p_kv[:], 512, 1024), (p_kw[:, 0:280], 1024, 1304), (p_kw[:, 280:288], C_DT, C_END), (p_z[:], C_Z, C_XBC)):
                    for k in range(KC):
                        mm = nc.tensor.matmul(dst, a[:, k, :], w[:, k, c0:c1], start=(k == 0), stop=(k == KC - 1))
                    if c0 != 1024:
                        mm.then_inc(proj_ready, 1)
                for c in range(6):
                    dst = (p_x0, p_x1)[c // 3][:, c % 3, :]
                    for k in range(KC):
                        mm = nc.tensor.matmul(dst, w[:, k, C_XBC + c * P:C_XBC + c * P + P], a[:, k, :], start=(k == 0), stop=(k == KC - 1))
                mm.then_inc(proj_ready, 1)
                pe.wait_ge(proj_ready, t * 5 + 5)
                pe.sem_inc(a_free, 1)
                pe.wait_ge(rot_ready, t + 1)
                for bank, src in ((p_q, qkv), (p_kv, qrot)):
                    for j in range(HPG):
                        mm = nc.tensor.transpose(bank[:, j * P:(j + 1) * P], src[:, j * P:(j + 1) * P], ident[:])
                    mm.then_inc(turn_ready, 1)
                for j, src in enumerate((qkv[:, 512:640], qkv[:, 640:768], krot[:, 0].rearrange("p h e -> p (h e)"), krot[:, 1].rearrange("p h e -> p (h e)"))):
                    mm = nc.tensor.transpose(p_kw[:, j * P:(j + 1) * P], src, ident[:])
                mm.then_inc(turn_ready, 1)


def conv_phase(nc, d):
    with Phase(nc, "conv") as ph:
        raw = ph.sb("raw", [P, 6, 3 + SEQ])
        raw_s = ph.sb("raw_s", [P, 6, P // DEC_SEQ, 3 + DEC_SEQ])
        acc = ph.sb("acc", [P, 6, TOK])
        e = ph.sb("e", [P, 6, TOK])
        cw = ph.sb("cw", [P, 6, CONV_W])
        cb = ph.sb("cb", [P, 6])
        zeroed, loaded, conv_ready, exp_ready = ph.sem("zeroed"), ph.sem("loaded"), ph.sem("conv_ready"), ph.sem("exp_ready")
        stored, dve_step, act_ready = ph.sem("stored"), ph.sem("dve_step"), ph.sem("act_ready")
        block = ph.enter_context(nc.Block())

        @block.sync
        def _(sp):
            sp.wait_ge(zeroed, 2)
            sp.dma_start(cw[:], d["conv_w"]).then_inc(loaded, 16)
            sp.dma_start(cb[:], d["conv_b"]).then_inc(loaded, 16)
            for c in range(6):
                sp.dma_start(raw[:, c, 3:], d["xbc"][:, c, 0:SEQ]).then_inc(loaded, 16)
                sp.dma_start(raw_s[:, c, :, 3:], d["xbc"][:, c, SEQ:TOK].rearrange("p (b l) -> p b l", l=DEC_SEQ)).then_inc(loaded, 16)
                sp.dma_start(raw_s[:, c, 0:DEC_BATCH, 0:3], d["state_conv"][:, c]).then_inc(loaded, 16)
            sp.wait_ge(loaded, 20 * 16)
            sp.dma_start(d["conv_p"], raw[:, :, SEQ:SEQ + 3]).then_inc(stored, 16)
            for c in range(6):
                sp.dma_start(d["conv_s"][:, c], raw_s[:, c, 0:DEC_BATCH, DEC_SEQ:DEC_SEQ + 3]).then_inc(stored, 16)
            for c in range(6):
                sp.wait_ge(act_ready, c + 1)
                sp.dma_start(d["cv"][:, c], acc[:, c]).then_inc(stored, 16)
            sp.wait_ge(stored, 13 * 16)

        @block.scalar
        def _(act):
            for c in range(6):
                act.wait_ge(conv_ready, 2 * c + 2)
                nc.scalar.activation(e[:, c], acc[:, c], ACT.Exp, scale=-1.0).then_inc(exp_ready, 1)

        @block.vector
        def _(dve):
            link = Chain(dve, dve_step)
            nc.vector.memset(raw[:, :, 0:3], 0.0).then_inc(zeroed, 1)
            nc.vector.memset(raw_s[:], 0.0).then_inc(zeroed, 1)
            dve.wait_ge(loaded, 20 * 16)
            for c in range(6):
                smp = acc[:, c, SEQ:].rearrange("p (b l) -> p b l", l=DEC_SEQ)
                nc.vector.tensor_scalar(acc[:, c, 0:SEQ], raw[:, c, 0:SEQ], cw[:, c, 0:1], cb[:, c:c + 1], ALU.mult, ALU.add)
                link(nc.vector.tensor_scalar(smp, raw_s[:, c, :, 0:DEC_SEQ], cw[:, c, 0:1], cb[:, c:c + 1], ALU.mult, ALU.add))
                for j in range(1, CONV_W):
                    w = cw[:, c, j:j + 1]
                    i1 = nc.vector.scalar_tensor_tensor(acc[:, c, 0:SEQ], raw[:, c, j:j + SEQ], w, acc[:, c, 0:SEQ], ALU.mult, ALU.add)
                    if j == CONV_W - 1:
                        i1.then_inc(conv_ready, 1)
                    i2 = nc.vector.scalar_tensor_tensor(smp, raw_s[:, c, :, j:j + DEC_SEQ], w, smp, ALU.mult, ALU.add)
                    if j == CONV_W - 1:
                        i2.then_inc(conv_ready, 1)
                    else:
                        link(i2)
            for c in range(6):
                dve.wait_ge(exp_ready, c + 1)
                link(nc.vector.tensor_scalar(e[:, c], e[:, c], 1.0, None, ALU.add))
                link(nc.vector.reciprocal(e[:, c], e[:, c]))
                nc.vector.tensor_tensor(acc[:, c], acc[:, c], e[:, c], ALU.mult).then_inc(act_ready, 1)


def ssd_phase(nc, d):
    NB = DEC_BATCH
    with Phase(nc, "ssd") as ph:
        cv = ph.sb("cv", [P, 6, P])
        z = ph.sb("z", [P, 512])
        gdt = ph.sb("gdt", [P, 32])
        tri = ph.sb("tri", [P, 2, P])
        mask = ph.sb("mask", [P, 2, P])
        same = ph.sb("same", [P, 2, P])
        seqcol = ph.sb("seqcol", [P, NB])
        seqrow = ph.sb("seqrow", [P, NB, P])
        hb = ph.sb("hb", [P, 3, SH])
        gnorm = ph.sb("gnorm", [P, 512])
        ident = ph.sb("ident", [P, P])
        eps = ph.sb("eps", [P, 1])
        one = ph.sb("one", [P, 1])
        ah = ph.sb("ah", [P, SH])
        xd, ax, ex, u, lnu, m1, dt, a = (ph.sb(n, [P, SH]) for n in ("xd", "ax", "ex", "u", "lnu", "m1", "dt", "a"))
        acum = ph.sb("acum", [P, 2, SH])
        wd = ph.sb("wd", [P, SH])
        edec = ph.sb("edec", [P, 3, SH])
        xs, xdt, xw, y, t2, ez = (ph.sb(n, [P, 512]) for n in ("xs", "xdt", "xw", "y", "t2", "ez"))
        btok = ph.sb("btok", [P, P])
        m = ph.sb("m", [P, SH, P])
        st = ph.sb("st", [P, 256])
        sst = ph.sb("sst", [P, NB, 256])
        cm = ph.sb("cm", [P, NB, P])
        bm = ph.sb("bm", [P, NB, P])
        am = ph.sb("am", [P, NB, SH])
        et = ph.sb("et", [P, NB, SH])
        ss, rr = ph.sb("ss", [P, 1]), ph.sb("rr", [P, 1])
        p_s, p_x, p_y, p_e = (ph.ps(n, [P, 512]) for n in ("p_s", "p_x", "p_y", "p_e"))
        p_d = [ph.ps(f"p_d{i}", [P, 4, P]) for i in range(2)]
        p_c = [ph.ps(f"p_c{i}", [P, 512]) for i in range(2)]

        names = ("const_ready", "setup", "ah_ready", "loaded", "in_free", "ex_ready", "u_ready", "lnu_ready", "a_ready", "acum_ready", "wd_ready",
                 "edec_ready", "turned", "cb_ready", "diff_ready", "dm_ready", "dexp_ready", "m_ready", "yd_ready", "yo_ready", "xw_ready",
                 "st_ready", "state_ready", "ez_ready", "y_ready", "sq_ready", "ln_ready", "rr_ready", "out_ready", "stored", "dve_step", "smp_step",
                 "sstate_loaded", "masked", "et_sum", "et_ready", "sst_ready", "sst_done", "states_stored")
        s = {n: ph.sem(n) for n in names}
        block = ph.enter_context(nc.Block())

        @block.sync
        def _(sp):
            sp.sem_inc(s["in_free"], 1)
            for dst, src in ((tri, "tri"), (mask, "mask"), (same, "same"), (seqcol, "seqcol"), (seqrow, "seqrow"), (hb, "head_ssm"), (gnorm, "ssm_norm"), (ident, "ident")):
                sp.dma_start(dst[:], d[src]).then_inc(s["const_ready"], 16)
            sp.dma_start(sst[:], d["state_ssm"]).then_inc(s["sstate_loaded"], 16)

            def chunk(c, tok):
                sp.wait_ge(s["in_free"], c + 1)
                sp.dma_start(cv[:], d["cv"][:, :, tok]).then_inc(s["loaded"], 16)
                sp.dma_start(z[:], d["z"][tok, :]).then_inc(s["loaded"], 16)
                sp.dma_start(gdt[:], d["gdt"][tok, :]).then_inc(s["loaded"], 16)
                sp.wait_ge(s["out_ready"], c + 1)
                sp.dma_start(d["ssd"][tok, :], y[:]).then_inc(s["stored"], 16)

            with sp.Fori(0, NT) as c:
                chunk(c, bass.ds(c * P, P))
            chunk(NT, slice(SEQ, TOK))
            sp.dma_start(d["ssm_p"], st[:]).then_inc(s["states_stored"], 16)
            sp.wait_ge(s["sst_done"], 1)
            sp.dma_start(d["ssm_s"], sst[:]).then_inc(s["states_stored"], 16)
            sp.wait_ge(s["stored"], 16 * TILES)
            sp.wait_ge(s["states_stored"], 32)

        @block.scalar
        def _(act):
            act.wait_ge(s["const_ready"], 128)
            act.wait_ge(s["setup"], 2)
            nc.scalar.activation(ah[:], hb[:, 1, :], ACT.Exp).then_inc(s["ah_ready"], 1)

            def chunk(c, smp):
                act.wait_ge(s["u_ready"], 2 * c + 1)
                nc.scalar.activation(ex[:], ax[:], ACT.Exp, scale=-1.0).then_inc(s["ex_ready"], 1)
                act.wait_ge(s["u_ready"], 2 * c + 2)
                nc.scalar.activation(lnu[:], u[:], ACT.Ln).then_inc(s["lnu_ready"], 1)
                act.wait_ge(s["wd_ready"], c + 1)
                nc.scalar.activation(edec[:, 0, :], acum[:, 0, :], ACT.Exp)
                nc.scalar.activation(edec[:, 1, :], wd[:], ACT.Exp)
                nc.scalar.activation(edec[:, 2, :], acum[:, 1, :], ACT.Exp).then_inc(s["edec_ready"], 1)
                nc.scalar.activation(ez[:], z[:], ACT.Exp, scale=-1.0).then_inc(s["ez_ready"], 1)
                act.wait_ge(s["dm_ready"], c + 1)
                nc.scalar.activation(m[:], m[:], ACT.Exp).then_inc(s["dexp_ready"], 1)
                if smp:
                    act.wait_ge(s["et_sum"], 1)
                    nc.scalar.activation(et[:], p_e[:, 0:NB * SH].rearrange("p (b h) -> p b h", h=SH), ACT.Exp).then_inc(s["et_ready"], 1)
                act.wait_ge(s["y_ready"], c + 1)
                nc.scalar.activation(t2[:], y[:], ACT.Square, accum_out=ss[:]).then_inc(s["sq_ready"], 1)
                act.wait_ge(s["sq_ready"], c + 1)
                nc.scalar.activation(rr[:], ss[:], ACT.Ln, bias=eps[:], scale=1.0 / D_INNER).then_inc(s["ln_ready"], 1)
                act.wait_ge(s["ln_ready"], c + 1)
                nc.scalar.activation(rr[:], rr[:], ACT.Exp, scale=-0.5).then_inc(s["rr_ready"], 1)

            with act.Fori(0, NT) as c:
                chunk(c, False)
            chunk(NT, True)

        @block.vector
        def _(dve):
            nc.vector.memset(eps[:], EPS).then_inc(s["setup"], 1)
            nc.vector.memset(st[:], 0.0).then_inc(s["setup"], 1)
            dve.wait_ge(s["setup"], 2)
            dve.wait_ge(s["const_ready"], 128)
            dve.wait_ge(s["ah_ready"], 1)

            def h3(ap):
                return ap.rearrange("p (h e) -> p h e", e=HD)

            def over(ap, n=HD):
                return ap.unsqueeze(2).broadcast_to([ap.shape[0], ap.shape[1], n])

            def chunk(c, smp, link):
                dve.wait_ge(s["loaded"], c * 48 + 48)
                link(nc.vector.tensor_tensor(xd[:], gdt[:, 24:32], hb[:, 0, :], ALU.add))
                nc.vector.scalar_tensor_tensor(ax[:], xd[:], -1.0, xd[:], ALU.mult, ALU.max).then_inc(s["u_ready"], 1)
                dve.wait_ge(s["ex_ready"], c + 1)
                nc.vector.tensor_scalar(u[:], ex[:], 1.0, None, ALU.add).then_inc(s["u_ready"], 1)
                dve.wait_ge(s["u_ready"], c * 2 + 2)
                link(nc.vector.tensor_scalar(m1[:], u[:], 1.0, None, ALU.is_equal))
                link(nc.vector.scalar_tensor_tensor(dt[:], u[:], 1.0, m1[:], ALU.subtract, ALU.add))
                link(nc.vector.reciprocal(dt[:], dt[:]))
                link(nc.vector.tensor_tensor(dt[:], dt[:], ex[:], ALU.mult))
                dve.wait_ge(s["lnu_ready"], c + 1)
                link(nc.vector.tensor_tensor(m1[:], m1[:], lnu[:], ALU.add))
                link(nc.vector.tensor_tensor(dt[:], dt[:], m1[:], ALU.mult))
                link(nc.vector.scalar_tensor_tensor(dt[:], xd[:], 0.0, dt[:], ALU.max, ALU.add))
                nc.vector.scalar_tensor_tensor(a[:], ah[:], -1.0, dt[:], ALU.mult, ALU.mult).then_inc(s["a_ready"], 1)
                dve.wait_ge(s["acum_ready"], c + 1)
                link(nc.vector.tensor_copy(acum[:], p_s[:, 0:16].rearrange("p (k h) -> p k h", k=2)))
                nc.vector.tensor_tensor(wd[:], acum[:, 1, :], acum[:, 0, :], ALU.subtract).then_inc(s["wd_ready"], 1)
                dve.wait_ge(s["turned"], c + 1)
                link(nc.vector.tensor_copy(btok[:], p_s[:, 128:256]))
                link(nc.vector.tensor_copy(xs[:], p_x[:]))
                link(nc.vector.tensor_tensor(h3(xdt[:]), h3(xs[:]), over(dt[:]), ALU.mult))
                dve.wait_ge(s["edec_ready"], c + 1)
                nc.vector.tensor_tensor(h3(xw[:]), h3(xdt[:]), over(edec[:, 1, :]), ALU.mult).then_inc(s["xw_ready"], 1)
                dve.wait_ge(s["diff_ready"], c + 1)
                for h in range(SH):
                    ins = nc.vector.scalar_tensor_tensor(m[:, h, :], p_d[h // 4][:, h % 4, :], acum[:, 0, h:h + 1], mask[:, int(smp), :], ALU.subtract, ALU.add)
                ins.then_inc(s["dm_ready"], 1)
                if smp:
                    link(nc.vector.tensor_tensor(cm[:], seqrow[:], cv[:, 5:6, :].broadcast_to([P, NB, P]), ALU.mult))
                    link(nc.vector.tensor_tensor(bm[:], seqcol[:].unsqueeze(2).broadcast_to([P, NB, P]), btok[:].unsqueeze(1).broadcast_to([P, NB, P]), ALU.mult))
                    nc.vector.tensor_tensor(am[:], seqcol[:].unsqueeze(2).broadcast_to([P, NB, SH]), a[:].unsqueeze(1).broadcast_to([P, NB, SH]), ALU.mult).then_inc(s["masked"], 1)
                dve.wait_ge(s["dexp_ready"], c + 1)
                dve.wait_ge(s["cb_ready"], c + 1)
                for g in range(2):
                    mg = m[:, 4 * g:4 * g + 4, :]
                    ins = nc.vector.tensor_tensor(mg, mg, p_c[g][:, 0:P].unsqueeze(1).broadcast_to([P, 4, P]), ALU.mult)
                ins.then_inc(s["m_ready"], 1)
                dve.wait_ge(s["yo_ready"], c + 1)
                for g in range(2):
                    link(nc.vector.tensor_tensor(h3(t2[:, 256 * g:256 * g + 256]), h3(p_c[g][:, 0:256]), over(edec[:, 0, 4 * g:4 * g + 4]), ALU.mult))
                link(nc.vector.tensor_tensor(y[:], t2[:], p_y[:], ALU.add))
                link(nc.vector.tensor_tensor(h3(t2[:]), h3(xs[:]), over(hb[:, 2, :]), ALU.mult))
                link(nc.vector.tensor_tensor(y[:], y[:], t2[:], ALU.add))
                dve.wait_ge(s["ez_ready"], c + 1)
                link(nc.vector.tensor_scalar(ez[:], ez[:], 1.0, None, ALU.add))
                link(nc.vector.reciprocal(ez[:], ez[:]))
                link(nc.vector.tensor_tensor(ez[:], ez[:], z[:], ALU.mult))
                nc.vector.tensor_tensor(y[:], y[:], ez[:], ALU.mult).then_inc(s["y_ready"], 1)
                if not smp:
                    dve.wait_ge(s["st_ready"], c + 1)
                    for g in range(2):
                        sg = h3(st[64 * g:64 * g + 64, :])
                        link(nc.vector.tensor_tensor(sg, sg, over(edec[64 * g:64 * g + 64, 2, 4 * g:4 * g + 4]), ALU.mult))
                    link(nc.vector.tensor_tensor(st[:], st[:], p_x[:, 0:256], ALU.add))
                    dve.sem_inc(s["state_ready"], 1)
                else:
                    dve.wait_ge(s["et_ready"], 1)
                    for g in range(2):
                        sg = sst[64 * g:64 * g + 64].rearrange("p b (h e) -> p b h e", e=HD)
                        for b in range(NB):
                            link(nc.vector.tensor_tensor(sg[:, b], sg[:, b], over(et[64 * g:64 * g + 64, b, 4 * g:4 * g + 4]), ALU.mult))
                    for q in range(4):
                        dve.wait_ge(s["sst_ready"], q + 1)
                        bank = (p_x, p_y, p_d[0], p_d[1])[q]
                        flat = bank[:] if q < 2 else bank[:].rearrange("p a b -> p (a b)")
                        ins = nc.vector.tensor_tensor(sst[:, 2 * q:2 * q + 2, :], sst[:, 2 * q:2 * q + 2, :], flat.rearrange("p (b n) -> p b n", b=2), ALU.add)
                    ins.then_inc(s["sst_done"], 1)
                dve.wait_ge(s["rr_ready"], c + 1)
                link(nc.vector.tensor_scalar(y[:], y[:], rr[:], None, ALU.mult))
                nc.vector.tensor_tensor(y[:], y[:], gnorm[:], ALU.mult).then_inc(s["out_ready"], 1)
                dve.wait_ge(s["stored"], c * 16 + 16)
                dve.sem_inc(s["in_free"], 1)

            with dve.Fori(0, NT) as c:
                link = Chain(dve, s["dve_step"], 24, c)
                chunk(c, False, link)
                link.close()
            chunk(NT, True, Chain(dve, s["smp_step"]))

        @block.tensor
        def _(pe):
            pe.wait_ge(s["const_ready"], 128)
            pe.wait_ge(s["setup"], 2)

            def chunk(c, smp):
                k = int(smp)
                pe.wait_ge(s["loaded"], c * 48 + 48)
                for i in range(4):
                    nc.tensor.transpose(p_x[:, i * P:(i + 1) * P], cv[:, i, :], ident[:])
                nc.tensor.transpose(p_s[:, 128:256], cv[:, 4, :], ident[:]).then_inc(s["turned"], 1)
                for g in range(2):
                    mm = nc.tensor.matmul(p_c[g][:, 0:P], cv[64 * g:64 * g + 64, 4, :], cv[64 * g:64 * g + 64, 5, :], start=True, stop=True)
                mm.then_inc(s["cb_ready"], 1)
                pe.wait_ge(s["a_ready"], c + 1)
                pe.wait_ge(s["turned"], c + 1)
                nc.tensor.matmul(p_s[:, 0:8], tri[:, k, :], a[:], start=True, stop=True)
                nc.tensor.matmul(p_s[:, 8:16], same[:, k, :], a[:], start=True, stop=True).then_inc(s["acum_ready"], 1)
                for h in range(SH):
                    mm = nc.tensor.matmul(p_d[h // 4][:, h % 4, :], a[:, h:h + 1].broadcast_to([P, P]), tri[:, k, :], start=True, stop=True)
                mm.then_inc(s["diff_ready"], 1)
                pe.wait_ge(s["m_ready"], c + 1)
                for h in range(SH):
                    nc.tensor.matmul(p_y[:, 64 * h:64 * h + 64], m[:, h, :], xdt[:, 64 * h:64 * h + 64], start=True, stop=True)
                if not smp:
                    for g in range(2):
                        mm = nc.tensor.matmul(p_c[g][:, 0:256], cv[64 * g:64 * g + 64, 5, :], st[64 * g:64 * g + 64, :], start=True, stop=True)
                else:
                    pe.wait_ge(s["sstate_loaded"], 16)
                    pe.wait_ge(s["masked"], 1)
                    for g in range(2):
                        for b in range(NB):
                            mm = nc.tensor.matmul(p_c[g][:, 0:256], cm[64 * g:64 * g + 64, b, :], sst[64 * g:64 * g + 64, b, :], start=(b == 0), stop=(b == NB - 1))
                mm.then_inc(s["yo_ready"], 1)
                pe.wait_ge(s["xw_ready"], c + 1)
                if not smp:
                    for g in range(2):
                        mm = nc.tensor.matmul(p_x[64 * g:64 * g + 64, 0:256], btok[:, 64 * g:64 * g + 64], xw[:, 256 * g:256 * g + 256], start=True, stop=True)
                    mm.then_inc(s["st_ready"], 1)
                    pe.wait_ge(s["in_free"], c + 2)
                    pe.wait_ge(s["state_ready"], c + 1)
                else:
                    nc.tensor.matmul(p_e[:, 0:NB * SH], same[:, 0, :], am[:].rearrange("p b h -> p (b h)"), start=True, stop=True).then_inc(s["et_sum"], 1)
                    pe.wait_ge(s["y_ready"], c + 1)
                    for q in range(4):
                        bank = (p_x, p_y, p_d[0], p_d[1])[q]
                        flat = bank[:] if q < 2 else bank[:].rearrange("p a b -> p (a b)")
                        for b in (2 * q, 2 * q + 1):
                            for g in range(2):
                                mm = nc.tensor.matmul(flat[64 * g:64 * g + 64, 256 * (b % 2):256 * (b % 2) + 256], bm[:, b, 64 * g:64 * g + 64], xw[:, 256 * g:256 * g + 256], start=True, stop=True)
                        mm.then_inc(s["sst_ready"], 1)

            with pe.Fori(0, NT) as c:
                chunk(c, False)
            chunk(NT, True)


def compress_prompt(nc, d):
    NS, NC = SEQ // S_CMP, N_CMP_P
    with Phase(nc, "cmp") as ph:
        kv = ph.sb("kv", [P, 2, SEQ])
        w1 = ph.sb("w1", [P, 2, S_CMP, P])
        pe_t = ph.sb("pe", [HD, 2, 2, S_CMP])
        w2 = ph.sb("w2", [HD, 2, HD])
        pe_hid = ph.sb("pe_hid", [HD, 2])
        pe_neg = ph.sb("pe_neg", [HD, 2])
        late = ph.sb("late", [HD, 2, 2, NS])
        hid = ph.sb("hid", [HD, 2, 2, NC])
        e = ph.sb("e", [HD, 2, 2, NC])
        kct = ph.sb("kct", [P, NC])
        vc = ph.sb("vc", [NC, P])
        p_h = [ph.ps(f"p_h{g}", [P, 2, NS]) for g in range(2)]
        p_pe, p_k, p_v = ph.ps("p_pe", [HD, 2]), ph.ps("p_k", [P, NC]), ph.ps("p_v", [NC, P])
        loaded, hid_ready, pe_ready, late_ready = ph.sem("loaded"), ph.sem("hid_ready"), ph.sem("pe_ready"), ph.sem("late_ready")
        sum_ready, exp_ready, act_ready, out_ready = ph.sem("sum_ready"), ph.sem("exp_ready"), ph.sem("act_ready"), ph.sem("out_ready")
        evac, stored, dve_step = ph.sem("evac"), ph.sem("stored"), ph.sem("dve_step")
        block = ph.enter_context(nc.Block())

        @block.sync
        def _(sp):
            sp.dma_start(w1[:], d["cmp_w1_sd"]).then_inc(loaded, 16)
            sp.dma_start(kv[:], d["turned"][:, 8:10, 0:SEQ]).then_inc(loaded, 16)
            sp.dma_start(pe_t[:], d["cmp_pe"]).then_inc(loaded, 16)
            sp.dma_start(w2[:], d["cmp_w2"]).then_inc(loaded, 16)
            sp.wait_ge(pe_ready, 2)
            sp.dma_start(d["pe_hid"], pe_hid[:]).then_inc(stored, 16)
            sp.wait_ge(evac, 2)
            sp.dma_start(d["kct"], kct[:]).then_inc(stored, 16)
            sp.dma_start(d["vc"], vc[:]).then_inc(stored, 16)
            sp.wait_ge(stored, 48)

        @block.tensor
        def _(pe):
            pe.wait_ge(loaded, 64)
            for slot in range(2):
                for n, (r, s) in enumerate((r, s) for r in range(2) for s in range(S_CMP)):
                    mm = nc.tensor.matmul(p_pe[:, slot:slot + 1], w1[0:HD, slot, s, HD * r:HD * r + HD], pe_t[:, slot, r, s:s + 1], start=(n == 0), stop=(n == 2 * S_CMP - 1))
            mm.then_inc(pe_ready, 1)
            for g in range(2):
                for slot in range(2):
                    seg = kv[64 * g:64 * g + 64, slot, :].rearrange("p (n s) -> p s n", s=S_CMP)
                    for s in range(S_CMP):
                        mm = nc.tensor.matmul(p_h[g][:, slot, :], w1[64 * g:64 * g + 64, slot, s, :], seg[:, s, :], start=(s == 0), stop=(s == S_CMP - 1))
            mm.then_inc(hid_ready, 1)
            pe.wait_ge(act_ready, 1)
            for g in range(2):
                nc.tensor.matmul(p_k[64 * g:64 * g + 64, :], w2[:, 0, :], hid[:, 0, g, :], start=True, stop=True)
                mm = nc.tensor.matmul(p_v[:, 64 * g:64 * g + 64], hid[:, 1, g, :], w2[:, 1, :], start=True, stop=True)
            mm.then_inc(out_ready, 1)

        @block.scalar
        def _(act):
            act.wait_ge(hid_ready, 1)
            for g in range(2):
                ins = nc.scalar.activation(late[:, :, g, :], p_h[g][64:128], ACT.Copy)
            ins.then_inc(late_ready, 1)
            act.wait_ge(sum_ready, 1)
            nc.scalar.activation(e[:], hid[:], ACT.Exp, scale=-1.0).then_inc(exp_ready, 1)

        @block.vector
        def _(dve):
            link = Chain(dve, dve_step)
            dve.wait_ge(pe_ready, 1)
            nc.vector.tensor_copy(pe_hid[:], p_pe[:]).then_inc(pe_ready, 1)
            dve.wait_ge(pe_ready, 2)
            dve.wait_ge(late_ready, 1)
            for g in range(2):
                ins = nc.vector.tensor_tensor(hid[:, :, g, :], p_h[g][0:HD, :, 0:NC], late[:, :, g, 1:NS], ALU.add)
            link(ins)
            for slot in range(2):
                ins = nc.vector.tensor_scalar(hid[:, slot], hid[:, slot], pe_hid[:, slot:slot + 1], None, ALU.add)
            ins.then_inc(sum_ready, 1)
            dve.wait_ge(exp_ready, 1)
            link(nc.vector.tensor_scalar(e[:], e[:], 1.0, None, ALU.add))
            link(nc.vector.reciprocal(e[:], e[:]))
            nc.vector.tensor_tensor(hid[:], hid[:], e[:], ALU.mult).then_inc(act_ready, 1)
            dve.wait_ge(out_ready, 1)
            nc.vector.tensor_copy(kct[:], p_k[:]).then_inc(evac, 1)
            nc.vector.tensor_copy(vc[:], p_v[:]).then_inc(evac, 1)


def attend_prompt(nc, d):
    assert SEQ // L_SLC <= N_SEL and WINDOW % P == 0
    NC = N_CMP_P
    WT = WINDOW // P
    CMP, SLC, WIN = range(3)
    units = [(qt, g, br, 0 if br != WIN else max(0, qt - WT), {CMP: 0, SLC: qt + 1, WIN: min(qt, WT) + 1}[br])
             for qt in range(NT) for g in range(2) for br in range(3)]
    NU = len(units)
    groups = []
    for u, (qt, g, br, k0, kn) in enumerate(units):
        groups += [(u, t, min(4, max(kn, 1) - t)) for t in range(0, max(kn, 1), 4)]
    of_unit = [[i for i, gr in enumerate(groups) if gr[0] == u] for u in range(NU)]
    per_bank = [len(groups) - len(groups) // 2, len(groups) // 2]
    with Phase(nc, "att") as ph:
        q = ph.sb("q", [P, 2, SEQ])
        kk = ph.sb("kk", [P, 2, SEQ])
        v = ph.sb("v", [P, 2, NT, P])
        kct = ph.sb("kct", [P, NC])
        vc = ph.sb("vc", [NC, P])
        gates = ph.sb("gates", [P, NT, 6])
        diag = ph.sb("diag", [P, P])
        old = ph.sb("old", [P, P])
        cmask = ph.sb("cmask", [P, NT, NC])
        valid = ph.sb("valid", [P, 1])
        ident = ph.sb("ident", [P, P])
        prob = [ph.sb(f"prob{i}", [P, SEQ]) for i in range(2)]
        pt = [ph.sb(f"pt{i}", [P, 4, P]) for i in range(2)]
        mx, nb, l, rg = (ph.sb(n, [P, 2]) for n in ("mx", "nb", "l", "rg"))
        o = ph.sb("o", [P, NT, P])
        p_s = [ph.ps(f"p_s{i}", [P, SEQ]) for i in range(2)]
        p_t = [ph.ps(f"p_t{i}", [P, 4, P]) for i in range(2)]
        p_o = [ph.ps(f"p_o{i}", [P, 512]) for i in range(2)]
        const_ready, q_ready, q_free = ph.sem("const_ready"), ph.sem("q_ready"), ph.sem("q_free")
        s_ready, nb_ready, p_ready, o_ready, o_done = (ph.sem(n) for n in ("s_ready", "nb_ready", "p_ready", "o_ready", "o_done"))
        t_ready = [ph.sem(f"t_ready{i}") for i in range(2)]
        t_done = [ph.sem(f"t_done{i}") for i in range(2)]
        zero = ph.sb("zero", [P, D_MODEL])
        rows_zeroed, rows_stored = ph.sem("rows_zeroed"), ph.sem("rows_stored")
        g_exp, o_stored, dve_step = ph.sem("g_exp"), ph.sem("o_stored"), ph.sem("dve_step")
        block = ph.enter_context(nc.Block())

        def unit(it, u, back=0):
            return it * NU + (u - back + 1 + 2)

        def group(it, i, back=0):
            return it * per_bank[i % 2] + (i // 2 - back + 1 + 1)

        @block.sync
        def _(sp):
            sp.wait_ge(rows_zeroed, 1)
            for n in range(OVER_BLOCKS):
                sp.dma_start(d["ypad"][(MAIN_BLOCKS + n) * P:(MAIN_BLOCKS + n + 1) * P, :], zero[:]).then_inc(rows_stored, 16)
            for s in (o_done, p_ready):
                sp.sem_inc(s, 2)
            for s in t_done:
                sp.sem_inc(s, 1)
            sp.sem_inc(q_free, 1)
            sp.sem_inc(o_stored, 16)
            for dst, src in ((kk[:], d["turned"][:, 10:12, 0:SEQ]), (kct[:], d["kct"]), (vc[:], d["vc"]), (diag[:], d["diag"]), (old[:], d["old"]),
                             (cmask[:], d["cmask"]), (valid[:], d["valid"]), (ident[:], d["ident"]),
                             (v[:, 0], d["kv_out"][0:SEQ, 384:512].rearrange("(t p) n -> p t n", p=P)),
                             (v[:, 1], d["win_new"][0:SEQ, 128:256].rearrange("(t p) n -> p t n", p=P))):
                sp.dma_start(dst, src).then_inc(const_ready, 16)
            with sp.Fori(0, HPG) as j:
                sp.wait_ge(q_free, j + 1)
                sp.dma_start(q[:, 0], d["turned"][:, bass.ds(j, 1), 0:SEQ].rearrange("p o n -> p (o n)")).then_inc(q_ready, 16)
                sp.dma_start(q[:, 1], d["turned"][:, bass.ds(j + HPG, 1), 0:SEQ].rearrange("p o n -> p (o n)")).then_inc(q_ready, 16)
                sp.dma_start(gates[:], d["gdt"][0:SEQ, bass.ds(j * 6, 6)].rearrange("(t p) n -> p t n", p=P)).then_inc(q_ready, 16)
                sp.wait_ge(o_done, j * NU + NU + 2)
                sp.dma_start(d["attn"][0:SEQ, bass.ds(j * P, P)].rearrange("(t p) n -> p t n", p=P), o[:]).then_inc(o_stored, 16)
            sp.wait_ge(o_stored, 16 * HPG + 16)
            sp.wait_ge(rows_stored, 16 * OVER_BLOCKS)

        @block.tensor
        def _(pe):
            pe.wait_ge(const_ready, 160)

            def scores(it, u):
                qt, g, br, k0, kn = units[u]
                pe.wait_ge(p_ready, unit(it, u, 2))
                rows = slice(64 * g, 64 * g + 64)
                lhs = q[rows, 0 if br == CMP else 1, qt * P:qt * P + P]
                if br == CMP:
                    mm = nc.tensor.matmul(p_s[u % 2][:, 0:NC], lhs, kct[rows, :], start=True, stop=True)
                else:
                    n = kn * P
                    for c in range(0, n, 512):
                        w = min(512, n - c)
                        mm = nc.tensor.matmul(p_s[u % 2][:, c:c + w], lhs, kk[rows, br - 1, k0 * P + c:k0 * P + c + w], start=True, stop=True)
                mm.then_inc(s_ready, 1)

            def turn(it, i):
                u, t0, n = groups[i]
                br = units[u][2]
                hold(pe, t_done[i % 2], group(it, i, 1), ph.passed)
                for t in range(n):
                    if br == CMP:
                        mm = nc.tensor.transpose(p_t[i % 2][0:NC, 0, :], prob[u % 2][:, 0:NC], ident[:])
                    else:
                        mm = nc.tensor.transpose(p_t[i % 2][:, t, :], prob[u % 2][:, (t0 + t) * P:(t0 + t + 1) * P], ident[:])
                mm.then_inc(t_ready[i % 2], 1)

            def values(it, i):
                u, t0, n = groups[i]
                qt, g, br, k0, kn = units[u]
                pe.wait_ge(t_done[i % 2], group(it, i))
                if t0 == 0:
                    pe.wait_ge(o_done, unit(it, u, 2))
                for t in range(n):
                    if br == CMP:
                        mm = nc.tensor.matmul(p_o[u % 2][:, 0:HD], pt[i % 2][0:NC, 0, :], vc[:, 64 * g:64 * g + 64], start=True, stop=True)
                    else:
                        k = t0 + t
                        mm = nc.tensor.matmul(p_o[u % 2][:, 0:HD], pt[i % 2][:, t, :], v[:, br - 1, k0 + k, 64 * g:64 * g + 64], start=(k == 0), stop=(k == kn - 1))
                if i == of_unit[u][-1]:
                    mm.then_inc(o_ready, 1)

            with pe.Fori(0, HPG) as it:
                pe.wait_ge(q_ready, it * 48 + 48)
                scores(it, 0)
                for u in range(NU):
                    if u + 1 < NU:
                        scores(it, u + 1)
                    pe.wait_ge(p_ready, unit(it, u))
                    turn(it, of_unit[u][0])
                    for i in of_unit[u]:
                        if i != of_unit[u][-1]:
                            turn(it, i + 1)
                        values(it, i)

        def copy_turned(eng, op, it, u, bank):
            for i in of_unit[u]:
                if i % 2 == bank:
                    n = groups[i][2]
                    rows = NC if units[u][2] == CMP else P
                    eng.wait_ge(t_ready[bank], it * per_bank[bank] + (i // 2 + 1))
                    op(pt[bank][0:rows, 0:n, :], p_t[bank][0:rows, 0:n, :]).then_inc(t_done[bank], 1)

        @block.scalar
        def _(act):
            def exponentials(it, u):
                qt, g, br, k0, kn = units[u]
                n = NC if br == CMP else kn * P
                act.wait_ge(nb_ready, it * NU + (u + 1))
                act.wait_ge(o_done, unit(it, u, 2))
                nc.scalar.activation(prob[u % 2][:, 0:n], p_s[u % 2][:, 0:n], ACT.Exp, bias=nb[:, u % 2:u % 2 + 1], scale=SCALE,
                                     accum_out=l[:, u % 2:u % 2 + 1]).then_inc(p_ready, 1)

            with act.Fori(0, HPG) as it:
                act.wait_ge(q_ready, it * 48 + 48)
                nc.scalar.activation(gates[:], gates[:], ACT.Exp, scale=-1.0).then_inc(g_exp, 1)
                exponentials(it, 0)
                for u in range(NU):
                    if u + 1 < NU:
                        exponentials(it, u + 1)
                    copy_turned(act, lambda a, b: nc.scalar.activation(a, b, ACT.Copy), it, u, 1)

        @block.vector
        def _(dve):
            nc.vector.memset(zero[:], 0.0).then_inc(rows_zeroed, 1)
            dve.wait_ge(const_ready, 160)
            with dve.Fori(0, HPG) as it:
                link = Chain(dve, dve_step, 2 + 3 * NU + sum(1 if br == CMP or qt < WT or br == SLC else 2 for qt, g, br, _, _ in units) + 2, it)

                def maxima(u):
                    qt, g, br, k0, kn = units[u]
                    S = p_s[u % 2]
                    dve.wait_ge(s_ready, it * NU + (u + 1))
                    if br == CMP:
                        n = NC
                        link(nc.vector.tensor_tensor(S[:, 0:NC], S[:, 0:NC], cmask[:, qt, :], ALU.add))
                    else:
                        n = kn * P
                        link(nc.vector.tensor_tensor(S[:, n - P:n], S[:, n - P:n], diag[:], ALU.add))
                        if br == WIN and qt >= WT:
                            link(nc.vector.tensor_tensor(S[:, 0:P], S[:, 0:P], old[:], ALU.add))
                    link(nc.vector.reduce_max(mx[:, u % 2:u % 2 + 1], S[:, 0:n], AX))
                    nc.vector.tensor_scalar(nb[:, u % 2:u % 2 + 1], mx[:, u % 2:u % 2 + 1], -SCALE, None, ALU.mult).then_inc(nb_ready, 1)

                dve.wait_ge(g_exp, it + 1)
                link(nc.vector.tensor_scalar(gates[:], gates[:], 1.0, None, ALU.add))
                link(nc.vector.reciprocal(gates[:], gates[:]))
                dve.wait_ge(o_stored, it * 16 + 16)
                maxima(0)
                for u in range(NU):
                    qt, g, br, k0, kn = units[u]
                    if u + 1 < NU:
                        maxima(u + 1)
                    copy_turned(dve, nc.vector.tensor_copy, it, u, 0)
                    dve.wait_ge(p_ready, unit(it, u))
                    r = rg[:, u % 2:u % 2 + 1]
                    link(nc.vector.reciprocal(r, l[:, u % 2:u % 2 + 1]))
                    ins = nc.vector.tensor_tensor(r, r, gates[:, qt, 3 * g + br:3 * g + br + 1], ALU.mult)
                    link(ins)
                    if br == CMP and qt == 0:
                        link(nc.vector.tensor_tensor(r, r, valid[:], ALU.mult))
                    dve.wait_ge(o_ready, it * NU + (u + 1))
                    out = o[:, qt, 64 * g:64 * g + 64]
                    if br == CMP:
                        nc.vector.tensor_scalar(out, p_o[u % 2][:, 0:HD], r, None, ALU.mult).then_inc(o_done, 1)
                    else:
                        nc.vector.scalar_tensor_tensor(out, p_o[u % 2][:, 0:HD], r, out, ALU.mult, ALU.add).then_inc(o_done, 1)
                    dve.wait_ge(o_done, unit(it, u))
                dve.sem_inc(q_free, 1)
                link.close()


def attend_samples(nc, d, n_pool):
    NC, NBK, Q = N_CMP_S, N_SLC_S, DEC_SEQ
    R = KVH * HPG * Q
    OLD = PAST
    W0, WN = OLD + Q, WINDOW + Q
    CUR = PAST // L_SLC
    FORCED = 1e9
    assert (PAST + Q - 1) // L_SLC == CUR and (NC - 1) * S_CMP + L_CMP - 1 <= PAST and R == 64
    with Phase(nc, "smp") as ph:
        page = ph.sb("page", [P, N_PAGES, 512])
        table = ph.sb("table", [1, N_PAGES], I32)
        win = ph.sb("win", [P, 2, 512])
        qbd = ph.sb("qbd", [P, 2, R])
        knew = ph.sb("knew", [P, 2, Q])
        vnew = ph.sb("vnew", [Q, 2, P])
        graw = ph.sb("graw", [R, 3])
        zero = ph.sb("zero", [TOK - SEQ - N_SMP, ATT_W])
        gate = ph.sb("gate", [R, 3])
        w1 = ph.sb("w1", [P, 2, 8, P])
        w2 = ph.sb("w2", [HD, 2, HD])
        pe_hid = ph.sb("pe_hid", [HD, 2])
        cover = ph.sb("cover", [P, 2, NBK])
        gsum = ph.sb("gsum", [R, R])
        nmask = ph.sb("nmask", [R, Q])
        wmask = ph.sb("wmask", [R, WN])
        ident = ph.sb("ident", [P, P])
        late = ph.sb("late", [HD, 2, 2, N_SEG_S])
        hid = ph.sb("hid", [HD, 2, 2, NC])
        e = ph.sb("e", [HD, 2, 2, NC])
        kct = ph.sb("kct", [P, NC])
        vc = ph.sb("vc", [P, 2, P])
        pc = ph.sb("pc", [R, NC])
        pct = ph.sb("pct", [P, 2, R])
        imp = ph.sb("imp", [R, NBK])
        score, score2, score3, unsel = (ph.sb(n, [R, NBK]) for n in ("score", "score2", "score3", "unsel"))
        top = ph.sb("top", [R, 2, 8])
        S = ph.sb("S", [R, W0 + WN])
        pst = ph.sb("pst", [P, N_PAGES + 4, R])
        pnew = ph.sb("pnew", [Q, 2, R])
        mx, nb, l, rg = (ph.sb(n, [R, 3]) for n in ("mx", "nb", "l", "rg"))
        o = ph.sb("o", [R, HD])
        p_h = [ph.ps(f"p_h{i}", [P, 512]) for i in range(2)]
        p_s = [ph.ps(f"p_s{i}", [P, 512]) for i in range(2)]
        p_t = [ph.ps(f"p_t{i}", [P, 8, R]) for i in range(2)]
        p_o, p_m = ph.ps("p_o", [P, 512]), ph.ps("p_m", [P, 512])
        names = ("const_ready", "zeroed", "table_ready", "in_free", "pages_ready", "small_ready", "old_copied", "hid_ready", "late_ready", "sum_ready", "exp_ready",
                 "act_ready", "kc_ready", "kc_copied", "vc_copied", "sc_ready", "nb_ready", "pc_ready", "pcn_ready", "pct_ready", "pct_copied", "imp_ready",
                 "imp_copied", "imps_ready", "unsel_ready", "ss_ready", "ss_taken", "new_ready", "new_taken", "sw_ready", "sw_taken", "nbs_ready", "ps_ready",
                 "t0_ready", "t0_done", "t1_ready", "t1_done", "tn_ready", "tn_done", "o_ready", "o_done", "stored", "dve_step", "gexp_ready")
        s = {n: ph.sem(n) for n in names}
        block = ph.enter_context(nc.Block())
        cmp_ops = page[:, :, 0:256].rearrange("p pg (sl c g sg) -> p sl c g pg sg", sl=2, c=8, g=2)
        NG_S = N_PAGES // 8

        @block.sync
        def _(sp):
            sp.sem_inc(s["in_free"], 1)
            sp.wait_ge(s["zeroed"], 2)
            for dst, src in ((w1, "cmp_w1_seg"), (w2, "cmp_w2"), (pe_hid, "pe_hid"), (cover, "cover"), (gsum, "gsum"), (nmask, "nmask"), (wmask, "wmask"), (ident, "ident")):
                sp.dma_start(dst[:], d[src]).then_inc(s["const_ready"], 16)
            sp.dma_start(d["attn"][SEQ + N_SMP:TOK, :], zero[:]).then_inc(s["old_copied"], 16)
            sp.dma_start(d["win_old"], d["cache_win"][:, Q:, :]).then_inc(s["old_copied"], 16)
            with sp.Fori(0, DEC_BATCH) as b:
                new = bass.ds(SEQ + b * Q, Q)
                sp.wait_ge(s["in_free"], b + 1)
                sp.dma_start(table[:], d["page_table"][bass.ds(b, 1), :]).then_inc(s["table_ready"], 16)
                sp.wait_ge(s["table_ready"], b * 16 + 16)
                for g in range(2):
                    for kind in range(2):
                        sp.dma_start(qbd[64 * g:64 * g + 64, kind, 32 * g:32 * g + 32].rearrange("p (j q) -> p j q", j=HPG),
                                     d["turned"][64 * g:64 * g + 64, 4 * kind:4 * kind + 4, new]).then_inc(s["small_ready"], 16)
                sp.dma_start(knew[:], d["turned"][:, 10:12, new]).then_inc(s["small_ready"], 16)
                sp.dma_start(vnew[:, 0], d["kv_out"][new, 384:512]).then_inc(s["small_ready"], 16)
                sp.dma_start(vnew[:, 1], d["win_new"][new, 128:256]).then_inc(s["small_ready"], 16)
                sp.dma_start(win[:].rearrange("p a n -> p (a n)"), d["win_pack"][bass.ds(b, 1)].rearrange("o p n -> (o p) n")).then_inc(s["small_ready"], 16)
                for g in range(2):
                    for j in range(HPG):
                        c = 3 * (2 * j + g)
                        sp.dma_start(graw[32 * g + 8 * j:32 * g + 8 * j + 8, :], d["gdt"][new, c:c + 3]).then_inc(s["small_ready"], 16)
                for n in range(N_PAGES):
                    at = sp.value_load(table[0:1, n:n + 1], min_val=0, max_val=n_pool - 1)
                    sp.dma_start(page[:, n, :], d["pool"][bass.ds(at, 1)].rearrange("o p n -> (o p) n")).then_inc(s["pages_ready"], 16)
                hold(sp, s["o_done"], b * 6 + 6, ph.passed)
                for g in range(2):
                    for j in range(HPG):
                        c = 64 * (2 * j + g)
                        sp.dma_start(d["attn"][new, c:c + 64], o[32 * g + 8 * j:32 * g + 8 * j + 8, :]).then_inc(s["stored"], 16)
            sp.wait_ge(s["stored"], DEC_BATCH * 128)
            sp.wait_ge(s["old_copied"], 32)

        @block.tensor
        def _(pe):
            pe.wait_ge(s["const_ready"], 128)
            with pe.Fori(0, DEC_BATCH) as b:
                hold(pe, s["pages_ready"], b * 16 * N_PAGES + 16 * N_PAGES, ph.passed)
                hold(pe, s["small_ready"], b * 256 + 256, ph.passed)
                for slot in range(2):
                    for c in range(8):
                        mm = nc.tensor.matmul(p_h[slot][:], w1[:, slot, c, :], cmp_ops[:, slot, c], start=(c == 0), stop=(c == 7))
                mm.then_inc(s["hid_ready"], 1)
                hold(pe, s["act_ready"], b + 1, ph.passed)
                for g in range(2):
                    nc.tensor.matmul(p_m[64 * g:64 * g + 64, 0:NC], w2[:, 0, :], hid[:, 0, g, :], start=True, stop=True)
                for g in range(2):
                    for h in range(2):
                        n = min(P, NC - P * h)
                        mm = nc.tensor.matmul(p_s[0][0:n, P * h + 64 * g:P * h + 64 * g + 64], hid[:, 1, g, P * h:P * h + n], w2[:, 1, :], start=True, stop=True)
                mm.then_inc(s["kc_ready"], 1)
                hold(pe, s["kc_copied"], b + 1, ph.passed)
                nc.tensor.matmul(p_s[1][0:R, 0:NC], qbd[:, 0, :], kct[:], start=True, stop=True).then_inc(s["sc_ready"], 1)
                hold(pe, s["pcn_ready"], b + 1, ph.passed)
                nc.tensor.transpose(p_t[0][:, 0, :], pc[:, 0:P], ident[0:R, 0:R])
                nc.tensor.transpose(p_t[0][0:NC - P, 1, :], pc[:, P:NC], ident[0:R, 0:R]).then_inc(s["pct_ready"], 1)
                hold(pe, s["pct_copied"], b + 1, ph.passed)
                hold(pe, s["vc_copied"], b + 1, ph.passed)
                for h in range(2):
                    n = min(P, NC - P * h)
                    nc.tensor.matmul(p_o[0:R, 0:P], pct[0:n, h, :], vc[0:n, h, :], start=(h == 0), stop=(h == 1))
                for h in range(2):
                    n = min(P, NC - P * h)
                    mm = nc.tensor.matmul(p_m[0:R, 0:NBK], pct[0:n, h, :], cover[0:n, h, :], start=(h == 0), stop=(h == 1))
                mm.then_inc(s["imp_ready"], 1)
                hold(pe, s["imp_copied"], b + 1, ph.passed)
                nc.tensor.matmul(p_m[0:R, 0:NBK], gsum[:], imp[:], start=True, stop=True).then_inc(s["imps_ready"], 1)
                for c in range(8):
                    if c >= 2:
                        hold(pe, s["ss_taken"], b * 8 + (c - 1), ph.passed)
                    nc.tensor.matmul(p_s[c % 2][0:R, :], qbd[:, 1, :], page[:, 4 * c:4 * c + 4, 256:384], start=True, stop=True).then_inc(s["ss_ready"], 1)
                hold(pe, s["unsel_ready"], b + 1, ph.passed)
                nc.tensor.matmul(p_m[0:R, 0:Q], qbd[:, 1, :], knew[:, 0, :], start=True, stop=True)
                nc.tensor.matmul(p_m[0:R, Q:2 * Q], qbd[:, 1, :], knew[:, 1, :], start=True, stop=True).then_inc(s["new_ready"], 1)
                hold(pe, s["ss_taken"], b * 8 + 7, ph.passed)
                nc.tensor.matmul(p_s[0][0:R, :], qbd[:, 1, :], win[:, 0, :], start=True, stop=True).then_inc(s["sw_ready"], 1)
                hold(pe, s["ps_ready"], b + 1, ph.passed)

                def turn(k):
                    n, c0 = (8, 1024 * k) if k < NG_S else (4, W0)
                    if k >= 2:
                        hold(pe, s[f"t{k % 2}_done"], b * (3 - k % 2) + k // 2, ph.passed)
                    for i in range(n):
                        mm = nc.tensor.transpose(p_t[k % 2][:, i, :], S[:, c0 + P * i:c0 + P * i + P], ident[0:R, 0:R])
                    mm.then_inc(s[f"t{k % 2}_ready"], 1)

                def values(k):
                    hold(pe, s[f"t{k % 2}_done"], b * (3 - k % 2) + (k // 2 + 1), ph.passed)
                    if k < NG_S:
                        for n in range(8 * k, 8 * k + 8):
                            nc.tensor.matmul(p_o[0:R, P:2 * P], pst[:, n, :], page[:, n, 384:512], start=(n == 0), stop=False)
                    else:
                        for n in range(4):
                            nc.tensor.matmul(p_o[0:R, 2 * P:3 * P], pst[:, N_PAGES + n, :], win[:, 1, P * n:P * n + P], start=(n == 0), stop=False)

                nc.tensor.transpose(p_m[0:Q, 0:R], S[:, OLD:W0], ident[0:R, 0:R])
                nc.tensor.transpose(p_m[0:Q, R:2 * R], S[:, W0 + WINDOW:W0 + WN], ident[0:R, 0:R]).then_inc(s["tn_ready"], 1)
                turn(0)
                for k in range(NG_S):
                    turn(k + 1)
                    values(k)
                hold(pe, s["tn_done"], b + 1, ph.passed)
                nc.tensor.matmul(p_o[0:R, P:2 * P], pnew[:, 0, :], vnew[:, 0, :], start=False, stop=True)
                values(NG_S)
                nc.tensor.matmul(p_o[0:R, 2 * P:3 * P], pnew[:, 1, :], vnew[:, 1, :], start=False, stop=True).then_inc(s["o_ready"], 1)

        @block.scalar
        def _(act):
            act.wait_ge(s["const_ready"], 128)
            with act.Fori(0, DEC_BATCH) as b:
                act.wait_ge(s["small_ready"], b * 256 + 256)
                nc.scalar.activation(gate[:], graw[:], ACT.Exp, scale=-1.0).then_inc(s["gexp_ready"], 1)
                act.wait_ge(s["hid_ready"], b + 1)
                for slot in range(2):
                    ins = nc.scalar.activation(late[:, slot], p_h[slot][64:128].rearrange("p (g n) -> p g n", g=2), ACT.Copy)
                ins.then_inc(s["late_ready"], 1)
                act.wait_ge(s["sum_ready"], b + 1)
                nc.scalar.activation(e[:], hid[:], ACT.Exp, scale=-1.0).then_inc(s["exp_ready"], 1)
                act.wait_ge(s["kc_ready"], b + 1)
                nc.scalar.activation(kct[:], p_m[:, 0:NC], ACT.Copy).then_inc(s["kc_copied"], 1)
                act.wait_ge(s["nb_ready"], b + 1)
                nc.scalar.activation(pc[:], p_s[1][0:R, 0:NC], ACT.Exp, bias=nb[:, 0:1], scale=SCALE, accum_out=l[:, 0:1]).then_inc(s["pc_ready"], 1)
                act.wait_ge(s["nbs_ready"], b + 1)
                nc.scalar.activation(S[:, 0:W0], S[:, 0:W0], ACT.Exp, bias=nb[:, 1:2], scale=SCALE, accum_out=l[:, 1:2])
                nc.scalar.activation(S[:, W0:], S[:, W0:], ACT.Exp, bias=nb[:, 2:3], scale=SCALE, accum_out=l[:, 2:3]).then_inc(s["ps_ready"], 1)
                for k in range(1, NG_S + 1, 2):
                    act.wait_ge(s["t1_ready"], b * 2 + (k // 2 + 1))
                    nc.scalar.activation(pst[:, 8 * k:8 * k + 8, :], p_t[1][:], ACT.Copy).then_inc(s["t1_done"], 1)

        @block.vector
        def _(dve):
            nc.vector.memset(qbd[:], 0.0).then_inc(s["zeroed"], 1)
            nc.vector.memset(zero[:], 0.0).then_inc(s["zeroed"], 1)
            dve.wait_ge(s["const_ready"], 128)
            with dve.Fori(0, DEC_BATCH) as b:
                link = Chain(dve, s["dve_step"], 19, b)
                dve.wait_ge(s["gexp_ready"], b + 1)
                link(nc.vector.tensor_scalar(gate[:], gate[:], 1.0, None, ALU.add))
                link(nc.vector.reciprocal(gate[:], gate[:]))
                dve.wait_ge(s["late_ready"], b + 1)
                for slot in range(2):
                    first = p_h[slot][0:HD].rearrange("p (g n) -> p g n", g=2)[:, :, 0:NC]
                    ins = nc.vector.tensor_tensor(hid[:, slot], first, late[:, slot, :, 1:N_SEG_S], ALU.add)
                link(ins)
                for slot in range(2):
                    ins = nc.vector.tensor_scalar(hid[:, slot], hid[:, slot], pe_hid[:, slot:slot + 1], None, ALU.add)
                ins.then_inc(s["sum_ready"], 1)
                dve.wait_ge(s["exp_ready"], b + 1)
                link(nc.vector.tensor_scalar(e[:], e[:], 1.0, None, ALU.add))
                link(nc.vector.reciprocal(e[:], e[:]))
                nc.vector.tensor_tensor(hid[:], hid[:], e[:], ALU.mult).then_inc(s["act_ready"], 1)
                dve.wait_ge(s["kc_ready"], b + 1)
                nc.vector.tensor_copy(vc[:, 0], p_s[0][:, 0:P])
                nc.vector.tensor_copy(vc[0:NC - P, 1], p_s[0][0:NC - P, P:2 * P]).then_inc(s["vc_copied"], 1)
                dve.wait_ge(s["sc_ready"], b + 1)
                link(nc.vector.reduce_max(mx[:, 0:1], p_s[1][0:R, 0:NC], AX))
                nc.vector.tensor_scalar(nb[:, 0:1], mx[:, 0:1], -SCALE, None, ALU.mult).then_inc(s["nb_ready"], 1)
                dve.wait_ge(s["pc_ready"], b + 1)
                link(nc.vector.reciprocal(rg[:, 0:1], l[:, 0:1]))
                nc.vector.tensor_scalar(pc[:], pc[:], rg[:, 0:1], None, ALU.mult).then_inc(s["pcn_ready"], 1)
                dve.wait_ge(s["pct_ready"], b + 1)
                nc.vector.tensor_copy(pct[:, 0], p_t[0][:, 0, :])
                nc.vector.tensor_copy(pct[0:NC - P, 1], p_t[0][0:NC - P, 1, :]).then_inc(s["pct_copied"], 1)
                dve.wait_ge(s["imp_ready"], b + 1)
                nc.vector.tensor_copy(imp[:], p_m[0:R, 0:NBK]).then_inc(s["imp_copied"], 1)
                dve.wait_ge(s["imps_ready"], b + 1)
                link(nc.vector.tensor_copy(score[:], p_m[0:R, 0:NBK]))
                nc.vector.memset(score[:, 0:1], FORCED)
                link(nc.vector.memset(score[:, CUR - 1:CUR + 1], FORCED), ph.passed)
                link(nc.vector.max(top[:, 0], score[:]), ph.passed)
                link(nc.vector.match_replace(score2[:], top[:, 0], score[:], -3e38), ph.passed)
                link(nc.vector.max(top[:, 1], score2[:]), ph.passed)
                link(nc.vector.match_replace(score3[:], top[:, 1], score2[:], -3e38))
                link(nc.vector.tensor_tensor(unsel[:], score[:], score3[:], ALU.is_equal))
                nc.vector.tensor_scalar(unsel[:], unsel[:], NEG, None, ALU.mult).then_inc(s["unsel_ready"], 1)
                dve.wait_ge(s["unsel_ready"], b + 1)
                for c in range(8):
                    dve.wait_ge(s["ss_ready"], b * 8 + (c + 1))
                    nc.vector.tensor_tensor(S[:, 512 * c:512 * c + 512].rearrange("p (k n) -> p k n", n=L_SLC), p_s[c % 2][0:R, :].rearrange("p (k n) -> p k n", n=L_SLC),
                                            unsel[:, 8 * c:8 * c + 8].unsqueeze(2).broadcast_to([R, 8, L_SLC]), ALU.add).then_inc(s["ss_taken"], 1)
                dve.wait_ge(s["new_ready"], b + 1)
                nc.vector.tensor_tensor(S[:, OLD:W0], p_m[0:R, 0:Q], nmask[:], ALU.add)
                nc.vector.tensor_tensor(S[:, W0 + WINDOW:], p_m[0:R, Q:2 * Q], wmask[:, WINDOW:], ALU.add)
                dve.wait_ge(s["sw_ready"], b + 1)
                link(nc.vector.tensor_tensor(S[:, W0:W0 + WINDOW], p_s[0][0:R, :], wmask[:, 0:WINDOW], ALU.add))
                nc.vector.reduce_max(mx[:, 1:2], S[:, 0:W0], AX)
                link(nc.vector.reduce_max(mx[:, 2:3], S[:, W0:], AX))
                nc.vector.tensor_scalar(nb[:, 1:3], mx[:, 1:3], -SCALE, None, ALU.mult).then_inc(s["nbs_ready"], 1)
                dve.wait_ge(s["ps_ready"], b + 1)
                link(nc.vector.reciprocal(rg[:, 1:3], l[:, 1:3]))
                link(nc.vector.memset(rg[:, 0:1], 1.0))
                link(nc.vector.tensor_tensor(rg[:], rg[:], gate[:], ALU.mult))
                dve.wait_ge(s["tn_ready"], b + 1)
                nc.vector.tensor_copy(pnew[:], p_m[0:Q, 0:2 * R].rearrange("p (a n) -> p a n", a=2)).then_inc(s["tn_done"], 1)
                for k in range(0, NG_S + 1, 2):
                    n = 8 if k < NG_S else 4
                    dve.wait_ge(s["t0_ready"], b * 3 + (k // 2 + 1))
                    nc.vector.tensor_copy(pst[:, 8 * k:8 * k + n, :], p_t[0][:, 0:n, :]).then_inc(s["t0_done"], 1)
                dve.wait_ge(s["o_ready"], b + 1)
                for br in range(3):
                    for g in range(2):
                        rows, cols = slice(32 * g, 32 * g + 32), slice(P * br + 64 * g, P * br + 64 * g + 64)
                        if br == 0:
                            nc.vector.tensor_scalar(o[rows, :], p_o[rows, cols], rg[rows, 0:1], None, ALU.mult).then_inc(s["o_done"], 1)
                        else:
                            dve.wait_ge(s["o_done"], b * 6 + (2 * br))
                            nc.vector.scalar_tensor_tensor(o[rows, :], p_o[rows, cols], rg[rows, br:br + 1], o[rows, :], ALU.mult, ALU.add).then_inc(s["o_done"], 1)
                dve.wait_ge(s["stored"], b * 128 + 128)
                dve.sem_inc(s["in_free"], 1)
                link.close()


def mix_phase(nc, d):
    BIG = 3e38
    with Phase(nc, "mix") as ph:
        w = ph.sb("w", [P, KC, D_MODEL])
        wr = ph.sb("wr", [P, KC, 36])
        rb = ph.sb("rb", [P, 36])
        gain = ph.sb("gain", [P, D_MODEL])
        real = ph.sb("real", [P, TILES])
        ident = ph.sb("ident", [P, P])
        eps = ph.sb("eps", [P, 1])
        cat, x, h, sq, f = (ph.sb(n, [P, D_MODEL]) for n in ("cat", "x", "h", "sq", "f"))
        catT = ph.sb("catT", [P, KC, P])
        fT = ph.sb("fT", [P, KC, P])
        valid = ph.sb("valid", [P, 1])
        ss, r, nm, z, ed, den = (ph.sb(n, [P, 1]) for n in ("ss", "r", "nm", "z", "ed", "den"))
        lg = ph.sb("lg", [P, 36])
        g16, g16r = ph.sb("g16", [P, 16]), ph.sb("g16r", [P, 16])
        ge = ph.sb("ge", [P, NG])
        pen = ph.sb("pen", [P, NG])
        el, el1, el2 = (ph.sb(n, [P, NE + 16]) for n in ("el", "el1", "el2"))
        top, pick = ph.sb("top", [P, 8]), ph.sb("pick", [P, 3, 8])
        route = ph.sb("route", [P, 66])
        p_t = [ph.ps(f"p_t{i}", [P, 4, P]) for i in range(2)]
        p_m = [ph.ps(f"p_m{i}", [P, 512]) for i in range(2)]
        p_f = [ph.ps(f"p_f{i}", [P, 4, P]) for i in range(2)]
        p_l = ph.ps("p_l", [P, 36])
        names = ("const_ready", "setup", "in_ready", "in_free", "cat_turned", "cat_copied", "mix_ready", "h_ready", "sq_ready", "ln_ready", "r_ready", "f_ready",
                 "f_turned", "f_copied", "lg_ready", "nm_ready", "ge_ready", "route_ready", "stored", "dve_step")
        s = {n: ph.sem(n) for n in names}
        block = ph.enter_context(nc.Block())

        @block.sync
        def _(sp):
            sp.sem_inc(s["in_free"], 1)
            for dst, src in ((wr, "w_route"), (rb, "b_route"), (gain, "ffn_norm"), (ident, "ident")):
                sp.dma_start(dst[:], d[src]).then_inc(s["const_ready"], 16)
            for k in range(KC):
                sp.dma_start(w[:, k], d["w_out"][:, k]).then_inc(s["const_ready"], 16)
            with sp.Fori(0, TILES) as t:
                tok = bass.ds(t * P, P)
                sp.wait_ge(s["in_free"], t + 1)
                sp.dma_start(cat[:, 0:512], d["attn"][tok, :]).then_inc(s["in_ready"], 16)
                sp.dma_start(cat[:, 512:], d["ssd"][tok, :]).then_inc(s["in_ready"], 16)
                sp.dma_start(x[:], d["x"][tok, :]).then_inc(s["in_ready"], 16)
                sp.dma_start(valid[:], d["real"][tok, :]).then_inc(s["in_ready"], 16)
                sp.wait_ge(s["h_ready"], t * 2 + 2)
                sp.dma_start(d["h"][tok, :], h[:]).then_inc(s["stored"], 16)
                sp.wait_ge(s["f_ready"], t + 1)
                sp.dma_start(d["f"][tok, :], f[:]).then_inc(s["stored"], 16)
                sp.wait_ge(s["route_ready"], t + 1)
                sp.dma_start(d["route"][tok, :], route[:]).then_inc(s["stored"], 16)
            sp.wait_ge(s["stored"], TILES * 48)

        @block.tensor
        def _(pe):
            pe.wait_ge(s["const_ready"], 16 * (4 + KC))
            with pe.Fori(0, TILES) as t:
                pe.wait_ge(s["in_ready"], t * 64 + 64)
                for k in range(KC):
                    mm = nc.tensor.transpose(p_t[k // 4][:, k % 4, :], cat[:, k * P:k * P + P], ident[:])
                mm.then_inc(s["cat_turned"], 1)
                pe.wait_ge(s["cat_copied"], t * 2 + 2)
                for n in range(2):
                    for k in range(KC):
                        mm = nc.tensor.matmul(p_m[n][:], catT[:, k, :], w[:, k, 512 * n:512 * n + 512], start=(k == 0), stop=(k == KC - 1))
                mm.then_inc(s["mix_ready"], 1)
                pe.wait_ge(s["f_ready"], t + 1)
                for k in range(KC):
                    mm = nc.tensor.transpose(p_f[k // 4][:, k % 4, :], f[:, k * P:k * P + P], ident[:])
                mm.then_inc(s["f_turned"], 1)
                pe.wait_ge(s["f_copied"], t * 2 + 2)
                for k in range(KC):
                    mm = nc.tensor.matmul(p_l[:], fT[:, k, :], wr[:, k, :], start=(k == 0), stop=(k == KC - 1))
                mm.then_inc(s["lg_ready"], 1)

        @block.scalar
        def _(act):
            act.wait_ge(s["setup"], 3)
            with act.Fori(0, TILES) as t:
                act.wait_ge(s["cat_turned"], t + 1)
                nc.scalar.activation(catT[:, 4:8], p_t[1][:], ACT.Copy).then_inc(s["cat_copied"], 1)
                act.wait_ge(s["h_ready"], t * 2 + 2)
                nc.scalar.activation(sq[:], h[:], ACT.Square, accum_out=ss[:]).then_inc(s["sq_ready"], 1)
                act.wait_ge(s["sq_ready"], t + 1)
                nc.scalar.activation(r[:], ss[:], ACT.Ln, bias=eps[:], scale=1.0 / D_MODEL).then_inc(s["ln_ready"], 1)
                act.wait_ge(s["ln_ready"], t + 1)
                nc.scalar.activation(r[:], r[:], ACT.Exp, scale=-0.5).then_inc(s["r_ready"], 1)
                act.wait_ge(s["f_turned"], t + 1)
                nc.scalar.activation(fT[:, 4:8], p_f[1][:], ACT.Copy).then_inc(s["f_copied"], 1)
                act.wait_ge(s["nm_ready"], t + 1)
                nc.scalar.activation(ge[:], lg[:, 0:NG], ACT.Exp, bias=nm[:], accum_out=z[:])
                nc.scalar.activation(ed[:], den[:], ACT.Exp).then_inc(s["ge_ready"], 1)

        @block.vector
        def _(dve):
            nc.vector.memset(eps[:], EPS).then_inc(s["setup"], 1)
            for i, tile in enumerate((g16, el, pick)):
                ins = nc.vector.memset(tile[:], -BIG)
            ins.then_inc(s["setup"], 2)
            dve.wait_ge(s["setup"], 3)
            dve.wait_ge(s["const_ready"], 16 * (4 + KC))
            with dve.Fori(0, TILES) as t:
                link = Chain(dve, s["dve_step"], 20, t)
                dve.wait_ge(s["cat_turned"], t + 1)
                nc.vector.tensor_copy(catT[:, 0:4], p_t[0][:]).then_inc(s["cat_copied"], 1)
                dve.wait_ge(s["mix_ready"], t + 1)
                for n in range(2):
                    nc.vector.tensor_tensor(h[:, 512 * n:512 * n + 512], x[:, 512 * n:512 * n + 512], p_m[n][:], ALU.add).then_inc(s["h_ready"], 1)
                dve.wait_ge(s["r_ready"], t + 1)
                nc.vector.scalar_tensor_tensor(f[:], h[:], r[:], gain[:], ALU.mult, ALU.mult).then_inc(s["f_ready"], 1)
                dve.wait_ge(s["f_turned"], t + 1)
                nc.vector.tensor_copy(fT[:, 0:4], p_f[0][:]).then_inc(s["f_copied"], 1)
                dve.wait_ge(s["lg_ready"], t + 1)
                link(nc.vector.tensor_tensor(lg[:], p_l[:], rb[:], ALU.add))
                link(nc.vector.tensor_copy(g16[:, 0:NG], lg[:, 0:NG]), ph.passed)
                link(nc.vector.max(top[:], g16[:]))
                link(nc.vector.tensor_copy(pick[:, 0, 0:1], top[:, 0:1]))
                link(nc.vector.tensor_scalar(nm[:], top[:, 0:1], -1.0, None, ALU.mult), ph.passed)
                link(nc.vector.match_replace(g16r[:], pick[:, 0], g16[:], BIG))
                link(nc.vector.tensor_scalar(pen[:], g16r[:, 0:NG], BIG, None, ALU.is_equal))
                link(nc.vector.tensor_scalar(pen[:], pen[:], -NEG, NEG, ALU.mult, ALU.add))
                link(nc.vector.tensor_tensor(el[:, 0:NE].rearrange("p (g e) -> p g e", g=NG), lg[:, NG:].rearrange("p (g e) -> p g e", g=NG),
                                             pen[:].unsqueeze(2).broadcast_to([P, NG, EPG]), ALU.add), ph.passed)
                link(nc.vector.max(top[:], el[:]))
                nc.vector.tensor_copy(pick[:, 1, 0:1], top[:, 0:1])
                link(nc.vector.tensor_copy(pick[:, 2, 0:1], top[:, 1:2]), ph.passed)
                nc.vector.tensor_tensor(den[:], top[:, 1:2], top[:, 0:1], ALU.subtract).then_inc(s["nm_ready"], 1)
                link(nc.vector.match_replace(el1[:], pick[:, 1], el[:], BIG), ph.passed)
                link(nc.vector.match_replace(el2[:], pick[:, 2], el1[:], BIG))
                link(nc.vector.tensor_scalar(route[:, 0:NE], el1[:, 0:NE], BIG, None, ALU.is_equal))
                link(nc.vector.tensor_scalar(route[:, NE:2 * NE], el2[:, 0:NE], BIG, None, ALU.is_equal))
                link(nc.vector.tensor_tensor(route[:, NE:2 * NE], route[:, NE:2 * NE], route[:, 0:NE], ALU.subtract))
                link(nc.vector.tensor_scalar(route[:, 0:2 * NE], route[:, 0:2 * NE], valid[:], None, ALU.mult))
                dve.wait_ge(s["ge_ready"], t + 1)
                link(nc.vector.scalar_tensor_tensor(den[:], ed[:], 1.0, z[:], ALU.add, ALU.mult))
                link(nc.vector.reciprocal(route[:, 64:65], den[:]))
                link(nc.vector.tensor_tensor(route[:, 65:66], route[:, 64:65], ed[:], ALU.mult))
                dve.sem_inc(s["route_ready"], 1)
                dve.wait_ge(s["stored"], t * 48 + 48)
                dve.sem_inc(s["in_free"], 1)
                link.close()


def dispatch_phase(nc, d):
    with Phase(nc, "dsp") as ph:
        route = ph.sb("route", [P, TILES, 66])
        before = ph.sb("before", [P, P])
        ones = ph.sb("ones", [P, P])
        first = ph.sb("first", [P, NE])
        padoff = ph.sb("padoff", [P, TILES, 2])
        ids = ph.sb("ids", [P, TILES], U32)
        blocks = ph.sb("blocks", [P, OVER_BLOCKS])
        m = ph.sb("m", [P, TILES, NE])
        pos = ph.sb("pos", [P, TILES, NE])
        late = ph.sb("late", [P, TILES, NE])
        n_e, ov, cum, cum2, base2 = (ph.sb(n, [P, NE]) for n in ("n_e", "ov", "cum", "cum2", "base2"))
        dest = ph.sb("dest", [P, TILES, 2])
        gidx = ph.sb("gidx", [P, TILES, 2], U32)
        sidx = ph.sb("sidx", [P, TILES, 2], U32)
        fill = ph.sb("fill", [P, SLOTS // P], U32)
        cmpj = ph.sb("cmpj", [P, OVER_BLOCKS, NE])
        over = ph.sb("over", [P, OVER_BLOCKS + 1])
        over_i = ph.sb("over_i", [P, OVER_BLOCKS + 1], I32)
        p_c = ph.ps("p_c", [P, TILES + 1, NE])
        loaded, m_ready, cnt_ready, idx_ready, over_ready = ph.sem("loaded"), ph.sem("m_ready"), ph.sem("cnt_ready"), ph.sem("idx_ready"), ph.sem("over_ready")
        filled, fill_ready, scattered, stored, dve_step = ph.sem("filled"), ph.sem("fill_ready"), ph.sem("scattered"), ph.sem("stored"), ph.sem("dve_step")
        block = ph.enter_context(nc.Block())

        @block.sync
        def _(sp):
            for dst, src in ((route[:], d["route"].rearrange("(t p) n -> p t n", p=P)), (before[:], d["before"]), (first[:], d["first"]), (padoff[:], d["padoff"]),
                             (ids[:], d["ids"]), (blocks[:], d["blocks"])):
                sp.dma_start(dst, src).then_inc(loaded, 16)
            sp.wait_ge(fill_ready, 1)
            sp.dma_start(d["slot_tok"].rearrange("(p n) o -> p (n o)", p=P), fill[:]).then_inc(filled, 16)
            sp.wait_ge(idx_ready, 1)
            sp.dma_start(d["gidx"].rearrange("(t p) n -> p t n", p=P), gidx[:]).then_inc(stored, 16)
            sp.wait_ge(over_ready, 1)
            sp.dma_start(d["over"], over_i[0:1, :]).then_inc(stored, 16)
            sp.wait_ge(stored, 32)

        @block.tensor
        def _(pe):
            pe.wait_ge(m_ready, 1)
            for t in range(TILES + 1):
                if t < TILES:
                    mm = nc.tensor.matmul(p_c[:, t, :], before[:], m[:, t, :], start=True, stop=(t == 0))
                for u in range(t):
                    mm = nc.tensor.matmul(p_c[:, t, :], ones[:], m[:, u, :], start=(t == TILES and u == 0), stop=(u == t - 1))
            mm.then_inc(cnt_ready, 1)

        @block.vector
        def _(dve):
            link = Chain(dve, dve_step)
            nc.vector.memset(fill[:], TOK - 1).then_inc(fill_ready, 1)
            link(nc.vector.memset(ones[:], 1.0))
            dve.wait_ge(loaded, 96)
            nc.vector.tensor_tensor(m[:], route[:, :, 0:NE], route[:, :, NE:2 * NE], ALU.add).then_inc(m_ready, 1)
            dve.wait_ge(cnt_ready, 1)
            link(nc.vector.tensor_copy(pos[:], p_c[:, 0:TILES, :]))
            link(nc.vector.tensor_copy(n_e[:], p_c[:, TILES, :]))
            link(nc.vector.tensor_scalar(ov[:], n_e[:], float(P), None, ALU.is_gt))
            for k in range(2, TILES):
                link(nc.vector.scalar_tensor_tensor(ov[:], n_e[:], float(P * k), ov[:], ALU.is_gt, ALU.add))
            link(nc.vector.tensor_copy(cum[:], ov[:]))
            a, b = cum, cum2
            for k in (1, 2, 4, 8, 16):
                nc.vector.tensor_copy(b[:, 0:k], a[:, 0:k])
                link(nc.vector.tensor_tensor(b[:, k:], a[:, k:], a[:, 0:NE - k], ALU.add))
                a, b = b, a
            link(nc.vector.tensor_tensor(base2[:], a[:], ov[:], ALU.subtract))
            link(nc.vector.tensor_scalar(base2[:], base2[:], float(P), float(P * (MAIN_BLOCKS - 1)), ALU.mult, ALU.add))
            link(nc.vector.tensor_tensor(base2[:], base2[:], first[:], ALU.subtract))
            link(nc.vector.tensor_scalar(late[:], pos[:], float(P), None, ALU.is_ge))
            link(nc.vector.tensor_tensor(late[:], late[:], base2[:].unsqueeze(1).broadcast_to([P, TILES, NE]), ALU.mult))
            link(nc.vector.tensor_tensor(pos[:], pos[:], first[:].unsqueeze(1).broadcast_to([P, TILES, NE]), ALU.add))
            link(nc.vector.tensor_tensor(pos[:], pos[:], late[:], ALU.add))
            for k in range(2):
                link(nc.vector.tensor_tensor(m[:], pos[:], route[:, :, NE * k:NE * k + NE], ALU.mult))
                link(nc.vector.reduce_sum(dest[:, :, k], m[:], AX))
            nc.vector.tensor_copy(gidx[:], dest[:])
            link(nc.vector.tensor_tensor(dest[:], dest[:], padoff[:], ALU.add))
            nc.vector.tensor_copy(sidx[:], dest[:]).then_inc(idx_ready, 1)
            link(nc.vector.tensor_tensor(cmpj[:], a[:].unsqueeze(1).broadcast_to([P, OVER_BLOCKS, NE]), blocks[:].unsqueeze(2).broadcast_to([P, OVER_BLOCKS, NE]), ALU.is_le))
            link(nc.vector.reduce_sum(over[:, 0:OVER_BLOCKS], cmpj[:], AX))
            link(nc.vector.tensor_scalar(over[:, 0:OVER_BLOCKS], over[:, 0:OVER_BLOCKS], float(NE - 1), None, ALU.min))
            link(nc.vector.tensor_copy(over[:, OVER_BLOCKS:], a[:, NE - 1:NE]))
            nc.vector.tensor_copy(over_i[:], over[:]).then_inc(over_ready, 1)

        @block.gpsimd
        def _(pool):
            pool.wait_ge(filled, 16)
            pool.wait_ge(idx_ready, 1)
            for t in range(TILES):
                for k in range(2):
                    pool.indirect_dma_start(d["slot_tok"], bass.IndirectOffsetOnAxis(ap=sidx[:, t, k:k + 1], axis=0), ids[:, t:t + 1], None).then_inc(scattered, 16)
            pool.wait_ge(scattered, 2 * TILES * 16)


def expert_phase(nc, d, overflow):
    NBUF = 1 if overflow else 2
    with Phase(nc, "ovf" if overflow else "exp") as ph:
        wg = [ph.sb(f"wg{i}", [P, KC, D_EXP]) for i in range(NBUF)]
        wu = [ph.sb(f"wu{i}", [P, KC, D_EXP]) for i in range(NBUF)]
        wd = [ph.sb(f"wd{i}", [P, D_EXP // P, D_MODEL]) for i in range(NBUF)]
        idx = [ph.sb(f"idx{i}", [P, 1], U32) for i in range(NBUF)]
        xg = [ph.sb(f"xg{i}", [P, D_MODEL]) for i in range(NBUF)]
        xT = ph.sb("xT", [P, KC, P])
        e = ph.sb("e", [P, D_EXP])
        hb = ph.sb("hb", [P, D_EXP])
        hT = ph.sb("hT", [P, 4, P])
        y = [ph.sb(f"y{i}", [P, D_MODEL]) for i in range(NBUF)]
        ident = ph.sb("ident", [P, P])
        over = ph.sb("over", [1, OVER_BLOCKS + 1], I32)
        p_t = [ph.ps(f"p_t{i}", [P, 4, P]) for i in range(2)]
        p_g, p_u, p_h = ph.ps("p_g", [P, D_EXP]), ph.ps("p_u", [P, D_EXP]), ph.ps("p_h", [P, 4, P])
        p_y = [ph.ps(f"p_y{i}", [P, 512]) for i in range(2)]
        const_ready = ph.sem("const_ready")
        per_buf = [{n: ph.sem(f"{n}{i}") for n in ("g_loaded", "u_loaded", "d_loaded", "idx_ready", "x_ready", "x_free", "gu_free", "d_free", "stored", "y_ready", "idx_free")} for i in range(NBUF)]
        s = {n: ph.sem(n) for n in ("x_turned", "x_copied", "g_ready", "u_ready", "e_ready", "h_ready", "h_turned", "h_copied", "y_done", "dve_step")}
        block = ph.enter_context(nc.Block())
        N = (OVER_BLOCKS if overflow else MAIN_BLOCKS) // NBUF

        def blocks(eng, body):
            if not overflow:
                with eng.Fori(0, N) as i:
                    for k in range(NBUF):
                        body(i, i * NBUF + k, k)
            else:
                eng.wait_ge(const_ready, 32)
                needed = eng.value_load(over[0:1, OVER_BLOCKS:OVER_BLOCKS + 1], min_val=0, max_val=OVER_BLOCKS)
                with eng.Fori(0, N) as i:
                    with eng.If(needed > i):
                        body(i, i, 0)
                    with eng.Else():
                        pass

        @block.sync
        def _(sp):
            sp.dma_start(ident[:], d["ident"]).then_inc(const_ready, 16)
            sp.dma_start(over[:], d["over"]).then_inc(const_ready, 16)
            for k in range(NBUF):
                for n in ("gu_free", "d_free"):
                    sp.sem_inc(per_buf[k][n], 1)

            def body(i, b, k):
                q = per_buf[k]
                ex = sp.value_load(over[0:1, bass.ds(b, 1)], min_val=0, max_val=NE - 1) if overflow else b
                sp.wait_ge(q["gu_free"], i + 1)
                sp.dma_start(wg[k][:], d["w_gate"][bass.ds(ex, 1)].rearrange("o (c p) n -> p (o c) n", p=P)).then_inc(q["g_loaded"], 16)
                sp.dma_start(wu[k][:], d["w_up"][bass.ds(ex, 1)].rearrange("o (c p) n -> p (o c) n", p=P)).then_inc(q["u_loaded"], 16)
                sp.wait_ge(q["d_free"], i + 1)
                sp.dma_start(wd[k][:], d["w_down"][bass.ds(ex, 1)].rearrange("o (c p) n -> p (o c) n", p=P)).then_inc(q["d_loaded"], 16)
            blocks(sp, body)

        @block.gpsimd
        def _(pool):
            for k in range(NBUF):
                pool.sem_inc(per_buf[k]["x_free"], 1)

            def body(i, b, k):
                q = per_buf[k]
                row0 = (b + (MAIN_BLOCKS if overflow else 0)) * P
                hold(pool, q["x_free"], i + 1, ph.passed)
                pool.dma_start(idx[k][:], d["slot_tok"][bass.ds(row0, P), :]).then_inc(q["idx_ready"], 16)
                hold(pool, q["idx_ready"], i * 16 + 16, ph.passed)
                pool.indirect_dma_start(xg[k][:], None, d["f"], bass.IndirectOffsetOnAxis(ap=idx[k][:, 0:1], axis=0)).then_inc(q["x_ready"], 16)
            blocks(pool, body)

        @block.tensor
        def _(pe):
            pe.wait_ge(const_ready, 32)

            def body(i, b, k):
                q = per_buf[k]
                pe.wait_ge(q["x_ready"], i * 16 + 16)
                for c in range(KC):
                    mm = nc.tensor.transpose(p_t[c // 4][:, c % 4, :], xg[k][:, c * P:c * P + P], ident[:])
                mm.then_inc(s["x_turned"], 1)
                pe.wait_ge(s["x_copied"], b * 2 + 2)
                pe.sem_inc(q["x_free"], 1)
                for n, (dst, w) in enumerate(((p_g, wg[k]), (p_u, wu[k]))):
                    pe.wait_ge(q[("g_loaded", "u_loaded")[n]], i * 16 + 16)
                    for c in range(KC):
                        mm = nc.tensor.matmul(dst[:], xT[:, c, :], w[:, c, :], start=(c == 0), stop=(c == KC - 1))
                    mm.then_inc(s[("g_ready", "u_ready")[n]], 1)
                pe.wait_ge(s["h_ready"], b + 1)
                pe.sem_inc(q["gu_free"], 1)
                for c in range(4):
                    mm = nc.tensor.transpose(p_h[:, c, :], hb[:, c * P:c * P + P], ident[:])
                mm.then_inc(s["h_turned"], 1)
                pe.wait_ge(s["h_copied"], b + 1)
                pe.wait_ge(q["d_loaded"], i * 16 + 16)
                for n in range(2):
                    for c in range(4):
                        mm = nc.tensor.matmul(p_y[n][:], hT[:, c, :], wd[k][:, c, 512 * n:512 * n + 512], start=(c == 0), stop=(c == 3))
                mm.then_inc(s["y_done"], 1)
            blocks(pe, body)

        @block.scalar
        def _(act):
            for k in range(NBUF):
                act.sem_inc(per_buf[k]["stored"], 16)

            def body(i, b, k):
                q = per_buf[k]
                act.wait_ge(s["x_turned"], b + 1)
                nc.scalar.activation(xT[:, 4:8], p_t[1][:], ACT.Copy).then_inc(s["x_copied"], 1)
                act.wait_ge(s["g_ready"], b + 1)
                nc.scalar.activation(e[:], p_g[:], ACT.Exp, scale=-1.0).then_inc(s["e_ready"], 1)
                act.wait_ge(s["y_done"], b + 1)
                act.sem_inc(q["d_free"], 1)
                act.wait_ge(q["stored"], i * 16 + 16)
                for n in range(2):
                    ins = nc.scalar.activation(y[k][:, 512 * n:512 * n + 512], p_y[n][:], ACT.Copy)
                ins.then_inc(q["y_ready"], 1)
                act.wait_ge(q["y_ready"], i + 1)
                row0 = (b + (MAIN_BLOCKS if overflow else 0)) * P
                act.dma_start(d["ypad"][bass.ds(row0, P), :], y[k][:]).then_inc(q["stored"], 16)
                if overflow:
                    hold(act, q["stored"], i * 16 + 32, ph.passed)
            blocks(act, body)
            if not overflow:
                for k in range(NBUF):
                    act.wait_ge(per_buf[k]["stored"], 16 * N + 16)

        @block.vector
        def _(dve):
            def body(i, b, k):
                dve.wait_ge(s["x_turned"], b + 1)
                nc.vector.tensor_copy(xT[:, 0:4], p_t[0][:]).then_inc(s["x_copied"], 1)
                link = Chain(dve, s["dve_step"], 3, b)
                dve.wait_ge(s["e_ready"], b + 1)
                link(nc.vector.tensor_scalar(e[:], e[:], 1.0, None, ALU.add))
                link(nc.vector.reciprocal(e[:], e[:]))
                link(nc.vector.tensor_tensor(e[:], e[:], p_g[:], ALU.mult))
                dve.wait_ge(s["u_ready"], b + 1)
                nc.vector.tensor_tensor(hb[:], e[:], p_u[:], ALU.mult).then_inc(s["h_ready"], 1)
                dve.wait_ge(s["h_turned"], b + 1)
                nc.vector.tensor_copy(hT[:], p_h[:]).then_inc(s["h_copied"], 1)
            blocks(dve, body)


def final_phase(nc, d):
    with Phase(nc, "fin") as ph:
        wg = ph.sb("wg", [P, KC, D_MODEL])
        wp = ph.sb("wp", [P, 2, D_MODEL])
        gain = ph.sb("gain", [P, D_MODEL])
        ident = ph.sb("ident", [P, P])
        eps = ph.sb("eps", [P, 1])
        gidx = ph.sb("gidx", [P, 2], U32)
        wt = ph.sb("wt", [P, 2])
        h, y1, y2, e, pn, sq = (ph.sb(n, [P, D_MODEL]) for n in ("h", "y1", "y2", "e", "pn", "sq"))
        pT = ph.sb("pT", [P, 2, P])
        hT = ph.sb("hT", [P, KC, P])
        ss, r = ph.sb("ss", [P, 2]), ph.sb("r", [P, 1])
        p_t = [ph.ps(f"p_t{i}", [P, 4, P]) for i in range(2)]
        p_g = [ph.ps(f"p_g{i}", [P, 512]) for i in range(2)]
        p_p = [ph.ps(f"p_p{i}", [P, 512]) for i in range(2)]
        names = ("const_ready", "setup", "idx_ready", "in_ready", "y_ready", "in_free", "h_ready", "h_turned", "h_copied", "g_ready", "p_ready", "e_ready",
                 "sq_ready", "ss_ready", "ln_ready", "r_ready", "out_ready", "stored", "dve_step")
        s = {n: ph.sem(n) for n in names}
        block = ph.enter_context(nc.Block())

        @block.sync
        def _(sp):
            sp.sem_inc(s["in_free"], 1)
            for dst, src in ((wp, "w_ple_proj"), (gain, "ple_norm"), (ident, "ident")):
                sp.dma_start(dst[:], d[src]).then_inc(s["const_ready"], 16)
            for k in range(KC):
                sp.dma_start(wg[:, k], d["w_ple_gate"][:, k]).then_inc(s["const_ready"], 16)
            with sp.Fori(0, TILES) as t:
                tok = bass.ds(t * P, P)
                sp.wait_ge(s["in_free"], t + 1)
                sp.dma_start(gidx[:], d["gidx"][tok, :]).then_inc(s["idx_ready"], 16)
                sp.dma_start(wt[:], d["route"][tok, 64:66]).then_inc(s["in_ready"], 16)
                sp.dma_start(h[:], d["h"][tok, :]).then_inc(s["in_ready"], 16)
                sp.dma_start(pT[:], d["pT"][bass.ds(t, 1)].rearrange("o p c n -> (o p) c n")).then_inc(s["in_ready"], 16)
                sp.wait_ge(s["out_ready"], t + 1)
                sp.dma_start(d["y"][tok, :], pn[:]).then_inc(s["stored"], 16)
            sp.wait_ge(s["stored"], TILES * 16)

        @block.gpsimd
        def _(pool):
            with pool.Fori(0, TILES) as t:
                hold(pool, s["idx_ready"], t * 16 + 16, ph.passed)
                for k, dst in enumerate((y1, y2)):
                    pool.indirect_dma_start(dst[:], None, d["ypad"], bass.IndirectOffsetOnAxis(ap=gidx[:, k:k + 1], axis=0)).then_inc(s["y_ready"], 16)

        @block.tensor
        def _(pe):
            pe.wait_ge(s["const_ready"], 16 * (3 + KC))
            with pe.Fori(0, TILES) as t:
                pe.wait_ge(s["in_ready"], t * 48 + 48)
                pe.wait_ge(s["in_free"], t + 1)
                for n in range(2):
                    for c in range(2):
                        mm = nc.tensor.matmul(p_p[n][:], pT[:, c, :], wp[:, c, 512 * n:512 * n + 512], start=(c == 0), stop=(c == 1))
                mm.then_inc(s["p_ready"], 1)
                pe.wait_ge(s["h_ready"], t + 1)
                for c in range(KC):
                    mm = nc.tensor.transpose(p_t[c // 4][:, c % 4, :], h[:, c * P:c * P + P], ident[:])
                mm.then_inc(s["h_turned"], 1)
                pe.wait_ge(s["h_copied"], t * 2 + 2)
                for n in range(2):
                    for c in range(KC):
                        mm = nc.tensor.matmul(p_g[n][:], hT[:, c, :], wg[:, c, 512 * n:512 * n + 512], start=(c == 0), stop=(c == KC - 1))
                mm.then_inc(s["g_ready"], 1)

        @block.scalar
        def _(act):
            act.wait_ge(s["setup"], 1)
            with act.Fori(0, TILES) as t:
                act.wait_ge(s["p_ready"], t + 1)
                for n in range(2):
                    ins = nc.scalar.activation(sq[:, 512 * n:512 * n + 512], p_p[n][:], ACT.Square, accum_out=ss[:, n:n + 1])
                ins.then_inc(s["sq_ready"], 1)
                act.wait_ge(s["ss_ready"], t + 1)
                nc.scalar.activation(r[:], ss[:, 0:1], ACT.Ln, bias=eps[:], scale=1.0 / D_MODEL).then_inc(s["ln_ready"], 1)
                act.wait_ge(s["ln_ready"], t + 1)
                nc.scalar.activation(r[:], r[:], ACT.Exp, scale=-0.5).then_inc(s["r_ready"], 1)
                act.wait_ge(s["h_turned"], t + 1)
                nc.scalar.activation(hT[:, 4:8], p_t[1][:], ACT.Copy).then_inc(s["h_copied"], 1)
                act.wait_ge(s["g_ready"], t + 1)
                for n in range(2):
                    ins = nc.scalar.activation(e[:, 512 * n:512 * n + 512], p_g[n][:], ACT.Exp, scale=-1.0)
                ins.then_inc(s["e_ready"], 1)

        @block.vector
        def _(dve):
            nc.vector.memset(eps[:], EPS).then_inc(s["setup"], 1)
            dve.wait_ge(s["const_ready"], 16 * (3 + KC))
            with dve.Fori(0, TILES) as t:
                link = Chain(dve, s["dve_step"], 6, t)
                dve.wait_ge(s["in_ready"], t * 48 + 48)
                dve.wait_ge(s["y_ready"], t * 32 + 32)
                link(nc.vector.scalar_tensor_tensor(h[:], y1[:], wt[:, 0:1], h[:], ALU.mult, ALU.add))
                nc.vector.scalar_tensor_tensor(h[:], y2[:], wt[:, 1:2], h[:], ALU.mult, ALU.add).then_inc(s["h_ready"], 1)
                dve.wait_ge(s["sq_ready"], t + 1)
                nc.vector.tensor_tensor(ss[:, 0:1], ss[:, 0:1], ss[:, 1:2], ALU.add).then_inc(s["ss_ready"], 1)
                dve.wait_ge(s["h_turned"], t + 1)
                nc.vector.tensor_copy(hT[:, 0:4], p_t[0][:]).then_inc(s["h_copied"], 1)
                dve.wait_ge(s["r_ready"], t + 1)
                for n in range(2):
                    c = slice(512 * n, 512 * n + 512)
                    ins = nc.vector.scalar_tensor_tensor(pn[:, c], p_p[n][:], r[:], gain[:, c], ALU.mult, ALU.mult)
                link(ins)
                dve.wait_ge(s["e_ready"], t + 1)
                link(nc.vector.tensor_scalar(e[:], e[:], 1.0, None, ALU.add))
                link(nc.vector.reciprocal(e[:], e[:]))
                link(nc.vector.tensor_tensor(pn[:], pn[:], e[:], ALU.mult))
                dve.wait_ge(s["h_ready"], t + 1)
                link(nc.vector.tensor_tensor(pn[:], pn[:], h[:], ALU.add))
                dve.sem_inc(s["out_ready"], 1)
                dve.wait_ge(s["stored"], t * 16 + 16)
                dve.sem_inc(s["in_free"], 1)
                link.close()



def _pool(cache):
    n = cache.shape[0]
    ops = cache[:, :, 0:2].reshape(n, 8, 8, 2, 2, KVH, HD)
    ops = ops.transpose(0, 3, 6, 4, 2, 5, 1).reshape(n, P, 256)
    keys = cache[:, :, 2].reshape(n, P, P).transpose(0, 2, 1)
    return np.concatenate([ops, keys, cache[:, :, 3].reshape(n, P, P)], 2)


def _layout(inputs):
    f = {k: np.asarray(v) for k, v in inputs.items()}
    pad = np.zeros((TOK - SEQ - N_SMP, D_MODEL), np.float32)
    x = np.concatenate([f["x_prompt"][0], f["x_sample"].reshape(N_SMP, D_MODEL), pad])
    pos = np.concatenate([np.arange(SEQ), PAST + np.arange(P) % DEC_SEQ]).astype(np.float32)
    half = HD // 2
    inv = np.float32(10000.0) ** (-np.arange(half, dtype=np.float32) / half)
    ang = (pos[:, None] * inv[None, :]).astype(np.float32)
    trig = np.stack([np.cos(ang), np.sin(ang)], 1).reshape(TILES, P, 2, half).astype(np.float32)
    w_in = f["w_in"][0].copy()
    w_in[:, :ATT_W] = w_in[:, :ATT_W].reshape(D_MODEL, KVH, HPG, HD).transpose(0, 2, 1, 3).reshape(D_MODEL, ATT_W)
    w_in[:, C_GL:C_Z] = w_in[:, C_GL:C_Z].reshape(D_MODEL, KVH, HPG, 3).transpose(0, 2, 1, 3).reshape(D_MODEL, 24)
    gains = np.concatenate([f["q_norm"][0][None], f["k_norm"][0]])
    tok = np.arange(P)
    seq = tok // DEC_SEQ
    same = np.stack([np.ones((P, P)), seq[:, None] == seq[None]], 1).astype(np.float32)
    tri = (same * (tok[:, None] <= tok[None])[:, None]).astype(np.float32)
    seqcol = (seq[:, None] == np.arange(DEC_BATCH)[None]).astype(np.float32)
    ends = np.arange(N_CMP_P) * S_CMP + L_CMP - 1
    w1 = f["cmp_w1"][0].reshape(2, 2, S_CMP, HD, HD)
    rg, rq = np.arange(64) // 32, np.arange(64) % DEC_SEQ
    gsum = ((rg[:, None] == rg[None]) & (rq[:, None] == rq[None])).astype(np.float32)
    nmask = np.where(np.arange(DEC_SEQ)[None] <= rq[:, None], 0, NEG).astype(np.float32)
    key = np.arange(WINDOW + DEC_SEQ)[None]
    wmask = np.where((key > rq[:, None]) & (key <= rq[:, None] + WINDOW), 0, NEG).astype(np.float32)
    c0, s0 = np.arange(2 * P)[:, None] * S_CMP, np.arange(N_SLC_S)[None] * L_SLC
    cover = np.maximum(np.minimum(c0 + L_CMP, s0 + L_SLC) - np.maximum(c0, s0), 0).astype(np.float32) / np.float32(L_CMP)
    cover = cover.reshape(2, P, N_SLC_S).transpose(1, 0, 2)
    cw = f["cache_win"][0].reshape(DEC_BATCH, WINDOW, 2, P)
    p_all = np.concatenate([f["p_prompt"][0, 0], f["p_sample"][0].reshape(N_SMP, PLE), np.zeros((TOK - SEQ - N_SMP, PLE), np.float32)])
    padoff = np.zeros((P, TILES, 2), np.float32)
    padoff[N_SMP:, NT, :] = DUMP + np.arange(2 * (P - N_SMP)).reshape(-1, 2)
    cm = {
        "xT": x.reshape(TILES, P, KC, P).transpose(0, 3, 2, 1),
        "trig": trig,
        "w_in": w_in.reshape(KC, P, C_END).transpose(1, 0, 2),
        "attn_norm": f["attn_norm"][0].reshape(KC, P).T,
        "head_gain": np.broadcast_to(gains, (P, 4, HD)),
        "ident": np.eye(P, dtype=np.float32),
        "cmp_w1_sd": np.tile(w1.transpose(3, 0, 2, 1, 4), (2, 1, 1, 1, 1)).reshape(P, 2, S_CMP, P),
        "cmp_pe": f["cmp_pe"][0].reshape(2, 2, S_CMP, HD).transpose(3, 0, 1, 2),
        "cmp_w2": f["cmp_w2"][0].transpose(1, 0, 2),
        "diag": np.where(tok[None] > tok[:, None], NEG, 0).astype(np.float32),
        "old": np.where(tok[None] <= tok[:, None], NEG, 0).astype(np.float32),
        "cmask": np.where(ends[None, None] <= (np.arange(NT)[None] * P + tok[:, None])[..., None], 0, NEG).astype(np.float32),
        "valid": (tok[:, None] >= L_CMP - 1).astype(np.float32),
        "cmp_w1_seg": w1.reshape(2, 2, 8, 2, HD, HD).transpose(3, 4, 0, 2, 1, 5).reshape(P, 2, 8, P),
        "cover": cover, "gsum": gsum, "nmask": nmask, "wmask": wmask,
        "page_table": f["page_table"],
        "pool": _pool(f["cache_kv"][0]),
        "win_pack": np.concatenate([cw[:, :, 0].transpose(0, 2, 1), cw[:, :, 1].reshape(DEC_BATCH, 4, P, P).transpose(0, 2, 1, 3).reshape(DEC_BATCH, P, 512)], 2),
        "cache_win": cw.reshape(DEC_BATCH, WINDOW, 256),
        "x": x,
        "w_out": np.concatenate([f["w_out"][0][:ATT_W].reshape(KVH, HPG, HD, D_MODEL).transpose(1, 0, 2, 3).reshape(ATT_W, D_MODEL), f["w_out"][0][ATT_W:]])
                   .reshape(KC, P, D_MODEL).transpose(1, 0, 2),
        "w_route": np.concatenate([f["w_rg"][0], f["w_re"][0]], 1).reshape(KC, P, 36).transpose(1, 0, 2),
        "b_route": np.broadcast_to(np.concatenate([f["b_rg"][0], f["b_re"][0]]), (P, 36)),
        "ffn_norm": np.broadcast_to(f["ffn_norm"][0], (P, D_MODEL)),
        "real": (np.arange(TOK) < SEQ + N_SMP).astype(np.float32)[:, None],
        "before": (tok[:, None] < tok[None]).astype(np.float32),
        "first": np.broadcast_to(np.arange(NE, dtype=np.float32) * P, (P, NE)),
        "padoff": padoff, "ids": np.arange(TOK, dtype=np.uint32).reshape(TILES, P).T,
        "blocks": np.broadcast_to(np.arange(OVER_BLOCKS, dtype=np.float32), (P, OVER_BLOCKS)),
        "w_gate": f["w_gate"][0], "w_up": f["w_up"][0], "w_down": f["w_down"][0],
        "w_ple_gate": f["w_ple_gate"][0].reshape(KC, P, D_MODEL).transpose(1, 0, 2),
        "w_ple_proj": f["w_ple_proj"][0].reshape(2, P, D_MODEL).transpose(1, 0, 2),
        "ple_norm": np.broadcast_to(f["ple_norm"][0], (P, D_MODEL)),
        "pT": p_all.reshape(TILES, P, 2, P).transpose(0, 3, 2, 1),
        "conv_w": f["conv_w"][0].T.reshape(6, P, CONV_W).transpose(1, 0, 2),
        "conv_b": f["conv_b"][0].reshape(6, P).T,
        "state_conv": f["state_conv"][0].transpose(2, 0, 1).reshape(6, P, DEC_BATCH, 3).transpose(1, 0, 2, 3),
        "tri": tri, "mask": np.where(tri > 0, 0, NEG).astype(np.float32), "same": same,
        "seqcol": seqcol, "seqrow": np.broadcast_to(seqcol.T, (P, DEC_BATCH, P)),
        "head_ssm": np.broadcast_to(np.stack([f["dt_bias"][0], f["a_log"][0], f["ssm_d"][0]]), (P, 3, SH)),
        "ssm_norm": np.broadcast_to(f["ssm_norm"][0], (P, D_INNER)),
        "state_ssm": f["state_ssm"][0].reshape(DEC_BATCH, 2, 4, HD, SN).transpose(1, 4, 0, 2, 3).reshape(P, DEC_BATCH, 256),
    }
    return {k: np.ascontiguousarray(v) for k, v in cm.items()}


_SCRATCH = {"z": (TOK, D_INNER), "gdt": (TOK, 32), "xbc": (P, 6, TOK), "turned": (P, 12, TOK),             "cv": (P, 6, TOK), "ssd": (TOK, 512), "pe_hid": (HD, 2), "kct": (P, N_CMP_P), "vc": (N_CMP_P, P), "attn": (TOK, 512),
            "h": (TOK, D_MODEL), "f": (TOK, D_MODEL), "route": (TOK, 66), "slot_tok": (SLOTS, 1, U32), "gidx": (TOK, 2, U32),
            "over": (1, OVER_BLOCKS + 1, I32), "ypad": (DUMP, D_MODEL)}
_OUTS = {"y": (TOK, D_MODEL), "win_new": (TOK, 256), "win_old": (DEC_BATCH, WINDOW - DEC_SEQ, 256), "kv_out": (TOK, 512), "conv_p": (P, 6, 3), "conv_s": (P, 6, DEC_BATCH, 3), "ssm_p": (P, 256), "ssm_s": (P, DEC_BATCH, 256)}


def build(nc, d):
    project_phase(nc, d)
    conv_phase(nc, d)
    ssd_phase(nc, d)
    compress_prompt(nc, d)
    attend_prompt(nc, d)
    attend_samples(nc, d, d["pool"].shape[0])
    mix_phase(nc, d)
    dispatch_phase(nc, d)
    expert_phase(nc, d, False)
    expert_phase(nc, d, True)
    final_phase(nc, d)


def kernel(**inputs):
    import concourse.bacc as _bacc
    from concourse.bass_utils import run_bass_kernel_spmd as _run

    nc = _bacc.Bacc("TRN2", target_bir_lowering=False, num_devices=1)
    arrays, d = {}, {}
    for name, a in _layout(inputs).items():
        arrays[f"in_{name}"] = a
        d[name] = nc.dram_tensor(f"in_{name}", a.shape, mybir.dt.from_np(a.dtype), kind="ExternalInput").ap()
    for kind, tensors in (("Internal", _SCRATCH), ("ExternalOutput", _OUTS)):
        for name, shape in tensors.items():
            dt = F32 if isinstance(shape[-1], int) else shape[-1]
            shape = [n for n in shape if isinstance(n, int)]
            prefix = "scratch" if kind == "Internal" else "out"
            d[name] = nc.dram_tensor(f"{prefix}_{name}", shape, dt, kind=kind).ap()
    build(nc, d)
    r = _run(nc, [arrays], core_ids=[0])
    got = {k: np.asarray(r.results[0][f"out_{k}"]) for k in _OUTS}
    y, kv, win = got["y"], got["kv_out"], got["win_new"]
    smp = slice(SEQ, SEQ + N_SMP)
    win_s = np.concatenate([got["win_old"], win[smp].reshape(DEC_BATCH, DEC_SEQ, 256)], 1)
    ssm_p = got["ssm_p"].reshape(KVH, SN, HPG, HD).transpose(0, 2, 3, 1)
    ssm_s = got["ssm_s"].reshape(KVH, SN, DEC_BATCH, HPG, HD).transpose(2, 0, 3, 4, 1)
    return (y[:SEQ].reshape(1, SEQ, D_MODEL), y[smp].reshape(DEC_BATCH, DEC_SEQ, D_MODEL),
            kv[:SEQ].reshape(1, 1, SEQ, 4, KVH, HD), kv[smp].reshape(1, DEC_BATCH, DEC_SEQ, 4, KVH, HD),
            win[SEQ - WINDOW:SEQ].reshape(1, 1, WINDOW, 2, KVH, HD), win_s.reshape(1, DEC_BATCH, WINDOW, 2, KVH, HD),
            ssm_p.reshape(1, 1, SH, HD, SN), ssm_s.reshape(1, DEC_BATCH, SH, HD, SN),
            got["conv_p"].transpose(2, 1, 0).reshape(1, 1, CONV_W - 1, CONV_DIM), got["conv_s"].transpose(2, 3, 1, 0).reshape(1, DEC_BATCH, CONV_W - 1, CONV_DIM))
```

```python
from contextlib import ExitStack

import numpy as np

import concourse.bass as bass
from concourse import mybir

ALU = mybir.AluOpType
ACT = mybir.ActivationFunctionType
F32 = mybir.dt.float32
I32 = mybir.dt.int32
U32 = mybir.dt.uint32
AX = mybir.AxisListType.X
P = 128

D_MODEL, SEQ, DEC_BATCH, DEC_SEQ, PAST, PAGE = 1024, 1024, 8, 8, 4096, 128
HEADS, HD, KVH = 8, 64, 2
HPG = HEADS // KVH
ATT_W = HEADS * HD
L_CMP, S_CMP, L_SLC, N_SEL, WINDOW = 32, 16, 64, 16, 512
SH, SN, D_INNER = 8, 64, 512
CONV_DIM, CONV_W = 768, 4
NG, EPG, NE = 4, 8, 32
D_EXP = 512
PLE = 256
EPS = 1e-6
KC = D_MODEL // P
NT = SEQ // P
TILES = NT + 1
TOK = TILES * P
N_SMP = DEC_BATCH * DEC_SEQ
N_PAGES = PAST // PAGE
N_CMP_P = (SEQ - L_CMP) // S_CMP + 1
N_SEG_S = PAST // S_CMP
N_CMP_S = (PAST + DEC_SEQ - L_CMP) // S_CMP + 1
N_SLC_S = -(-(PAST + DEC_SEQ) // L_SLC)
SCALE = HD ** -0.5
NEG = -1e30
C_KV, C_GL, C_Z, C_XBC, C_DT, C_END = 512, 1280, 1304, 1816, 2584, 2592
QKV = 20 * HD
MAIN_BLOCKS = NE
OVER_BLOCKS = 2 * (SEQ + N_SMP) // P - 1
DUMP = (MAIN_BLOCKS + OVER_BLOCKS) * P
SLOTS = DUMP + 2 * P


class Chain:

    def __init__(self, eng, sem, per=0, i=None):
        self.eng, self.sem, self.per, self.i, self.k = eng, sem, per, i, 0

    def __call__(self, ins, passed=None):
        self.k += 1
        ins.then_inc(self.sem, 1)
        base = self.k if self.i is None else self.i * self.per + self.k
        self.eng.wait_ge(self.sem, base)
        if passed is not None:
            self.eng.sem_inc(passed, 1)

    def close(self):
        assert self.k == self.per, (self.k, self.per)


def hold(eng, sem, value, passed):
    eng.wait_ge(sem, value)
    eng.sem_inc(passed, 1)


class Phase(ExitStack):

    def __init__(self, nc, name):
        super().__init__()
        self.nc, self.name, self.own = nc, name, []
        self.passed = self.sem("passed")
        self.callback(self.release)

    def release(self):
        self.nc.clear_and_free_semaphores(self.own)
        self.nc.all_engine_barrier()

    def sb(self, name, shape, dt=F32):
        return self.enter_context(self.nc.sbuf_tensor(f"{self.name}_{name}", shape, dt))

    def ps(self, name, shape):
        return self.enter_context(self.nc.psum_tensor(f"{self.name}_{name}", shape, F32))

    def sem(self, name):
        self.own.append(self.nc.alloc_semaphore(name=f"{self.name}_{name}"))
        return self.own[-1]


def project_phase(nc, d):
    with Phase(nc, "proj") as ph:
        w = ph.sb("w", [P, KC, C_END])
        x = ph.sb("x", [P, KC, P])
        sq = ph.sb("sq", [P, KC, P])
        a = ph.sb("a", [P, KC, P])
        lnv = ph.sb("lnv", [P, P])
        rinv = ph.sb("rinv", [P, P])
        gain = ph.sb("gain", [P, KC])
        qkv = ph.sb("qkv", [P, QKV])
        qkv_sq = ph.sb("qkv_sq", [P, QKV])
        qrot = ph.sb("qrot", [P, ATT_W])
        krot = ph.sb("krot", [P, 2, 2, HD])
        tmp = ph.sb("tmp", [P, HEADS, HD // 2])
        ss = ph.sb("ss", [P, 20])
        hr = ph.sb("hr", [P, 20])
        hgain = ph.sb("hgain", [P, 4, HD])
        trig = ph.sb("trig", [P, 2, HD // 2])
        gdt = ph.sb("gdt", [P, 32])
        z = ph.sb("z", [P, D_INNER])
        xbc = ph.sb("xbc", [P, 6, P])
        turned = ph.sb("turned", [P, 12, P])
        ones = ph.sb("ones", [P, P])
        ident = ph.sb("ident", [P, P])
        eps = ph.sb("eps", [P, 1])
        p_q, p_kv, p_kw = ph.ps("p_q", [P, 512]), ph.ps("p_kv", [P, 512]), ph.ps("p_kw", [P, 512])
        p_z, p_x0, p_x1 = ph.ps("p_z", [P, 512]), ph.ps("p_x0", [P, 3, P]), ph.ps("p_x1", [P, 3, P])
        p_ss = ph.ps("p_ss", [P, 512])

        const_ready, w_ready = ph.sem("const_ready"), ph.sem("w_ready")
        x_ready, x_free = ph.sem("x_ready"), ph.sem("x_free")
        trig_ready, trig_free = ph.sem("trig_ready"), ph.sem("trig_free")
        sq_ready, ss_ready, ln_ready, rinv_ready = ph.sem("sq_ready"), ph.sem("ss_ready"), ph.sem("ln_ready"), ph.sem("rinv_ready")
        a_ready, proj_ready = ph.sem("a_ready"), ph.sem("proj_ready")
        qkv_ready, z_ready, banks_free = ph.sem("qkv_ready"), ph.sem("z_ready"), ph.sem("banks_free")
        hss_ready, hln_ready, hr_ready, rot_ready = ph.sem("hss_ready"), ph.sem("hln_ready"), ph.sem("hr_ready"), ph.sem("rot_ready")
        turn_ready, turned_ready = ph.sem("turn_ready"), ph.sem("turned_ready")
        stored, a_free, dve_step = ph.sem("stored"), ph.sem("a_free"), ph.sem("dve_step")
        STORES = 8

        block = ph.enter_context(nc.Block())

        @block.sync
        def _(sp):
            sp.sem_inc(x_free, 1)
            sp.sem_inc(trig_free, 1)
            sp.sem_inc(a_free, 1)
            sp.sem_inc(banks_free, 1)
            sp.dma_start(ident[:], d["ident"]).then_inc(const_ready, 16)
            sp.dma_start(gain[:], d["attn_norm"]).then_inc(const_ready, 16)
            sp.dma_start(hgain[:], d["head_gain"]).then_inc(const_ready, 16)
            for k in range(KC):
                sp.dma_start(w[:, k, :], d["w_in"][:, k, :]).then_inc(w_ready, 16)
            with sp.Fori(0, TILES) as t:
                sp.wait_ge(x_free, t + 1)
                sp.dma_start(x[:], d["xT"][bass.ds(t, 1)].rearrange("o p c n -> (o p) c n")).then_inc(x_ready, 16)
                sp.wait_ge(trig_free, t + 1)
                sp.dma_start(trig[:], d["trig"][bass.ds(t, 1)].rearrange("o p c n -> (o p) c n")).then_inc(trig_ready, 16)

        @block.gpsimd
        def _(pool):
            with pool.Fori(0, TILES) as t:
                tok = bass.ds(t * P, P)
                hold(pool, z_ready, t * 3 + 3, ph.passed)
                pool.dma_start(d["z"][tok, :], z[:]).then_inc(stored, 16)
                pool.dma_start(d["gdt"][tok, :], gdt[:]).then_inc(stored, 16)
                pool.dma_start(d["xbc"][:, :, tok], xbc[:]).then_inc(stored, 16)
                hold(pool, rot_ready, t + 1, ph.passed)
                pool.dma_start(d["kv_out"][tok, 0:256], qkv[:, 512:768]).then_inc(stored, 16)
                pool.dma_start(d["kv_out"][tok, 256:384], krot[:, 0]).then_inc(stored, 16)
                pool.dma_start(d["kv_out"][tok, 384:512], qkv[:, 896:1024]).then_inc(stored, 16)
                pool.dma_start(d["win_new"][tok, 0:128], krot[:, 1]).then_inc(stored, 16)
                pool.dma_start(d["win_new"][tok, 128:256], qkv[:, 1152:1280]).then_inc(stored, 16)
                hold(pool, turned_ready, t * 3 + 3, ph.passed)
                pool.dma_start(d["turned"][:, :, tok], turned[:]).then_inc(stored, 16)
            pool.wait_ge(stored, TILES * 9 * 16)

        @block.scalar
        def _(act):
            act.wait_ge(const_ready, 49)
            with act.Fori(0, TILES) as t:
                act.wait_ge(x_ready, t * 16 + 16)
                nc.scalar.activation(sq[:], x[:], ACT.Square).then_inc(sq_ready, 1)
                act.wait_ge(ss_ready, t + 1)
                nc.scalar.activation(lnv[:], p_ss[:, 0:P], ACT.Ln, bias=eps[:], scale=1.0 / D_MODEL).then_inc(ln_ready, 1)
                act.wait_ge(ln_ready, t + 1)
                nc.scalar.activation(rinv[:], lnv[:], ACT.Exp, scale=-0.5).then_inc(rinv_ready, 1)
                act.wait_ge(proj_ready, t * 5 + 3)
                act.wait_ge(banks_free, t + 1)
                nc.scalar.activation(qkv[:, 0:512], p_q[:], ACT.Copy)
                nc.scalar.activation(qkv[:, 512:1024], p_kv[:], ACT.Copy)
                nc.scalar.activation(qkv[:, 1024:1280], p_kw[:, 0:256], ACT.Copy)
                nc.scalar.activation(gdt[:], p_kw[:, 256:288], ACT.Copy).then_inc(qkv_ready, 1)
                act.wait_ge(hss_ready, t + 1)
                nc.scalar.activation(ss[:], ss[:], ACT.Ln, bias=eps[:], scale=1.0 / HD).then_inc(hln_ready, 1)
                act.wait_ge(hln_ready, t + 1)
                nc.scalar.activation(hr[:], ss[:], ACT.Exp, scale=-0.5).then_inc(hr_ready, 1)
                act.wait_ge(turn_ready, t * 3 + 2)
                nc.scalar.activation(turned[:, 4:8, :], p_kv[:].rearrange("p (a b) -> p a b", a=4), ACT.Copy, scale=SCALE).then_inc(turned_ready, 1)

        @block.vector
        def _(dve):
            nc.vector.memset(ones[:], 1.0)
            nc.vector.memset(eps[:], EPS).then_inc(const_ready, 1)
            dve.wait_ge(const_ready, 49)
            with dve.Fori(0, TILES) as t:
                link = Chain(dve, dve_step, 21, t)
                dve.wait_ge(rinv_ready, t + 1)
                dve.wait_ge(a_free, t + 1)
                link(nc.vector.tensor_tensor(a[:], x[:], rinv[:].unsqueeze(1).broadcast_to([P, KC, P]), ALU.mult))
                dve.sem_inc(x_free, 1)
                nc.vector.tensor_tensor(a[:], a[:], gain[:].unsqueeze(2).broadcast_to([P, KC, P]), ALU.mult).then_inc(a_ready, 1)
                dve.wait_ge(proj_ready, t * 5 + 5)
                dve.wait_ge(banks_free, t + 1)
                nc.vector.tensor_copy(z[:], p_z[:]).then_inc(z_ready, 1)
                nc.vector.tensor_copy(xbc[:, 0:3, :], p_x0[:]).then_inc(z_ready, 1)
                dve.wait_ge(qkv_ready, t + 1)
                nc.vector.tensor_copy(xbc[:, 3:6, :], p_x1[:]).then_inc(z_ready, 1)
                link(nc.vector.tensor_tensor(qkv_sq[:], qkv[:], qkv[:], ALU.mult))
                nc.vector.reduce_sum(ss[:], qkv_sq[:].rearrange("p (h e) -> p h e", e=HD), AX).then_inc(hss_ready, 1)
                dve.wait_ge(hr_ready, t + 1)
                q3 = qkv[:, 0:512].rearrange("p (h e) -> p h e", e=HD)
                link(nc.vector.tensor_tensor(q3, q3, hr[:, 0:8].unsqueeze(2).broadcast_to([P, 8, HD]), ALU.mult))
                link(nc.vector.tensor_tensor(q3, q3, hgain[:, 0:1, :].broadcast_to([P, 8, HD]), ALU.mult))
                for b in range(3):
                    k3 = qkv[:, 512 + 256 * b:640 + 256 * b].rearrange("p (h e) -> p h e", e=HD)
                    link(nc.vector.tensor_tensor(k3, k3, hr[:, 8 + 4 * b:10 + 4 * b].unsqueeze(2).broadcast_to([P, 2, HD]), ALU.mult))
                    link(nc.vector.tensor_tensor(k3, k3, hgain[:, 1 + b:2 + b, :].broadcast_to([P, 2, HD]), ALU.mult))
                dve.wait_ge(trig_ready, t * 16 + 16)
                sets = [(q3, qrot[:].rearrange("p (h e) -> p h e", e=HD), 8)]
                sets += [(qkv[:, 768 + 256 * b:896 + 256 * b].rearrange("p (h e) -> p h e", e=HD), krot[:, b], 2) for b in range(2)]
                H2 = HD // 2
                for src, dst, n in sets:
                    cos = trig[:, 0:1, :].broadcast_to([P, n, H2])
                    sin = trig[:, 1:2, :].broadcast_to([P, n, H2])
                    x1, x2, t2 = src[:, :, 0:H2], src[:, :, H2:HD], tmp[:, 0:n, :]
                    nc.vector.tensor_tensor(dst[:, :, 0:H2], x1, cos, ALU.mult)
                    link(nc.vector.tensor_tensor(t2, x2, sin, ALU.mult))
                    link(nc.vector.tensor_tensor(dst[:, :, 0:H2], dst[:, :, 0:H2], t2, ALU.subtract))
                    nc.vector.tensor_tensor(dst[:, :, H2:HD], x2, cos, ALU.mult)
                    link(nc.vector.tensor_tensor(t2, x1, sin, ALU.mult))
                    last = nc.vector.tensor_tensor(dst[:, :, H2:HD], dst[:, :, H2:HD], t2, ALU.add)
                    if n == 2 and dst is not sets[1][1]:
                        last.then_inc(rot_ready, 1)
                    else:
                        link(last)
                dve.wait_ge(turn_ready, t * 3 + 3)
                nc.vector.tensor_scalar(turned[:, 0:4, :], p_q[:].rearrange("p (a b) -> p a b", a=4), SCALE, None, ALU.mult).then_inc(turned_ready, 1)
                nc.vector.tensor_copy(turned[:, 8:12, :], p_kw[:].rearrange("p (a b) -> p a b", a=4)).then_inc(turned_ready, 1)
                dve.sem_inc(trig_free, 1)
                dve.wait_ge(turned_ready, t * 3 + 3)
                dve.wait_ge(stored, t * 144 + 144)
                dve.sem_inc(banks_free, 1)
                link.close()

        @block.tensor
        def _(pe):
            pe.wait_ge(const_ready, 49)
            pe.wait_ge(w_ready, 16 * KC)
            with pe.Fori(0, TILES) as t:
                pe.wait_ge(sq_ready, t + 1)
                for k in range(KC):
                    mm = nc.tensor.matmul(p_ss[:, 0:P], ones[:], sq[:, k, :], start=(k == 0), stop=(k == KC - 1))
                mm.then_inc(ss_ready, 1)
                pe.wait_ge(a_ready, t + 1)
                pe.wait_ge(banks_free, t + 1)
                for dst, c0, c1 in ((p_q[:], 0, 512), (p_kv[:], 512, 1024), (p_kw[:, 0:280], 1024, 1304), (p_kw[:, 280:288], C_DT, C_END), (p_z[:], C_Z, C_XBC)):
                    for k in range(KC):
                        mm = nc.tensor.matmul(dst, a[:, k, :], w[:, k, c0:c1], start=(k == 0), stop=(k == KC - 1))
                    if c0 != 1024:
                        mm.then_inc(proj_ready, 1)
                for c in range(6):
                    dst = (p_x0, p_x1)[c // 3][:, c % 3, :]
                    for k in range(KC):
                        mm = nc.tensor.matmul(dst, w[:, k, C_XBC + c * P:C_XBC + c * P + P], a[:, k, :], start=(k == 0), stop=(k == KC - 1))
                mm.then_inc(proj_ready, 1)
                pe.wait_ge(proj_ready, t * 5 + 5)
                pe.sem_inc(a_free, 1)
                pe.wait_ge(rot_ready, t + 1)
                for bank, src in ((p_q, qkv), (p_kv, qrot)):
                    for j in range(HPG):
                        mm = nc.tensor.transpose(bank[:, j * P:(j + 1) * P], src[:, j * P:(j + 1) * P], ident[:])
                    mm.then_inc(turn_ready, 1)
                for j, src in enumerate((qkv[:, 512:640], qkv[:, 640:768], krot[:, 0].rearrange("p h e -> p (h e)"), krot[:, 1].rearrange("p h e -> p (h e)"))):
                    mm = nc.tensor.transpose(p_kw[:, j * P:(j + 1) * P], src, ident[:])
                mm.then_inc(turn_ready, 1)


def conv_phase(nc, d):
    with Phase(nc, "conv") as ph:
        raw = ph.sb("raw", [P, 6, 3 + SEQ])
        raw_s = ph.sb("raw_s", [P, 6, P // DEC_SEQ, 3 + DEC_SEQ])
        acc = ph.sb("acc", [P, 6, TOK])
        e = ph.sb("e", [P, 6, TOK])
        cw = ph.sb("cw", [P, 6, CONV_W])
        cb = ph.sb("cb", [P, 6])
        zeroed, loaded, conv_ready, exp_ready = ph.sem("zeroed"), ph.sem("loaded"), ph.sem("conv_ready"), ph.sem("exp_ready")
        stored, dve_step, act_ready = ph.sem("stored"), ph.sem("dve_step"), ph.sem("act_ready")
        block = ph.enter_context(nc.Block())

        @block.sync
        def _(sp):
            sp.wait_ge(zeroed, 2)
            sp.dma_start(cw[:], d["conv_w"]).then_inc(loaded, 16)
            sp.dma_start(cb[:], d["conv_b"]).then_inc(loaded, 16)
            for c in range(6):
                sp.dma_start(raw[:, c, 3:], d["xbc"][:, c, 0:SEQ]).then_inc(loaded, 16)
                sp.dma_start(raw_s[:, c, :, 3:], d["xbc"][:, c, SEQ:TOK].rearrange("p (b l) -> p b l", l=DEC_SEQ)).then_inc(loaded, 16)
                sp.dma_start(raw_s[:, c, 0:DEC_BATCH, 0:3], d["state_conv"][:, c]).then_inc(loaded, 16)
            sp.wait_ge(loaded, 20 * 16)
            sp.dma_start(d["conv_p"], raw[:, :, SEQ:SEQ + 3]).then_inc(stored, 16)
            for c in range(6):
                sp.dma_start(d["conv_s"][:, c], raw_s[:, c, 0:DEC_BATCH, DEC_SEQ:DEC_SEQ + 3]).then_inc(stored, 16)
            for c in range(6):
                sp.wait_ge(act_ready, c + 1)
                sp.dma_start(d["cv"][:, c], acc[:, c]).then_inc(stored, 16)
            sp.wait_ge(stored, 13 * 16)

        @block.scalar
        def _(act):
            for c in range(6):
                act.wait_ge(conv_ready, 2 * c + 2)
                nc.scalar.activation(e[:, c], acc[:, c], ACT.Exp, scale=-1.0).then_inc(exp_ready, 1)

        @block.vector
        def _(dve):
            link = Chain(dve, dve_step)
            nc.vector.memset(raw[:, :, 0:3], 0.0).then_inc(zeroed, 1)
            nc.vector.memset(raw_s[:], 0.0).then_inc(zeroed, 1)
            dve.wait_ge(loaded, 20 * 16)
            for c in range(6):
                smp = acc[:, c, SEQ:].rearrange("p (b l) -> p b l", l=DEC_SEQ)
                nc.vector.tensor_scalar(acc[:, c, 0:SEQ], raw[:, c, 0:SEQ], cw[:, c, 0:1], cb[:, c:c + 1], ALU.mult, ALU.add)
                link(nc.vector.tensor_scalar(smp, raw_s[:, c, :, 0:DEC_SEQ], cw[:, c, 0:1], cb[:, c:c + 1], ALU.mult, ALU.add))
                for j in range(1, CONV_W):
                    w = cw[:, c, j:j + 1]
                    i1 = nc.vector.scalar_tensor_tensor(acc[:, c, 0:SEQ], raw[:, c, j:j + SEQ], w, acc[:, c, 0:SEQ], ALU.mult, ALU.add)
                    if j == CONV_W - 1:
                        i1.then_inc(conv_ready, 1)
                    i2 = nc.vector.scalar_tensor_tensor(smp, raw_s[:, c, :, j:j + DEC_SEQ], w, smp, ALU.mult, ALU.add)
                    if j == CONV_W - 1:
                        i2.then_inc(conv_ready, 1)
                    else:
                        link(i2)
            for c in range(6):
                dve.wait_ge(exp_ready, c + 1)
                link(nc.vector.tensor_scalar(e[:, c], e[:, c], 1.0, None, ALU.add))
                link(nc.vector.reciprocal(e[:, c], e[:, c]))
                nc.vector.tensor_tensor(acc[:, c], acc[:, c], e[:, c], ALU.mult).then_inc(act_ready, 1)


def ssd_phase(nc, d):
    NB = DEC_BATCH
    with Phase(nc, "ssd") as ph:
        cv = ph.sb("cv", [P, 6, P])
        z = ph.sb("z", [P, 512])
        gdt = ph.sb("gdt", [P, 32])
        tri = ph.sb("tri", [P, 2, P])
        mask = ph.sb("mask", [P, 2, P])
        same = ph.sb("same", [P, 2, P])
        seqcol = ph.sb("seqcol", [P, NB])
        seqrow = ph.sb("seqrow", [P, NB, P])
        hb = ph.sb("hb", [P, 3, SH])
        gnorm = ph.sb("gnorm", [P, 512])
        ident = ph.sb("ident", [P, P])
        eps = ph.sb("eps", [P, 1])
        one = ph.sb("one", [P, 1])
        ah = ph.sb("ah", [P, SH])
        xd, ax, ex, u, lnu, m1, dt, a = (ph.sb(n, [P, SH]) for n in ("xd", "ax", "ex", "u", "lnu", "m1", "dt", "a"))
        acum = ph.sb("acum", [P, 2, SH])
        wd = ph.sb("wd", [P, SH])
        edec = ph.sb("edec", [P, 3, SH])
        xs, xdt, xw, y, t2, ez = (ph.sb(n, [P, 512]) for n in ("xs", "xdt", "xw", "y", "t2", "ez"))
        btok = ph.sb("btok", [P, P])
        m = ph.sb("m", [P, SH, P])
        st = ph.sb("st", [P, 256])
        sst = ph.sb("sst", [P, NB, 256])
        cm = ph.sb("cm", [P, NB, P])
        bm = ph.sb("bm", [P, NB, P])
        am = ph.sb("am", [P, NB, SH])
        et = ph.sb("et", [P, NB, SH])
        ss, rr = ph.sb("ss", [P, 1]), ph.sb("rr", [P, 1])
        p_s, p_x, p_y, p_e = (ph.ps(n, [P, 512]) for n in ("p_s", "p_x", "p_y", "p_e"))
        p_d = [ph.ps(f"p_d{i}", [P, 4, P]) for i in range(2)]
        p_c = [ph.ps(f"p_c{i}", [P, 512]) for i in range(2)]

        names = ("const_ready", "setup", "ah_ready", "loaded", "in_free", "ex_ready", "u_ready", "lnu_ready", "a_ready", "acum_ready", "wd_ready",
                 "edec_ready", "turned", "cb_ready", "diff_ready", "dm_ready", "dexp_ready", "m_ready", "yd_ready", "yo_ready", "xw_ready",
                 "st_ready", "state_ready", "ez_ready", "y_ready", "sq_ready", "ln_ready", "rr_ready", "out_ready", "stored", "dve_step", "smp_step",
                 "sstate_loaded", "masked", "et_sum", "et_ready", "sst_ready", "sst_done", "states_stored")
        s = {n: ph.sem(n) for n in names}
        block = ph.enter_context(nc.Block())

        @block.sync
        def _(sp):
            sp.sem_inc(s["in_free"], 1)
            for dst, src in ((tri, "tri"), (mask, "mask"), (same, "same"), (seqcol, "seqcol"), (seqrow, "seqrow"), (hb, "head_ssm"), (gnorm, "ssm_norm"), (ident, "ident")):
                sp.dma_start(dst[:], d[src]).then_inc(s["const_ready"], 16)
            sp.dma_start(sst[:], d["state_ssm"]).then_inc(s["sstate_loaded"], 16)

            def chunk(c, tok):
                sp.wait_ge(s["in_free"], c + 1)
                sp.dma_start(cv[:], d["cv"][:, :, tok]).then_inc(s["loaded"], 16)
                sp.dma_start(z[:], d["z"][tok, :]).then_inc(s["loaded"], 16)
                sp.dma_start(gdt[:], d["gdt"][tok, :]).then_inc(s["loaded"], 16)
                sp.wait_ge(s["out_ready"], c + 1)
                sp.dma_start(d["ssd"][tok, :], y[:]).then_inc(s["stored"], 16)

            with sp.Fori(0, NT) as c:
                chunk(c, bass.ds(c * P, P))
            chunk(NT, slice(SEQ, TOK))
            sp.dma_start(d["ssm_p"], st[:]).then_inc(s["states_stored"], 16)
            sp.wait_ge(s["sst_done"], 1)
            sp.dma_start(d["ssm_s"], sst[:]).then_inc(s["states_stored"], 16)
            sp.wait_ge(s["stored"], 16 * TILES)
            sp.wait_ge(s["states_stored"], 32)

        @block.scalar
        def _(act):
            act.wait_ge(s["const_ready"], 128)
            act.wait_ge(s["setup"], 2)
            nc.scalar.activation(ah[:], hb[:, 1, :], ACT.Exp).then_inc(s["ah_ready"], 1)

            def chunk(c, smp):
                act.wait_ge(s["u_ready"], 2 * c + 1)
                nc.scalar.activation(ex[:], ax[:], ACT.Exp, scale=-1.0).then_inc(s["ex_ready"], 1)
                act.wait_ge(s["u_ready"], 2 * c + 2)
                nc.scalar.activation(lnu[:], u[:], ACT.Ln).then_inc(s["lnu_ready"], 1)
                act.wait_ge(s["wd_ready"], c + 1)
                nc.scalar.activation(edec[:, 0, :], acum[:, 0, :], ACT.Exp)
                nc.scalar.activation(edec[:, 1, :], wd[:], ACT.Exp)
                nc.scalar.activation(edec[:, 2, :], acum[:, 1, :], ACT.Exp).then_inc(s["edec_ready"], 1)
                nc.scalar.activation(ez[:], z[:], ACT.Exp, scale=-1.0).then_inc(s["ez_ready"], 1)
                act.wait_ge(s["dm_ready"], c + 1)
                nc.scalar.activation(m[:], m[:], ACT.Exp).then_inc(s["dexp_ready"], 1)
                if smp:
                    act.wait_ge(s["et_sum"], 1)
                    nc.scalar.activation(et[:], p_e[:, 0:NB * SH].rearrange("p (b h) -> p b h", h=SH), ACT.Exp).then_inc(s["et_ready"], 1)
                act.wait_ge(s["y_ready"], c + 1)
                nc.scalar.activation(t2[:], y[:], ACT.Square, accum_out=ss[:]).then_inc(s["sq_ready"], 1)
                act.wait_ge(s["sq_ready"], c + 1)
                nc.scalar.activation(rr[:], ss[:], ACT.Ln, bias=eps[:], scale=1.0 / D_INNER).then_inc(s["ln_ready"], 1)
                act.wait_ge(s["ln_ready"], c + 1)
                nc.scalar.activation(rr[:], rr[:], ACT.Exp, scale=-0.5).then_inc(s["rr_ready"], 1)

            with act.Fori(0, NT) as c:
                chunk(c, False)
            chunk(NT, True)

        @block.vector
        def _(dve):
            nc.vector.memset(eps[:], EPS).then_inc(s["setup"], 1)
            nc.vector.memset(st[:], 0.0).then_inc(s["setup"], 1)
            dve.wait_ge(s["setup"], 2)
            dve.wait_ge(s["const_ready"], 128)
            dve.wait_ge(s["ah_ready"], 1)

            def h3(ap):
                return ap.rearrange("p (h e) -> p h e", e=HD)

            def over(ap, n=HD):
                return ap.unsqueeze(2).broadcast_to([ap.shape[0], ap.shape[1], n])

            def chunk(c, smp, link):
                dve.wait_ge(s["loaded"], c * 48 + 48)
                link(nc.vector.tensor_tensor(xd[:], gdt[:, 24:32], hb[:, 0, :], ALU.add))
                nc.vector.scalar_tensor_tensor(ax[:], xd[:], -1.0, xd[:], ALU.mult, ALU.max).then_inc(s["u_ready"], 1)
                dve.wait_ge(s["ex_ready"], c + 1)
                nc.vector.tensor_scalar(u[:], ex[:], 1.0, None, ALU.add).then_inc(s["u_ready"], 1)
                dve.wait_ge(s["u_ready"], c * 2 + 2)
                link(nc.vector.tensor_scalar(m1[:], u[:], 1.0, None, ALU.is_equal))
                link(nc.vector.scalar_tensor_tensor(dt[:], u[:], 1.0, m1[:], ALU.subtract, ALU.add))
                link(nc.vector.reciprocal(dt[:], dt[:]))
                link(nc.vector.tensor_tensor(dt[:], dt[:], ex[:], ALU.mult))
                dve.wait_ge(s["lnu_ready"], c + 1)
                link(nc.vector.tensor_tensor(m1[:], m1[:], lnu[:], ALU.add))
                link(nc.vector.tensor_tensor(dt[:], dt[:], m1[:], ALU.mult))
                link(nc.vector.scalar_tensor_tensor(dt[:], xd[:], 0.0, dt[:], ALU.max, ALU.add))
                nc.vector.scalar_tensor_tensor(a[:], ah[:], -1.0, dt[:], ALU.mult, ALU.mult).then_inc(s["a_ready"], 1)
                dve.wait_ge(s["acum_ready"], c + 1)
                link(nc.vector.tensor_copy(acum[:], p_s[:, 0:16].rearrange("p (k h) -> p k h", k=2)))
                nc.vector.tensor_tensor(wd[:], acum[:, 1, :], acum[:, 0, :], ALU.subtract).then_inc(s["wd_ready"], 1)
                dve.wait_ge(s["turned"], c + 1)
                link(nc.vector.tensor_copy(btok[:], p_s[:, 128:256]))
                link(nc.vector.tensor_copy(xs[:], p_x[:]))
                link(nc.vector.tensor_tensor(h3(xdt[:]), h3(xs[:]), over(dt[:]), ALU.mult))
                dve.wait_ge(s["edec_ready"], c + 1)
                nc.vector.tensor_tensor(h3(xw[:]), h3(xdt[:]), over(edec[:, 1, :]), ALU.mult).then_inc(s["xw_ready"], 1)
                dve.wait_ge(s["diff_ready"], c + 1)
                for h in range(SH):
                    ins = nc.vector.scalar_tensor_tensor(m[:, h, :], p_d[h // 4][:, h % 4, :], acum[:, 0, h:h + 1], mask[:, int(smp), :], ALU.subtract, ALU.add)
                ins.then_inc(s["dm_ready"], 1)
                if smp:
                    link(nc.vector.tensor_tensor(cm[:], seqrow[:], cv[:, 5:6, :].broadcast_to([P, NB, P]), ALU.mult))
                    link(nc.vector.tensor_tensor(bm[:], seqcol[:].unsqueeze(2).broadcast_to([P, NB, P]), btok[:].unsqueeze(1).broadcast_to([P, NB, P]), ALU.mult))
                    nc.vector.tensor_tensor(am[:], seqcol[:].unsqueeze(2).broadcast_to([P, NB, SH]), a[:].unsqueeze(1).broadcast_to([P, NB, SH]), ALU.mult).then_inc(s["masked"], 1)
                dve.wait_ge(s["dexp_ready"], c + 1)
                dve.wait_ge(s["cb_ready"], c + 1)
                for g in range(2):
                    mg = m[:, 4 * g:4 * g + 4, :]
                    ins = nc.vector.tensor_tensor(mg, mg, p_c[g][:, 0:P].unsqueeze(1).broadcast_to([P, 4, P]), ALU.mult)
                ins.then_inc(s["m_ready"], 1)
                dve.wait_ge(s["yo_ready"], c + 1)
                for g in range(2):
                    link(nc.vector.tensor_tensor(h3(t2[:, 256 * g:256 * g + 256]), h3(p_c[g][:, 0:256]), over(edec[:, 0, 4 * g:4 * g + 4]), ALU.mult))
                link(nc.vector.tensor_tensor(y[:], t2[:], p_y[:], ALU.add))
                link(nc.vector.tensor_tensor(h3(t2[:]), h3(xs[:]), over(hb[:, 2, :]), ALU.mult))
                link(nc.vector.tensor_tensor(y[:], y[:], t2[:], ALU.add))
                dve.wait_ge(s["ez_ready"], c + 1)
                link(nc.vector.tensor_scalar(ez[:], ez[:], 1.0, None, ALU.add))
                link(nc.vector.reciprocal(ez[:], ez[:]))
                link(nc.vector.tensor_tensor(ez[:], ez[:], z[:], ALU.mult))
                nc.vector.tensor_tensor(y[:], y[:], ez[:], ALU.mult).then_inc(s["y_ready"], 1)
                if not smp:
                    dve.wait_ge(s["st_ready"], c + 1)
                    for g in range(2):
                        sg = h3(st[64 * g:64 * g + 64, :])
                        link(nc.vector.tensor_tensor(sg, sg, over(edec[64 * g:64 * g + 64, 2, 4 * g:4 * g + 4]), ALU.mult))
                    link(nc.vector.tensor_tensor(st[:], st[:], p_x[:, 0:256], ALU.add))
                    dve.sem_inc(s["state_ready"], 1)
                else:
                    dve.wait_ge(s["et_ready"], 1)
                    for g in range(2):
                        sg = sst[64 * g:64 * g + 64].rearrange("p b (h e) -> p b h e", e=HD)
                        for b in range(NB):
                            link(nc.vector.tensor_tensor(sg[:, b], sg[:, b], over(et[64 * g:64 * g + 64, b, 4 * g:4 * g + 4]), ALU.mult))
                    for q in range(4):
                        dve.wait_ge(s["sst_ready"], q + 1)
                        bank = (p_x, p_y, p_d[0], p_d[1])[q]
                        flat = bank[:] if q < 2 else bank[:].rearrange("p a b -> p (a b)")
                        ins = nc.vector.tensor_tensor(sst[:, 2 * q:2 * q + 2, :], sst[:, 2 * q:2 * q + 2, :], flat.rearrange("p (b n) -> p b n", b=2), ALU.add)
                    ins.then_inc(s["sst_done"], 1)
                dve.wait_ge(s["rr_ready"], c + 1)
                link(nc.vector.tensor_scalar(y[:], y[:], rr[:], None, ALU.mult))
                nc.vector.tensor_tensor(y[:], y[:], gnorm[:], ALU.mult).then_inc(s["out_ready"], 1)
                dve.wait_ge(s["stored"], c * 16 + 16)
                dve.sem_inc(s["in_free"], 1)

            with dve.Fori(0, NT) as c:
                link = Chain(dve, s["dve_step"], 24, c)
                chunk(c, False, link)
                link.close()
            chunk(NT, True, Chain(dve, s["smp_step"]))

        @block.tensor
        def _(pe):
            pe.wait_ge(s["const_ready"], 128)
            pe.wait_ge(s["setup"], 2)

            def chunk(c, smp):
                k = int(smp)
                pe.wait_ge(s["loaded"], c * 48 + 48)
                for i in range(4):
                    nc.tensor.transpose(p_x[:, i * P:(i + 1) * P], cv[:, i, :], ident[:])
                nc.tensor.transpose(p_s[:, 128:256], cv[:, 4, :], ident[:]).then_inc(s["turned"], 1)
                for g in range(2):
                    mm = nc.tensor.matmul(p_c[g][:, 0:P], cv[64 * g:64 * g + 64, 4, :], cv[64 * g:64 * g + 64, 5, :], start=True, stop=True)
                mm.then_inc(s["cb_ready"], 1)
                pe.wait_ge(s["a_ready"], c + 1)
                pe.wait_ge(s["turned"], c + 1)
                nc.tensor.matmul(p_s[:, 0:8], tri[:, k, :], a[:], start=True, stop=True)
                nc.tensor.matmul(p_s[:, 8:16], same[:, k, :], a[:], start=True, stop=True).then_inc(s["acum_ready"], 1)
                for h in range(SH):
                    mm = nc.tensor.matmul(p_d[h // 4][:, h % 4, :], a[:, h:h + 1].broadcast_to([P, P]), tri[:, k, :], start=True, stop=True)
                mm.then_inc(s["diff_ready"], 1)
                pe.wait_ge(s["m_ready"], c + 1)
                for h in range(SH):
                    nc.tensor.matmul(p_y[:, 64 * h:64 * h + 64], m[:, h, :], xdt[:, 64 * h:64 * h + 64], start=True, stop=True)
                if not smp:
                    for g in range(2):
                        mm = nc.tensor.matmul(p_c[g][:, 0:256], cv[64 * g:64 * g + 64, 5, :], st[64 * g:64 * g + 64, :], start=True, stop=True)
                else:
                    pe.wait_ge(s["sstate_loaded"], 16)
                    pe.wait_ge(s["masked"], 1)
                    for g in range(2):
                        for b in range(NB):
                            mm = nc.tensor.matmul(p_c[g][:, 0:256], cm[64 * g:64 * g + 64, b, :], sst[64 * g:64 * g + 64, b, :], start=(b == 0), stop=(b == NB - 1))
                mm.then_inc(s["yo_ready"], 1)
                pe.wait_ge(s["xw_ready"], c + 1)
                if not smp:
                    for g in range(2):
                        mm = nc.tensor.matmul(p_x[64 * g:64 * g + 64, 0:256], btok[:, 64 * g:64 * g + 64], xw[:, 256 * g:256 * g + 256], start=True, stop=True)
                    mm.then_inc(s["st_ready"], 1)
                    pe.wait_ge(s["in_free"], c + 2)
                    pe.wait_ge(s["state_ready"], c + 1)
                else:
                    nc.tensor.matmul(p_e[:, 0:NB * SH], same[:, 0, :], am[:].rearrange("p b h -> p (b h)"), start=True, stop=True).then_inc(s["et_sum"], 1)
                    pe.wait_ge(s["y_ready"], c + 1)
                    for q in range(4):
                        bank = (p_x, p_y, p_d[0], p_d[1])[q]
                        flat = bank[:] if q < 2 else bank[:].rearrange("p a b -> p (a b)")
                        for b in (2 * q, 2 * q + 1):
                            for g in range(2):
                                mm = nc.tensor.matmul(flat[64 * g:64 * g + 64, 256 * (b % 2):256 * (b % 2) + 256], bm[:, b, 64 * g:64 * g + 64], xw[:, 256 * g:256 * g + 256], start=True, stop=True)
                        mm.then_inc(s["sst_ready"], 1)

            with pe.Fori(0, NT) as c:
                chunk(c, False)
            chunk(NT, True)


def compress_prompt(nc, d):
    NS, NC = SEQ // S_CMP, N_CMP_P
    with Phase(nc, "cmp") as ph:
        kv = ph.sb("kv", [P, 2, SEQ])
        w1 = ph.sb("w1", [P, 2, S_CMP, P])
        pe_t = ph.sb("pe", [HD, 2, 2, S_CMP])
        w2 = ph.sb("w2", [HD, 2, HD])
        pe_hid = ph.sb("pe_hid", [HD, 2])
        pe_neg = ph.sb("pe_neg", [HD, 2])
        late = ph.sb("late", [HD, 2, 2, NS])
        hid = ph.sb("hid", [HD, 2, 2, NC])
        e = ph.sb("e", [HD, 2, 2, NC])
        kct = ph.sb("kct", [P, NC])
        vc = ph.sb("vc", [NC, P])
        p_h = [ph.ps(f"p_h{g}", [P, 2, NS]) for g in range(2)]
        p_pe, p_k, p_v = ph.ps("p_pe", [HD, 2]), ph.ps("p_k", [P, NC]), ph.ps("p_v", [NC, P])
        loaded, hid_ready, pe_ready, late_ready = ph.sem("loaded"), ph.sem("hid_ready"), ph.sem("pe_ready"), ph.sem("late_ready")
        sum_ready, exp_ready, act_ready, out_ready = ph.sem("sum_ready"), ph.sem("exp_ready"), ph.sem("act_ready"), ph.sem("out_ready")
        evac, stored, dve_step = ph.sem("evac"), ph.sem("stored"), ph.sem("dve_step")
        block = ph.enter_context(nc.Block())

        @block.sync
        def _(sp):
            sp.dma_start(w1[:], d["cmp_w1_sd"]).then_inc(loaded, 16)
            sp.dma_start(kv[:], d["turned"][:, 8:10, 0:SEQ]).then_inc(loaded, 16)
            sp.dma_start(pe_t[:], d["cmp_pe"]).then_inc(loaded, 16)
            sp.dma_start(w2[:], d["cmp_w2"]).then_inc(loaded, 16)
            sp.wait_ge(pe_ready, 2)
            sp.dma_start(d["pe_hid"], pe_hid[:]).then_inc(stored, 16)
            sp.wait_ge(evac, 2)
            sp.dma_start(d["kct"], kct[:]).then_inc(stored, 16)
            sp.dma_start(d["vc"], vc[:]).then_inc(stored, 16)
            sp.wait_ge(stored, 48)

        @block.tensor
        def _(pe):
            pe.wait_ge(loaded, 64)
            for slot in range(2):
                for n, (r, s) in enumerate((r, s) for r in range(2) for s in range(S_CMP)):
                    mm = nc.tensor.matmul(p_pe[:, slot:slot + 1], w1[0:HD, slot, s, HD * r:HD * r + HD], pe_t[:, slot, r, s:s + 1], start=(n == 0), stop=(n == 2 * S_CMP - 1))
            mm.then_inc(pe_ready, 1)
            for g in range(2):
                for slot in range(2):
                    seg = kv[64 * g:64 * g + 64, slot, :].rearrange("p (n s) -> p s n", s=S_CMP)
                    for s in range(S_CMP):
                        mm = nc.tensor.matmul(p_h[g][:, slot, :], w1[64 * g:64 * g + 64, slot, s, :], seg[:, s, :], start=(s == 0), stop=(s == S_CMP - 1))
            mm.then_inc(hid_ready, 1)
            pe.wait_ge(act_ready, 1)
            for g in range(2):
                nc.tensor.matmul(p_k[64 * g:64 * g + 64, :], w2[:, 0, :], hid[:, 0, g, :], start=True, stop=True)
                mm = nc.tensor.matmul(p_v[:, 64 * g:64 * g + 64], hid[:, 1, g, :], w2[:, 1, :], start=True, stop=True)
            mm.then_inc(out_ready, 1)

        @block.scalar
        def _(act):
            act.wait_ge(hid_ready, 1)
            for g in range(2):
                ins = nc.scalar.activation(late[:, :, g, :], p_h[g][64:128], ACT.Copy)
            ins.then_inc(late_ready, 1)
            act.wait_ge(sum_ready, 1)
            nc.scalar.activation(e[:], hid[:], ACT.Exp, scale=-1.0).then_inc(exp_ready, 1)

        @block.vector
        def _(dve):
            link = Chain(dve, dve_step)
            dve.wait_ge(pe_ready, 1)
            nc.vector.tensor_copy(pe_hid[:], p_pe[:]).then_inc(pe_ready, 1)
            dve.wait_ge(pe_ready, 2)
            dve.wait_ge(late_ready, 1)
            for g in range(2):
                ins = nc.vector.tensor_tensor(hid[:, :, g, :], p_h[g][0:HD, :, 0:NC], late[:, :, g, 1:NS], ALU.add)
            link(ins)
            for slot in range(2):
                ins = nc.vector.tensor_scalar(hid[:, slot], hid[:, slot], pe_hid[:, slot:slot + 1], None, ALU.add)
            ins.then_inc(sum_ready, 1)
            dve.wait_ge(exp_ready, 1)
            link(nc.vector.tensor_scalar(e[:], e[:], 1.0, None, ALU.add))
            link(nc.vector.reciprocal(e[:], e[:]))
            nc.vector.tensor_tensor(hid[:], hid[:], e[:], ALU.mult).then_inc(act_ready, 1)
            dve.wait_ge(out_ready, 1)
            nc.vector.tensor_copy(kct[:], p_k[:]).then_inc(evac, 1)
            nc.vector.tensor_copy(vc[:], p_v[:]).then_inc(evac, 1)


def attend_prompt(nc, d):
    assert SEQ // L_SLC <= N_SEL and WINDOW % P == 0
    NC = N_CMP_P
    WT = WINDOW // P
    CMP, SLC, WIN = range(3)
    units = [(qt, g, br, 0 if br != WIN else max(0, qt - WT), {CMP: 0, SLC: qt + 1, WIN: min(qt, WT) + 1}[br])
             for qt in range(NT) for g in range(2) for br in range(3)]
    NU = len(units)
    groups = []
    for u, (qt, g, br, k0, kn) in enumerate(units):
        groups += [(u, t, min(4, max(kn, 1) - t)) for t in range(0, max(kn, 1), 4)]
    of_unit = [[i for i, gr in enumerate(groups) if gr[0] == u] for u in range(NU)]
    per_bank = [len(groups) - len(groups) // 2, len(groups) // 2]
    with Phase(nc, "att") as ph:
        q = ph.sb("q", [P, 2, SEQ])
        kk = ph.sb("kk", [P, 2, SEQ])
        v = ph.sb("v", [P, 2, NT, P])
        kct = ph.sb("kct", [P, NC])
        vc = ph.sb("vc", [NC, P])
        gates = ph.sb("gates", [P, NT, 6])
        diag = ph.sb("diag", [P, P])
        old = ph.sb("old", [P, P])
        cmask = ph.sb("cmask", [P, NT, NC])
        valid = ph.sb("valid", [P, 1])
        ident = ph.sb("ident", [P, P])
        prob = [ph.sb(f"prob{i}", [P, SEQ]) for i in range(3)]
        pt = [ph.sb(f"pt{i}", [P, 4, P]) for i in range(2)]
        nb, l, rg = (ph.sb(n, [P, 3]) for n in ("nb", "l", "rg"))
        o = ph.sb("o", [P, NT, P])
        p_s = [ph.ps(f"p_s{i}", [P, SEQ]) for i in range(2)]
        p_t = [ph.ps(f"p_t{i}", [P, 4, P]) for i in range(2)]
        p_o = [ph.ps(f"p_o{i}", [P, 512]) for i in range(2)]
        const_ready, q_ready, q_free = ph.sem("const_ready"), ph.sem("q_ready"), ph.sem("q_free")
        s_ready, nb_ready, p_ready, o_ready, o_done = (ph.sem(n) for n in ("s_ready", "nb_ready", "p_ready", "o_ready", "o_done"))
        t_ready = [ph.sem(f"t_ready{i}") for i in range(2)]
        t_done = [ph.sem(f"t_done{i}") for i in range(2)]
        zero = ph.sb("zero", [P, D_MODEL])
        rows_zeroed, rows_stored = ph.sem("rows_zeroed"), ph.sem("rows_stored")
        g_exp, o_stored, dve_step = ph.sem("g_exp"), ph.sem("o_stored"), ph.sem("dve_step")
        block = ph.enter_context(nc.Block())

        HEAD = 3

        def unit(it, u, back=0):
            return it * NU + (u - back + 1 + HEAD)

        def group(it, i, back=0):
            return it * per_bank[i % 2] + (i // 2 - back + 1 + 1)

        @block.sync
        def _(sp):
            sp.wait_ge(rows_zeroed, 1)
            sp.dma_start(d["attn"][SEQ + N_SMP:TOK, :], zero[0:TOK - SEQ - N_SMP, 0:ATT_W]).then_inc(rows_stored, 16)
            for n in range(OVER_BLOCKS):
                sp.dma_start(d["ypad"][(MAIN_BLOCKS + n) * P:(MAIN_BLOCKS + n + 1) * P, :], zero[:]).then_inc(rows_stored, 16)
            for s in (o_done, p_ready):
                sp.sem_inc(s, HEAD)
            for s in t_done:
                sp.sem_inc(s, 1)
            sp.sem_inc(q_free, 1)
            sp.sem_inc(o_stored, 16)
            for dst, src in ((kk[:], d["turned"][:, 10:12, 0:SEQ]), (kct[:], d["kct"]), (vc[:], d["vc"]), (diag[:], d["diag"]), (old[:], d["old"]),
                             (cmask[:], d["cmask"]), (valid[:], d["valid"]), (ident[:], d["ident"]),
                             (v[:, 0], d["kv_out"][0:SEQ, 384:512].rearrange("(t p) n -> p t n", p=P)),
                             (v[:, 1], d["win_new"][0:SEQ, 128:256].rearrange("(t p) n -> p t n", p=P))):
                sp.dma_start(dst, src).then_inc(const_ready, 16)
            with sp.Fori(0, HPG) as j:
                sp.wait_ge(q_free, j + 1)
                sp.dma_start(q[:, 0], d["turned"][:, bass.ds(j, 1), 0:SEQ].rearrange("p o n -> p (o n)")).then_inc(q_ready, 16)
                sp.dma_start(q[:, 1], d["turned"][:, bass.ds(j + HPG, 1), 0:SEQ].rearrange("p o n -> p (o n)")).then_inc(q_ready, 16)
                sp.dma_start(gates[:], d["gdt"][0:SEQ, bass.ds(j * 6, 6)].rearrange("(t p) n -> p t n", p=P)).then_inc(q_ready, 16)
                sp.wait_ge(o_done, unit(j, NU - 1))
                sp.dma_start(d["attn"][0:SEQ, bass.ds(j * P, P)].rearrange("(t p) n -> p t n", p=P), o[:]).then_inc(o_stored, 16)
            sp.wait_ge(o_stored, 16 * HPG + 16)
            sp.wait_ge(rows_stored, 16 * (OVER_BLOCKS + 1))

        @block.tensor
        def _(pe):
            pe.wait_ge(const_ready, 160)

            def scores(it, u):
                qt, g, br, k0, kn = units[u]
                pe.wait_ge(p_ready, unit(it, u, 2))
                rows = slice(64 * g, 64 * g + 64)
                lhs = q[rows, 0 if br == CMP else 1, qt * P:qt * P + P]
                if br == CMP:
                    mm = nc.tensor.matmul(p_s[u % 2][:, 0:NC], lhs, kct[rows, :], start=True, stop=True)
                else:
                    n = kn * P
                    for c in range(0, n, 512):
                        w = min(512, n - c)
                        mm = nc.tensor.matmul(p_s[u % 2][:, c:c + w], lhs, kk[rows, br - 1, k0 * P + c:k0 * P + c + w], start=True, stop=True)
                mm.then_inc(s_ready, 1)

            def turn(it, i):
                u, t0, n = groups[i]
                br = units[u][2]
                hold(pe, t_done[i % 2], group(it, i, 1), ph.passed)
                for t in range(n):
                    if br == CMP:
                        mm = nc.tensor.transpose(p_t[i % 2][0:NC, 0, :], prob[u % 3][:, 0:NC], ident[:])
                    else:
                        mm = nc.tensor.transpose(p_t[i % 2][:, t, :], prob[u % 3][:, (t0 + t) * P:(t0 + t + 1) * P], ident[:])
                mm.then_inc(t_ready[i % 2], 1)

            def values(it, i):
                u, t0, n = groups[i]
                qt, g, br, k0, kn = units[u]
                pe.wait_ge(t_done[i % 2], group(it, i))
                if t0 == 0:
                    pe.wait_ge(o_done, unit(it, u, 2))
                for t in range(n):
                    if br == CMP:
                        mm = nc.tensor.matmul(p_o[u % 2][:, 0:HD], pt[i % 2][0:NC, 0, :], vc[:, 64 * g:64 * g + 64], start=True, stop=True)
                    else:
                        k = t0 + t
                        mm = nc.tensor.matmul(p_o[u % 2][:, 0:HD], pt[i % 2][:, t, :], v[:, br - 1, k0 + k, 64 * g:64 * g + 64], start=(k == 0), stop=(k == kn - 1))
                if i == of_unit[u][-1]:
                    mm.then_inc(o_ready, 1)

            with pe.Fori(0, HPG) as it:
                pe.wait_ge(q_ready, it * 48 + 48)
                scores(it, 0)
                scores(it, 1)
                for i, (u, t0, _) in enumerate(groups):
                    if t0 == 0:
                        pe.wait_ge(p_ready, unit(it, u))
                    turn(it, i)
                    if t0 == 0 and u + 2 < NU:
                        scores(it, u + 2)
                    if i > 0:
                        values(it, i - 1)
                values(it, len(groups) - 1)

        def copy_turned(eng, op, it, some, bank):
            for i in some:
                u = groups[i][0]
                if i % 2 == bank:
                    n = groups[i][2]
                    rows = NC if units[u][2] == CMP else P
                    eng.wait_ge(t_ready[bank], it * per_bank[bank] + (i // 2 + 1))
                    op(pt[bank][0:rows, 0:n, :], p_t[bank][0:rows, 0:n, :]).then_inc(t_done[bank], 1)

        @block.scalar
        def _(act):
            def exponentials(it, u):
                qt, g, br, k0, kn = units[u]
                n = NC if br == CMP else kn * P
                act.wait_ge(nb_ready, it * NU + (u + 1))
                act.wait_ge(o_done, unit(it, u, 3))
                nc.scalar.activation(prob[u % 3][:, 0:n], p_s[u % 2][:, 0:n], ACT.Exp, bias=nb[:, u % 3:u % 3 + 1],
                                     accum_out=l[:, u % 3:u % 3 + 1]).then_inc(p_ready, 1)

            with act.Fori(0, HPG) as it:
                act.wait_ge(q_ready, it * 48 + 48)
                nc.scalar.activation(gates[:], gates[:], ACT.Exp, scale=-1.0).then_inc(g_exp, 1)
                exponentials(it, 0)
                exponentials(it, 1)
                for u in range(NU):
                    copy_turned(act, lambda a, b: nc.scalar.activation(a, b, ACT.Copy), it, of_unit[u], 1)
                    if u + 2 < NU:
                        exponentials(it, u + 2)

        @block.vector
        def _(dve):
            nc.vector.memset(zero[:], 0.0).then_inc(rows_zeroed, 1)
            dve.wait_ge(const_ready, 160)
            with dve.Fori(0, HPG) as it:
                link = Chain(dve, dve_step, 2 + 2 * NU + sum(1 if br == CMP or qt < WT or br == SLC else 2 for qt, g, br, _, _ in units) + 2, it)

                def maxima(u):
                    qt, g, br, k0, kn = units[u]
                    S = p_s[u % 2]
                    dve.wait_ge(s_ready, it * NU + (u + 1))
                    if br == CMP:
                        n = NC
                        link(nc.vector.tensor_tensor(S[:, 0:NC], S[:, 0:NC], cmask[:, qt, :], ALU.add))
                    else:
                        n = kn * P
                        link(nc.vector.tensor_tensor(S[:, n - P:n], S[:, n - P:n], diag[:], ALU.add))
                        if br == WIN and qt >= WT:
                            link(nc.vector.tensor_tensor(S[:, 0:P], S[:, 0:P], old[:], ALU.add))
                    nc.vector.tensor_reduce(nb[:, u % 3:u % 3 + 1], S[:, 0:n], AX, ALU.max, negate=True).then_inc(nb_ready, 1)

                dve.wait_ge(g_exp, it + 1)
                link(nc.vector.tensor_scalar(gates[:], gates[:], 1.0, None, ALU.add))
                link(nc.vector.reciprocal(gates[:], gates[:]))
                dve.wait_ge(o_stored, it * 16 + 16)

                def output(u):
                    qt, g, br, k0, kn = units[u]
                    r = rg[:, u % 3:u % 3 + 1]
                    link(nc.vector.reciprocal(r, l[:, u % 3:u % 3 + 1]))
                    link(nc.vector.tensor_tensor(r, r, gates[:, qt, 3 * g + br:3 * g + br + 1], ALU.mult))
                    if br == CMP and qt == 0:
                        link(nc.vector.tensor_tensor(r, r, valid[:], ALU.mult))
                    dve.wait_ge(o_ready, it * NU + (u + 1))
                    if br > CMP:
                        dve.wait_ge(o_done, unit(it, u, 1))
                    out = o[:, qt, 64 * g:64 * g + 64]
                    if br == CMP:
                        nc.vector.tensor_scalar(out, p_o[u % 2][:, 0:HD], r, None, ALU.mult).then_inc(o_done, 1)
                    else:
                        nc.vector.scalar_tensor_tensor(out, p_o[u % 2][:, 0:HD], r, out, ALU.mult, ALU.add).then_inc(o_done, 1)

                maxima(0)
                maxima(1)
                for u in range(NU):
                    dve.wait_ge(p_ready, unit(it, u))
                    copy_turned(dve, nc.vector.tensor_copy, it, of_unit[u][:1], 0)
                    if u > 0:
                        output(u - 1)
                    copy_turned(dve, nc.vector.tensor_copy, it, of_unit[u][1:], 0)
                    if u + 2 < NU:
                        maxima(u + 2)
                output(NU - 1)
                dve.wait_ge(o_done, unit(it, NU - 1))
                dve.sem_inc(q_free, 1)
                link.close()


def attend_samples(nc, d, n_pool):
    NC, NBK, Q, NB = N_CMP_S, N_SLC_S, DEC_SEQ, DEC_BATCH
    R = KVH * HPG * Q
    OLD = PAST
    W0, WN = OLD + Q, WINDOW + Q
    CUR = PAST // L_SLC
    FORCED = 1e9
    NG_S = N_PAGES // 8
    CHUNKS = PAST // 512
    assert (PAST + Q - 1) // L_SLC == CUR and (NC - 1) * S_CMP + L_CMP - 1 <= PAST and R == 64 and NB % 2 == 0
    with Phase(nc, "smp") as ph:
        cmp_page = ph.sb("cmp_page", [P, N_PAGES, 256])
        kv_page = [ph.sb(f"kv_page{u}", [P, N_PAGES, 256]) for u in range(2)]
        win = [ph.sb(f"win{u}", [P, 2, 512]) for u in range(2)]
        table = ph.sb("table", [1, NB * N_PAGES], I32)
        tnew = ph.sb("tnew", [P, 12, N_SMP])
        vnew = ph.sb("vnew", [Q, NB, 2, P])
        gate = ph.sb("gate", [R, NB, 3])
        qbd = [ph.sb(f"qbd{u}", [P, 2, R]) for u in range(2)]
        w1 = ph.sb("w1", [P, 2, 8, P])
        w2 = ph.sb("w2", [HD, 2, HD])
        pe_hid = ph.sb("pe_hid", [HD, 2])
        cover = ph.sb("cover", [P, 2, NBK])
        gsum = ph.sb("gsum", [R, R])
        nmask = ph.sb("nmask", [R, Q])
        wmask = ph.sb("wmask", [R, WN])
        ident = ph.sb("ident", [P, P])
        late = ph.sb("late", [HD, 2, 2, N_SEG_S])
        hid = ph.sb("hid", [HD, 2, 2, NC])
        kct = ph.sb("kct", [P, NC])
        vc = ph.sb("vc", [P, 2, P])
        pc = ph.sb("pc", [R, NC])
        pct = ph.sb("pct", [P, 2, R])
        imp = ph.sb("imp", [R, NBK])
        score, score2, score3, unsel = (ph.sb(n, [R, NBK]) for n in ("score", "score2", "score3", "unsel"))
        top = ph.sb("top", [R, 2, 8])
        S = ph.sb("S", [R, W0 + WN])
        pst = ph.sb("pst", [P, N_PAGES + 4, R])
        pnew = ph.sb("pnew", [Q, 2, R])
        vcur = ph.sb("vcur", [Q, 2, P])
        nbc, lc, rc, gc = (ph.sb(n, [R, 1]) for n in ("nbc", "lc", "rc", "gc"))
        nbs, ls, rs = (ph.sb(n, [R, 2]) for n in ("nbs", "ls", "rs"))
        o = [ph.sb(f"o{u}", [R, HD]) for u in range(2)]
        o_all = ph.sb("o_all", [R, NB, HD])
        p_h = [ph.ps(f"p_h{i}", [P, 512]) for i in range(2)]
        p_s = [ph.ps(f"p_s{i}", [P, 512]) for i in range(2)]
        p_t = [ph.ps(f"p_t{i}", [P, 8, R]) for i in range(2)]
        p_o, p_m = ph.ps("p_o", [P, 512]), ph.ps("p_m", [P, 512])
        names = ("const_ready", "zeroed", "table_ready", "gate_step", "old_copied", "stored",
                 "cmp_ready", "cmp_rest_ready", "kv0_ready", "kv1_ready", "q_ready", "hid_ready", "late_ready", "sum_ready", "act_ready",
                 "kc_ready", "kc_copied", "vc_copied", "sc_ready", "nb_ready", "pc_ready", "pcn_ready", "pct_ready", "pct_copied",
                 "imp_ready", "imp_copied", "imps_ready", "picked", "unsel_ready", "a_step",
                 "ss_ready", "ss_taken", "new_ready", "sw_ready", "nbs_ready", "ps_ready", "tn_ready", "tn_done",
                 "t0_ready", "t0_done", "t1_ready", "t1_done", "o_ready", "o_done", "b_step")
        s = {n: ph.sem(n) for n in names}
        CONSTS = 8 + 3 + 8
        SP_PAGES = 24
        block = ph.enter_context(nc.Block())
        cmp_ops = cmp_page[:].rearrange("p pg (sl c g sg) -> p sl c g pg sg", sl=2, c=8, g=2)

        def steps(eng, step):
            with eng.Fori(0, NB // 2 - 1) as i:
                for u in range(2):
                    step(i * 2 + u, u, i * 2 + (u + 1))
            step(NB - 2, 0, NB - 1)
            step(NB - 1, 1, None)

        def cmp_load(eng, b, n, ready):
            at = eng.value_load(table[0:1, bass.ds(b * N_PAGES + n, 1)], min_val=0, max_val=n_pool - 1)
            eng.dma_start(cmp_page[:, n, :], d["pool"][bass.ds(at, 1), :, 0:256].rearrange("o p n -> (o p) n")).then_inc(s[ready], 16)

        @block.sync
        def _(sp):
            sp.dma_start(table[:], d["page_table"].rearrange("b n -> (b n)").unsqueeze(0)).then_inc(s["table_ready"], 16)
            for dst, src in ((w1, "cmp_w1_seg"), (w2, "cmp_w2"), (pe_hid, "pe_hid"), (cover, "cover"), (gsum, "gsum"), (nmask, "nmask"), (wmask, "wmask"), (ident, "ident")):
                sp.dma_start(dst[:], d[src]).then_inc(s["const_ready"], 16)
            sp.wait_ge(s["table_ready"], 16)

            def cmp_loads(b):
                for n in range(SP_PAGES):
                    cmp_load(sp, b, n, "cmp_ready")

            cmp_loads(0)
            smp = slice(SEQ, SEQ + N_SMP)
            sp.dma_start(tnew[:], d["turned"][:, :, smp]).then_inc(s["const_ready"], 16)
            sp.dma_start(vnew[:, :, 0], d["kv_out"][smp, 384:512].rearrange("(b q) n -> q b n", q=Q)).then_inc(s["const_ready"], 16)
            sp.dma_start(vnew[:, :, 1], d["win_new"][smp, 128:256].rearrange("(b q) n -> q b n", q=Q)).then_inc(s["const_ready"], 16)
            for g in range(2):
                for j in range(HPG):
                    c = 3 * (2 * j + g)
                    sp.dma_start(gate[32 * g + 8 * j:32 * g + 8 * j + 8], d["gdt"][smp, c:c + 3].rearrange("(b q) c -> q b c", q=Q)).then_inc(s["const_ready"], 16)
            sp.wait_ge(s["hid_ready"], 1)
            cmp_loads(1)
            sp.dma_start(d["win_old"], d["cache_win"][:, Q:, :]).then_inc(s["old_copied"], 16)
            with sp.Fori(0, NB - 2) as b:
                hold(sp, s["hid_ready"], b + 2, ph.passed)
                cmp_loads(b + 2)
            sp.wait_ge(s["o_done"], 2 * NB)
            for g in range(2):
                for j in range(HPG):
                    c = 64 * (2 * j + g)
                    sp.dma_start(d["attn"][smp, c:c + 64].rearrange("(b q) c -> q b c", q=Q), o_all[32 * g + 8 * j:32 * g + 8 * j + 8]).then_inc(s["stored"], 16)
            sp.wait_ge(s["stored"], 128)
            sp.wait_ge(s["old_copied"], 16)

        @block.gpsimd
        def _(pool):
            pool.wait_ge(s["table_ready"], 16)

            def kv_loads(b, u):
                pool.dma_start(win[u][:].rearrange("p a n -> p (a n)"), d["win_pack"][bass.ds(b, 1)].rearrange("o p n -> (o p) n")).then_inc(s[f"kv{u}_ready"], 16)
                for n in range(N_PAGES):
                    at = pool.value_load(table[0:1, bass.ds(b * N_PAGES + n, 1)], min_val=0, max_val=n_pool - 1)
                    pool.dma_start(kv_page[u][:, n, :], d["pool"][bass.ds(at, 1), :, 256:512].rearrange("o p n -> (o p) n")).then_inc(s[f"kv{u}_ready"], 16)

            def cmp_rest(b):
                for n in range(SP_PAGES, N_PAGES):
                    cmp_load(pool, b, n, "cmp_rest_ready")

            cmp_rest(0)
            kv_loads(0, 0)
            pool.wait_ge(s["hid_ready"], 1)
            cmp_rest(1)
            kv_loads(1, 1)
            with pool.Fori(0, NB // 2 - 1) as i:
                for u in range(2):
                    hold(pool, s["hid_ready"], i * 2 + (u + 2), ph.passed)
                    cmp_rest(i * 2 + (u + 2))
                    hold(pool, s["o_ready"], i * 2 + (u + 1), ph.passed)
                    kv_loads(i * 2 + (u + 2), u)

        @block.tensor
        def _(pe):
            pe.wait_ge(s["const_ready"], CONSTS * 16)

            def hidden(b):
                hold(pe, s["cmp_ready"], b * (16 * SP_PAGES) + 16 * SP_PAGES, ph.passed)
                hold(pe, s["cmp_rest_ready"], b * (16 * (N_PAGES - SP_PAGES)) + 16 * (N_PAGES - SP_PAGES), ph.passed)
                for slot in range(2):
                    for c in range(8):
                        mm = nc.tensor.matmul(p_h[slot][:], w1[:, slot, c, :], cmp_ops[:, slot, c], start=(c == 0), stop=(c == 7))
                mm.then_inc(s["hid_ready"], 1)

            def compressed(b):
                hold(pe, s["act_ready"], b + 1, ph.passed)
                for g in range(2):
                    nc.tensor.matmul(p_h[0][64 * g:64 * g + 64, 0:NC], w2[:, 0, :], hid[:, 0, g, :], start=True, stop=True)
                for g in range(2):
                    for h in range(2):
                        n = min(P, NC - P * h)
                        mm = nc.tensor.matmul(p_h[1][0:n, P * h + 64 * g:P * h + 64 * g + 64], hid[:, 1, g, P * h:P * h + n], w2[:, 1, :], start=True, stop=True)
                mm.then_inc(s["kc_ready"], 1)

            def cmp_scores(b, u):
                hold(pe, s["kc_copied"], b + 1, ph.passed)
                hold(pe, s["q_ready"], b + 1, ph.passed)
                nc.tensor.matmul(p_h[0][0:R, 256:256 + NC], qbd[u][:, 0, :], kct[:], start=True, stop=True).then_inc(s["sc_ready"], 1)

            def cmp_turn(b):
                hold(pe, s["pcn_ready"], b + 1, ph.passed)
                nc.tensor.transpose(p_h[1][:, 256:256 + R], pc[:, 0:P], ident[0:R, 0:R])
                nc.tensor.transpose(p_h[1][0:NC - P, 256 + R:256 + 2 * R], pc[:, P:NC], ident[0:R, 0:R]).then_inc(s["pct_ready"], 1)

            def cmp_out(b):
                hold(pe, s["vc_copied"], b + 1, ph.passed)
                hold(pe, s["pct_copied"], b + 1, ph.passed)
                for h in range(2):
                    n = min(P, NC - P * h)
                    nc.tensor.matmul(p_h[1][0:R, 384:384 + NBK], pct[0:n, h, :], cover[0:n, h, :], start=(h == 0), stop=(h == 1))
                for h in range(2):
                    n = min(P, NC - P * h)
                    mm = nc.tensor.matmul(p_h[0][0:R, 0:P], pct[0:n, h, :], vc[0:n, h, :], start=(h == 0), stop=(h == 1))
                mm.then_inc(s["imp_ready"], 1)

            def importance(b):
                hold(pe, s["imp_copied"], b + 1, ph.passed)
                nc.tensor.matmul(p_h[1][0:R, 384:384 + NBK], gsum[:], imp[:], start=True, stop=True).then_inc(s["imps_ready"], 1)

            def step(b, u, a):
                def turn(k):
                    n, c0 = (8, 1024 * k) if k < NG_S else (4, W0)
                    if k >= 2:
                        hold(pe, s[f"t{k % 2}_done"], b * (3 - k % 2) + k // 2, ph.passed)
                    for i in range(n):
                        mm = nc.tensor.transpose(p_t[k % 2][:, i, :], S[:, c0 + P * i:c0 + P * i + P], ident[0:R, 0:R])
                    mm.then_inc(s[f"t{k % 2}_ready"], 1)

                def values(k):
                    hold(pe, s[f"t{k % 2}_done"], b * (3 - k % 2) + (k // 2 + 1), ph.passed)
                    if k < NG_S:
                        for n in range(8 * k, 8 * k + 8):
                            nc.tensor.matmul(p_o[0:R, P:2 * P], pst[:, n, :], kv_page[u][:, n, 128:256], start=(n == 0), stop=False)
                    else:
                        for n in range(4):
                            nc.tensor.matmul(p_o[0:R, 2 * P:3 * P], pst[:, N_PAGES + n, :], win[u][:, 1, P * n:P * n + P], start=(n == 0), stop=False)

                hold(pe, s[f"kv{u}_ready"], b * (8 * N_PAGES + 8) + (2 - u) * (8 * N_PAGES + 8), ph.passed)
                nc.tensor.matmul(p_m[0:R, 0:Q], qbd[u][:, 1, :], tnew[:, 10, bass.ds(b * Q, Q)], start=True, stop=True)
                nc.tensor.matmul(p_m[0:R, Q:2 * Q], qbd[u][:, 1, :], tnew[:, 11, bass.ds(b * Q, Q)], start=True, stop=True).then_inc(s["new_ready"], 1)
                for c in range(CHUNKS):
                    if c >= 2:
                        hold(pe, s["ss_taken"], b * (CHUNKS + 1) + (c - 1), ph.passed)
                    nc.tensor.matmul(p_s[c % 2][0:R, :], qbd[u][:, 1, :], kv_page[u][:, 4 * c:4 * c + 4, 0:128], start=True, stop=True).then_inc(s["ss_ready"], 1)
                hold(pe, s["ss_taken"], b * (CHUNKS + 1) + (CHUNKS - 1), ph.passed)
                nc.tensor.matmul(p_s[0][0:R, :], qbd[u][:, 1, :], win[u][:, 0, :], start=True, stop=True).then_inc(s["ss_ready"], 1)
                if a is not None:
                    hold(pe, s["picked"], b + 1, ph.passed)
                    hidden(a)
                hold(pe, s["ps_ready"], b + 1, ph.passed)
                nc.tensor.transpose(p_m[0:Q, 0:R], S[:, OLD:W0], ident[0:R, 0:R])
                nc.tensor.transpose(p_m[0:Q, R:2 * R], S[:, W0 + WINDOW:W0 + WN], ident[0:R, 0:R]).then_inc(s["tn_ready"], 1)
                turn(0)
                turn(1)
                values(0)
                if a is not None:
                    compressed(a)
                turn(2)
                values(1)
                if a is not None:
                    cmp_scores(a, 1 - u)
                turn(3)
                values(2)
                if a is not None:
                    cmp_turn(a)
                turn(4)
                values(3)
                if a is not None:
                    cmp_out(a)
                hold(pe, s["tn_done"], b + 1, ph.passed)
                nc.tensor.matmul(p_o[0:R, P:2 * P], pnew[:, 0, :], vcur[:, 0, :], start=False, stop=True)
                values(4)
                nc.tensor.matmul(p_o[0:R, 2 * P:3 * P], pnew[:, 1, :], vcur[:, 1, :], start=False, stop=True).then_inc(s["o_ready"], 1)
                if a is not None:
                    importance(a)

            hidden(0)
            compressed(0)
            cmp_scores(0, 0)
            cmp_turn(0)
            cmp_out(0)
            importance(0)
            steps(pe, step)

        @block.scalar
        def _(act):
            act.wait_ge(s["const_ready"], CONSTS * 16)
            nc.scalar.activation(gate[:], gate[:], ACT.Exp, scale=-1.0).then_inc(s["gate_step"], 1)

            def halves(b):
                act.wait_ge(s["hid_ready"], b + 1)
                for slot in range(2):
                    ins = nc.scalar.activation(late[:, slot], p_h[slot][64:128].rearrange("p (g n) -> p g n", g=2), ACT.Copy)
                ins.then_inc(s["late_ready"], 1)
                act.wait_ge(s["sum_ready"], b + 1)
                for slot in range(2):
                    ins = nc.scalar.activation(hid[:, slot], hid[:, slot], ACT.Silu, bias=pe_hid[:, slot:slot + 1])
                ins.then_inc(s["act_ready"], 1)

            def cmp_keys(b):
                act.wait_ge(s["kc_ready"], b + 1)
                nc.scalar.activation(kct[:], p_h[0][:, 0:NC], ACT.Copy).then_inc(s["kc_copied"], 1)

            def cmp_exp(b):
                act.wait_ge(s["nb_ready"], b + 1)
                nc.scalar.activation(pc[:], p_h[0][0:R, 256:256 + NC], ACT.Exp, bias=nbc[:], accum_out=lc[:]).then_inc(s["pc_ready"], 1)

            def step(b, u, a):
                def turned(k):
                    act.wait_ge(s["t1_ready"], b * 2 + (k // 2 + 1))
                    nc.scalar.activation(pst[:, 8 * k:8 * k + 8, :], p_t[1][:], ACT.Copy).then_inc(s["t1_done"], 1)

                act.wait_ge(s["nbs_ready"], b + 1)
                nc.scalar.activation(S[:, 0:W0], S[:, 0:W0], ACT.Exp, bias=nbs[:, 0:1], accum_out=ls[:, 0:1])
                nc.scalar.activation(S[:, W0:], S[:, W0:], ACT.Exp, bias=nbs[:, 1:2], accum_out=ls[:, 1:2]).then_inc(s["ps_ready"], 1)
                if a is not None:
                    halves(a)
                turned(1)
                if a is not None:
                    cmp_keys(a)
                    cmp_exp(a)
                turned(3)

            halves(0)
            cmp_keys(0)
            cmp_exp(0)
            steps(act, step)

        @block.vector
        def _(dve):
            for u in range(2):
                nc.vector.memset(qbd[u][:], 0.0).then_inc(s["zeroed"], 1)
            dve.wait_ge(s["zeroed"], 2)
            dve.wait_ge(s["const_ready"], CONSTS * 16)
            dve.wait_ge(s["gate_step"], 1)
            nc.vector.tensor_scalar(gate[:], gate[:], 1.0, None, ALU.add).then_inc(s["gate_step"], 1)
            dve.wait_ge(s["gate_step"], 2)
            nc.vector.reciprocal(gate[:], gate[:]).then_inc(s["gate_step"], 1)
            dve.wait_ge(s["gate_step"], 3)

            def halves(b, u, link):
                for g in range(2):
                    for kind in range(2):
                        ins = nc.vector.tensor_copy(qbd[u][64 * g:64 * g + 64, kind, 32 * g:32 * g + 32].rearrange("p (j q) -> p j q", j=HPG),
                                                    tnew[64 * g:64 * g + 64, 4 * kind:4 * kind + 4, bass.ds(b * Q, Q)])
                ins.then_inc(s["q_ready"], 1)
                dve.wait_ge(s["late_ready"], b + 1)
                for slot in range(2):
                    first = p_h[slot][0:HD].rearrange("p (g n) -> p g n", g=2)[:, :, 0:NC]
                    ins = nc.vector.tensor_tensor(hid[:, slot], first, late[:, slot, :, 1:N_SEG_S], ALU.add)
                ins.then_inc(s["sum_ready"], 1)

            def cmp_values(b):
                dve.wait_ge(s["kc_ready"], b + 1)
                nc.vector.tensor_copy(vc[:, 0], p_h[1][:, 0:P])
                nc.vector.tensor_copy(vc[0:NC - P, 1], p_h[1][0:NC - P, P:2 * P]).then_inc(s["vc_copied"], 1)

            def cmp_max(b):
                dve.wait_ge(s["sc_ready"], b + 1)
                nc.vector.tensor_reduce(nbc[:], p_h[0][0:R, 256:256 + NC], AX, ALU.max, negate=True).then_inc(s["nb_ready"], 1)

            def cmp_norm(b, link):
                dve.wait_ge(s["pc_ready"], b + 1)
                link(nc.vector.reciprocal(rc[:], lc[:]))
                nc.vector.tensor_scalar(pc[:], pc[:], rc[:], None, ALU.mult).then_inc(s["pcn_ready"], 1)

            def cmp_turned(b):
                dve.wait_ge(s["pct_ready"], b + 1)
                nc.vector.tensor_copy(pct[:, 0], p_h[1][:, 256:256 + R])
                nc.vector.tensor_copy(pct[0:NC - P, 1], p_h[1][0:NC - P, 256 + R:256 + 2 * R]).then_inc(s["pct_copied"], 1)

            def pick(b, u, link):
                dve.wait_ge(s["imp_ready"], b + 1)
                nc.vector.tensor_copy(imp[:], p_h[1][0:R, 384:384 + NBK]).then_inc(s["imp_copied"], 1)
                link(nc.vector.tensor_copy(gc[:], gate[:, bass.ds(b, 1), 0]))
                for g in range(2):
                    rows = slice(32 * g, 32 * g + 32)
                    link(nc.vector.tensor_scalar(o[u][rows, :], p_h[0][rows, 64 * g:64 * g + 64], gc[rows, 0:1], None, ALU.mult))
                dve.wait_ge(s["imps_ready"], b + 1)
                nc.vector.tensor_copy(score[:], p_h[1][0:R, 384:384 + NBK]).then_inc(s["picked"], 1)
                dve.wait_ge(s["picked"], b + 1)
                nc.vector.memset(score[:, 0:1], FORCED)
                link(nc.vector.memset(score[:, CUR - 1:CUR + 1], FORCED), ph.passed)
                link(nc.vector.max(top[:, 0], score[:]), ph.passed)
                link(nc.vector.match_replace(score2[:], top[:, 0], score[:], -3e38), ph.passed)
                link(nc.vector.max(top[:, 1], score2[:]), ph.passed)
                link(nc.vector.match_replace(score3[:], top[:, 1], score2[:], -3e38))
                link(nc.vector.tensor_tensor(unsel[:], score[:], score3[:], ALU.is_equal))
                nc.vector.tensor_scalar(unsel[:], unsel[:], NEG, None, ALU.mult).then_inc(s["unsel_ready"], 1)
                link.close()

            def step(b, u, a):
                link = Chain(dve, s["b_step"], 4, b)
                more = None if a is None else Chain(dve, s["a_step"], A_STEPS, a)

                def turned(k):
                    n = 8 if k < NG_S else 4
                    dve.wait_ge(s["t0_ready"], b * 3 + (k // 2 + 1))
                    nc.vector.tensor_copy(pst[:, 8 * k:8 * k + n, :], p_t[0][:, 0:n, :]).then_inc(s["t0_done"], 1)

                dve.wait_ge(s["unsel_ready"], b + 1)
                for c in range(CHUNKS):
                    dve.wait_ge(s["ss_ready"], b * (CHUNKS + 1) + (c + 1))
                    nc.vector.tensor_tensor(S[:, 512 * c:512 * c + 512].rearrange("p (k n) -> p k n", n=L_SLC), p_s[c % 2][0:R, :].rearrange("p (k n) -> p k n", n=L_SLC),
                                            unsel[:, 8 * c:8 * c + 8].unsqueeze(2).broadcast_to([R, 8, L_SLC]), ALU.add).then_inc(s["ss_taken"], 1)
                dve.wait_ge(s["new_ready"], b + 1)
                nc.vector.tensor_tensor(S[:, OLD:W0], p_m[0:R, 0:Q], nmask[:], ALU.add)
                nc.vector.tensor_tensor(S[:, W0 + WINDOW:], p_m[0:R, Q:2 * Q], wmask[:, WINDOW:], ALU.add)
                dve.wait_ge(s["ss_ready"], b * (CHUNKS + 1) + (CHUNKS + 1))
                nc.vector.tensor_tensor(S[:, W0:W0 + WINDOW], p_s[0][0:R, :], wmask[:, 0:WINDOW], ALU.add).then_inc(s["ss_taken"], 1)
                dve.wait_ge(s["ss_taken"], b * (CHUNKS + 1) + (CHUNKS + 1))
                nc.vector.tensor_reduce(nbs[:, 0:1], S[:, 0:W0], AX, ALU.max, negate=True)
                nc.vector.tensor_reduce(nbs[:, 1:2], S[:, W0:], AX, ALU.max, negate=True).then_inc(s["nbs_ready"], 1)
                if a is not None:
                    halves(a, 1 - u, more)
                dve.wait_ge(s["tn_ready"], b + 1)
                nc.vector.tensor_copy(vcur[:], vnew[:, bass.ds(b, 1)].rearrange("q o k n -> q (o k) n"))
                nc.vector.tensor_copy(pnew[:], p_m[0:Q, 0:2 * R].rearrange("p (a n) -> p a n", a=2)).then_inc(s["tn_done"], 1)
                turned(0)
                if a is not None:
                    cmp_values(a)
                turned(2)
                if a is not None:
                    cmp_max(a)
                    cmp_norm(a, more)
                    cmp_turned(a)
                turned(4)
                dve.wait_ge(s["ps_ready"], b + 1)
                link(nc.vector.reciprocal(rs[:], ls[:]))
                link(nc.vector.tensor_tensor(rs[:], rs[:], gate[:, bass.ds(b, 1), 1:3].rearrange("r o n -> r (o n)"), ALU.mult))
                if a is not None:
                    pick(a, 1 - u, more)
                dve.wait_ge(s["o_ready"], b + 1)
                for g in range(2):
                    rows = slice(32 * g, 32 * g + 32)
                    link(nc.vector.scalar_tensor_tensor(o[u][rows, :], p_o[rows, P + 64 * g:P + 64 * g + 64], rs[rows, 0:1], o[u][rows, :], ALU.mult, ALU.add))
                for g in range(2):
                    rows = slice(32 * g, 32 * g + 32)
                    nc.vector.scalar_tensor_tensor(o_all[rows, bass.ds(b, 1), :].rearrange("r o n -> r (o n)"), p_o[rows, 2 * P + 64 * g:2 * P + 64 * g + 64], rs[rows, 1:2], o[u][rows, :], ALU.mult, ALU.add).then_inc(s["o_done"], 1)
                dve.wait_ge(s["o_done"], b * 2 + 2)
                link.close()

            A_STEPS = 10
            more = Chain(dve, s["a_step"], A_STEPS, 0)
            halves(0, 0, more)
            cmp_values(0)
            cmp_max(0)
            cmp_norm(0, more)
            cmp_turned(0)
            pick(0, 0, more)
            steps(dve, step)


def after_tile(t, n, b):
    return t + 1, n + b, 1 - b


def before_tile(t, n, b):
    return t - 1, n - (1 - b), 1 - b


def tile_loop(eng, body):
    body(0, 0, 0, True, 0)
    with eng.Fori(0, (TILES - 3) // 2) as i:
        body(i * 2 + 1, i, 1, False, 0)
        body(i * 2 + 2, i + 1, 0, False, 0)
    body(TILES - 2, (TILES - 2) // 2, (TILES - 2) % 2, False, 1)
    body(TILES - 1, (TILES - 1) // 2, (TILES - 1) % 2, False, 2)


def mix_phase(nc, d):
    BIG = 3e38
    with Phase(nc, "mix") as ph:
        w = ph.sb("w", [P, KC, D_MODEL])
        wr = ph.sb("wr", [P, KC, 36])
        rb = ph.sb("rb", [P, 36])
        gain = ph.sb("gain", [P, D_MODEL])
        ident = ph.sb("ident", [P, P])
        eps = ph.sb("eps", [P, 1])
        cat, x, h, f = ([ph.sb(f"{n}{b}", [P, D_MODEL]) for b in range(2)] for n in ("cat", "x", "h", "f"))
        sq = ph.sb("sq", [P, D_MODEL])
        catT = ph.sb("catT", [P, KC, P])
        fT = ph.sb("fT", [P, KC, P])
        real = ph.sb("real", [P, 1])
        ss, r, nm, z, ed, den = (ph.sb(n, [P, 1]) for n in ("ss", "r", "nm", "z", "ed", "den"))
        lg = ph.sb("lg", [P, 36])
        g16, g16r = ph.sb("g16", [P, 16]), ph.sb("g16r", [P, 16])
        ge = ph.sb("ge", [P, NG])
        pen = ph.sb("pen", [P, NG])
        el, el1, el2 = (ph.sb(n, [P, NE + 16]) for n in ("el", "el1", "el2"))
        top, pick = ph.sb("top", [P, 8]), ph.sb("pick", [P, 3, 8])
        route = [ph.sb(f"route{b}", [P, 66]) for b in range(2)]
        p_t = [ph.ps(f"p_t{i}", [P, 4, P]) for i in range(2)]
        p_m = [ph.ps(f"p_m{i}", [P, 512]) for i in range(2)]
        p_f = [ph.ps(f"p_f{i}", [P, 4, P]) for i in range(2)]
        p_l = ph.ps("p_l", [P, 36])
        names = ("const_ready", "setup", "cat_turned", "cat_copied", "mix_ready", "h_ready", "sq_ready", "ln_ready", "r_ready", "f_ready",
                 "f_turned", "f_copied", "lg_ready", "nm_ready", "ge_ready", "route_ready", "dve_step")
        s = {n: ph.sem(n) for n in names}
        in_ready, h_stored, f_stored, route_stored = ([ph.sem(f"{n}{b}") for b in range(2)] for n in ("in_ready", "h_stored", "f_stored", "route_stored"))
        block = ph.enter_context(nc.Block())

        @block.sync
        def _(sp):
            for dst, src in ((wr, "w_route"), (rb, "b_route"), (gain, "ffn_norm"), (ident, "ident"), (real, "real")):
                sp.dma_start(dst[:], d[src]).then_inc(s["const_ready"], 16)

            def load(t, n, b):
                tok = bass.ds(t * P, P)
                for dst, src in ((cat[b][:, 0:512], d["attn"]), (cat[b][:, 512:], d["ssd"]), (x[b][:], d["x"])):
                    sp.dma_start(dst, src[tok, :]).then_inc(in_ready[b], 16)

            def store_route(t, n, b):
                sp.wait_ge(s["route_ready"], t + 1)
                sp.dma_start(d["route"][bass.ds(t * P, P), :], route[b][:]).then_inc(route_stored[b], 16)

            def body(t, n, b, first, last):
                tok = bass.ds(t * P, P)
                sp.wait_ge(s["h_ready"], t * 2 + 2)
                sp.dma_start(d["h"][tok, :], h[b][:]).then_inc(h_stored[b], 16)
                if not first:
                    store_route(*before_tile(t, n, b))
                if last < 2:
                    sp.wait_ge(s["f_ready"], t + 1)
                    sp.dma_start(d["f"][tok, :], f[b][:]).then_inc(f_stored[b], 16)
                if last == 0:
                    load(t + 2, n + 1, b)
                if last == 2:
                    sp.wait_ge(s["f_ready"], t + 1)
                    sp.dma_start(d["f"][tok, :], f[b][:]).then_inc(f_stored[b], 16)

            load(0, 0, 0)
            for k in range(KC):
                sp.dma_start(w[:, k], d["w_out"][:, k]).then_inc(s["const_ready"], 16)
            load(1, 0, 1)
            tile_loop(sp, body)
            store_route(TILES - 1, TILES // 2, (TILES - 1) % 2)
            for b in range(2):
                n = (TILES + 1 - b) // 2
                for q in (h_stored, f_stored, route_stored):
                    sp.wait_ge(q[b], 16 * n + 16)

        @block.tensor
        def _(pe):
            pe.wait_ge(s["const_ready"], 16 * (5 + KC))

            def turn_cat(t, n, b):
                pe.wait_ge(in_ready[b], n * 48 + 48)
                for k in range(KC):
                    mm = nc.tensor.transpose(p_t[k // 4][:, k % 4, :], cat[b][:, k * P:k * P + P], ident[:])
                mm.then_inc(s["cat_turned"], 1)

            def turn_f(t, n, b):
                pe.wait_ge(s["f_ready"], t + 1)
                for k in range(KC):
                    mm = nc.tensor.transpose(p_f[k // 4][:, k % 4, :], f[b][:, k * P:k * P + P], ident[:])
                mm.then_inc(s["f_turned"], 1)

            def logits(t, n, b):
                pe.wait_ge(s["f_copied"], t * 2 + 2)
                for k in range(KC):
                    mm = nc.tensor.matmul(p_l[:], fT[:, k, :], wr[:, k, :], start=(k == 0), stop=(k == KC - 1))
                mm.then_inc(s["lg_ready"], 1)

            def body(t, n, b, first, last):
                pe.wait_ge(s["cat_copied"], t * 2 + 2)
                if not first:
                    pe.wait_ge(s["h_ready"], t * 2)
                for h2 in range(2):
                    for k in range(KC):
                        mm = nc.tensor.matmul(p_m[h2][:], catT[:, k, :], w[:, k, 512 * h2:512 * h2 + 512], start=(k == 0), stop=(k == KC - 1))
                mm.then_inc(s["mix_ready"], 1)
                if not first:
                    turn_f(*before_tile(t, n, b))
                if last < 2:
                    turn_cat(*after_tile(t, n, b))
                if not first:
                    logits(*before_tile(t, n, b))

            turn_cat(0, 0, 0)
            tile_loop(pe, body)
            end = (TILES - 1, TILES // 2, (TILES - 1) % 2)
            turn_f(*end)
            logits(*end)

        @block.scalar
        def _(act):
            act.wait_ge(s["setup"], 3)

            def copy_cat(t, n, b):
                act.wait_ge(s["cat_turned"], t + 1)
                nc.scalar.activation(catT[:, 4:8], p_t[1][:], ACT.Copy).then_inc(s["cat_copied"], 1)

            def copy_f(t, n, b):
                act.wait_ge(s["f_turned"], t + 1)
                nc.scalar.activation(fT[:, 4:8], p_f[1][:], ACT.Copy).then_inc(s["f_copied"], 1)

            def router(t, n, b):
                act.wait_ge(s["nm_ready"], t + 1)
                nc.scalar.activation(ge[:], lg[:, 0:NG], ACT.Exp, bias=nm[:], accum_out=z[:])
                nc.scalar.activation(ed[:], den[:], ACT.Exp).then_inc(s["ge_ready"], 1)

            def body(t, n, b, first, last):
                if not first:
                    copy_f(*before_tile(t, n, b))
                if last < 2:
                    copy_cat(*after_tile(t, n, b))
                act.wait_ge(s["h_ready"], t * 2 + 2)
                nc.scalar.activation(sq[:], h[b][:], ACT.Square, accum_out=ss[:]).then_inc(s["sq_ready"], 1)
                act.wait_ge(s["sq_ready"], t + 1)
                if not first:
                    act.wait_ge(s["f_ready"], t)
                nc.scalar.activation(ss[:], ss[:], ACT.Ln, bias=eps[:], scale=1.0 / D_MODEL).then_inc(s["ln_ready"], 1)
                act.wait_ge(s["ln_ready"], t + 1)
                nc.scalar.activation(r[:], ss[:], ACT.Exp, scale=-0.5).then_inc(s["r_ready"], 1)
                if not first:
                    router(*before_tile(t, n, b))

            copy_cat(0, 0, 0)
            tile_loop(act, body)
            end = (TILES - 1, TILES // 2, (TILES - 1) % 2)
            copy_f(*end)
            router(*end)

        @block.vector
        def _(dve):
            nc.vector.memset(eps[:], EPS).then_inc(s["setup"], 1)
            for i, tile in enumerate((g16, el, pick)):
                ins = nc.vector.memset(tile[:], -BIG)
            ins.then_inc(s["setup"], 2)
            for b in range(2):
                for q in (h_stored, f_stored, route_stored):
                    dve.sem_inc(q[b], 16)
            dve.wait_ge(s["setup"], 3)
            dve.wait_ge(s["const_ready"], 16 * (5 + KC))

            def copy_cat(t, n, b):
                dve.wait_ge(s["cat_turned"], t + 1)
                nc.vector.tensor_copy(catT[:, 0:4], p_t[0][:]).then_inc(s["cat_copied"], 1)

            def copy_f(t, n, b):
                dve.wait_ge(s["f_turned"], t + 1)
                nc.vector.tensor_copy(fT[:, 0:4], p_f[0][:]).then_inc(s["f_copied"], 1)

            def router(t, n, b):
                link = Chain(dve, s["dve_step"], 19, t)
                rt = route[b]
                dve.wait_ge(route_stored[b], n * 16 + 16)
                dve.wait_ge(s["lg_ready"], t + 1)
                link(nc.vector.tensor_tensor(lg[:], p_l[:], rb[:], ALU.add))
                link(nc.vector.tensor_copy(g16[:, 0:NG], lg[:, 0:NG]), ph.passed)
                link(nc.vector.max(top[:], g16[:]))
                link(nc.vector.tensor_copy(pick[:, 0, 0:1], top[:, 0:1]))
                link(nc.vector.tensor_scalar(nm[:], top[:, 0:1], -1.0, None, ALU.mult), ph.passed)
                link(nc.vector.match_replace(g16r[:], pick[:, 0], g16[:], BIG))
                link(nc.vector.tensor_scalar(pen[:], g16r[:, 0:NG], BIG, None, ALU.is_equal))
                link(nc.vector.tensor_scalar(pen[:], pen[:], -NEG, NEG, ALU.mult, ALU.add))
                link(nc.vector.tensor_tensor(el[:, 0:NE].rearrange("p (g e) -> p g e", g=NG), lg[:, NG:].rearrange("p (g e) -> p g e", g=NG),
                                             pen[:].unsqueeze(2).broadcast_to([P, NG, EPG]), ALU.add), ph.passed)
                link(nc.vector.max(top[:], el[:]))
                nc.vector.tensor_copy(pick[:, 1, 0:1], top[:, 0:1])
                link(nc.vector.tensor_copy(pick[:, 2, 0:1], top[:, 1:2]))
                nc.vector.tensor_tensor(den[:], top[:, 1:2], top[:, 0:1], ALU.subtract).then_inc(s["nm_ready"], 1)
                hold(dve, s["nm_ready"], t + 1, ph.passed)
                link(nc.vector.match_replace(el1[:], pick[:, 1], el[:], BIG), ph.passed)
                link(nc.vector.match_replace(el2[:], pick[:, 2], el1[:], BIG))
                link(nc.vector.tensor_scalar(rt[:, 0:NE], el1[:, 0:NE], BIG, None, ALU.is_equal))
                link(nc.vector.tensor_scalar(rt[:, NE:2 * NE], el2[:, 0:NE], BIG, None, ALU.is_equal))
                link(nc.vector.tensor_tensor(rt[:, NE:2 * NE], rt[:, NE:2 * NE], rt[:, 0:NE], ALU.subtract))
                if isinstance(t, int) and t == TILES - 1:
                    link(nc.vector.tensor_scalar(rt[:, 0:2 * NE], rt[:, 0:2 * NE], real[:], None, ALU.mult))
                dve.wait_ge(s["ge_ready"], t + 1)
                link(nc.vector.scalar_tensor_tensor(den[:], ed[:], 1.0, z[:], ALU.add, ALU.mult))
                link(nc.vector.reciprocal(rt[:, 64:65], den[:]))
                link(nc.vector.tensor_tensor(rt[:, 65:66], rt[:, 64:65], ed[:], ALU.mult))
                dve.sem_inc(s["route_ready"], 1)
                if not isinstance(t, int):
                    link.close()

            def body(t, n, b, first, last):
                dve.wait_ge(s["mix_ready"], t + 1)
                dve.wait_ge(h_stored[b], n * 16 + 16)
                for h2 in range(2):
                    c = slice(512 * h2, 512 * h2 + 512)
                    nc.vector.tensor_tensor(h[b][:, c], x[b][:, c], p_m[h2][:], ALU.add).then_inc(s["h_ready"], 1)
                if not first:
                    copy_f(*before_tile(t, n, b))
                if last < 2:
                    copy_cat(*after_tile(t, n, b))
                dve.wait_ge(s["r_ready"], t + 1)
                dve.wait_ge(f_stored[b], n * 16 + 16)
                nc.vector.scalar_tensor_tensor(f[b][:], h[b][:], r[:], gain[:], ALU.mult, ALU.mult).then_inc(s["f_ready"], 1)
                if not first:
                    router(*before_tile(t, n, b))

            copy_cat(0, 0, 0)
            tile_loop(dve, body)
            end = (TILES - 1, TILES // 2, (TILES - 1) % 2)
            copy_f(*end)
            router(*end)


def dispatch_phase(nc, d):
    with Phase(nc, "dsp") as ph:
        route = ph.sb("route", [P, TILES, 66])
        before = ph.sb("before", [P, P])
        ones = ph.sb("ones", [P, P])
        first = ph.sb("first", [P, NE])
        padoff = ph.sb("padoff", [P, TILES, 2])
        ids = ph.sb("ids", [P, TILES], U32)
        blocks = ph.sb("blocks", [P, OVER_BLOCKS])
        m = ph.sb("m", [P, TILES, NE])
        pos = ph.sb("pos", [P, TILES, NE])
        late = ph.sb("late", [P, TILES, NE])
        n_e, ov, cum, cum2, base2 = (ph.sb(n, [P, NE]) for n in ("n_e", "ov", "cum", "cum2", "base2"))
        dest = ph.sb("dest", [P, TILES, 2])
        gidx = ph.sb("gidx", [P, TILES, 2], U32)
        sidx = ph.sb("sidx", [P, TILES, 2], U32)
        fill = ph.sb("fill", [P, SLOTS // P], U32)
        cmpj = ph.sb("cmpj", [P, OVER_BLOCKS, NE])
        over = ph.sb("over", [P, OVER_BLOCKS + 1])
        over_i = ph.sb("over_i", [P, OVER_BLOCKS + 1], I32)
        p_c = ph.ps("p_c", [P, TILES + 1, NE])
        loaded, m_ready, cnt_ready, idx_ready, over_ready = ph.sem("loaded"), ph.sem("m_ready"), ph.sem("cnt_ready"), ph.sem("idx_ready"), ph.sem("over_ready")
        filled, fill_ready, scattered, stored, dve_step = ph.sem("filled"), ph.sem("fill_ready"), ph.sem("scattered"), ph.sem("stored"), ph.sem("dve_step")
        block = ph.enter_context(nc.Block())

        @block.sync
        def _(sp):
            for dst, src in ((route[:], d["route"].rearrange("(t p) n -> p t n", p=P)), (before[:], d["before"]), (first[:], d["first"]), (padoff[:], d["padoff"]),
                             (ids[:], d["ids"]), (blocks[:], d["blocks"])):
                sp.dma_start(dst, src).then_inc(loaded, 16)
            sp.wait_ge(fill_ready, 1)
            sp.dma_start(d["slot_tok"].rearrange("(p n) o -> p (n o)", p=P), fill[:]).then_inc(filled, 16)
            sp.wait_ge(idx_ready, 1)
            sp.dma_start(d["gidx"].rearrange("(t p) n -> p t n", p=P), gidx[:]).then_inc(stored, 16)
            sp.wait_ge(over_ready, 1)
            sp.dma_start(d["over"], over_i[0:1, :]).then_inc(stored, 16)
            sp.wait_ge(stored, 32)

        @block.tensor
        def _(pe):
            pe.wait_ge(m_ready, 1)
            for t in range(TILES + 1):
                if t < TILES:
                    mm = nc.tensor.matmul(p_c[:, t, :], before[:], m[:, t, :], start=True, stop=(t == 0))
                for u in range(t):
                    mm = nc.tensor.matmul(p_c[:, t, :], ones[:], m[:, u, :], start=(t == TILES and u == 0), stop=(u == t - 1))
            mm.then_inc(cnt_ready, 1)

        @block.vector
        def _(dve):
            link = Chain(dve, dve_step)
            nc.vector.memset(fill[:], TOK - 1).then_inc(fill_ready, 1)
            link(nc.vector.memset(ones[:], 1.0))
            dve.wait_ge(loaded, 96)
            nc.vector.tensor_tensor(m[:], route[:, :, 0:NE], route[:, :, NE:2 * NE], ALU.add).then_inc(m_ready, 1)
            dve.wait_ge(cnt_ready, 1)
            link(nc.vector.tensor_copy(pos[:], p_c[:, 0:TILES, :]))
            link(nc.vector.tensor_copy(n_e[:], p_c[:, TILES, :]))
            link(nc.vector.tensor_scalar(ov[:], n_e[:], float(P), None, ALU.is_gt))
            for k in range(2, TILES):
                link(nc.vector.scalar_tensor_tensor(ov[:], n_e[:], float(P * k), ov[:], ALU.is_gt, ALU.add))
            link(nc.vector.tensor_copy(cum[:], ov[:]))
            a, b = cum, cum2
            for k in (1, 2, 4, 8, 16):
                nc.vector.tensor_copy(b[:, 0:k], a[:, 0:k])
                link(nc.vector.tensor_tensor(b[:, k:], a[:, k:], a[:, 0:NE - k], ALU.add))
                a, b = b, a
            link(nc.vector.tensor_tensor(base2[:], a[:], ov[:], ALU.subtract))
            link(nc.vector.tensor_scalar(base2[:], base2[:], float(P), float(P * (MAIN_BLOCKS - 1)), ALU.mult, ALU.add))
            link(nc.vector.tensor_tensor(base2[:], base2[:], first[:], ALU.subtract))
            link(nc.vector.tensor_scalar(late[:], pos[:], float(P), None, ALU.is_ge))
            link(nc.vector.tensor_tensor(late[:], late[:], base2[:].unsqueeze(1).broadcast_to([P, TILES, NE]), ALU.mult))
            link(nc.vector.tensor_tensor(pos[:], pos[:], first[:].unsqueeze(1).broadcast_to([P, TILES, NE]), ALU.add))
            link(nc.vector.tensor_tensor(pos[:], pos[:], late[:], ALU.add))
            for k in range(2):
                link(nc.vector.tensor_tensor(m[:], pos[:], route[:, :, NE * k:NE * k + NE], ALU.mult))
                link(nc.vector.reduce_sum(dest[:, :, k], m[:], AX))
            nc.vector.tensor_copy(gidx[:], dest[:])
            link(nc.vector.tensor_tensor(dest[:], dest[:], padoff[:], ALU.add))
            nc.vector.tensor_copy(sidx[:], dest[:]).then_inc(idx_ready, 1)
            link(nc.vector.tensor_tensor(cmpj[:], a[:].unsqueeze(1).broadcast_to([P, OVER_BLOCKS, NE]), blocks[:].unsqueeze(2).broadcast_to([P, OVER_BLOCKS, NE]), ALU.is_le))
            link(nc.vector.reduce_sum(over[:, 0:OVER_BLOCKS], cmpj[:], AX))
            link(nc.vector.tensor_scalar(over[:, 0:OVER_BLOCKS], over[:, 0:OVER_BLOCKS], float(NE - 1), None, ALU.min))
            link(nc.vector.tensor_copy(over[:, OVER_BLOCKS:], a[:, NE - 1:NE]))
            nc.vector.tensor_copy(over_i[:], over[:]).then_inc(over_ready, 1)

        @block.gpsimd
        def _(pool):
            pool.wait_ge(filled, 16)
            pool.wait_ge(idx_ready, 1)
            for t in range(TILES):
                for k in range(2):
                    pool.indirect_dma_start(d["slot_tok"], bass.IndirectOffsetOnAxis(ap=sidx[:, t, k:k + 1], axis=0), ids[:, t:t + 1], None).then_inc(scattered, 16)
            pool.wait_ge(scattered, 2 * TILES * 16)


def expert_phase(nc, d, overflow):
    NBUF = 1 if overflow else 2
    FIRST = MAIN_BLOCKS if overflow else 0
    with Phase(nc, "ovf" if overflow else "exp") as ph:
        wg = [ph.sb(f"wg{i}", [P, KC, D_EXP]) for i in range(NBUF)]
        wu = [ph.sb(f"wu{i}", [P, KC, D_EXP]) for i in range(NBUF)]
        wd = [ph.sb(f"wd{i}", [P, D_EXP // P, D_MODEL]) for i in range(NBUF)]
        idx = [ph.sb(f"idx{i}", [P, 1], U32) for i in range(NBUF)]
        xg = [ph.sb(f"xg{i}", [P, D_MODEL]) for i in range(NBUF)]
        xT = [ph.sb(f"xT{i}", [P, KC, P]) for i in range(NBUF)]
        act_g = ph.sb("act_g", [P, D_EXP])
        hb = ph.sb("hb", [P, D_EXP])
        hT = ph.sb("hT", [P, 4, P])
        y = [ph.sb(f"y{i}", [P, D_MODEL]) for i in range(NBUF)]
        ident = ph.sb("ident", [P, P])
        over = ph.sb("over", [1, OVER_BLOCKS + 1], I32)
        p_t = [ph.ps(f"p_t{i}", [P, 4, P]) for i in range(2)]
        p_g, p_u, p_h = ph.ps("p_g", [P, D_EXP]), ph.ps("p_u", [P, D_EXP]), ph.ps("p_h", [P, 4, P])
        p_y = [ph.ps(f"p_y{i}", [P, 512]) for i in range(2)]
        const_ready = ph.sem("const_ready")
        per_buf = [{n: ph.sem(f"{n}{i}") for n in ("g_loaded", "u_loaded", "d_loaded", "idx_ready", "x_ready", "x_free", "g_free", "u_free", "d_free", "stored", "y_ready")} for i in range(NBUF)]
        s = {n: ph.sem(n) for n in ("x_turned", "x_copied", "g_ready", "u_ready", "act_ready", "h_ready", "h_turned", "h_copied", "y_done", "y_free")}
        block = ph.enter_context(nc.Block())
        N = (OVER_BLOCKS if overflow else MAIN_BLOCKS) // NBUF

        def blocks(eng, body):
            if not overflow:
                with eng.Fori(0, N - 1) as i:
                    for k in range(NBUF):
                        body(i, i * NBUF + k, k, False)
                for k in range(NBUF):
                    body(N - 1, (N - 1) * NBUF + k, k, k == NBUF - 1)
            else:
                eng.wait_ge(const_ready, 32)
                needed = eng.value_load(over[0:1, OVER_BLOCKS:OVER_BLOCKS + 1], min_val=0, max_val=OVER_BLOCKS)
                with eng.Fori(0, N) as i:
                    with eng.If(needed > i):
                        body(i, i, 0, False)
                    with eng.Else():
                        pass

        @block.sync
        def _(sp):
            sp.dma_start(ident[:], d["ident"]).then_inc(const_ready, 16)
            sp.dma_start(over[:], d["over"]).then_inc(const_ready, 16)
            for k in range(NBUF):
                for n in ("g_free", "u_free", "d_free"):
                    sp.sem_inc(per_buf[k][n], 1)

            def body(i, b, k, last):
                q = per_buf[k]
                ex = sp.value_load(over[0:1, bass.ds(b, 1)], min_val=0, max_val=NE - 1) if overflow else b
                for name, dst in (("g", wg), ("u", wu), ("d", wd)):
                    src = d[{"g": "w_gate", "u": "w_up", "d": "w_down"}[name]]
                    sp.wait_ge(q[name + "_free"], i + 1)
                    sp.dma_start(dst[k][:], src[bass.ds(ex, 1)].rearrange("o (c p) n -> p (o c) n", p=P)).then_inc(q[name + "_loaded"], 16)
            blocks(sp, body)

        @block.gpsimd
        def _(pool):
            for k in range(NBUF):
                pool.sem_inc(per_buf[k]["x_free"], 1)

            def body(i, b, k, last):
                q = per_buf[k]
                hold(pool, q["x_free"], i + 1, ph.passed)
                pool.dma_start(idx[k][:], d["slot_tok"][bass.ds((b + FIRST) * P, P), :]).then_inc(q["idx_ready"], 16)
                hold(pool, q["idx_ready"], i * 16 + 16, ph.passed)
                pool.indirect_dma_start(xg[k][:], None, d["f"], bass.IndirectOffsetOnAxis(ap=idx[k][:, 0:1], axis=0)).then_inc(q["x_ready"], 16)
            blocks(pool, body)

        @block.tensor
        def _(pe):
            pe.wait_ge(const_ready, 32)

            def turn_x(i, b, k):
                pe.wait_ge(per_buf[k]["x_ready"], i * 16 + 16)
                for c in range(KC):
                    mm = nc.tensor.transpose(p_t[c // 4][:, c % 4, :], xg[k][:, c * P:c * P + P], ident[:])
                mm.then_inc(s["x_turned"], 1)

            def gate(i, b, k):
                pe.wait_ge(s["x_copied"], b * 2 + 2)
                pe.sem_inc(per_buf[k]["x_free"], 1)
                pe.wait_ge(per_buf[k]["g_loaded"], i * 16 + 16)
                for c in range(KC):
                    mm = nc.tensor.matmul(p_g[:], xT[k][:, c, :], wg[k][:, c, :], start=(c == 0), stop=(c == KC - 1))
                mm.then_inc(s["g_ready"], 1)

            def up(i, b, k):
                pe.wait_ge(per_buf[k]["u_loaded"], i * 16 + 16)
                for c in range(KC):
                    mm = nc.tensor.matmul(p_u[:], xT[k][:, c, :], wu[k][:, c, :], start=(c == 0), stop=(c == KC - 1))
                mm.then_inc(s["u_ready"], 1)

            def turn_h(i, b, k):
                pe.wait_ge(s["h_ready"], b + 1)
                pe.sem_inc(per_buf[k]["g_free"], 1)
                pe.sem_inc(per_buf[k]["u_free"], 1)
                for c in range(4):
                    mm = nc.tensor.transpose(p_h[:, c, :], hb[:, c * P:c * P + P], ident[:])
                mm.then_inc(s["h_turned"], 1)

            def down(i, b, k):
                pe.wait_ge(s["h_copied"], b + 1)
                pe.wait_ge(s["y_free"], b + 1)
                pe.wait_ge(per_buf[k]["d_loaded"], i * 16 + 16)
                for n in range(2):
                    for c in range(4):
                        mm = nc.tensor.matmul(p_y[n][:], hT[:, c, :], wd[k][:, c, 512 * n:512 * n + 512], start=(c == 0), stop=(c == 3))
                mm.then_inc(s["y_done"], 1)

            def body(i, b, k, last):
                if overflow:
                    for part in (turn_x, gate, up, turn_h, down):
                        part(i, b, k)
                    return
                nxt = (i + k, b + 1, 1 - k)
                if not last:
                    turn_x(*nxt)
                turn_h(i, b, k)
                if not last:
                    gate(*nxt)
                down(i, b, k)
                if not last:
                    up(*nxt)

            if not overflow:
                for part in (turn_x, gate, up):
                    part(0, 0, 0)
            blocks(pe, body)

        @block.scalar
        def _(act):
            act.sem_inc(s["y_free"], 1)
            for k in range(NBUF):
                act.sem_inc(per_buf[k]["stored"], 16)

            def first(b, k):
                act.wait_ge(s["x_turned"], b + 1)
                nc.scalar.activation(xT[k][:, 4:8], p_t[1][:], ACT.Copy).then_inc(s["x_copied"], 1)

            def silu(b):
                act.wait_ge(s["g_ready"], b + 1)
                if not overflow:
                    act.wait_ge(s["h_ready"], b)
                nc.scalar.activation(act_g[:], p_g[:], ACT.Silu).then_inc(s["act_ready"], 1)

            def body(i, b, k, last):
                q = per_buf[k]
                if overflow:
                    first(b, k)
                    silu(b)
                elif not last:
                    first(b + 1, 1 - k)
                    silu(b + 1)
                act.wait_ge(s["y_done"], b + 1)
                act.sem_inc(q["d_free"], 1)
                act.wait_ge(q["stored"], i * 16 + 16)
                for n in range(2):
                    ins = nc.scalar.activation(y[k][:, 512 * n:512 * n + 512], p_y[n][:], ACT.Copy)
                ins.then_inc(q["y_ready"], 1)
                act.wait_ge(q["y_ready"], i + 1)
                act.sem_inc(s["y_free"], 1)
                act.dma_start(d["ypad"][bass.ds((b + FIRST) * P, P), :], y[k][:]).then_inc(q["stored"], 16)
                if overflow:
                    hold(act, q["stored"], i * 16 + 32, ph.passed)

            if not overflow:
                first(0, 0)
                act.wait_ge(s["g_ready"], 1)
                nc.scalar.activation(act_g[:], p_g[:], ACT.Silu).then_inc(s["act_ready"], 1)
            blocks(act, body)
            if not overflow:
                for k in range(NBUF):
                    act.wait_ge(per_buf[k]["stored"], 16 * N + 16)

        @block.vector
        def _(dve):
            def first(b, k):
                dve.wait_ge(s["x_turned"], b + 1)
                nc.vector.tensor_copy(xT[k][:, 0:4], p_t[0][:]).then_inc(s["x_copied"], 1)

            def product(b):
                dve.wait_ge(s["act_ready"], b + 1)
                dve.wait_ge(s["u_ready"], b + 1)
                nc.vector.tensor_tensor(hb[:], act_g[:], p_u[:], ALU.mult).then_inc(s["h_ready"], 1)

            def body(i, b, k, last):
                if overflow:
                    first(b, k)
                    product(b)
                elif not last:
                    first(b + 1, 1 - k)
                dve.wait_ge(s["h_turned"], b + 1)
                nc.vector.tensor_copy(hT[:], p_h[:]).then_inc(s["h_copied"], 1)
                if not overflow and not last:
                    product(b + 1)

            if not overflow:
                first(0, 0)
                product(0)
            blocks(dve, body)


def final_phase(nc, d):
    with Phase(nc, "fin") as ph:
        wg = ph.sb("wg", [P, KC, D_MODEL])
        wp = ph.sb("wp", [P, 2, D_MODEL])
        gain = ph.sb("gain", [P, D_MODEL])
        ident = ph.sb("ident", [P, P])
        eps = ph.sb("eps", [P, 1])
        gidx, wt = [ph.sb(f"gidx{b}", [P, 2], U32) for b in range(2)], [ph.sb(f"wt{b}", [P, 2]) for b in range(2)]
        h, y1, y2, pn = ([ph.sb(f"{n}{b}", [P, D_MODEL]) for b in range(2)] for n in ("h", "y1", "y2", "pn"))
        e, sq = ph.sb("e", [P, D_MODEL]), ph.sb("sq", [P, D_MODEL])
        pT = [ph.sb(f"pT{b}", [P, 2, P]) for b in range(2)]
        hT = [ph.sb(f"hT{b}", [P, KC, P]) for b in range(2)]
        ss, r = ph.sb("ss", [P, 2]), ph.sb("r", [P, 1])
        p_t = [ph.ps(f"p_t{i}", [P, 4, P]) for i in range(2)]
        p_g = [ph.ps(f"p_g{i}", [P, 512]) for i in range(2)]
        p_p = [ph.ps(f"p_p{i}", [P, 512]) for i in range(2)]
        names = ("const_ready", "setup", "h_ready", "h_turned", "h_copied", "g_ready", "p_ready", "pn_ready", "e_ready",
                 "sq_ready", "ss_ready", "ln_ready", "r_ready", "out_ready", "gated", "dve_step")
        s = {n: ph.sem(n) for n in names}
        in_free, idx_ready, in_ready, y_ready, stored = ([ph.sem(f"{n}{b}") for b in range(2)] for n in ("in_free", "idx_ready", "in_ready", "y_ready", "stored"))
        block = ph.enter_context(nc.Block())

        @block.sync
        def _(sp):
            for b in range(2):
                sp.sem_inc(in_free[b], 1)
            for dst, src in ((wp, "w_ple_proj"), (gain, "ple_norm"), (ident, "ident")):
                sp.dma_start(dst[:], d[src]).then_inc(s["const_ready"], 16)

            def load(t, n, b):
                tok = bass.ds(t * P, P)
                sp.wait_ge(in_free[b], n + 1)
                sp.dma_start(gidx[b][:], d["gidx"][tok, :]).then_inc(idx_ready[b], 16)
                sp.dma_start(wt[b][:], d["route"][tok, 64:66]).then_inc(in_ready[b], 16)
                sp.dma_start(h[b][:], d["h"][tok, :]).then_inc(in_ready[b], 16)
                sp.dma_start(pT[b][:], d["pT"][bass.ds(t, 1)].rearrange("o p c n -> (o p) c n")).then_inc(in_ready[b], 16)

            def body(t, n, b, first, last):
                if last < 2:
                    load(*after_tile(t, n, b))
                sp.wait_ge(s["out_ready"], t + 1)
                sp.dma_start(d["y"][bass.ds(t * P, P), :], pn[b][:]).then_inc(stored[b], 16)

            load(0, 0, 0)
            for k in range(KC):
                sp.dma_start(wg[:, k], d["w_ple_gate"][:, k]).then_inc(s["const_ready"], 16)
            tile_loop(sp, body)
            for b in range(2):
                sp.wait_ge(stored[b], 16 * ((TILES + 1 - b) // 2) + 16)

        @block.gpsimd
        def _(pool):
            def gather(t, n, b):
                hold(pool, idx_ready[b], n * 16 + 16, ph.passed)
                for k, dst in enumerate((y1[b], y2[b])):
                    pool.indirect_dma_start(dst[:], None, d["ypad"], bass.IndirectOffsetOnAxis(ap=gidx[b][:, k:k + 1], axis=0)).then_inc(y_ready[b], 16)

            tile_loop(pool, lambda t, n, b, first, last: gather(t, n, b))

        @block.tensor
        def _(pe):
            pe.wait_ge(s["const_ready"], 16 * (3 + KC))

            def prepare(t, n, b, first):
                pe.wait_ge(in_ready[b], n * 48 + 48)
                if not first:
                    pe.wait_ge(s["pn_ready"], t)
                for h2 in range(2):
                    for c in range(2):
                        mm = nc.tensor.matmul(p_p[h2][:], pT[b][:, c, :], wp[:, c, 512 * h2:512 * h2 + 512], start=(c == 0), stop=(c == 1))
                mm.then_inc(s["p_ready"], 1)
                pe.wait_ge(s["h_ready"], t + 1)
                if not first:
                    pe.wait_ge(s["h_copied"], t * 2)
                for c in range(KC):
                    mm = nc.tensor.transpose(p_t[c // 4][:, c % 4, :], h[b][:, c * P:c * P + P], ident[:])
                mm.then_inc(s["h_turned"], 1)

            def body(t, n, b, first, last):
                if last < 2:
                    prepare(*after_tile(t, n, b), False)
                pe.wait_ge(s["h_copied"], t * 2 + 2)
                if not first:
                    pe.wait_ge(s["e_ready"], t)
                for h2 in range(2):
                    for c in range(KC):
                        mm = nc.tensor.matmul(p_g[h2][:], hT[b][:, c, :], wg[:, c, 512 * h2:512 * h2 + 512], start=(c == 0), stop=(c == KC - 1))
                mm.then_inc(s["g_ready"], 1)

            prepare(0, 0, 0, True)
            tile_loop(pe, body)

        @block.scalar
        def _(act):
            act.wait_ge(s["setup"], 1)

            def prepare(t, n, b):
                act.wait_ge(s["p_ready"], t + 1)
                for h2 in range(2):
                    ins = nc.scalar.activation(sq[:, 512 * h2:512 * h2 + 512], p_p[h2][:], ACT.Square, accum_out=ss[:, h2:h2 + 1])
                ins.then_inc(s["sq_ready"], 1)
                act.wait_ge(s["ss_ready"], t + 1)
                nc.scalar.activation(ss[:, 0:1], ss[:, 0:1], ACT.Ln, bias=eps[:], scale=1.0 / D_MODEL).then_inc(s["ln_ready"], 1)
                act.wait_ge(s["ln_ready"], t + 1)
                nc.scalar.activation(r[:], ss[:, 0:1], ACT.Exp, scale=-0.5).then_inc(s["r_ready"], 1)
                act.wait_ge(s["h_turned"], t + 1)
                nc.scalar.activation(hT[b][:, 4:8], p_t[1][:], ACT.Copy).then_inc(s["h_copied"], 1)

            def body(t, n, b, first, last):
                if last < 2:
                    prepare(*after_tile(t, n, b))
                act.wait_ge(s["g_ready"], t + 1)
                if not first:
                    act.wait_ge(s["out_ready"], t)
                for h2 in range(2):
                    ins = nc.scalar.activation(e[:, 512 * h2:512 * h2 + 512], p_g[h2][:], ACT.Sigmoid)
                ins.then_inc(s["e_ready"], 1)

            prepare(0, 0, 0)
            tile_loop(act, body)

        @block.vector
        def _(dve):
            nc.vector.memset(eps[:], EPS).then_inc(s["setup"], 1)
            for b in range(2):
                dve.sem_inc(stored[b], 16)
            dve.wait_ge(s["const_ready"], 16 * (3 + KC))

            def prepare(t, n, b):
                dve.wait_ge(in_ready[b], n * 48 + 48)
                dve.wait_ge(y_ready[b], n * 32 + 32)
                link = Chain(dve, s["dve_step"], 1, t)
                link(nc.vector.scalar_tensor_tensor(h[b][:], y1[b][:], wt[b][:, 0:1], h[b][:], ALU.mult, ALU.add))
                nc.vector.scalar_tensor_tensor(h[b][:], y2[b][:], wt[b][:, 1:2], h[b][:], ALU.mult, ALU.add).then_inc(s["h_ready"], 1)
                dve.wait_ge(s["sq_ready"], t + 1)
                nc.vector.tensor_tensor(ss[:, 0:1], ss[:, 0:1], ss[:, 1:2], ALU.add).then_inc(s["ss_ready"], 1)
                dve.wait_ge(s["h_turned"], t + 1)
                nc.vector.tensor_copy(hT[b][:, 0:4], p_t[0][:]).then_inc(s["h_copied"], 1)
                dve.wait_ge(s["r_ready"], t + 1)
                dve.wait_ge(stored[b], n * 16 + 16)
                for h2 in range(2):
                    c = slice(512 * h2, 512 * h2 + 512)
                    ins = nc.vector.scalar_tensor_tensor(pn[b][:, c], p_p[h2][:], r[:], gain[:, c], ALU.mult, ALU.mult)
                ins.then_inc(s["pn_ready"], 1)

            def body(t, n, b, first, last):
                if last < 2:
                    prepare(*after_tile(t, n, b))
                dve.wait_ge(s["e_ready"], t + 1)
                dve.wait_ge(s["pn_ready"], t + 1)
                mul = nc.vector.tensor_tensor(pn[b][:], pn[b][:], e[:], ALU.mult)
                mul.then_inc(s["gated"], 1)
                dve.wait_ge(s["gated"], t + 1)
                nc.vector.tensor_tensor(pn[b][:], pn[b][:], h[b][:], ALU.add).then_inc(s["out_ready"], 1)
                dve.wait_ge(s["out_ready"], t + 1)
                dve.sem_inc(in_free[b], 1)

            prepare(0, 0, 0)
            tile_loop(dve, body)



def _pool(cache):
    n = cache.shape[0]
    ops = cache[:, :, 0:2].reshape(n, 8, 8, 2, 2, KVH, HD)
    ops = ops.transpose(0, 3, 6, 4, 2, 5, 1).reshape(n, P, 256)
    keys = cache[:, :, 2].reshape(n, P, P).transpose(0, 2, 1)
    return np.concatenate([ops, keys, cache[:, :, 3].reshape(n, P, P)], 2)


def _layout(inputs):
    f = {k: np.asarray(v) for k, v in inputs.items()}
    pad = np.zeros((TOK - SEQ - N_SMP, D_MODEL), np.float32)
    x = np.concatenate([f["x_prompt"][0], f["x_sample"].reshape(N_SMP, D_MODEL), pad])
    pos = np.concatenate([np.arange(SEQ), PAST + np.arange(P) % DEC_SEQ]).astype(np.float32)
    half = HD // 2
    inv = np.float32(10000.0) ** (-np.arange(half, dtype=np.float32) / half)
    ang = (pos[:, None] * inv[None, :]).astype(np.float32)
    trig = np.stack([np.cos(ang), np.sin(ang)], 1).reshape(TILES, P, 2, half).astype(np.float32)
    w_in = f["w_in"][0].copy()
    w_in[:, :ATT_W] = w_in[:, :ATT_W].reshape(D_MODEL, KVH, HPG, HD).transpose(0, 2, 1, 3).reshape(D_MODEL, ATT_W)
    w_in[:, C_GL:C_Z] = w_in[:, C_GL:C_Z].reshape(D_MODEL, KVH, HPG, 3).transpose(0, 2, 1, 3).reshape(D_MODEL, 24)
    gains = np.concatenate([f["q_norm"][0][None], f["k_norm"][0]])
    tok = np.arange(P)
    seq = tok // DEC_SEQ
    same = np.stack([np.ones((P, P)), seq[:, None] == seq[None]], 1).astype(np.float32)
    tri = (same * (tok[:, None] <= tok[None])[:, None]).astype(np.float32)
    seqcol = (seq[:, None] == np.arange(DEC_BATCH)[None]).astype(np.float32)
    ends = np.arange(N_CMP_P) * S_CMP + L_CMP - 1
    w1 = f["cmp_w1"][0].reshape(2, 2, S_CMP, HD, HD)
    rg, rq = np.arange(64) // 32, np.arange(64) % DEC_SEQ
    gsum = ((rg[:, None] == rg[None]) & (rq[:, None] == rq[None])).astype(np.float32)
    nmask = np.where(np.arange(DEC_SEQ)[None] <= rq[:, None], 0, NEG).astype(np.float32)
    key = np.arange(WINDOW + DEC_SEQ)[None]
    wmask = np.where((key > rq[:, None]) & (key <= rq[:, None] + WINDOW), 0, NEG).astype(np.float32)
    c0, s0 = np.arange(2 * P)[:, None] * S_CMP, np.arange(N_SLC_S)[None] * L_SLC
    cover = np.maximum(np.minimum(c0 + L_CMP, s0 + L_SLC) - np.maximum(c0, s0), 0).astype(np.float32) / np.float32(L_CMP)
    cover = cover.reshape(2, P, N_SLC_S).transpose(1, 0, 2)
    cw = f["cache_win"][0].reshape(DEC_BATCH, WINDOW, 2, P)
    p_all = np.concatenate([f["p_prompt"][0, 0], f["p_sample"][0].reshape(N_SMP, PLE), np.zeros((TOK - SEQ - N_SMP, PLE), np.float32)])
    padoff = np.zeros((P, TILES, 2), np.float32)
    padoff[N_SMP:, NT, :] = DUMP + np.arange(2 * (P - N_SMP)).reshape(-1, 2)
    cm = {
        "xT": x.reshape(TILES, P, KC, P).transpose(0, 3, 2, 1),
        "trig": trig,
        "w_in": w_in.reshape(KC, P, C_END).transpose(1, 0, 2),
        "attn_norm": f["attn_norm"][0].reshape(KC, P).T,
        "head_gain": np.broadcast_to(gains, (P, 4, HD)),
        "ident": np.eye(P, dtype=np.float32),
        "cmp_w1_sd": np.tile(w1.transpose(3, 0, 2, 1, 4), (2, 1, 1, 1, 1)).reshape(P, 2, S_CMP, P),
        "cmp_pe": f["cmp_pe"][0].reshape(2, 2, S_CMP, HD).transpose(3, 0, 1, 2),
        "cmp_w2": f["cmp_w2"][0].transpose(1, 0, 2),
        "diag": np.where(tok[None] > tok[:, None], NEG, 0).astype(np.float32),
        "old": np.where(tok[None] <= tok[:, None], NEG, 0).astype(np.float32),
        "cmask": np.where(ends[None, None] <= (np.arange(NT)[None] * P + tok[:, None])[..., None], 0, NEG).astype(np.float32),
        "valid": (tok[:, None] >= L_CMP - 1).astype(np.float32),
        "cmp_w1_seg": w1.reshape(2, 2, 8, 2, HD, HD).transpose(3, 4, 0, 2, 1, 5).reshape(P, 2, 8, P),
        "cover": cover, "gsum": gsum, "nmask": nmask, "wmask": wmask,
        "page_table": f["page_table"],
        "pool": _pool(f["cache_kv"][0]),
        "win_pack": np.concatenate([cw[:, :, 0].transpose(0, 2, 1), cw[:, :, 1].reshape(DEC_BATCH, 4, P, P).transpose(0, 2, 1, 3).reshape(DEC_BATCH, P, 512)], 2),
        "cache_win": cw.reshape(DEC_BATCH, WINDOW, 256),
        "x": x,
        "w_out": np.concatenate([f["w_out"][0][:ATT_W].reshape(KVH, HPG, HD, D_MODEL).transpose(1, 0, 2, 3).reshape(ATT_W, D_MODEL), f["w_out"][0][ATT_W:]])
                   .reshape(KC, P, D_MODEL).transpose(1, 0, 2),
        "w_route": np.concatenate([f["w_rg"][0], f["w_re"][0]], 1).reshape(KC, P, 36).transpose(1, 0, 2),
        "b_route": np.broadcast_to(np.concatenate([f["b_rg"][0], f["b_re"][0]]), (P, 36)),
        "ffn_norm": np.broadcast_to(f["ffn_norm"][0], (P, D_MODEL)),
        "real": (tok < N_SMP).astype(np.float32)[:, None],
        "before": (tok[:, None] < tok[None]).astype(np.float32),
        "first": np.broadcast_to(np.arange(NE, dtype=np.float32) * P, (P, NE)),
        "padoff": padoff, "ids": np.arange(TOK, dtype=np.uint32).reshape(TILES, P).T,
        "blocks": np.broadcast_to(np.arange(OVER_BLOCKS, dtype=np.float32), (P, OVER_BLOCKS)),
        "w_gate": f["w_gate"][0], "w_up": f["w_up"][0], "w_down": f["w_down"][0],
        "w_ple_gate": f["w_ple_gate"][0].reshape(KC, P, D_MODEL).transpose(1, 0, 2),
        "w_ple_proj": f["w_ple_proj"][0].reshape(2, P, D_MODEL).transpose(1, 0, 2),
        "ple_norm": np.broadcast_to(f["ple_norm"][0], (P, D_MODEL)),
        "pT": p_all.reshape(TILES, P, 2, P).transpose(0, 3, 2, 1),
        "conv_w": f["conv_w"][0].T.reshape(6, P, CONV_W).transpose(1, 0, 2),
        "conv_b": f["conv_b"][0].reshape(6, P).T,
        "state_conv": f["state_conv"][0].transpose(2, 0, 1).reshape(6, P, DEC_BATCH, 3).transpose(1, 0, 2, 3),
        "tri": tri, "mask": np.where(tri > 0, 0, NEG).astype(np.float32), "same": same,
        "seqcol": seqcol, "seqrow": np.broadcast_to(seqcol.T, (P, DEC_BATCH, P)),
        "head_ssm": np.broadcast_to(np.stack([f["dt_bias"][0], f["a_log"][0], f["ssm_d"][0]]), (P, 3, SH)),
        "ssm_norm": np.broadcast_to(f["ssm_norm"][0], (P, D_INNER)),
        "state_ssm": f["state_ssm"][0].reshape(DEC_BATCH, 2, 4, HD, SN).transpose(1, 4, 0, 2, 3).reshape(P, DEC_BATCH, 256),
    }
    return {k: np.ascontiguousarray(v) for k, v in cm.items()}


_SCRATCH = {"z": (TOK, D_INNER), "gdt": (TOK, 32), "xbc": (P, 6, TOK), "turned": (P, 12, TOK),             "cv": (P, 6, TOK), "ssd": (TOK, 512), "pe_hid": (HD, 2), "kct": (P, N_CMP_P), "vc": (N_CMP_P, P), "attn": (TOK, 512),
            "h": (TOK, D_MODEL), "f": (TOK, D_MODEL), "route": (TOK, 66), "slot_tok": (SLOTS, 1, U32), "gidx": (TOK, 2, U32),
            "over": (1, OVER_BLOCKS + 1, I32), "ypad": (DUMP, D_MODEL)}
_OUTS = {"y": (TOK, D_MODEL), "win_new": (TOK, 256), "win_old": (DEC_BATCH, WINDOW - DEC_SEQ, 256), "kv_out": (TOK, 512), "conv_p": (P, 6, 3), "conv_s": (P, 6, DEC_BATCH, 3), "ssm_p": (P, 256), "ssm_s": (P, DEC_BATCH, 256)}


def build(nc, d):
    project_phase(nc, d)
    conv_phase(nc, d)
    ssd_phase(nc, d)
    compress_prompt(nc, d)
    attend_prompt(nc, d)
    attend_samples(nc, d, d["pool"].shape[0])
    mix_phase(nc, d)
    dispatch_phase(nc, d)
    expert_phase(nc, d, False)
    expert_phase(nc, d, True)
    final_phase(nc, d)


def kernel(**inputs):
    import concourse.bacc as _bacc
    from concourse.bass_utils import run_bass_kernel_spmd as _run

    nc = _bacc.Bacc("TRN2", target_bir_lowering=False, num_devices=1)
    arrays, d = {}, {}
    for name, a in _layout(inputs).items():
        arrays[f"in_{name}"] = a
        d[name] = nc.dram_tensor(f"in_{name}", a.shape, mybir.dt.from_np(a.dtype), kind="ExternalInput").ap()
    for kind, tensors in (("Internal", _SCRATCH), ("ExternalOutput", _OUTS)):
        for name, shape in tensors.items():
            dt = F32 if isinstance(shape[-1], int) else shape[-1]
            shape = [n for n in shape if isinstance(n, int)]
            prefix = "scratch" if kind == "Internal" else "out"
            d[name] = nc.dram_tensor(f"{prefix}_{name}", shape, dt, kind=kind).ap()
    build(nc, d)
    r = _run(nc, [arrays], core_ids=[0])
    got = {k: np.asarray(r.results[0][f"out_{k}"]) for k in _OUTS}
    y, kv, win = got["y"], got["kv_out"], got["win_new"]
    smp = slice(SEQ, SEQ + N_SMP)
    win_s = np.concatenate([got["win_old"], win[smp].reshape(DEC_BATCH, DEC_SEQ, 256)], 1)
    ssm_p = got["ssm_p"].reshape(KVH, SN, HPG, HD).transpose(0, 2, 3, 1)
    ssm_s = got["ssm_s"].reshape(KVH, SN, DEC_BATCH, HPG, HD).transpose(2, 0, 3, 4, 1)
    return (y[:SEQ].reshape(1, SEQ, D_MODEL), y[smp].reshape(DEC_BATCH, DEC_SEQ, D_MODEL),
            kv[:SEQ].reshape(1, 1, SEQ, 4, KVH, HD), kv[smp].reshape(1, DEC_BATCH, DEC_SEQ, 4, KVH, HD),
            win[SEQ - WINDOW:SEQ].reshape(1, 1, WINDOW, 2, KVH, HD), win_s.reshape(1, DEC_BATCH, WINDOW, 2, KVH, HD),
            ssm_p.reshape(1, 1, SH, HD, SN), ssm_s.reshape(1, DEC_BATCH, SH, HD, SN),
            got["conv_p"].transpose(2, 1, 0).reshape(1, 1, CONV_W - 1, CONV_DIM), got["conv_s"].transpose(2, 3, 1, 0).reshape(1, DEC_BATCH, CONV_W - 1, CONV_DIM))
```

```python
from contextlib import ExitStack

import numpy as np

import concourse.bass as bass
from concourse import mybir

ALU = mybir.AluOpType
ACT = mybir.ActivationFunctionType
F32 = mybir.dt.float32
I32 = mybir.dt.int32
U32 = mybir.dt.uint32
AX = mybir.AxisListType.X
P = 128

D_MODEL, SEQ, DEC_BATCH, DEC_SEQ, PAST, PAGE = 1024, 1024, 8, 8, 4096, 128
HEADS, HD, KVH = 8, 64, 2
HPG = HEADS // KVH
ATT_W = HEADS * HD
L_CMP, S_CMP, L_SLC, N_SEL, WINDOW = 32, 16, 64, 16, 512
SH, SN, D_INNER = 8, 64, 512
CONV_DIM, CONV_W = 768, 4
NG, EPG, NE = 4, 8, 32
D_EXP = 512
PLE = 256
EPS = 1e-6
KC = D_MODEL // P
NT = SEQ // P
TILES = NT + 1
TOK = TILES * P
N_SMP = DEC_BATCH * DEC_SEQ
N_PAGES = PAST // PAGE
N_CMP_P = (SEQ - L_CMP) // S_CMP + 1
N_SEG_S = PAST // S_CMP
N_CMP_S = (PAST + DEC_SEQ - L_CMP) // S_CMP + 1
N_SLC_S = -(-(PAST + DEC_SEQ) // L_SLC)
SCALE = HD ** -0.5
NEG = -1e30
C_KV, C_GL, C_Z, C_XBC, C_DT, C_END = 512, 1280, 1304, 1816, 2584, 2592
QKV = 20 * HD
MAIN_BLOCKS = NE
OVER_BLOCKS = 2 * (SEQ + N_SMP) // P - 1
DUMP = (MAIN_BLOCKS + OVER_BLOCKS) * P
SLOTS = DUMP + 2 * P


class Chain:

    def __init__(self, eng, sem, per=0, i=None):
        self.eng, self.sem, self.per, self.i, self.k = eng, sem, per, i, 0

    def __call__(self, ins, passed=None):
        self.k += 1
        ins.then_inc(self.sem, 1)
        base = self.k if self.i is None else self.i * self.per + self.k
        self.eng.wait_ge(self.sem, base)
        if passed is not None:
            self.eng.sem_inc(passed, 1)

    def close(self):
        assert self.k == self.per, (self.k, self.per)


def hold(eng, sem, value, passed):
    eng.wait_ge(sem, value)
    eng.sem_inc(passed, 1)


class Phase(ExitStack):

    def __init__(self, nc, name):
        super().__init__()
        self.nc, self.name, self.own = nc, name, []
        self.passed = self.sem("passed")
        self.callback(self.release)

    def release(self):
        self.nc.clear_and_free_semaphores(self.own)
        self.nc.all_engine_barrier()

    def sb(self, name, shape, dt=F32):
        return self.enter_context(self.nc.sbuf_tensor(f"{self.name}_{name}", shape, dt))

    def ps(self, name, shape):
        return self.enter_context(self.nc.psum_tensor(f"{self.name}_{name}", shape, F32))

    def sem(self, name):
        self.own.append(self.nc.alloc_semaphore(name=f"{self.name}_{name}"))
        return self.own[-1]


def project_phase(nc, d):
    CH = CONV_DIM // P
    with Phase(nc, "proj") as ph:
        w = ph.sb("w", [P, KC, C_END])
        x = ph.sb("x", [P, KC, P])
        sq = ph.sb("sq", [P, KC, P])
        a = ph.sb("a", [P, KC, P])
        lnv = ph.sb("lnv", [P, P])
        rinv = ph.sb("rinv", [P, P])
        gain = ph.sb("gain", [P, KC])
        qkv = ph.sb("qkv", [P, QKV])
        qkv_sq = ph.sb("qkv_sq", [P, QKV])
        qrot = ph.sb("qrot", [P, ATT_W])
        krot = ph.sb("krot", [P, 2, 2, HD])
        tmp = ph.sb("tmp", [P, HEADS, HD // 2])
        ss = ph.sb("ss", [P, 20])
        hr = ph.sb("hr", [P, 20])
        hgain = ph.sb("hgain", [P, 4, HD])
        trig = ph.sb("trig", [P, 2, HD // 2])
        gdt = ph.sb("gdt", [P, 32])
        z = ph.sb("z", [P, D_INNER])
        raw = ph.sb("raw", [P, CH, 3 + P])
        raw_s = ph.sb("raw_s", [P, CH, P // DEC_SEQ, 3 + DEC_SEQ])
        acc = ph.sb("acc", [P, CH, P])
        conv = ph.sb("conv", [P, CH, P])
        cw = ph.sb("cw", [P, CH, CONV_W])
        cb = ph.sb("cb", [P, CH])
        turned = ph.sb("turned", [P, 12, P])
        ones = ph.sb("ones", [P, P])
        ident = ph.sb("ident", [P, P])
        eps = ph.sb("eps", [P, 1])
        p_q, p_kv, p_kw = ph.ps("p_q", [P, 512]), ph.ps("p_kv", [P, 512]), ph.ps("p_kw", [P, 512])
        p_z, p_x0, p_x1 = ph.ps("p_z", [P, 512]), ph.ps("p_x0", [P, 3, P]), ph.ps("p_x1", [P, 3, P])
        p_ss, p_turn = ph.ps("p_ss", [P, 512]), ph.ps("p_turn", [P, 512])

        const_ready, gain_ready = ph.sem("const_ready"), ph.sem("gain_ready")
        x_ready, x_free = ph.sem("x_ready"), ph.sem("x_free")
        trig_ready, trig_free = ph.sem("trig_ready"), ph.sem("trig_free")
        sq_ready, ss_ready, ln_ready, rinv_ready = ph.sem("sq_ready"), ph.sem("ss_ready"), ph.sem("ln_ready"), ph.sem("rinv_ready")
        a_ready, proj_ready = ph.sem("a_ready"), ph.sem("proj_ready")
        qkv_ready, z_ready = ph.sem("qkv_ready"), ph.sem("z_ready")
        hss_ready, hln_ready, hr_ready, rot_ready = ph.sem("hss_ready"), ph.sem("hln_ready"), ph.sem("hr_ready"), ph.sem("rot_ready")
        turn_ready, turned_ready, dve_step = ph.sem("turn_ready"), ph.sem("turned_ready"), ph.sem("dve_step")
        state_zeroed, state_ready, acc_ready, conv_ready = ph.sem("state_zeroed"), ph.sem("state_ready"), ph.sem("acc_ready"), ph.sem("conv_ready")
        conv_step, conv_free, conv_stored, state_stored = ph.sem("conv_step"), ph.sem("conv_free"), ph.sem("conv_stored"), ph.sem("state_stored")
        z_stored, kv_stored, turned_stored = ph.sem("z_stored"), ph.sem("kv_stored"), ph.sem("turned_stored")
        W_BLOCKS = ((0, 512), (512, 1024), (1024, C_Z), (C_DT, C_END), (C_Z, C_XBC), (C_XBC, C_DT))
        w_ready = [ph.sem(f"w{i}_ready") for i in range(len(W_BLOCKS))]

        block = ph.enter_context(nc.Block())

        def tiles(eng, tile):
            tile(0, True, False)
            with eng.Fori(1, TILES - 1) as t:
                tile(t, False, False)
            tile(TILES - 1, False, True)

        @block.sync
        def _(sp):
            sp.sem_inc(x_free, 2)
            sp.sem_inc(trig_free, 1)
            sp.sem_inc(conv_free, 1)
            sp.dma_start(x[:], d["xT"][0]).then_inc(x_ready, 16)
            sp.dma_start(gain[:], d["attn_norm"]).then_inc(gain_ready, 16)
            for i, (c0, c1) in enumerate(W_BLOCKS):
                sp.dma_start(w[:, :, c0:c1], d["w_in"][:, :, c0:c1]).then_inc(w_ready[i], 16)
                if i == 0:
                    sp.dma_start(hgain[:], d["head_gain"]).then_inc(const_ready, 16)
                    sp.dma_start(ident[:], d["ident"]).then_inc(const_ready, 16)
                    sp.dma_start(trig[:], d["trig"][0]).then_inc(trig_ready, 16)
            sp.dma_start(cw[:], d["conv_w"]).then_inc(state_ready, 16)
            sp.dma_start(cb[:], d["conv_b"]).then_inc(state_ready, 16)
            sp.wait_ge(state_zeroed, 1)
            for c in range(CH):
                sp.dma_start(raw_s[:, c, 0:DEC_BATCH, 0:3], d["state_conv"][:, c]).then_inc(state_ready, 16)
            with sp.Fori(1, TILES) as t:
                sp.wait_ge(x_free, t * 2 + 2)
                sp.dma_start(x[:], d["xT"][bass.ds(t, 1)].rearrange("o p c n -> (o p) c n")).then_inc(x_ready, 16)
                sp.wait_ge(trig_free, t + 1)
                sp.dma_start(trig[:], d["trig"][bass.ds(t, 1)].rearrange("o p c n -> (o p) c n")).then_inc(trig_ready, 16)
            sp.wait_ge(z_ready, TILES * 3)
            sp.dma_start(d["conv_p"], raw[:, :, P:P + 3]).then_inc(state_stored, 16)
            for c in range(CH):
                sp.dma_start(d["conv_s"][:, c], raw_s[:, c, 0:DEC_BATCH, DEC_SEQ:DEC_SEQ + 3]).then_inc(state_stored, 16)
            sp.wait_ge(state_stored, 16 * (CH + 1))

        @block.gpsimd
        def _(pool):
            with pool.Fori(0, TILES) as t:
                tok = bass.ds(t * P, P)
                hold(pool, rot_ready, t + 1, ph.passed)
                pool.dma_start(d["kv_out"][tok, 0:256], qkv[:, 512:768]).then_inc(kv_stored, 16)
                pool.dma_start(d["kv_out"][tok, 256:384], krot[:, 0]).then_inc(kv_stored, 16)
                pool.dma_start(d["kv_out"][tok, 384:512], qkv[:, 896:1024]).then_inc(kv_stored, 16)
                pool.dma_start(d["win_new"][tok, 0:128], krot[:, 1]).then_inc(kv_stored, 16)
                pool.dma_start(d["win_new"][tok, 128:256], qkv[:, 1152:1280]).then_inc(kv_stored, 16)
                hold(pool, z_ready, t * 3 + 3, ph.passed)
                pool.dma_start(d["z"][tok, :], z[:]).then_inc(z_stored, 16)
                pool.dma_start(d["gdt"][tok, :], gdt[:]).then_inc(z_stored, 16)
                hold(pool, turned_ready, t * 3 + 3, ph.passed)
                pool.dma_start(d["turned"][:, :, tok], turned[:]).then_inc(turned_stored, 16)
                hold(pool, conv_ready, t + 1, ph.passed)
                pool.dma_start(d["cv"][:, :, tok], conv[:]).then_inc(conv_stored, 16)
                hold(pool, conv_stored, t * 16 + 16, conv_free)
            pool.wait_ge(kv_stored, TILES * 80)
            pool.wait_ge(z_stored, TILES * 32)
            pool.wait_ge(conv_stored, TILES * 16)
            pool.wait_ge(turned_stored, TILES * 16)

        @block.scalar
        def _(act):
            act.wait_ge(gain_ready, 17)

            def square(t):
                act.wait_ge(x_ready, t * 16 + 16)
                nc.scalar.activation(sq[:], x[:], ACT.Square).then_inc(sq_ready, 1)
                act.wait_ge(sq_ready, t + 1)
                act.sem_inc(x_free, 1)

            def rms(t):
                act.wait_ge(ss_ready, t + 1)
                nc.scalar.activation(lnv[:], p_ss[:, 0:P], ACT.Ln, bias=eps[:], scale=1.0 / D_MODEL).then_inc(ln_ready, 1)
                act.wait_ge(ln_ready, t + 1)
                nc.scalar.activation(rinv[:], lnv[:], ACT.Exp, scale=-0.5).then_inc(rinv_ready, 1)

            def silu(t):
                act.wait_ge(acc_ready, t + 1)
                act.wait_ge(conv_free, t + 1)
                nc.scalar.activation(conv[:], acc[:], ACT.Silu).then_inc(conv_ready, 1)

            def tile(t, first, last):
                if not last:
                    act.wait_ge(ss_ready, t + 1)
                    square(t + 1)
                if not first:
                    act.wait_ge(kv_stored, t * 80)
                    act.wait_ge(turn_ready, t * 3)
                act.wait_ge(proj_ready, t * 6 + 1)
                nc.scalar.activation(qkv[:, 0:512], p_q[:], ACT.Copy)
                act.wait_ge(proj_ready, t * 6 + 2)
                nc.scalar.activation(qkv[:, 512:1024], p_kv[:], ACT.Copy)
                act.wait_ge(proj_ready, t * 6 + 3)
                nc.scalar.activation(qkv[:, 1024:1280], p_kw[:, 0:256], ACT.Copy)
                if not first:
                    act.wait_ge(z_stored, t * 32)
                nc.scalar.activation(gdt[:], p_kw[:, 256:288], ACT.Copy).then_inc(qkv_ready, 1)
                act.wait_ge(hss_ready, t + 1)
                nc.scalar.activation(ss[:], ss[:], ACT.Ln, bias=eps[:], scale=1.0 / HD).then_inc(hln_ready, 1)
                act.wait_ge(hln_ready, t + 1)
                nc.scalar.activation(hr[:], ss[:], ACT.Exp, scale=-0.5).then_inc(hr_ready, 1)
                if not last:
                    rms(t + 1)
                if not first:
                    silu(t - 1)
                    act.wait_ge(turned_stored, t * 16)
                act.wait_ge(turn_ready, t * 3 + 2)
                nc.scalar.activation(turned[:, 4:8, :], p_z[:].rearrange("p (a b) -> p a b", a=4), ACT.Copy, scale=SCALE).then_inc(turned_ready, 1)
                act.wait_ge(turn_ready, t * 3 + 3)
                nc.scalar.activation(turned[:, 8:12, :], p_kw[:].rearrange("p (a b) -> p a b", a=4), ACT.Copy).then_inc(turned_ready, 1)

            square(0)
            rms(0)
            tiles(act, tile)
            silu(TILES - 1)

        @block.vector
        def _(dve):
            nc.vector.memset(ones[:], 1.0)
            nc.vector.memset(eps[:], EPS).then_inc(gain_ready, 1)
            nc.vector.memset(raw[:, :, 0:3], 0.0)
            nc.vector.memset(raw_s[:], 0.0).then_inc(state_zeroed, 1)
            dve.wait_ge(state_zeroed, 1)
            dve.wait_ge(gain_ready, 17)
            dve.wait_ge(const_ready, 32)

            def normed(t):
                dve.wait_ge(rinv_ready, t + 1)
                dve.wait_ge(x_ready, t * 16 + 16)
                for k in range(KC):
                    ins = nc.vector.scalar_tensor_tensor(a[:, k, :], x[:, k, :], gain[:, k:k + 1], rinv[:], ALU.mult, ALU.mult)
                ins.then_inc(a_ready, 1)
                dve.wait_ge(a_ready, t + 1)
                dve.sem_inc(x_free, 1)

            def fresh(smp, i):
                return raw_s[:, 3 * i:3 * i + 3, :, 3:] if smp else raw[:, 3 * i:3 * i + 3, 3:]

            def bank_view(bank, smp):
                return bank[:].rearrange("p c (b l) -> p c b l", l=DEC_SEQ) if smp else bank[:]

            def convolve(t, first, smp):
                link = Chain(dve, conv_step, CONV_W, t)
                dve.wait_ge(z_ready, t * 3 + 3)
                if first or smp:
                    dve.wait_ge(state_ready, 16 * (CH + 2))
                if not first:
                    dve.wait_ge(conv_ready, t)
                for j in range(CONV_W):
                    for c in range(CH):
                        w = cw[:, c, j:j + 1]
                        src = raw_s[:, c, :, j:j + DEC_SEQ] if smp else raw[:, c, j:j + P]
                        dst = acc[:, c].rearrange("p (b l) -> p b l", l=DEC_SEQ) if smp else acc[:, c]
                        if j == 0:
                            ins = nc.vector.tensor_scalar(dst, src, w, cb[:, c:c + 1], ALU.mult, ALU.add)
                        else:
                            ins = nc.vector.scalar_tensor_tensor(dst, src, w, dst, ALU.mult, ALU.add)
                    if j < CONV_W - 1:
                        link(ins)
                ins.then_inc(acc_ready, 1)
                if not smp:
                    dve.wait_ge(acc_ready, t + 1)
                    link(nc.vector.tensor_copy(raw[:, :, 0:3], raw[:, :, P:P + 3]))
                    link.close()

            def tile(t, first, last):
                link = Chain(dve, dve_step, 20, t)
                dve.wait_ge(qkv_ready, t + 1)
                link(nc.vector.tensor_tensor(qkv_sq[:], qkv[:], qkv[:], ALU.mult))
                nc.vector.reduce_sum(ss[:], qkv_sq[:].rearrange("p (h e) -> p h e", e=HD), AX).then_inc(hss_ready, 1)
                dve.wait_ge(hr_ready, t + 1)
                q3 = qkv[:, 0:512].rearrange("p (h e) -> p h e", e=HD)
                link(nc.vector.tensor_tensor(q3, q3, hr[:, 0:8].unsqueeze(2).broadcast_to([P, 8, HD]), ALU.mult))
                link(nc.vector.tensor_tensor(q3, q3, hgain[:, 0:1, :].broadcast_to([P, 8, HD]), ALU.mult))
                for b in range(3):
                    k3 = qkv[:, 512 + 256 * b:640 + 256 * b].rearrange("p (h e) -> p h e", e=HD)
                    link(nc.vector.tensor_tensor(k3, k3, hr[:, 8 + 4 * b:10 + 4 * b].unsqueeze(2).broadcast_to([P, 2, HD]), ALU.mult))
                    link(nc.vector.tensor_tensor(k3, k3, hgain[:, 1 + b:2 + b, :].broadcast_to([P, 2, HD]), ALU.mult))
                dve.wait_ge(trig_ready, t * 16 + 16)
                if not first:
                    dve.wait_ge(kv_stored, t * 80)
                    dve.wait_ge(turn_ready, t * 3)
                sets = [(q3, qrot[:].rearrange("p (h e) -> p h e", e=HD), 8)]
                sets += [(qkv[:, 768 + 256 * b:896 + 256 * b].rearrange("p (h e) -> p h e", e=HD), krot[:, b], 2) for b in range(2)]
                H2 = HD // 2
                for src, dst, n in sets:
                    cos = trig[:, 0:1, :].broadcast_to([P, n, H2])
                    sin = trig[:, 1:2, :].broadcast_to([P, n, H2])
                    x1, x2, t2 = src[:, :, 0:H2], src[:, :, H2:HD], tmp[:, 0:n, :]
                    nc.vector.tensor_tensor(dst[:, :, 0:H2], x1, cos, ALU.mult)
                    link(nc.vector.tensor_tensor(t2, x2, sin, ALU.mult))
                    link(nc.vector.tensor_tensor(dst[:, :, 0:H2], dst[:, :, 0:H2], t2, ALU.subtract))
                    nc.vector.tensor_tensor(dst[:, :, H2:HD], x2, cos, ALU.mult)
                    link(nc.vector.tensor_tensor(t2, x1, sin, ALU.mult))
                    last_of = nc.vector.tensor_tensor(dst[:, :, H2:HD], dst[:, :, H2:HD], t2, ALU.add)
                    if n == 2 and dst is not sets[1][1]:
                        last_of.then_inc(rot_ready, 1)
                    else:
                        link(last_of)
                dve.wait_ge(rot_ready, t + 1)
                dve.sem_inc(trig_free, 1)
                if not first:
                    dve.wait_ge(z_stored, t * 32)
                dve.wait_ge(proj_ready, t * 6 + 4)
                nc.vector.tensor_copy(z[:], p_z[:]).then_inc(z_ready, 1)
                dve.wait_ge(proj_ready, t * 6 + 5)
                nc.vector.tensor_copy(fresh(last, 0), bank_view(p_x0, last)).then_inc(z_ready, 1)
                dve.wait_ge(proj_ready, t * 6 + 6)
                if not last:
                    normed(t + 1)
                nc.vector.tensor_copy(fresh(last, 1), bank_view(p_x1, last)).then_inc(z_ready, 1)
                if not first:
                    dve.wait_ge(turned_stored, t * 16)
                dve.wait_ge(turn_ready, t * 3 + 1)
                nc.vector.tensor_scalar(turned[:, 0:4, :], p_turn[:].rearrange("p (a b) -> p a b", a=4), SCALE, None, ALU.mult).then_inc(turned_ready, 1)
                link.close()
                convolve(t, first, last)

            normed(0)
            tiles(dve, tile)

        @block.tensor
        def _(pe):
            pe.wait_ge(gain_ready, 17)

            def squares(t):
                pe.wait_ge(sq_ready, t + 1)
                for k in range(KC):
                    mm = nc.tensor.matmul(p_ss[:, 0:P], ones[:], sq[:, k, :], start=(k == 0), stop=(k == KC - 1))
                mm.then_inc(ss_ready, 1)

            def tile(t, first, last):
                def rows(dst, i):
                    c0, c1 = W_BLOCKS[i]
                    if first:
                        pe.wait_ge(w_ready[i], 16)
                    for k in range(KC):
                        mm = nc.tensor.matmul(dst, a[:, k, :], w[:, k, c0:c1], start=(k == 0), stop=(k == KC - 1))
                    return mm

                pe.wait_ge(a_ready, t + 1)
                rows(p_q[:], 0).then_inc(proj_ready, 1)
                rows(p_kv[:], 1).then_inc(proj_ready, 1)
                if not first:
                    pe.wait_ge(turned_ready, t * 3)
                rows(p_kw[:, 0:280], 2)
                rows(p_kw[:, 280:288], 3).then_inc(proj_ready, 1)
                if not last:
                    squares(t + 1)
                rows(p_z[:], 4).then_inc(proj_ready, 1)
                if first:
                    pe.wait_ge(w_ready[5], 16)
                else:
                    pe.wait_ge(z_ready, t * 3)
                for c in range(6):
                    dst = (p_x0, p_x1)[c // 3][:, c % 3, :]
                    for k in range(KC):
                        mm = nc.tensor.matmul(dst, w[:, k, C_XBC + c * P:C_XBC + c * P + P], a[:, k, :], start=(k == 0), stop=(k == KC - 1))
                    if c % 3 == 2:
                        mm.then_inc(proj_ready, 1)
                if first:
                    pe.wait_ge(const_ready, 32)
                pe.wait_ge(rot_ready, t + 1)
                pe.wait_ge(z_ready, t * 3 + 1)
                for bank, src in ((p_turn, qkv), (p_z, qrot)):
                    for j in range(HPG):
                        mm = nc.tensor.transpose(bank[:, j * P:(j + 1) * P], src[:, j * P:(j + 1) * P], ident[:])
                    mm.then_inc(turn_ready, 1)
                for j, src in enumerate((qkv[:, 512:640], qkv[:, 640:768], krot[:, 0].rearrange("p h e -> p (h e)"), krot[:, 1].rearrange("p h e -> p (h e)"))):
                    mm = nc.tensor.transpose(p_kw[:, j * P:(j + 1) * P], src, ident[:])
                mm.then_inc(turn_ready, 1)

            squares(0)
            tiles(pe, tile)


def ssd_phase(nc, d):
    NB = DEC_BATCH
    A, DT, ACUM, EIN, EOUT, ETOT = range(6)
    with Phase(nc, "ssd") as ph:
        cv = [ph.sb(f"cv{u}", [P, 6, P]) for u in range(2)]
        z = ph.sb("z", [P, TILES, D_INNER])
        y = ph.sb("y", [P, TILES, D_INNER])
        gdt = ph.sb("gdt", [P, TILES, 32])
        tri = ph.sb("tri", [P, 2, P])
        mask = ph.sb("mask", [P, 2, P])
        same = ph.sb("same", [P, 2, P])
        seqcol = ph.sb("seqcol", [P, NB])
        seqrow = ph.sb("seqrow", [P, NB, P])
        hb = ph.sb("hb", [P, 3, SH])
        gnorm = ph.sb("gnorm", [P, D_INNER])
        ident = ph.sb("ident", [P, P])
        eps = ph.sb("eps", [P, 1])
        ah = ph.sb("ah", [P, SH])
        xd, ax, ex, uu, lnu, m1, tot, wd = (ph.sb(n, [P, TILES, SH]) for n in ("xd", "ax", "ex", "uu", "lnu", "m1", "tot", "wd"))
        steps_all = ph.sb("steps_all", [P, 6, TILES, SH])
        cur = [ph.sb(f"cur{u}", [P, 6, SH]) for u in range(2)]
        xs, xsd, xdt, xw = ([ph.sb(f"{n}{u}", [P, D_INNER]) for u in range(2)] for n in ("xs", "xsd", "xdt", "xw"))
        btok = [ph.sb(f"btok{u}", [P, P]) for u in range(2)]
        m = [ph.sb(f"decay{u}", [P, SH, P]) for u in range(2)]
        t2, sq = ph.sb("t2", [P, D_INNER]), ph.sb("sq", [P, D_INNER])
        st = ph.sb("st", [P, 256])
        sst = ph.sb("sst", [P, NB, 256])
        cm = ph.sb("cm", [P, NB, P])
        bm = ph.sb("bm", [P, NB, P])
        am = ph.sb("am", [P, NB, SH])
        et = ph.sb("et", [P, NB, SH])
        ss, rr, rcur = ph.sb("ss", [P, TILES]), ph.sb("rr", [P, TILES]), ph.sb("rcur", [P, 1])
        p_x, p_b, p_y, p_yo, p_c1, p_st = (ph.ps(n, [P, 512]) for n in ("p_x", "p_b", "p_y", "p_yo", "p_c1", "p_st"))
        p_d = [ph.ps(f"p_d{i}", [P, 4, P]) for i in range(2)]
        p_cb = (p_b[:, P:2 * P], p_c1[:, 0:P])
        p_cs = (p_yo[:, 0:256], p_c1[:, 256:512])

        names = ("const_ready", "setup", "gdt_ready", "z_ready", "zs_ready", "cv0_ready", "cv1_ready", "prep", "ah_ready", "ex_ready", "lnu_ready",
                 "a_ready", "sums_ready", "wd_ready", "edec_ready", "cur_ready", "turned", "diff_ready", "xs_ready", "xsd_ready", "dm_ready", "dexp_ready",
                 "m_ready", "rows_ready", "state_ready", "y_summed", "y_ready", "sq_ready", "ln_ready", "rr_ready", "out_ready", "stored", "cur_step", "row_step",
                 "smp_step", "out_step", "sstate_loaded", "masked", "et_sum", "et_ready", "sst_ready", "sst_done", "states_stored")
        s = {n: ph.sem(n) for n in names}
        block = ph.enter_context(nc.Block())

        def steps(eng, step):
            step(0, 0, 1, True, False)
            with eng.Fori(0, NT // 2 - 1) as i:
                for u in (1, 2):
                    step(i * 2 + u, u % 2, i * 2 + (u + 1), False, False)
            step(NT - 1, 1, NT, False, True)

        def h3(ap):
            return ap.rearrange("p (h e) -> p h e", e=HD)

        def over(ap, n=HD):
            return ap.unsqueeze(2).broadcast_to([ap.shape[0], ap.shape[1], n])

        @block.sync
        def _(sp):
            sp.dma_start(gdt[:], d["gdt"].rearrange("(t p) c -> p t c", p=P)).then_inc(s["gdt_ready"], 16)
            for dst, src in ((hb, "head_ssm"), (tri, "tri"), (same, "same"), (ident, "ident"), (mask, "mask")):
                sp.dma_start(dst[:], d[src]).then_inc(s["const_ready"], 16)
            sp.dma_start(cv[0][:], d["cv"][:, :, 0:P]).then_inc(s["cv0_ready"], 16)
            sp.dma_start(z[:], d["z"].rearrange("(t p) c -> p t c", p=P)).then_inc(s["z_ready"], 16)
            sp.dma_start(cv[1][:], d["cv"][:, :, P:2 * P]).then_inc(s["cv1_ready"], 16)
            for dst, src in ((seqcol, "seqcol"), (seqrow, "seqrow"), (gnorm, "ssm_norm"), (sst, "state_ssm")):
                sp.dma_start(dst[:], d[src]).then_inc(s["sstate_loaded"], 16)

            def channels(c, u):
                sp.wait_ge(s["rows_ready"], c - 1)
                sp.dma_start(cv[u][:], d["cv"][:, :, bass.ds(c * P, P)]).then_inc(s[f"cv{u}_ready"], 16)

            with sp.Fori(0, NT // 2 - 1) as i:
                for u in range(2):
                    channels(i * 2 + (u + 2), u)
            channels(NT, 0)
            sp.wait_ge(s["state_ready"], NT)
            sp.dma_start(d["ssm_p"], st[:]).then_inc(s["states_stored"], 16)
            sp.wait_ge(s["sst_done"], 1)
            sp.dma_start(d["ssm_s"], sst[:]).then_inc(s["states_stored"], 16)
            with sp.Fori(0, TILES) as t:
                sp.wait_ge(s["out_ready"], t + 1)
                sp.dma_start(d["ssd"][bass.ds(t * P, P), :], y[:, bass.ds(t, 1), :].rearrange("p o n -> p (o n)")).then_inc(s["stored"], 16)
            sp.wait_ge(s["stored"], 16 * TILES)
            sp.wait_ge(s["states_stored"], 32)

        @block.gpsimd
        def _(pool):
            pool.wait_ge(s["const_ready"], 80)

            def skip(c, u, first=False):
                pool.wait_ge(s["xs_ready"], c + 1)
                if not first:
                    pool.wait_ge(s["y_ready"], c - 1)
                nc.gpsimd.tensor_tensor(h3(xsd[u][:]), h3(xs[u][:]), over(hb[:, 2, :]), ALU.mult).then_inc(s["xsd_ready"], 1)

            skip(0, 0, True)
            skip(1, 1, True)
            with pool.Fori(0, NT // 2 - 1) as i:
                for u in range(2):
                    skip(i * 2 + (u + 2), u)
            skip(NT, 0)

        @block.scalar
        def _(act):
            act.wait_ge(s["const_ready"], 80)
            act.wait_ge(s["setup"], 2)
            nc.scalar.activation(ah[:], hb[:, 1, :], ACT.Exp).then_inc(s["ah_ready"], 1)
            act.wait_ge(s["prep"], 2)
            nc.scalar.activation(ex[:], ax[:], ACT.Exp, scale=-1.0).then_inc(s["ex_ready"], 1)
            act.wait_ge(s["prep"], 3)
            nc.scalar.activation(lnu[:], uu[:], ACT.Ln).then_inc(s["lnu_ready"], 1)
            act.wait_ge(s["z_ready"], 16)
            nc.scalar.activation(z[:], z[:], ACT.Silu).then_inc(s["zs_ready"], 1)
            act.wait_ge(s["wd_ready"], 1)
            nc.scalar.activation(steps_all[:, EIN], steps_all[:, ACUM], ACT.Exp)
            nc.scalar.activation(steps_all[:, EOUT], wd[:], ACT.Exp)
            nc.scalar.activation(steps_all[:, ETOT], tot[:], ACT.Exp).then_inc(s["edec_ready"], 1)

            def prepare(c, u, first=False):
                act.wait_ge(s["turned"], c + 1)
                if not first:
                    act.wait_ge(s["xsd_ready"], c - 1)
                nc.scalar.activation(xs[u][:], p_x[:], ACT.Copy).then_inc(s["xs_ready"], 1)
                act.wait_ge(s["dm_ready"], c + 1)
                nc.scalar.activation(m[u][:], m[u][:], ACT.Exp).then_inc(s["dexp_ready"], 1)

            def square(c):
                act.wait_ge(s["y_ready"], c + 1)
                nc.scalar.activation(sq[:], y[:, bass.ds(c, 1), :].rearrange("p o n -> p (o n)"), ACT.Square, accum_out=ss[:, bass.ds(c, 1)]).then_inc(s["sq_ready"], 1)
                act.wait_ge(s["sq_ready"], c + 1)

            def step(c, u, n, first, smp):
                prepare(n, 1 - u, first)
                square(c)

            prepare(0, 0, True)
            steps(act, step)
            act.wait_ge(s["et_sum"], 1)
            nc.scalar.activation(et[:], p_st[:, 256:256 + NB * SH].rearrange("p (b h) -> p b h", h=SH), ACT.Exp).then_inc(s["et_ready"], 1)
            square(NT)
            nc.scalar.activation(rr[:], ss[:], ACT.Ln, bias=eps[:], scale=1.0 / D_INNER).then_inc(s["ln_ready"], 1)
            act.wait_ge(s["ln_ready"], 1)
            nc.scalar.activation(rr[:], rr[:], ACT.Exp, scale=-0.5).then_inc(s["rr_ready"], 1)

        @block.vector
        def _(dve):
            nc.vector.memset(eps[:], EPS).then_inc(s["setup"], 1)
            nc.vector.memset(st[:], 0.0).then_inc(s["setup"], 1)
            dve.wait_ge(s["setup"], 2)
            dve.wait_ge(s["const_ready"], 80)
            dve.wait_ge(s["gdt_ready"], 16)
            link = Chain(dve, s["prep"])
            dt, a, acum = (steps_all[:, i] for i in (DT, A, ACUM))
            link(nc.vector.tensor_tensor(xd[:], gdt[:, :, 24:32], hb[:, 0:1, :].broadcast_to([P, TILES, SH]), ALU.add))
            link(nc.vector.scalar_tensor_tensor(ax[:], xd[:], -1.0, xd[:], ALU.mult, ALU.max))
            dve.wait_ge(s["ex_ready"], 1)
            link(nc.vector.tensor_scalar(uu[:], ex[:], 1.0, None, ALU.add))
            link(nc.vector.tensor_scalar(m1[:], uu[:], 1.0, None, ALU.is_equal))
            link(nc.vector.scalar_tensor_tensor(dt, uu[:], 1.0, m1[:], ALU.subtract, ALU.add))
            link(nc.vector.reciprocal(dt, dt))
            link(nc.vector.tensor_tensor(dt, dt, ex[:], ALU.mult))
            dve.wait_ge(s["lnu_ready"], 1)
            link(nc.vector.tensor_tensor(m1[:], m1[:], lnu[:], ALU.add))
            link(nc.vector.tensor_tensor(dt, dt, m1[:], ALU.mult))
            link(nc.vector.scalar_tensor_tensor(dt, xd[:], 0.0, dt, ALU.max, ALU.add))
            dve.wait_ge(s["ah_ready"], 1)
            nc.vector.scalar_tensor_tensor(a, ah[:].unsqueeze(1).broadcast_to([P, TILES, SH]), -1.0, dt, ALU.mult, ALU.mult).then_inc(s["a_ready"], 1)
            dve.wait_ge(s["sums_ready"], 1)
            nc.vector.tensor_copy(acum, p_y[:, 0:TILES * SH].rearrange("p (t h) -> p t h", h=SH))
            link(nc.vector.tensor_copy(tot[:], p_y[:, TILES * SH:2 * TILES * SH].rearrange("p (t h) -> p t h", h=SH)))
            nc.vector.tensor_tensor(wd[:], tot[:], acum, ALU.subtract).then_inc(s["wd_ready"], 1)
            dve.wait_ge(s["edec_ready"], 1)

            def prepare(c, u, smp, link):
                nc.vector.tensor_copy(cur[u][:], steps_all[:, :, bass.ds(c, 1), :].rearrange("p k o h -> p k (o h)")).then_inc(s["cur_ready"], 1)
                dve.wait_ge(s["cur_ready"], c + 1)
                dve.wait_ge(s["turned"], c + 1)
                nc.vector.tensor_copy(btok[u][:], p_b[:, 0:P])
                dve.wait_ge(s["xs_ready"], c + 1)
                link(nc.vector.tensor_tensor(h3(xdt[u][:]), h3(xs[u][:]), over(cur[u][:, DT]), ALU.mult))
                nc.vector.tensor_tensor(h3(xw[u][:]), h3(xdt[u][:]), over(cur[u][:, EOUT]), ALU.mult)
                dve.wait_ge(s["diff_ready"], c + 1)
                for h in range(SH):
                    ins = nc.vector.scalar_tensor_tensor(m[u][:, h, :], p_d[h // 4][:, h % 4, :], cur[u][:, ACUM, h:h + 1], mask[:, int(smp), :], ALU.subtract, ALU.add)
                ins.then_inc(s["dm_ready"], 1)

            def decays(c, u):
                dve.wait_ge(s["dexp_ready"], c + 1)
                for g in range(2):
                    mg = m[u][:, 4 * g:4 * g + 4, :]
                    ins = nc.vector.tensor_tensor(mg, mg, p_cb[g].unsqueeze(1).broadcast_to([P, 4, P]), ALU.mult)
                ins.then_inc(s["m_ready"], 1)

            def state(c, u, link):
                dve.wait_ge(s["rows_ready"], c + 1)
                for g in range(2):
                    sg = h3(st[64 * g:64 * g + 64, :])
                    ins = nc.vector.tensor_tensor(sg, sg, over(cur[u][64 * g:64 * g + 64, ETOT, 4 * g:4 * g + 4]), ALU.mult)
                link(ins)
                nc.vector.tensor_tensor(st[:], st[:], p_st[:, 0:256], ALU.add).then_inc(s["state_ready"], 1)

            def rows(c, u, link):
                for g in range(2):
                    ins = nc.vector.tensor_tensor(h3(t2[:, 256 * g:256 * g + 256]), h3(p_cs[g]), over(cur[u][:, EIN, 4 * g:4 * g + 4]), ALU.mult)
                link(ins)
                nc.vector.tensor_tensor(t2[:], t2[:], p_y[:], ALU.add).then_inc(s["y_summed"], 1)

            def gated(c, u, link):
                dve.wait_ge(s["xsd_ready"], c + 1)
                dve.wait_ge(s["y_summed"], c + 1)
                link(nc.vector.tensor_tensor(t2[:], t2[:], xsd[u][:], ALU.add))
                nc.vector.tensor_tensor(y[:, bass.ds(c, 1), :].rearrange("p o n -> p (o n)"), t2[:], z[:, bass.ds(c, 1), :].rearrange("p o n -> p (o n)"), ALU.mult).then_inc(s["y_ready"], 1)
                dve.wait_ge(s["y_ready"], c + 1)

            def step(c, u, n, first, smp):
                link = Chain(dve, s["row_step"], 3, c)
                more = Chain(dve, s["cur_step"], 1, n)
                prepare(n, 1 - u, smp, more)
                state(c, u, link)
                rows(c, u, link)
                decays(n, 1 - u)
                gated(c, u, link)
                link.close()
                more.close()

            prepare(0, 0, False, Chain(dve, s["cur_step"], 1, 0))
            decays(0, 0)
            dve.wait_ge(s["zs_ready"], 1)
            steps(dve, step)
            link = Chain(dve, s["smp_step"])
            dve.wait_ge(s["sstate_loaded"], 64)
            link(nc.vector.tensor_tensor(cm[:], seqrow[:], cv[0][:, 5:6, :].broadcast_to([P, NB, P]), ALU.mult))
            nc.vector.tensor_tensor(bm[:], seqcol[:].unsqueeze(2).broadcast_to([P, NB, P]), btok[0][:].unsqueeze(1).broadcast_to([P, NB, P]), ALU.mult)
            nc.vector.tensor_tensor(am[:], seqcol[:].unsqueeze(2).broadcast_to([P, NB, SH]), cur[0][:, A].unsqueeze(1).broadcast_to([P, NB, SH]), ALU.mult).then_inc(s["masked"], 1)
            dve.wait_ge(s["rows_ready"], TILES)
            rows(NT, 0, link)
            gated(NT, 0, link)
            dve.wait_ge(s["et_ready"], 1)
            for g in range(2):
                sg = sst[64 * g:64 * g + 64].rearrange("p b (h e) -> p b h e", e=HD)
                ins = nc.vector.tensor_tensor(sg, sg, et[64 * g:64 * g + 64, :, 4 * g:4 * g + 4].unsqueeze(3).broadcast_to([64, NB, 4, HD]), ALU.mult)
            link(ins)
            for q in range(4):
                dve.wait_ge(s["sst_ready"], q + 1)
                bank = (p_x, p_b, p_d[0], p_d[1])[q]
                flat = bank[:] if q < 2 else bank[:].rearrange("p a b -> p (a b)")
                ins = nc.vector.tensor_tensor(sst[:, 2 * q:2 * q + 2, :], sst[:, 2 * q:2 * q + 2, :], flat.rearrange("p (b n) -> p b n", b=2), ALU.add)
            ins.then_inc(s["sst_done"], 1)
            dve.wait_ge(s["rr_ready"], 1)
            with dve.Fori(0, TILES) as t:
                link = Chain(dve, s["out_step"], 1, t)
                link(nc.vector.tensor_copy(rcur[:], rr[:, bass.ds(t, 1)]))
                yt = y[:, bass.ds(t, 1), :].rearrange("p o n -> p (o n)")
                nc.vector.scalar_tensor_tensor(yt, yt, rcur[:], gnorm[:], ALU.mult, ALU.mult).then_inc(s["out_ready"], 1)
                dve.wait_ge(s["out_ready"], t + 1)

        @block.tensor
        def _(pe):
            pe.wait_ge(s["const_ready"], 80)
            pe.wait_ge(s["setup"], 2)
            pe.wait_ge(s["a_ready"], 1)
            for i, w in enumerate((tri, same)):
                base = i * TILES * SH
                nc.tensor.matmul(p_y[:, base:base + NT * SH], w[:, 0, :], steps_all[:, A, 0:NT, :].rearrange("p t h -> p (t h)"), start=True, stop=True)
                mm = nc.tensor.matmul(p_y[:, base + NT * SH:base + TILES * SH], w[:, 1, :], steps_all[:, A, NT, :], start=True, stop=True)
            mm.then_inc(s["sums_ready"], 1)

            def prepare(c, u, smp, first=False):
                if not first:
                    pe.wait_ge(s["xs_ready"], c)
                    pe.wait_ge(s["m_ready"], c)
                pe.wait_ge(s[f"cv{u}_ready"], c * 8 + (16 - 8 * u))
                for i in range(4):
                    nc.tensor.transpose(p_x[:, i * P:(i + 1) * P], cv[u][:, i, :], ident[:])
                nc.tensor.transpose(p_b[:, 0:P], cv[u][:, 4, :], ident[:])
                for g in range(2):
                    mm = nc.tensor.matmul(p_cb[g], cv[u][64 * g:64 * g + 64, 4, :], cv[u][64 * g:64 * g + 64, 5, :], start=True, stop=True)
                mm.then_inc(s["turned"], 1)
                pe.wait_ge(s["cur_ready"], c + 1)
                for h in range(SH):
                    mm = nc.tensor.matmul(p_d[h // 4][:, h % 4, :], cur[u][:, A, h:h + 1].broadcast_to([P, P]), tri[:, int(smp), :], start=True, stop=True)
                mm.then_inc(s["diff_ready"], 1)

            def within(c, u, first):
                pe.wait_ge(s["m_ready"], c + 1)
                if not first:
                    pe.wait_ge(s["y_summed"], c)
                for h in range(SH):
                    nc.tensor.matmul(p_y[:, 64 * h:64 * h + 64], m[u][:, h, :], xdt[u][:, 64 * h:64 * h + 64], start=True, stop=True)

            def step(c, u, n, first, smp):
                prepare(n, 1 - u, smp)
                within(c, u, first)
                if not first:
                    pe.wait_ge(s["state_ready"], c)
                for g in range(2):
                    nc.tensor.matmul(p_cs[g], cv[u][64 * g:64 * g + 64, 5, :], st[64 * g:64 * g + 64, :], start=True, stop=True)
                for g in range(2):
                    mm = nc.tensor.matmul(p_st[64 * g:64 * g + 64, 0:256], btok[u][:, 64 * g:64 * g + 64], xw[u][:, 256 * g:256 * g + 256], start=True, stop=True)
                mm.then_inc(s["rows_ready"], 1)

            prepare(0, 0, False, True)
            steps(pe, step)
            within(NT, 0, False)
            pe.wait_ge(s["masked"], 1)
            pe.wait_ge(s["state_ready"], NT)
            for g in range(2):
                for b in range(NB):
                    mm = nc.tensor.matmul(p_cs[g], cm[64 * g:64 * g + 64, b, :], sst[64 * g:64 * g + 64, b, :], start=(b == 0), stop=(b == NB - 1))
            mm.then_inc(s["rows_ready"], 1)
            nc.tensor.matmul(p_st[:, 256:256 + NB * SH], same[:, 0, :], am[:].rearrange("p b h -> p (b h)"), start=True, stop=True).then_inc(s["et_sum"], 1)
            pe.wait_ge(s["xs_ready"], TILES)
            for q in range(4):
                bank = (p_x, p_b, p_d[0], p_d[1])[q]
                flat = bank[:] if q < 2 else bank[:].rearrange("p a b -> p (a b)")
                for b in (2 * q, 2 * q + 1):
                    for g in range(2):
                        mm = nc.tensor.matmul(flat[64 * g:64 * g + 64, 256 * (b % 2):256 * (b % 2) + 256], bm[:, b, 64 * g:64 * g + 64], xw[0][:, 256 * g:256 * g + 256], start=True, stop=True)
                mm.then_inc(s["sst_ready"], 1)


def compress_prompt(nc, d):
    NS, NC, C = SEQ // S_CMP, N_CMP_P, S_CMP // 2
    N = KVH * NS
    with Phase(nc, "cmp") as ph:
        kv = ph.sb("kv", [P, 2, SEQ])
        ops = ph.sb("ops", [P, 2, C, N + 2])
        w1 = ph.sb("w1", [P, 2, C, P])
        pe_t = ph.sb("pe", [P, 2, C, 2])
        w2 = ph.sb("w2", [HD, 2, HD])
        pe_hid = ph.sb("pe_hid", [HD, 2])
        late = ph.sb("late", [HD, 2, N + 2])
        hid = ph.sb("hid", [HD, 2, 2, NC])
        kct = ph.sb("kct", [P, NC])
        vc = ph.sb("vc", [NC, P])
        p_h = [ph.ps(f"p_h{slot}", [P, N + 2]) for slot in range(2)]
        p_k, p_v = ph.ps("p_k", [P, NC]), ph.ps("p_v", [NC, P])
        kv_ready, const_ready, ops_ready, hid_ready = ph.sem("kv_ready"), ph.sem("const_ready"), ph.sem("ops_ready"), ph.sem("hid_ready")
        late_ready, sum_ready, act_ready, out_ready = ph.sem("late_ready"), ph.sem("sum_ready"), ph.sem("act_ready"), ph.sem("out_ready")
        pe_ready, evac, stored = ph.sem("pe_ready"), ph.sem("evac"), ph.sem("stored")
        block = ph.enter_context(nc.Block())

        @block.sync
        def _(sp):
            sp.dma_start(kv[:], d["turned"][:, 8:10, 0:SEQ]).then_inc(kv_ready, 16)
            sp.dma_start(pe_t[:], d["cmp_pe"]).then_inc(const_ready, 16)
            sp.dma_start(w1[:], d["cmp_w1_seg"]).then_inc(const_ready, 16)
            sp.dma_start(w2[:], d["cmp_w2"]).then_inc(const_ready, 16)
            sp.wait_ge(pe_ready, 1)
            sp.dma_start(d["pe_hid"], pe_hid[:]).then_inc(stored, 16)
            sp.wait_ge(evac, 2)
            sp.dma_start(d["kct"], kct[:]).then_inc(stored, 16)
            sp.dma_start(d["vc"], vc[:]).then_inc(stored, 16)
            sp.wait_ge(stored, 48)

        def pairs(op, g):
            seg = kv[64 * g:64 * g + 64].rearrange("p k (n c s) -> p k c n s", c=C, s=2)
            for s2 in range(2):
                ins = op(ops[64 * s2:64 * s2 + 64, :, :, NS * g:NS * g + NS], seg[:, :, :, :, s2])
            return ins

        @block.tensor
        def _(pe):
            pe.wait_ge(const_ready, 48)
            pe.wait_ge(ops_ready, 2)
            for slot in range(2):
                for c in range(C):
                    mm = nc.tensor.matmul(p_h[slot][:], w1[:, slot, c, :], ops[:, slot, c, :], start=(c == 0), stop=(c == C - 1))
            mm.then_inc(hid_ready, 1)
            pe.wait_ge(act_ready, 1)
            for g in range(2):
                nc.tensor.matmul(p_k[64 * g:64 * g + 64, :], w2[:, 0, :], hid[:, 0, g, :], start=True, stop=True)
                mm = nc.tensor.matmul(p_v[:, 64 * g:64 * g + 64], hid[:, 1, g, :], w2[:, 1, :], start=True, stop=True)
            mm.then_inc(out_ready, 1)

        @block.scalar
        def _(act):
            act.wait_ge(kv_ready, 16)
            pairs(lambda dst, src: nc.scalar.activation(dst, src, ACT.Copy), 1).then_inc(ops_ready, 1)
            act.wait_ge(hid_ready, 1)
            for slot in range(2):
                ins = nc.scalar.activation(late[:, slot], p_h[slot][64:128], ACT.Copy)
            ins.then_inc(late_ready, 1)
            act.wait_ge(sum_ready, 1)
            for slot in range(2):
                ins = nc.scalar.activation(hid[:, slot], hid[:, slot], ACT.Silu, bias=pe_hid[:, slot:slot + 1])
            ins.then_inc(act_ready, 1)

        @block.vector
        def _(dve):
            dve.wait_ge(kv_ready, 16)
            pairs(nc.vector.tensor_copy, 0)
            dve.wait_ge(const_ready, 48)
            nc.vector.tensor_copy(ops[:, :, :, N:N + 2], pe_t[:]).then_inc(ops_ready, 1)
            dve.wait_ge(late_ready, 1)
            for slot in range(2):
                ins = nc.vector.tensor_tensor(pe_hid[:, slot:slot + 1], p_h[slot][0:HD, N:N + 1], late[:, slot, N + 1:N + 2], ALU.add)
            ins.then_inc(pe_ready, 1)
            for slot in range(2):
                ins = nc.vector.tensor_tensor(hid[:, slot], p_h[slot][0:HD, 0:N].rearrange("p (g n) -> p g n", g=2)[:, :, 0:NC],
                                              late[:, slot, 0:N].rearrange("p (g n) -> p g n", g=2)[:, :, 1:NS], ALU.add)
            ins.then_inc(sum_ready, 1)
            dve.wait_ge(out_ready, 1)
            nc.vector.tensor_copy(kct[:], p_k[:]).then_inc(evac, 1)
            nc.vector.tensor_copy(vc[:], p_v[:]).then_inc(evac, 1)


def attend_prompt(nc, d):
    assert SEQ // L_SLC <= N_SEL and WINDOW % P == 0
    NC = N_CMP_P
    WT = WINDOW // P
    CMP, SLC, WIN = range(3)
    units = [(qt, g, br, 0 if br != WIN else max(0, qt - WT), {CMP: 0, SLC: qt + 1, WIN: min(qt, WT) + 1}[br])
             for qt in range(NT) for g in range(2) for br in range(3)]
    NU = len(units)
    groups = []
    for u, (qt, g, br, k0, kn) in enumerate(units):
        groups += [(u, t, min(4, max(kn, 1) - t)) for t in range(0, max(kn, 1), 4)]
    of_unit = [[i for i, gr in enumerate(groups) if gr[0] == u] for u in range(NU)]
    AHEAD = 4
    HEAD = AHEAD
    per_bank = [len(groups) - len(groups) // 2, len(groups) // 2]
    with Phase(nc, "att") as ph:
        q = ph.sb("q", [P, 2, SEQ])
        kk = ph.sb("kk", [P, 2, SEQ])
        v = ph.sb("v", [P, 2, NT, P])
        kct = ph.sb("kct", [P, NC])
        vc = ph.sb("vc", [NC, P])
        all_gates = ph.sb("all_gates", [P, NT, 3 * HEADS])
        gates = ph.sb("gates", [P, NT, 6])
        diag = ph.sb("diag", [P, P])
        old = ph.sb("old", [P, P])
        cmask = ph.sb("cmask", [P, NT, NC])
        valid = ph.sb("valid", [P, 1])
        ident = ph.sb("ident", [P, P])
        prob = [ph.sb(f"prob{i}", [P, SEQ]) for i in range(AHEAD)]
        pt = [ph.sb(f"pt{i}", [P, 4, P]) for i in range(2)]
        nb, l, rg = (ph.sb(n, [P, AHEAD]) for n in ("nb", "l", "rg"))
        o = ph.sb("o", [P, NT, P])
        p_s = [ph.ps(f"p_s{i}", [P, SEQ]) for i in range(2)]
        p_t = [ph.ps(f"p_t{i}", [P, 4, P]) for i in range(2)]
        p_o = [ph.ps(f"p_o{i}", [P, 512]) for i in range(2)]
        const_ready, gates_ready = ph.sem("const_ready"), ph.sem("gates_ready")
        q_ready = [ph.sem(f"q_ready{i}") for i in range(2)]
        s_ready, nb_ready, p_ready, o_ready, o_done = (ph.sem(n) for n in ("s_ready", "nb_ready", "p_ready", "o_ready", "o_done"))
        t_ready = [ph.sem(f"t_ready{i}") for i in range(2)]
        t_done = [ph.sem(f"t_done{i}") for i in range(2)]
        zero = ph.sb("zero", [P, D_MODEL])
        rows_zeroed, rows_stored = ph.sem("rows_zeroed"), ph.sem("rows_stored")
        g_exp, o_stored, dve_step = ph.sem("g_exp"), ph.sem("o_stored"), ph.sem("dve_step")
        block = ph.enter_context(nc.Block())

        def unit(it, u, back=0):
            return it * NU + (u - back + 1 + HEAD)

        def group(it, i, back=0):
            return it * per_bank[i % 2] + (i // 2 - back + 1 + 1)

        @block.sync
        def _(sp):
            for s in (o_done, p_ready):
                sp.sem_inc(s, HEAD)
            for s in t_done:
                sp.sem_inc(s, 1)
            sp.sem_inc(o_stored, 16)

            def queries(j, half):
                c = slice(half * SEQ // 2, (half + 1) * SEQ // 2)
                for kind in range(2):
                    sp.dma_start(q[:, kind, c], d["turned"][:, bass.ds(j + kind * HPG, 1), c].rearrange("p o n -> p (o n)")).then_inc(q_ready[half], 16)

            def store(j):
                sp.wait_ge(o_done, unit(j, NU - 1))
                sp.dma_start(d["attn"][0:SEQ, bass.ds(j * P, P)].rearrange("(t p) n -> p t n", p=P), o[:]).then_inc(o_stored, 16)

            sp.dma_start(all_gates[:], d["gdt"][0:SEQ, 0:3 * HEADS].rearrange("(t p) n -> p t n", p=P)).then_inc(gates_ready, 16)
            queries(0, 0)
            for dst, src in ((kct[:], d["kct"]), (cmask[:], d["cmask"]), (ident[:], d["ident"]), (vc[:], d["vc"]), (diag[:], d["diag"]), (old[:], d["old"]),
                             (valid[:], d["valid"]), (kk[:], d["turned"][:, 10:12, 0:SEQ]),
                             (v[:, 0], d["kv_out"][0:SEQ, 384:512].rearrange("(t p) n -> p t n", p=P)),
                             (v[:, 1], d["win_new"][0:SEQ, 128:256].rearrange("(t p) n -> p t n", p=P))):
                sp.dma_start(dst, src).then_inc(const_ready, 16)
            queries(0, 1)
            sp.wait_ge(rows_zeroed, 1)
            sp.dma_start(d["attn"][SEQ + N_SMP:TOK, :], zero[0:TOK - SEQ - N_SMP, 0:ATT_W]).then_inc(rows_stored, 16)
            for n in range(OVER_BLOCKS):
                sp.dma_start(d["ypad"][(MAIN_BLOCKS + n) * P:(MAIN_BLOCKS + n + 1) * P, :], zero[:]).then_inc(rows_stored, 16)
            with sp.Fori(0, HPG - 1) as j:
                sp.wait_ge(p_ready, unit(j, NU // 2 - 1))
                queries(j + 1, 0)
                sp.wait_ge(p_ready, unit(j, NU - 1))
                queries(j + 1, 1)
                store(j)
            store(HPG - 1)
            sp.wait_ge(o_stored, 16 * HPG + 16)
            sp.wait_ge(rows_stored, 16 * (OVER_BLOCKS + 1))

        @block.tensor
        def _(pe):
            pe.wait_ge(const_ready, 160)

            def scores(it, u):
                qt, g, br, k0, kn = units[u]
                pe.wait_ge(p_ready, unit(it, u, 2))
                rows = slice(64 * g, 64 * g + 64)
                lhs = q[rows, 0 if br == CMP else 1, qt * P:qt * P + P]
                if br == CMP:
                    mm = nc.tensor.matmul(p_s[u % 2][:, 0:NC], lhs, kct[rows, :], start=True, stop=True)
                else:
                    n = kn * P
                    for c in range(0, n, 512):
                        w = min(512, n - c)
                        mm = nc.tensor.matmul(p_s[u % 2][:, c:c + w], lhs, kk[rows, br - 1, k0 * P + c:k0 * P + c + w], start=True, stop=True)
                mm.then_inc(s_ready, 1)

            def turn(it, i):
                u, t0, n = groups[i]
                br = units[u][2]
                hold(pe, t_done[i % 2], group(it, i, 1), ph.passed)
                for t in range(n):
                    if br == CMP:
                        mm = nc.tensor.transpose(p_t[i % 2][0:NC, 0, :], prob[u % AHEAD][:, 0:NC], ident[:])
                    else:
                        mm = nc.tensor.transpose(p_t[i % 2][:, t, :], prob[u % AHEAD][:, (t0 + t) * P:(t0 + t + 1) * P], ident[:])
                mm.then_inc(t_ready[i % 2], 1)

            def values(it, i):
                u, t0, n = groups[i]
                qt, g, br, k0, kn = units[u]
                pe.wait_ge(t_done[i % 2], group(it, i))
                if t0 == 0:
                    pe.wait_ge(o_done, unit(it, u, 2))
                for t in range(n):
                    if br == CMP:
                        mm = nc.tensor.matmul(p_o[u % 2][:, 0:P], pt[i % 2][0:NC, 0, :], vc[:], start=True, stop=True)
                    else:
                        k = t0 + t
                        mm = nc.tensor.matmul(p_o[u % 2][:, 0:P], pt[i % 2][:, t, :], v[:, br - 1, k0 + k], start=(k == 0), stop=(k == kn - 1))
                if i == of_unit[u][-1]:
                    mm.then_inc(o_ready, 1)

            with pe.Fori(0, HPG) as it:
                pe.wait_ge(q_ready[0], it * 32 + 32)
                scores(it, 0)
                scores(it, 1)
                for i, (u, t0, _) in enumerate(groups):
                    if t0 == 0:
                        pe.wait_ge(p_ready, unit(it, u))
                    turn(it, i)
                    if t0 == 0 and u + 2 < NU:
                        if u + 2 == NU // 2:
                            pe.wait_ge(q_ready[1], it * 32 + 32)
                        scores(it, u + 2)
                    if i > 0:
                        values(it, i - 1)
                values(it, len(groups) - 1)

        def copy_turned(eng, op, it, some, bank):
            for i in some:
                u = groups[i][0]
                if i % 2 == bank:
                    n = groups[i][2]
                    rows = NC if units[u][2] == CMP else P
                    eng.wait_ge(t_ready[bank], it * per_bank[bank] + (i // 2 + 1))
                    op(pt[bank][0:rows, 0:n, :], p_t[bank][0:rows, 0:n, :]).then_inc(t_done[bank], 1)

        @block.scalar
        def _(act):
            def exponentials(it, u):
                qt, g, br, k0, kn = units[u]
                n = NC if br == CMP else kn * P
                act.wait_ge(nb_ready, it * NU + (u + 1))
                act.wait_ge(o_done, unit(it, u, AHEAD))
                nc.scalar.activation(prob[u % AHEAD][:, 0:n], p_s[u % 2][:, 0:n], ACT.Exp, bias=nb[:, u % AHEAD:u % AHEAD + 1],
                                     accum_out=l[:, u % AHEAD:u % AHEAD + 1]).then_inc(p_ready, 1)

            act.wait_ge(gates_ready, 16)
            nc.scalar.activation(all_gates[:], all_gates[:], ACT.Exp, scale=-1.0).then_inc(g_exp, 1)
            with act.Fori(0, HPG) as it:
                exponentials(it, 0)
                exponentials(it, 1)
                for u in range(NU):
                    copy_turned(act, lambda a, b: nc.scalar.activation(a, b, ACT.Copy), it, of_unit[u], 1)
                    if u + 2 < NU:
                        exponentials(it, u + 2)

        @block.vector
        def _(dve):
            nc.vector.memset(zero[:], 0.0).then_inc(rows_zeroed, 1)
            dve.wait_ge(g_exp, 1)
            nc.vector.tensor_scalar(all_gates[:], all_gates[:], 1.0, None, ALU.add).then_inc(g_exp, 1)
            dve.wait_ge(g_exp, 2)
            nc.vector.reciprocal(all_gates[:], all_gates[:]).then_inc(g_exp, 1)
            dve.wait_ge(g_exp, 3)
            dve.wait_ge(const_ready, 160)
            with dve.Fori(0, HPG) as it:
                link = Chain(dve, dve_step, 1 + 2 * NU + sum(1 if br == CMP or qt < WT or br == SLC else 2 for qt, g, br, _, _ in units) + 2, it)

                def maxima(u):
                    qt, g, br, k0, kn = units[u]
                    S = p_s[u % 2]
                    dve.wait_ge(s_ready, it * NU + (u + 1))
                    if br == CMP:
                        n = NC
                        link(nc.vector.tensor_tensor(S[:, 0:NC], S[:, 0:NC], cmask[:, qt, :], ALU.add))
                    else:
                        n = kn * P
                        link(nc.vector.tensor_tensor(S[:, n - P:n], S[:, n - P:n], diag[:], ALU.add))
                        if br == WIN and qt >= WT:
                            link(nc.vector.tensor_tensor(S[:, 0:P], S[:, 0:P], old[:], ALU.add))
                    nc.vector.tensor_reduce(nb[:, u % AHEAD:u % AHEAD + 1], S[:, 0:n], AX, ALU.max, negate=True).then_inc(nb_ready, 1)

                link(nc.vector.tensor_copy(gates[:], all_gates[:, :, bass.ds(it * 6, 6)]))
                def output(u):
                    qt, g, br, k0, kn = units[u]
                    r = rg[:, u % AHEAD:u % AHEAD + 1]
                    link(nc.vector.reciprocal(r, l[:, u % AHEAD:u % AHEAD + 1]))
                    link(nc.vector.tensor_tensor(r, r, gates[:, qt, 3 * g + br:3 * g + br + 1], ALU.mult))
                    if br == CMP and qt == 0:
                        link(nc.vector.tensor_tensor(r, r, valid[:], ALU.mult))
                    dve.wait_ge(o_ready, it * NU + (u + 1))
                    if br > CMP:
                        dve.wait_ge(o_done, unit(it, u, 1))
                    out = o[:, qt, 64 * g:64 * g + 64]
                    if br == CMP:
                        nc.vector.tensor_scalar(out, p_o[u % 2][:, 64 * g:64 * g + 64], r, None, ALU.mult).then_inc(o_done, 1)
                    else:
                        nc.vector.scalar_tensor_tensor(out, p_o[u % 2][:, 64 * g:64 * g + 64], r, out, ALU.mult, ALU.add).then_inc(o_done, 1)

                maxima(0)
                maxima(1)
                dve.wait_ge(o_stored, it * 16 + 16)
                for u in range(NU):
                    dve.wait_ge(p_ready, unit(it, u))
                    copy_turned(dve, nc.vector.tensor_copy, it, of_unit[u][:1], 0)
                    if u + 2 < NU:
                        maxima(u + 2)
                    if u > 0:
                        output(u - 1)
                    copy_turned(dve, nc.vector.tensor_copy, it, of_unit[u][1:], 0)
                output(NU - 1)
                link.close()


def attend_samples(nc, d, n_pool):
    NC, NBK, Q, NB = N_CMP_S, N_SLC_S, DEC_SEQ, DEC_BATCH
    R = KVH * HPG * Q
    OLD = PAST
    W0, WN = OLD + Q, WINDOW + Q
    CUR = PAST // L_SLC
    FORCED = 1e9
    NG_S = N_PAGES // 8
    CHUNKS = PAST // 512
    assert (PAST + Q - 1) // L_SLC == CUR and (NC - 1) * S_CMP + L_CMP - 1 <= PAST and R == 64 and NB % 2 == 0
    with Phase(nc, "smp") as ph:
        cmp_page = ph.sb("cmp_page", [P, N_PAGES, 256])
        kv_page = [ph.sb(f"kv_page{u}", [P, N_PAGES, 256]) for u in range(2)]
        win = [ph.sb(f"win{u}", [P, 2, 512]) for u in range(2)]
        table = ph.sb("table", [1, NB * N_PAGES], I32)
        tnew = ph.sb("tnew", [P, 12, N_SMP])
        vnew = ph.sb("vnew", [Q, NB, 2, P])
        gate = ph.sb("gate", [R, NB, 3])
        qbd = [ph.sb(f"qbd{u}", [P, 2, R]) for u in range(2)]
        w1 = ph.sb("w1", [P, 2, 8, P])
        w2 = ph.sb("w2", [HD, 2, HD])
        pe_hid = ph.sb("pe_hid", [HD, 2])
        cover = ph.sb("cover", [P, 2, NBK])
        gsum = ph.sb("gsum", [R, R])
        nmask = ph.sb("nmask", [R, Q])
        wmask = ph.sb("wmask", [R, WN])
        ident = ph.sb("ident", [P, P])
        late = ph.sb("late", [HD, 2, 2, N_SEG_S])
        hid = ph.sb("hid", [HD, 2, 2, NC])
        kct = ph.sb("kct", [P, NC])
        vc = ph.sb("vc", [P, 2, P])
        pc = ph.sb("pc", [R, NC])
        pct = ph.sb("pct", [P, 2, R])
        imp = ph.sb("imp", [R, NBK])
        score, score2, score3, unsel = (ph.sb(n, [R, NBK]) for n in ("score", "score2", "score3", "unsel"))
        top = ph.sb("top", [R, 2, 8])
        S = ph.sb("S", [R, W0 + WN])
        pst = ph.sb("pst", [P, N_PAGES + 4, R])
        pnew = ph.sb("pnew", [Q, 2, R])
        vcur = ph.sb("vcur", [Q, 2, P])
        nbc, lc, rc, gc = (ph.sb(n, [R, 1]) for n in ("nbc", "lc", "rc", "gc"))
        nbs, ls, rs = (ph.sb(n, [R, 2]) for n in ("nbs", "ls", "rs"))
        o = [ph.sb(f"o{u}", [R, HD]) for u in range(2)]
        o_all = ph.sb("o_all", [R, NB, HD])
        p_h = [ph.ps(f"p_h{i}", [P, 512]) for i in range(2)]
        p_s = [ph.ps(f"p_s{i}", [P, 512]) for i in range(2)]
        p_t = [ph.ps(f"p_t{i}", [P, 8, R]) for i in range(2)]
        p_o, p_m = ph.ps("p_o", [P, 512]), ph.ps("p_m", [P, 512])
        names = ("const_ready", "zeroed", "table_ready", "gate_step", "old_copied", "stored",
                 "cmp_ready", "cmp_rest_ready", "kv0_ready", "kv1_ready", "q_ready", "hid_ready", "late_ready", "sum_ready", "act_ready",
                 "kc_ready", "kc_copied", "vc_copied", "sc_ready", "nb_ready", "pc_ready", "pcn_ready", "pct_ready", "pct_copied",
                 "imp_ready", "imp_copied", "imps_ready", "picked", "unsel_ready", "a_step",
                 "ss_ready", "ss_taken", "new_ready", "nbs_ready", "ps_ready", "tn_ready", "tn_done",
                 "t0_ready", "t0_done", "t1_ready", "t1_done", "o_ready", "o_done", "b_step")
        s = {n: ph.sem(n) for n in names}
        CONSTS = 8 + 3 + 8
        A_STEPS = 10
        SP_PAGES = 22
        block = ph.enter_context(nc.Block())
        cmp_ops = cmp_page[:].rearrange("p pg (sl c g sg) -> p sl c g pg sg", sl=2, c=8, g=2)

        def steps(eng, step):
            with eng.Fori(0, NB // 2 - 1) as i:
                for u in range(2):
                    step(i * 2 + u, u, i * 2 + (u + 1))
            step(NB - 2, 0, NB - 1)
            step(NB - 1, 1, None)

        def cmp_load(eng, b, n, ready):
            at = eng.value_load(table[0:1, bass.ds(b * N_PAGES + n, 1)], min_val=0, max_val=n_pool - 1)
            eng.dma_start(cmp_page[:, n, :], d["pool"][bass.ds(at, 1), :, 0:256].rearrange("o p n -> (o p) n")).then_inc(s[ready], 16)

        @block.sync
        def _(sp):
            sp.dma_start(table[:], d["page_table"].rearrange("b n -> (b n)").unsqueeze(0)).then_inc(s["table_ready"], 16)
            for dst, src in ((w1, "cmp_w1_seg"), (w2, "cmp_w2"), (pe_hid, "pe_hid"), (cover, "cover"), (gsum, "gsum"), (nmask, "nmask"), (wmask, "wmask"), (ident, "ident")):
                sp.dma_start(dst[:], d[src]).then_inc(s["const_ready"], 16)
            sp.wait_ge(s["table_ready"], 16)

            def cmp_loads(b):
                for n in range(SP_PAGES):
                    cmp_load(sp, b, n, "cmp_ready")

            cmp_loads(0)
            smp = slice(SEQ, SEQ + N_SMP)
            sp.dma_start(tnew[:], d["turned"][:, :, smp]).then_inc(s["const_ready"], 16)
            sp.dma_start(vnew[:, :, 0], d["kv_out"][smp, 384:512].rearrange("(b q) n -> q b n", q=Q)).then_inc(s["const_ready"], 16)
            sp.dma_start(vnew[:, :, 1], d["win_new"][smp, 128:256].rearrange("(b q) n -> q b n", q=Q)).then_inc(s["const_ready"], 16)
            for g in range(2):
                for j in range(HPG):
                    c = 3 * (2 * j + g)
                    sp.dma_start(gate[32 * g + 8 * j:32 * g + 8 * j + 8], d["gdt"][smp, c:c + 3].rearrange("(b q) c -> q b c", q=Q)).then_inc(s["const_ready"], 16)
            sp.wait_ge(s["hid_ready"], 1)
            cmp_loads(1)
            sp.dma_start(d["win_old"], d["cache_win"][:, Q:, :]).then_inc(s["old_copied"], 16)
            with sp.Fori(0, NB - 2) as b:
                hold(sp, s["hid_ready"], b + 2, ph.passed)
                cmp_loads(b + 2)
            sp.wait_ge(s["o_done"], 2 * NB)
            for g in range(2):
                for j in range(HPG):
                    c = 64 * (2 * j + g)
                    sp.dma_start(d["attn"][smp, c:c + 64].rearrange("(b q) c -> q b c", q=Q), o_all[32 * g + 8 * j:32 * g + 8 * j + 8]).then_inc(s["stored"], 16)
            sp.wait_ge(s["stored"], 128)
            sp.wait_ge(s["old_copied"], 16)

        @block.gpsimd
        def _(pool):
            pool.wait_ge(s["table_ready"], 16)

            def kv_loads(b, u):
                pool.dma_start(win[u][:].rearrange("p a n -> p (a n)"), d["win_pack"][bass.ds(b, 1)].rearrange("o p n -> (o p) n")).then_inc(s[f"kv{u}_ready"], 16)
                for n in range(N_PAGES):
                    at = pool.value_load(table[0:1, bass.ds(b * N_PAGES + n, 1)], min_val=0, max_val=n_pool - 1)
                    pool.dma_start(kv_page[u][:, n, :], d["pool"][bass.ds(at, 1), :, 256:512].rearrange("o p n -> (o p) n")).then_inc(s[f"kv{u}_ready"], 16)

            def cmp_rest(b):
                for n in range(SP_PAGES, N_PAGES):
                    cmp_load(pool, b, n, "cmp_rest_ready")

            cmp_rest(0)
            kv_loads(0, 0)
            pool.wait_ge(s["hid_ready"], 1)
            cmp_rest(1)
            kv_loads(1, 1)
            with pool.Fori(0, NB // 2 - 1) as i:
                for u in range(2):
                    hold(pool, s["hid_ready"], i * 2 + (u + 2), ph.passed)
                    cmp_rest(i * 2 + (u + 2))
                    hold(pool, s["o_ready"], i * 2 + (u + 1), ph.passed)
                    kv_loads(i * 2 + (u + 2), u)

        @block.tensor
        def _(pe):
            pe.wait_ge(s["const_ready"], CONSTS * 16)

            def hidden(b):
                hold(pe, s["cmp_ready"], b * (16 * SP_PAGES) + 16 * SP_PAGES, ph.passed)
                hold(pe, s["cmp_rest_ready"], b * (16 * (N_PAGES - SP_PAGES)) + 16 * (N_PAGES - SP_PAGES), ph.passed)
                for slot in range(2):
                    for c in range(8):
                        mm = nc.tensor.matmul(p_h[slot][:], w1[:, slot, c, :], cmp_ops[:, slot, c], start=(c == 0), stop=(c == 7))
                mm.then_inc(s["hid_ready"], 1)

            def compressed(b):
                hold(pe, s["act_ready"], b + 1, ph.passed)
                for g in range(2):
                    nc.tensor.matmul(p_h[0][64 * g:64 * g + 64, 0:NC], w2[:, 0, :], hid[:, 0, g, :], start=True, stop=True)
                for g in range(2):
                    for h in range(2):
                        n = min(P, NC - P * h)
                        mm = nc.tensor.matmul(p_h[1][0:n, P * h + 64 * g:P * h + 64 * g + 64], hid[:, 1, g, P * h:P * h + n], w2[:, 1, :], start=True, stop=True)
                mm.then_inc(s["kc_ready"], 1)

            def cmp_scores(b, u):
                hold(pe, s["kc_copied"], b + 1, ph.passed)
                hold(pe, s["q_ready"], b + 1, ph.passed)
                nc.tensor.matmul(p_h[0][0:R, 256:256 + NC], qbd[u][:, 0, :], kct[:], start=True, stop=True).then_inc(s["sc_ready"], 1)

            def cmp_turn(b):
                hold(pe, s["pcn_ready"], b + 1, ph.passed)
                nc.tensor.transpose(p_h[1][:, 256:256 + R], pc[:, 0:P], ident[0:R, 0:R])
                nc.tensor.transpose(p_h[1][0:NC - P, 256 + R:256 + 2 * R], pc[:, P:NC], ident[0:R, 0:R]).then_inc(s["pct_ready"], 1)

            def cmp_out(b):
                hold(pe, s["vc_copied"], b + 1, ph.passed)
                hold(pe, s["pct_copied"], b + 1, ph.passed)
                for h in range(2):
                    n = min(P, NC - P * h)
                    nc.tensor.matmul(p_h[1][0:R, 384:384 + NBK], pct[0:n, h, :], cover[0:n, h, :], start=(h == 0), stop=(h == 1))
                for h in range(2):
                    n = min(P, NC - P * h)
                    mm = nc.tensor.matmul(p_h[0][0:R, 0:P], pct[0:n, h, :], vc[0:n, h, :], start=(h == 0), stop=(h == 1))
                mm.then_inc(s["imp_ready"], 1)

            def importance(b):
                hold(pe, s["imp_copied"], b + 1, ph.passed)
                nc.tensor.matmul(p_h[1][0:R, 384:384 + NBK], gsum[:], imp[:], start=True, stop=True).then_inc(s["imps_ready"], 1)

            def step(b, u, a):
                def turn(k):
                    n, c0 = (8, 1024 * k) if k < NG_S else (4, W0)
                    if k >= 2:
                        hold(pe, s[f"t{k % 2}_done"], b * (3 - k % 2) + k // 2, ph.passed)
                    for i in range(n):
                        mm = nc.tensor.transpose(p_t[k % 2][:, i, :], S[:, c0 + P * i:c0 + P * i + P], ident[0:R, 0:R])
                    mm.then_inc(s[f"t{k % 2}_ready"], 1)

                def values(k):
                    hold(pe, s[f"t{k % 2}_done"], b * (3 - k % 2) + (k // 2 + 1), ph.passed)
                    if k < NG_S:
                        for n in range(8 * k, 8 * k + 8):
                            nc.tensor.matmul(p_o[0:R, P:2 * P], pst[:, n, :], kv_page[u][:, n, 128:256], start=(n == 0), stop=False)
                    else:
                        for n in range(4):
                            nc.tensor.matmul(p_o[0:R, 2 * P:3 * P], pst[:, N_PAGES + n, :], win[u][:, 1, P * n:P * n + P], start=(n == 0), stop=False)

                hold(pe, s[f"kv{u}_ready"], b * (8 * N_PAGES + 8) + (2 - u) * (8 * N_PAGES + 8), ph.passed)
                nc.tensor.matmul(p_m[0:R, 0:Q], qbd[u][:, 1, :], tnew[:, 10, bass.ds(b * Q, Q)], start=True, stop=True)
                nc.tensor.matmul(p_m[0:R, Q:2 * Q], qbd[u][:, 1, :], tnew[:, 11, bass.ds(b * Q, Q)], start=True, stop=True).then_inc(s["new_ready"], 1)
                for c in range(CHUNKS):
                    if c >= 2:
                        hold(pe, s["ss_taken"], b * (CHUNKS + 1) + (c - 1), ph.passed)
                    nc.tensor.matmul(p_s[c % 2][0:R, :], qbd[u][:, 1, :], kv_page[u][:, 4 * c:4 * c + 4, 0:128], start=True, stop=True).then_inc(s["ss_ready"], 1)
                hold(pe, s["ss_taken"], b * (CHUNKS + 1) + (CHUNKS - 1), ph.passed)
                nc.tensor.matmul(p_s[0][0:R, :], qbd[u][:, 1, :], win[u][:, 0, :], start=True, stop=True).then_inc(s["ss_ready"], 1)
                if a is not None:
                    hold(pe, s["picked"], b + 1, ph.passed)
                    hidden(a)
                hold(pe, s["ps_ready"], b + 1, ph.passed)
                nc.tensor.transpose(p_m[0:Q, 0:R], S[:, OLD:W0], ident[0:R, 0:R])
                nc.tensor.transpose(p_m[0:Q, R:2 * R], S[:, W0 + WINDOW:W0 + WN], ident[0:R, 0:R]).then_inc(s["tn_ready"], 1)
                turn(0)
                turn(1)
                values(0)
                if a is not None:
                    compressed(a)
                turn(2)
                values(1)
                if a is not None:
                    cmp_scores(a, 1 - u)
                turn(3)
                values(2)
                if a is not None:
                    cmp_turn(a)
                turn(4)
                values(3)
                if a is not None:
                    cmp_out(a)
                hold(pe, s["tn_done"], b + 1, ph.passed)
                nc.tensor.matmul(p_o[0:R, P:2 * P], pnew[:, 0, :], vcur[:, 0, :], start=False, stop=True)
                values(4)
                nc.tensor.matmul(p_o[0:R, 2 * P:3 * P], pnew[:, 1, :], vcur[:, 1, :], start=False, stop=True).then_inc(s["o_ready"], 1)
                if a is not None:
                    importance(a)

            hidden(0)
            compressed(0)
            cmp_scores(0, 0)
            cmp_turn(0)
            cmp_out(0)
            importance(0)
            steps(pe, step)

        @block.scalar
        def _(act):
            act.wait_ge(s["const_ready"], CONSTS * 16)
            nc.scalar.activation(gate[:], gate[:], ACT.Exp, scale=-1.0).then_inc(s["gate_step"], 1)

            def halves(b):
                act.wait_ge(s["hid_ready"], b + 1)
                for slot in range(2):
                    ins = nc.scalar.activation(late[:, slot], p_h[slot][64:128].rearrange("p (g n) -> p g n", g=2), ACT.Copy)
                ins.then_inc(s["late_ready"], 1)
                act.wait_ge(s["sum_ready"], b + 1)
                for slot in range(2):
                    ins = nc.scalar.activation(hid[:, slot], hid[:, slot], ACT.Silu, bias=pe_hid[:, slot:slot + 1])
                ins.then_inc(s["act_ready"], 1)

            def cmp_keys(b):
                act.wait_ge(s["kc_ready"], b + 1)
                nc.scalar.activation(kct[:], p_h[0][:, 0:NC], ACT.Copy).then_inc(s["kc_copied"], 1)

            def cmp_exp(b):
                act.wait_ge(s["nb_ready"], b + 1)
                nc.scalar.activation(pc[:], p_h[0][0:R, 256:256 + NC], ACT.Exp, bias=nbc[:], accum_out=lc[:]).then_inc(s["pc_ready"], 1)

            def step(b, u, a):
                def turned(k):
                    act.wait_ge(s["t1_ready"], b * 2 + (k // 2 + 1))
                    nc.scalar.activation(pst[:, 8 * k:8 * k + 8, :], p_t[1][:], ACT.Copy).then_inc(s["t1_done"], 1)

                act.wait_ge(s["nbs_ready"], b + 1)
                nc.scalar.activation(S[:, 0:W0], S[:, 0:W0], ACT.Exp, bias=nbs[:, 0:1], accum_out=ls[:, 0:1])
                nc.scalar.activation(S[:, W0:], S[:, W0:], ACT.Exp, bias=nbs[:, 1:2], accum_out=ls[:, 1:2]).then_inc(s["ps_ready"], 1)
                if a is not None:
                    halves(a)
                turned(1)
                if a is not None:
                    cmp_keys(a)
                    cmp_exp(a)
                turned(3)

            halves(0)
            cmp_keys(0)
            cmp_exp(0)
            steps(act, step)

        @block.vector
        def _(dve):
            for u in range(2):
                nc.vector.memset(qbd[u][:], 0.0).then_inc(s["zeroed"], 1)
            dve.wait_ge(s["zeroed"], 2)
            dve.wait_ge(s["const_ready"], CONSTS * 16)
            dve.wait_ge(s["gate_step"], 1)
            nc.vector.tensor_scalar(gate[:], gate[:], 1.0, None, ALU.add).then_inc(s["gate_step"], 1)
            dve.wait_ge(s["gate_step"], 2)
            nc.vector.reciprocal(gate[:], gate[:]).then_inc(s["gate_step"], 1)
            dve.wait_ge(s["gate_step"], 3)

            def halves(b, u):
                for g in range(2):
                    for kind in range(2):
                        ins = nc.vector.tensor_copy(qbd[u][64 * g:64 * g + 64, kind, 32 * g:32 * g + 32].rearrange("p (j q) -> p j q", j=HPG),
                                                    tnew[64 * g:64 * g + 64, 4 * kind:4 * kind + 4, bass.ds(b * Q, Q)])
                ins.then_inc(s["q_ready"], 1)
                dve.wait_ge(s["late_ready"], b + 1)
                for slot in range(2):
                    first = p_h[slot][0:HD].rearrange("p (g n) -> p g n", g=2)[:, :, 0:NC]
                    ins = nc.vector.tensor_tensor(hid[:, slot], first, late[:, slot, :, 1:N_SEG_S], ALU.add)
                ins.then_inc(s["sum_ready"], 1)

            def cmp_values(b):
                dve.wait_ge(s["kc_ready"], b + 1)
                nc.vector.tensor_copy(vc[:, 0], p_h[1][:, 0:P])
                nc.vector.tensor_copy(vc[0:NC - P, 1], p_h[1][0:NC - P, P:2 * P]).then_inc(s["vc_copied"], 1)

            def cmp_max(b):
                dve.wait_ge(s["sc_ready"], b + 1)
                nc.vector.tensor_reduce(nbc[:], p_h[0][0:R, 256:256 + NC], AX, ALU.max, negate=True).then_inc(s["nb_ready"], 1)

            def cmp_norm(b, link):
                dve.wait_ge(s["pc_ready"], b + 1)
                link(nc.vector.reciprocal(rc[:], lc[:]))
                nc.vector.tensor_scalar(pc[:], pc[:], rc[:], None, ALU.mult).then_inc(s["pcn_ready"], 1)

            def cmp_turned(b):
                dve.wait_ge(s["pct_ready"], b + 1)
                nc.vector.tensor_copy(pct[:, 0], p_h[1][:, 256:256 + R])
                nc.vector.tensor_copy(pct[0:NC - P, 1], p_h[1][0:NC - P, 256 + R:256 + 2 * R]).then_inc(s["pct_copied"], 1)

            def pick(b, u, link):
                dve.wait_ge(s["imp_ready"], b + 1)
                nc.vector.tensor_copy(imp[:], p_h[1][0:R, 384:384 + NBK]).then_inc(s["imp_copied"], 1)
                link(nc.vector.tensor_copy(gc[:], gate[:, bass.ds(b, 1), 0]))
                for g in range(2):
                    rows = slice(32 * g, 32 * g + 32)
                    link(nc.vector.tensor_scalar(o[u][rows, :], p_h[0][rows, 64 * g:64 * g + 64], gc[rows, 0:1], None, ALU.mult))
                dve.wait_ge(s["imps_ready"], b + 1)
                nc.vector.tensor_copy(score[:], p_h[1][0:R, 384:384 + NBK]).then_inc(s["picked"], 1)
                dve.wait_ge(s["picked"], b + 1)
                nc.vector.memset(score[:, 0:1], FORCED)
                link(nc.vector.memset(score[:, CUR - 1:CUR + 1], FORCED), ph.passed)
                link(nc.vector.max(top[:, 0], score[:]), ph.passed)
                link(nc.vector.match_replace(score2[:], top[:, 0], score[:], -3e38), ph.passed)
                link(nc.vector.max(top[:, 1], score2[:]), ph.passed)
                link(nc.vector.match_replace(score3[:], top[:, 1], score2[:], -3e38))
                link(nc.vector.tensor_tensor(unsel[:], score[:], score3[:], ALU.is_equal))
                nc.vector.tensor_scalar(unsel[:], unsel[:], NEG, None, ALU.mult).then_inc(s["unsel_ready"], 1)
                link.close()

            def step(b, u, a):
                link = Chain(dve, s["b_step"], 4, b)
                more = None if a is None else Chain(dve, s["a_step"], A_STEPS, a)

                def turned(k):
                    n = 8 if k < NG_S else 4
                    dve.wait_ge(s["t0_ready"], b * 3 + (k // 2 + 1))
                    nc.vector.tensor_copy(pst[:, 8 * k:8 * k + n, :], p_t[0][:, 0:n, :]).then_inc(s["t0_done"], 1)

                dve.wait_ge(s["unsel_ready"], b + 1)
                for c in range(CHUNKS):
                    dve.wait_ge(s["ss_ready"], b * (CHUNKS + 1) + (c + 1))
                    nc.vector.tensor_tensor(S[:, 512 * c:512 * c + 512].rearrange("p (k n) -> p k n", n=L_SLC), p_s[c % 2][0:R, :].rearrange("p (k n) -> p k n", n=L_SLC),
                                            unsel[:, 8 * c:8 * c + 8].unsqueeze(2).broadcast_to([R, 8, L_SLC]), ALU.add).then_inc(s["ss_taken"], 1)
                dve.wait_ge(s["new_ready"], b + 1)
                nc.vector.tensor_tensor(S[:, OLD:W0], p_m[0:R, 0:Q], nmask[:], ALU.add)
                nc.vector.tensor_tensor(S[:, W0 + WINDOW:], p_m[0:R, Q:2 * Q], wmask[:, WINDOW:], ALU.add)
                dve.wait_ge(s["ss_ready"], b * (CHUNKS + 1) + (CHUNKS + 1))
                nc.vector.tensor_tensor(S[:, W0:W0 + WINDOW], p_s[0][0:R, :], wmask[:, 0:WINDOW], ALU.add).then_inc(s["ss_taken"], 1)
                dve.wait_ge(s["ss_taken"], b * (CHUNKS + 1) + (CHUNKS + 1))
                nc.vector.tensor_reduce(nbs[:, 0:1], S[:, 0:W0], AX, ALU.max, negate=True)
                nc.vector.tensor_reduce(nbs[:, 1:2], S[:, W0:], AX, ALU.max, negate=True).then_inc(s["nbs_ready"], 1)
                if a is not None:
                    halves(a, 1 - u)
                dve.wait_ge(s["tn_ready"], b + 1)
                nc.vector.tensor_copy(vcur[:], vnew[:, bass.ds(b, 1)].rearrange("q o k n -> q (o k) n"))
                nc.vector.tensor_copy(pnew[:], p_m[0:Q, 0:2 * R].rearrange("p (a n) -> p a n", a=2)).then_inc(s["tn_done"], 1)
                turned(0)
                if a is not None:
                    cmp_values(a)
                turned(2)
                if a is not None:
                    cmp_max(a)
                    cmp_norm(a, more)
                    cmp_turned(a)
                turned(4)
                dve.wait_ge(s["ps_ready"], b + 1)
                link(nc.vector.reciprocal(rs[:], ls[:]))
                link(nc.vector.tensor_tensor(rs[:], rs[:], gate[:, bass.ds(b, 1), 1:3].rearrange("r o n -> r (o n)"), ALU.mult))
                if a is not None:
                    pick(a, 1 - u, more)
                dve.wait_ge(s["o_ready"], b + 1)
                for g in range(2):
                    rows = slice(32 * g, 32 * g + 32)
                    link(nc.vector.scalar_tensor_tensor(o[u][rows, :], p_o[rows, P + 64 * g:P + 64 * g + 64], rs[rows, 0:1], o[u][rows, :], ALU.mult, ALU.add))
                for g in range(2):
                    rows = slice(32 * g, 32 * g + 32)
                    nc.vector.scalar_tensor_tensor(o_all[rows, bass.ds(b, 1), :].rearrange("r o n -> r (o n)"), p_o[rows, 2 * P + 64 * g:2 * P + 64 * g + 64], rs[rows, 1:2], o[u][rows, :], ALU.mult, ALU.add).then_inc(s["o_done"], 1)
                dve.wait_ge(s["o_done"], b * 2 + 2)
                link.close()

            more = Chain(dve, s["a_step"], A_STEPS, 0)
            halves(0, 0)
            cmp_values(0)
            cmp_max(0)
            cmp_norm(0, more)
            cmp_turned(0)
            pick(0, 0, more)
            steps(dve, step)


def after_tile(t, n, b):
    return t + 1, n + b, 1 - b


def before_tile(t, n, b):
    return t - 1, n - (1 - b), 1 - b


def tile_loop(eng, body):
    body(0, 0, 0, True, 0)
    with eng.Fori(0, (TILES - 3) // 2) as i:
        body(i * 2 + 1, i, 1, False, 0)
        body(i * 2 + 2, i + 1, 0, False, 0)
    body(TILES - 2, (TILES - 2) // 2, (TILES - 2) % 2, False, 1)
    body(TILES - 1, (TILES - 1) // 2, (TILES - 1) % 2, False, 2)


def mix_phase(nc, d):
    BIG = 3e38
    with Phase(nc, "mix") as ph:
        w = ph.sb("w", [P, KC, D_MODEL])
        wr = ph.sb("wr", [P, KC, 36])
        rb = ph.sb("rb", [P, 36])
        gain = ph.sb("gain", [P, D_MODEL])
        ident = ph.sb("ident", [P, P])
        eps = ph.sb("eps", [P, 1])
        cat, x, h, f = ([ph.sb(f"{n}{b}", [P, D_MODEL]) for b in range(2)] for n in ("cat", "x", "h", "f"))
        sq = ph.sb("sq", [P, D_MODEL])
        catT = ph.sb("catT", [P, KC, P])
        fT = ph.sb("fT", [P, KC, P])
        real = ph.sb("real", [P, 1])
        ss, r, nm, z, ed, den = (ph.sb(n, [P, 1]) for n in ("ss", "r", "nm", "z", "ed", "den"))
        lg = ph.sb("lg", [P, 36])
        g16, g16r = ph.sb("g16", [P, 16]), ph.sb("g16r", [P, 16])
        ge = ph.sb("ge", [P, NG])
        pen = ph.sb("pen", [P, NG])
        el, el1, el2 = (ph.sb(n, [P, NE + 16]) for n in ("el", "el1", "el2"))
        top, pick = ph.sb("top", [P, 8]), ph.sb("pick", [P, 3, 8])
        route = [ph.sb(f"route{b}", [P, 66]) for b in range(2)]
        p_t = [ph.ps(f"p_t{i}", [P, 4, P]) for i in range(2)]
        p_m = [ph.ps(f"p_m{i}", [P, 512]) for i in range(2)]
        p_f = [ph.ps(f"p_f{i}", [P, 4, P]) for i in range(2)]
        p_l = ph.ps("p_l", [P, 36])
        names = ("const_ready", "setup", "cat_turned", "cat_copied", "mix_ready", "h_ready", "sq_ready", "ln_ready", "r_ready", "f_ready",
                 "f_turned", "f_copied", "lg_ready", "nm_ready", "ge_ready", "route_ready", "dve_step")
        s = {n: ph.sem(n) for n in names}
        w_ready = [ph.sem(f"w_ready{h2}") for h2 in range(2)]
        in_ready, h_stored, f_stored, route_stored = ([ph.sem(f"{n}{b}") for b in range(2)] for n in ("in_ready", "h_stored", "f_stored", "route_stored"))
        block = ph.enter_context(nc.Block())

        @block.sync
        def _(sp):
            for dst, src in ((wr, "w_route"), (rb, "b_route"), (gain, "ffn_norm"), (ident, "ident"), (real, "real")):
                sp.dma_start(dst[:], d[src]).then_inc(s["const_ready"], 16)

            def load(t, n, b):
                tok = bass.ds(t * P, P)
                for dst, src in ((cat[b][:, 0:512], d["attn"]), (cat[b][:, 512:], d["ssd"]), (x[b][:], d["x"])):
                    sp.dma_start(dst, src[tok, :]).then_inc(in_ready[b], 16)

            def store_route(t, n, b):
                sp.wait_ge(s["route_ready"], t + 1)
                sp.dma_start(d["route"][bass.ds(t * P, P), :], route[b][:]).then_inc(route_stored[b], 16)

            def body(t, n, b, first, last):
                tok = bass.ds(t * P, P)
                sp.wait_ge(s["h_ready"], t * 2 + 2)
                sp.dma_start(d["h"][tok, :], h[b][:]).then_inc(h_stored[b], 16)
                if last == 0:
                    load(t + 2, n + 1, b)
                if not first:
                    store_route(*before_tile(t, n, b))
                sp.wait_ge(s["f_ready"], t + 1)
                sp.dma_start(d["f"][tok, :], f[b][:]).then_inc(f_stored[b], 16)

            load(0, 0, 0)
            for h2 in range(2):
                c = slice(512 * h2, 512 * h2 + 512)
                sp.dma_start(w[:, :, c], d["w_out"][:, :, c]).then_inc(w_ready[h2], 16)
            load(1, 0, 1)
            tile_loop(sp, body)
            store_route(TILES - 1, TILES // 2, (TILES - 1) % 2)
            for b in range(2):
                n = (TILES + 1 - b) // 2
                for q in (h_stored, f_stored, route_stored):
                    sp.wait_ge(q[b], 16 * n + 16)

        @block.tensor
        def _(pe):
            pe.wait_ge(s["const_ready"], 80)

            def turn_cat(t, n, b):
                pe.wait_ge(in_ready[b], n * 48 + 48)
                for k in range(KC):
                    mm = nc.tensor.transpose(p_t[k // 4][:, k % 4, :], cat[b][:, k * P:k * P + P], ident[:])
                mm.then_inc(s["cat_turned"], 1)

            def turn_f(t, n, b):
                pe.wait_ge(s["f_ready"], t + 1)
                for k in range(KC):
                    mm = nc.tensor.transpose(p_f[k // 4][:, k % 4, :], f[b][:, k * P:k * P + P], ident[:])
                mm.then_inc(s["f_turned"], 1)

            def logits(t, n, b):
                pe.wait_ge(s["f_copied"], t * 2 + 2)
                for k in range(KC):
                    mm = nc.tensor.matmul(p_l[:], fT[:, k, :], wr[:, k, :], start=(k == 0), stop=(k == KC - 1))
                mm.then_inc(s["lg_ready"], 1)

            def body(t, n, b, first, last):
                pe.wait_ge(s["cat_copied"], t * 2 + 2)
                if not first:
                    pe.wait_ge(s["h_ready"], t * 2)
                for h2 in range(2):
                    if first:
                        pe.wait_ge(w_ready[h2], 16)
                    for k in range(KC):
                        mm = nc.tensor.matmul(p_m[h2][:], catT[:, k, :], w[:, k, 512 * h2:512 * h2 + 512], start=(k == 0), stop=(k == KC - 1))
                mm.then_inc(s["mix_ready"], 1)
                if not first:
                    turn_f(*before_tile(t, n, b))
                if last < 2:
                    turn_cat(*after_tile(t, n, b))
                if not first:
                    logits(*before_tile(t, n, b))

            turn_cat(0, 0, 0)
            tile_loop(pe, body)
            end = (TILES - 1, TILES // 2, (TILES - 1) % 2)
            turn_f(*end)
            logits(*end)

        @block.scalar
        def _(act):
            act.wait_ge(s["setup"], 3)

            def copy_cat(t, n, b):
                act.wait_ge(s["cat_turned"], t + 1)
                nc.scalar.activation(catT[:, 4:8], p_t[1][:], ACT.Copy).then_inc(s["cat_copied"], 1)

            def copy_f(t, n, b):
                act.wait_ge(s["f_turned"], t + 1)
                nc.scalar.activation(fT[:, 4:8], p_f[1][:], ACT.Copy).then_inc(s["f_copied"], 1)

            def router(t, n, b):
                act.wait_ge(s["nm_ready"], t + 1)
                nc.scalar.activation(ge[:], lg[:, 0:NG], ACT.Exp, bias=nm[:], accum_out=z[:])
                nc.scalar.activation(ed[:], den[:], ACT.Exp).then_inc(s["ge_ready"], 1)

            def body(t, n, b, first, last):
                if not first:
                    copy_f(*before_tile(t, n, b))
                if last < 2:
                    copy_cat(*after_tile(t, n, b))
                act.wait_ge(s["h_ready"], t * 2 + 2)
                nc.scalar.activation(sq[:], h[b][:], ACT.Square, accum_out=ss[:]).then_inc(s["sq_ready"], 1)
                act.wait_ge(s["sq_ready"], t + 1)
                if not first:
                    act.wait_ge(s["f_ready"], t)
                nc.scalar.activation(ss[:], ss[:], ACT.Ln, bias=eps[:], scale=1.0 / D_MODEL).then_inc(s["ln_ready"], 1)
                act.wait_ge(s["ln_ready"], t + 1)
                nc.scalar.activation(r[:], ss[:], ACT.Exp, scale=-0.5).then_inc(s["r_ready"], 1)
                if not first:
                    router(*before_tile(t, n, b))

            copy_cat(0, 0, 0)
            tile_loop(act, body)
            end = (TILES - 1, TILES // 2, (TILES - 1) % 2)
            copy_f(*end)
            router(*end)

        @block.vector
        def _(dve):
            nc.vector.memset(eps[:], EPS).then_inc(s["setup"], 1)
            for i, tile in enumerate((g16, el, pick)):
                ins = nc.vector.memset(tile[:], -BIG)
            ins.then_inc(s["setup"], 2)
            for b in range(2):
                for q in (h_stored, f_stored, route_stored):
                    dve.sem_inc(q[b], 16)
            dve.wait_ge(s["setup"], 3)
            dve.wait_ge(s["const_ready"], 80)

            def copy_cat(t, n, b):
                dve.wait_ge(s["cat_turned"], t + 1)
                nc.vector.tensor_copy(catT[:, 0:4], p_t[0][:]).then_inc(s["cat_copied"], 1)

            def copy_f(t, n, b):
                dve.wait_ge(s["f_turned"], t + 1)
                nc.vector.tensor_copy(fT[:, 0:4], p_f[0][:]).then_inc(s["f_copied"], 1)

            def router(t, n, b):
                link = Chain(dve, s["dve_step"], 19, t)
                rt = route[b]
                dve.wait_ge(route_stored[b], n * 16 + 16)
                dve.wait_ge(s["lg_ready"], t + 1)
                link(nc.vector.tensor_tensor(lg[:], p_l[:], rb[:], ALU.add))
                link(nc.vector.tensor_copy(g16[:, 0:NG], lg[:, 0:NG]), ph.passed)
                link(nc.vector.max(top[:], g16[:]))
                link(nc.vector.tensor_copy(pick[:, 0, 0:1], top[:, 0:1]))
                link(nc.vector.tensor_scalar(nm[:], top[:, 0:1], -1.0, None, ALU.mult), ph.passed)
                link(nc.vector.match_replace(g16r[:], pick[:, 0], g16[:], BIG))
                link(nc.vector.tensor_scalar(pen[:], g16r[:, 0:NG], BIG, None, ALU.is_equal))
                link(nc.vector.tensor_scalar(pen[:], pen[:], -NEG, NEG, ALU.mult, ALU.add))
                link(nc.vector.tensor_tensor(el[:, 0:NE].rearrange("p (g e) -> p g e", g=NG), lg[:, NG:].rearrange("p (g e) -> p g e", g=NG),
                                             pen[:].unsqueeze(2).broadcast_to([P, NG, EPG]), ALU.add), ph.passed)
                link(nc.vector.max(top[:], el[:]))
                nc.vector.tensor_copy(pick[:, 1, 0:1], top[:, 0:1])
                link(nc.vector.tensor_copy(pick[:, 2, 0:1], top[:, 1:2]))
                nc.vector.tensor_tensor(den[:], top[:, 1:2], top[:, 0:1], ALU.subtract).then_inc(s["nm_ready"], 1)
                hold(dve, s["nm_ready"], t + 1, ph.passed)
                link(nc.vector.match_replace(el1[:], pick[:, 1], el[:], BIG), ph.passed)
                link(nc.vector.match_replace(el2[:], pick[:, 2], el1[:], BIG))
                link(nc.vector.tensor_scalar(rt[:, 0:NE], el1[:, 0:NE], BIG, None, ALU.is_equal))
                link(nc.vector.tensor_scalar(rt[:, NE:2 * NE], el2[:, 0:NE], BIG, None, ALU.is_equal))
                link(nc.vector.tensor_tensor(rt[:, NE:2 * NE], rt[:, NE:2 * NE], rt[:, 0:NE], ALU.subtract))
                if isinstance(t, int) and t == TILES - 1:
                    link(nc.vector.tensor_scalar(rt[:, 0:2 * NE], rt[:, 0:2 * NE], real[:], None, ALU.mult))
                dve.wait_ge(s["ge_ready"], t + 1)
                link(nc.vector.scalar_tensor_tensor(den[:], ed[:], 1.0, z[:], ALU.add, ALU.mult))
                link(nc.vector.reciprocal(rt[:, 64:65], den[:]))
                link(nc.vector.tensor_tensor(rt[:, 65:66], rt[:, 64:65], ed[:], ALU.mult))
                dve.sem_inc(s["route_ready"], 1)
                if not isinstance(t, int):
                    link.close()

            def body(t, n, b, first, last):
                dve.wait_ge(s["mix_ready"], t + 1)
                dve.wait_ge(h_stored[b], n * 16 + 16)
                for h2 in range(2):
                    c = slice(512 * h2, 512 * h2 + 512)
                    nc.vector.tensor_tensor(h[b][:, c], x[b][:, c], p_m[h2][:], ALU.add).then_inc(s["h_ready"], 1)
                if not first:
                    copy_f(*before_tile(t, n, b))
                if last < 2:
                    copy_cat(*after_tile(t, n, b))
                dve.wait_ge(s["r_ready"], t + 1)
                dve.wait_ge(f_stored[b], n * 16 + 16)
                nc.vector.scalar_tensor_tensor(f[b][:], h[b][:], r[:], gain[:], ALU.mult, ALU.mult).then_inc(s["f_ready"], 1)
                if not first:
                    router(*before_tile(t, n, b))

            copy_cat(0, 0, 0)
            tile_loop(dve, body)
            end = (TILES - 1, TILES // 2, (TILES - 1) % 2)
            copy_f(*end)
            router(*end)


def dispatch_phase(nc, d):
    with Phase(nc, "dsp") as ph:
        route = ph.sb("route", [P, TILES, 66])
        before = ph.sb("before", [P, P])
        ones = ph.sb("ones", [P, P])
        first = ph.sb("first", [P, NE])
        padoff = ph.sb("padoff", [P, TILES, 2])
        ids = ph.sb("ids", [P, TILES], U32)
        blocks = ph.sb("blocks", [P, OVER_BLOCKS])
        m = ph.sb("m", [P, TILES, NE])
        pos = ph.sb("pos", [P, TILES, NE])
        late = ph.sb("late", [P, TILES, NE])
        n_e, ov, cum, cum2, base2 = (ph.sb(n, [P, NE]) for n in ("n_e", "ov", "cum", "cum2", "base2"))
        dest = ph.sb("dest", [P, TILES, 2])
        gidx = ph.sb("gidx", [P, TILES, 2], U32)
        sidx = ph.sb("sidx", [P, TILES, 2], U32)
        fill = ph.sb("fill", [P, SLOTS // P], U32)
        cmpj = ph.sb("cmpj", [P, OVER_BLOCKS, NE])
        over = ph.sb("over", [P, OVER_BLOCKS + 1])
        over_i = ph.sb("over_i", [P, OVER_BLOCKS + 1], I32)
        p_c = ph.ps("p_c", [P, TILES + 1, NE])
        loaded, m_ready, cnt_ready, idx_ready, over_ready = ph.sem("loaded"), ph.sem("m_ready"), ph.sem("cnt_ready"), ph.sem("idx_ready"), ph.sem("over_ready")
        filled, fill_ready, scattered, stored, dve_step = ph.sem("filled"), ph.sem("fill_ready"), ph.sem("scattered"), ph.sem("stored"), ph.sem("dve_step")
        block = ph.enter_context(nc.Block())

        @block.sync
        def _(sp):
            for dst, src in ((route[:], d["route"].rearrange("(t p) n -> p t n", p=P)), (before[:], d["before"]), (first[:], d["first"]), (padoff[:], d["padoff"]),
                             (ids[:], d["ids"]), (blocks[:], d["blocks"])):
                sp.dma_start(dst, src).then_inc(loaded, 16)
            sp.wait_ge(fill_ready, 1)
            sp.dma_start(d["slot_tok"].rearrange("(p n) o -> p (n o)", p=P), fill[:]).then_inc(filled, 16)
            sp.wait_ge(idx_ready, 1)
            sp.dma_start(d["gidx"].rearrange("(t p) n -> p t n", p=P), gidx[:]).then_inc(stored, 16)
            sp.wait_ge(over_ready, 1)
            sp.dma_start(d["over"], over_i[0:1, :]).then_inc(stored, 16)
            sp.wait_ge(stored, 32)

        @block.tensor
        def _(pe):
            pe.wait_ge(m_ready, 1)
            for t in range(TILES + 1):
                if t < TILES:
                    mm = nc.tensor.matmul(p_c[:, t, :], before[:], m[:, t, :], start=True, stop=(t == 0))
                for u in range(t):
                    mm = nc.tensor.matmul(p_c[:, t, :], ones[:], m[:, u, :], start=(t == TILES and u == 0), stop=(u == t - 1))
            mm.then_inc(cnt_ready, 1)

        @block.vector
        def _(dve):
            link = Chain(dve, dve_step)
            nc.vector.memset(fill[:], TOK - 1).then_inc(fill_ready, 1)
            link(nc.vector.memset(ones[:], 1.0))
            dve.wait_ge(loaded, 96)
            nc.vector.tensor_tensor(m[:], route[:, :, 0:NE], route[:, :, NE:2 * NE], ALU.add).then_inc(m_ready, 1)
            dve.wait_ge(cnt_ready, 1)
            link(nc.vector.tensor_copy(pos[:], p_c[:, 0:TILES, :]))
            link(nc.vector.tensor_copy(n_e[:], p_c[:, TILES, :]))
            link(nc.vector.tensor_scalar(ov[:], n_e[:], float(P), None, ALU.is_gt))
            for k in range(2, TILES):
                link(nc.vector.scalar_tensor_tensor(ov[:], n_e[:], float(P * k), ov[:], ALU.is_gt, ALU.add))
            link(nc.vector.tensor_copy(cum[:], ov[:]))
            a, b = cum, cum2
            for k in (1, 2, 4, 8, 16):
                nc.vector.tensor_copy(b[:, 0:k], a[:, 0:k])
                link(nc.vector.tensor_tensor(b[:, k:], a[:, k:], a[:, 0:NE - k], ALU.add))
                a, b = b, a
            link(nc.vector.tensor_tensor(base2[:], a[:], ov[:], ALU.subtract))
            link(nc.vector.tensor_scalar(base2[:], base2[:], float(P), float(P * (MAIN_BLOCKS - 1)), ALU.mult, ALU.add))
            link(nc.vector.tensor_tensor(base2[:], base2[:], first[:], ALU.subtract))
            link(nc.vector.tensor_scalar(late[:], pos[:], float(P), None, ALU.is_ge))
            link(nc.vector.tensor_tensor(late[:], late[:], base2[:].unsqueeze(1).broadcast_to([P, TILES, NE]), ALU.mult))
            link(nc.vector.tensor_tensor(pos[:], pos[:], first[:].unsqueeze(1).broadcast_to([P, TILES, NE]), ALU.add))
            link(nc.vector.tensor_tensor(pos[:], pos[:], late[:], ALU.add))
            for k in range(2):
                link(nc.vector.tensor_tensor(m[:], pos[:], route[:, :, NE * k:NE * k + NE], ALU.mult))
                link(nc.vector.reduce_sum(dest[:, :, k], m[:], AX))
            nc.vector.tensor_copy(gidx[:], dest[:])
            link(nc.vector.tensor_tensor(dest[:], dest[:], padoff[:], ALU.add))
            nc.vector.tensor_copy(sidx[:], dest[:]).then_inc(idx_ready, 1)
            link(nc.vector.tensor_tensor(cmpj[:], a[:].unsqueeze(1).broadcast_to([P, OVER_BLOCKS, NE]), blocks[:].unsqueeze(2).broadcast_to([P, OVER_BLOCKS, NE]), ALU.is_le))
            link(nc.vector.reduce_sum(over[:, 0:OVER_BLOCKS], cmpj[:], AX))
            link(nc.vector.tensor_scalar(over[:, 0:OVER_BLOCKS], over[:, 0:OVER_BLOCKS], float(NE - 1), None, ALU.min))
            link(nc.vector.tensor_copy(over[:, OVER_BLOCKS:], a[:, NE - 1:NE]))
            nc.vector.tensor_copy(over_i[:], over[:]).then_inc(over_ready, 1)

        @block.gpsimd
        def _(pool):
            pool.wait_ge(filled, 16)
            pool.wait_ge(idx_ready, 1)
            for t in range(TILES):
                for k in range(2):
                    pool.indirect_dma_start(d["slot_tok"], bass.IndirectOffsetOnAxis(ap=sidx[:, t, k:k + 1], axis=0), ids[:, t:t + 1], None).then_inc(scattered, 16)
            pool.wait_ge(scattered, 2 * TILES * 16)


def expert_phase(nc, d, overflow):
    NBUF = 1 if overflow else 2
    FIRST = MAIN_BLOCKS if overflow else 0
    with Phase(nc, "ovf" if overflow else "exp") as ph:
        wg = [ph.sb(f"wg{i}", [P, KC, D_EXP]) for i in range(NBUF)]
        wu = [ph.sb(f"wu{i}", [P, KC, D_EXP]) for i in range(NBUF)]
        wd = [ph.sb(f"wd{i}", [P, D_EXP // P, D_MODEL]) for i in range(NBUF)]
        idx = [ph.sb(f"idx{i}", [P, 1], U32) for i in range(NBUF)]
        xg = [ph.sb(f"xg{i}", [P, D_MODEL]) for i in range(NBUF)]
        xT = [ph.sb(f"xT{i}", [P, KC, P]) for i in range(NBUF)]
        act_g = ph.sb("act_g", [P, D_EXP])
        hb = ph.sb("hb", [P, D_EXP])
        hT = ph.sb("hT", [P, 4, P])
        y = [ph.sb(f"y{i}", [P, D_MODEL]) for i in range(NBUF)]
        ident = ph.sb("ident", [P, P])
        over = ph.sb("over", [1, OVER_BLOCKS + 1], I32)
        p_t = [ph.ps(f"p_t{i}", [P, 4, P]) for i in range(2)]
        p_g, p_u, p_h = ph.ps("p_g", [P, D_EXP]), ph.ps("p_u", [P, D_EXP]), ph.ps("p_h", [P, 4, P])
        p_y = [ph.ps(f"p_y{i}", [P, 512]) for i in range(2)]
        const_ready = ph.sem("const_ready")
        per_buf = [{n: ph.sem(f"{n}{i}") for n in ("g_loaded", "u_loaded", "d_loaded", "idx_ready", "x_ready", "x_free", "g_free", "u_free", "d_free", "stored", "y_ready")} for i in range(NBUF)]
        s = {n: ph.sem(n) for n in ("x_turned", "x_copied", "g_ready", "u_ready", "act_ready", "h_ready", "h_turned", "h_copied", "y_done", "y_free")}
        block = ph.enter_context(nc.Block())
        N = (OVER_BLOCKS if overflow else MAIN_BLOCKS) // NBUF

        def blocks(eng, body):
            if not overflow:
                with eng.Fori(0, N - 1) as i:
                    for k in range(NBUF):
                        body(i, i * NBUF + k, k, False)
                for k in range(NBUF):
                    body(N - 1, (N - 1) * NBUF + k, k, k == NBUF - 1)
            else:
                eng.wait_ge(const_ready, 32)
                needed = eng.value_load(over[0:1, OVER_BLOCKS:OVER_BLOCKS + 1], min_val=0, max_val=OVER_BLOCKS)
                with eng.Fori(0, N) as i:
                    with eng.If(needed > i):
                        body(i, i, 0, False)
                    with eng.Else():
                        pass

        @block.sync
        def _(sp):
            sp.dma_start(ident[:], d["ident"]).then_inc(const_ready, 16)
            sp.dma_start(over[:], d["over"]).then_inc(const_ready, 16)
            for k in range(NBUF):
                for n in ("g_free", "u_free", "d_free"):
                    sp.sem_inc(per_buf[k][n], 1)

            def body(i, b, k, last):
                q = per_buf[k]
                ex = sp.value_load(over[0:1, bass.ds(b, 1)], min_val=0, max_val=NE - 1) if overflow else b
                for name, dst in (("g", wg), ("u", wu), ("d", wd)):
                    src = d[{"g": "w_gate", "u": "w_up", "d": "w_down"}[name]]
                    sp.wait_ge(q[name + "_free"], i + 1)
                    sp.dma_start(dst[k][:], src[bass.ds(ex, 1)].rearrange("o (c p) n -> p (o c) n", p=P)).then_inc(q[name + "_loaded"], 16)
            blocks(sp, body)

        @block.gpsimd
        def _(pool):
            for k in range(NBUF):
                pool.sem_inc(per_buf[k]["x_free"], 1)

            def body(i, b, k, last):
                q = per_buf[k]
                hold(pool, q["x_free"], i + 1, ph.passed)
                pool.dma_start(idx[k][:], d["slot_tok"][bass.ds((b + FIRST) * P, P), :]).then_inc(q["idx_ready"], 16)
                hold(pool, q["idx_ready"], i * 16 + 16, ph.passed)
                pool.indirect_dma_start(xg[k][:], None, d["f"], bass.IndirectOffsetOnAxis(ap=idx[k][:, 0:1], axis=0)).then_inc(q["x_ready"], 16)
            blocks(pool, body)

        @block.tensor
        def _(pe):
            pe.wait_ge(const_ready, 32)

            def turn_x(i, b, k):
                pe.wait_ge(per_buf[k]["x_ready"], i * 16 + 16)
                for c in range(KC):
                    mm = nc.tensor.transpose(p_t[c // 4][:, c % 4, :], xg[k][:, c * P:c * P + P], ident[:])
                mm.then_inc(s["x_turned"], 1)

            def gate(i, b, k):
                pe.wait_ge(s["x_copied"], b * 2 + 2)
                pe.sem_inc(per_buf[k]["x_free"], 1)
                pe.wait_ge(per_buf[k]["g_loaded"], i * 16 + 16)
                for c in range(KC):
                    mm = nc.tensor.matmul(p_g[:], xT[k][:, c, :], wg[k][:, c, :], start=(c == 0), stop=(c == KC - 1))
                mm.then_inc(s["g_ready"], 1)

            def up(i, b, k):
                pe.wait_ge(per_buf[k]["u_loaded"], i * 16 + 16)
                for c in range(KC):
                    mm = nc.tensor.matmul(p_u[:], xT[k][:, c, :], wu[k][:, c, :], start=(c == 0), stop=(c == KC - 1))
                mm.then_inc(s["u_ready"], 1)

            def turn_h(i, b, k):
                pe.wait_ge(s["h_ready"], b + 1)
                pe.sem_inc(per_buf[k]["g_free"], 1)
                pe.sem_inc(per_buf[k]["u_free"], 1)
                for c in range(4):
                    mm = nc.tensor.transpose(p_h[:, c, :], hb[:, c * P:c * P + P], ident[:])
                mm.then_inc(s["h_turned"], 1)

            def down(i, b, k):
                pe.wait_ge(s["h_copied"], b + 1)
                pe.wait_ge(s["y_free"], b + 1)
                pe.wait_ge(per_buf[k]["d_loaded"], i * 16 + 16)
                for n in range(2):
                    for c in range(4):
                        mm = nc.tensor.matmul(p_y[n][:], hT[:, c, :], wd[k][:, c, 512 * n:512 * n + 512], start=(c == 0), stop=(c == 3))
                mm.then_inc(s["y_done"], 1)

            def body(i, b, k, last):
                if overflow:
                    for part in (turn_x, gate, up, turn_h, down):
                        part(i, b, k)
                    return
                nxt = (i + k, b + 1, 1 - k)
                if not last:
                    turn_x(*nxt)
                turn_h(i, b, k)
                if not last:
                    gate(*nxt)
                down(i, b, k)
                if not last:
                    up(*nxt)

            if not overflow:
                for part in (turn_x, gate, up):
                    part(0, 0, 0)
            blocks(pe, body)

        @block.scalar
        def _(act):
            act.sem_inc(s["y_free"], 1)
            for k in range(NBUF):
                act.sem_inc(per_buf[k]["stored"], 16)

            def first(b, k):
                act.wait_ge(s["x_turned"], b + 1)
                nc.scalar.activation(xT[k][:, 4:8], p_t[1][:], ACT.Copy).then_inc(s["x_copied"], 1)

            def silu(b):
                act.wait_ge(s["g_ready"], b + 1)
                if not overflow:
                    act.wait_ge(s["h_ready"], b)
                nc.scalar.activation(act_g[:], p_g[:], ACT.Silu).then_inc(s["act_ready"], 1)

            def body(i, b, k, last):
                q = per_buf[k]
                if overflow:
                    first(b, k)
                    silu(b)
                elif not last:
                    first(b + 1, 1 - k)
                    silu(b + 1)
                act.wait_ge(s["y_done"], b + 1)
                act.sem_inc(q["d_free"], 1)
                act.wait_ge(q["stored"], i * 16 + 16)
                for n in range(2):
                    ins = nc.scalar.activation(y[k][:, 512 * n:512 * n + 512], p_y[n][:], ACT.Copy)
                ins.then_inc(q["y_ready"], 1)
                act.wait_ge(q["y_ready"], i + 1)
                act.sem_inc(s["y_free"], 1)
                act.dma_start(d["ypad"][bass.ds((b + FIRST) * P, P), :], y[k][:]).then_inc(q["stored"], 16)
                if overflow:
                    hold(act, q["stored"], i * 16 + 32, ph.passed)

            if not overflow:
                first(0, 0)
                act.wait_ge(s["g_ready"], 1)
                nc.scalar.activation(act_g[:], p_g[:], ACT.Silu).then_inc(s["act_ready"], 1)
            blocks(act, body)
            if not overflow:
                for k in range(NBUF):
                    act.wait_ge(per_buf[k]["stored"], 16 * N + 16)

        @block.vector
        def _(dve):
            def first(b, k):
                dve.wait_ge(s["x_turned"], b + 1)
                nc.vector.tensor_copy(xT[k][:, 0:4], p_t[0][:]).then_inc(s["x_copied"], 1)

            def product(b):
                dve.wait_ge(s["act_ready"], b + 1)
                dve.wait_ge(s["u_ready"], b + 1)
                nc.vector.tensor_tensor(hb[:], act_g[:], p_u[:], ALU.mult).then_inc(s["h_ready"], 1)

            def body(i, b, k, last):
                if overflow:
                    first(b, k)
                    product(b)
                elif not last:
                    first(b + 1, 1 - k)
                dve.wait_ge(s["h_turned"], b + 1)
                nc.vector.tensor_copy(hT[:], p_h[:]).then_inc(s["h_copied"], 1)
                if not overflow and not last:
                    product(b + 1)

            if not overflow:
                first(0, 0)
                product(0)
            blocks(dve, body)


def final_phase(nc, d):
    with Phase(nc, "fin") as ph:
        wg = ph.sb("wg", [P, KC, D_MODEL])
        wp = ph.sb("wp", [P, 2, D_MODEL])
        gain = ph.sb("gain", [P, D_MODEL])
        ident = ph.sb("ident", [P, P])
        eps = ph.sb("eps", [P, 1])
        gidx, wt = [ph.sb(f"gidx{b}", [P, 2], U32) for b in range(2)], [ph.sb(f"wt{b}", [P, 2]) for b in range(2)]
        h_in, h, y1, y2, pn = ([ph.sb(f"{n}{b}", [P, D_MODEL]) for b in range(2)] for n in ("h_in", "h", "y1", "y2", "pn"))
        e, sq = ph.sb("e", [P, D_MODEL]), ph.sb("sq", [P, D_MODEL])
        pT = [ph.sb(f"pT{b}", [P, 2, P]) for b in range(2)]
        hT = [ph.sb(f"hT{b}", [P, KC, P]) for b in range(2)]
        ss, r = ph.sb("ss", [P, 2]), ph.sb("r", [P, 1])
        p_t = [ph.ps(f"p_t{i}", [P, 4, P]) for i in range(2)]
        p_g = [ph.ps(f"p_g{i}", [P, 512]) for i in range(2)]
        p_p = [ph.ps(f"p_p{i}", [P, 512]) for i in range(2)]
        names = ("const_ready", "setup", "h_ready", "h_turned", "h_copied", "g_ready", "p_ready", "pn_ready", "e_ready",
                 "sq_ready", "ss_ready", "ln_ready", "r_ready", "out_ready", "gated", "dve_step")
        s = {n: ph.sem(n) for n in names}
        w_ready = [ph.sem(f"w_ready{h2}") for h2 in range(2)]
        in_free, idx_ready, in_ready, y_ready, stored = ([ph.sem(f"{n}{b}") for b in range(2)] for n in ("in_free", "idx_ready", "in_ready", "y_ready", "stored"))
        block = ph.enter_context(nc.Block())

        @block.sync
        def _(sp):
            for b in range(2):
                sp.sem_inc(in_free[b], 1)
            for dst, src in ((wp, "w_ple_proj"), (gain, "ple_norm"), (ident, "ident")):
                sp.dma_start(dst[:], d[src]).then_inc(s["const_ready"], 16)

            def load(t, n, b):
                tok = bass.ds(t * P, P)
                sp.wait_ge(in_free[b], n + 1)
                sp.dma_start(gidx[b][:], d["gidx"][tok, :]).then_inc(idx_ready[b], 16)
                sp.dma_start(wt[b][:], d["route"][tok, 64:66]).then_inc(in_ready[b], 16)
                sp.dma_start(h_in[b][:], d["h"][tok, :]).then_inc(in_ready[b], 16)
                sp.dma_start(pT[b][:], d["pT"][bass.ds(t, 1)].rearrange("o p c n -> (o p) c n")).then_inc(in_ready[b], 16)

            def body(t, n, b, first, last):
                if last == 0:
                    load(t + 2, n + 1, b)
                sp.wait_ge(s["out_ready"], t + 1)
                sp.dma_start(d["y"][bass.ds(t * P, P), :], pn[b][:]).then_inc(stored[b], 16)

            load(0, 0, 0)
            load(1, 0, 1)
            for h2 in range(2):
                c = slice(512 * h2, 512 * h2 + 512)
                sp.dma_start(wg[:, :, c], d["w_ple_gate"][:, :, c]).then_inc(w_ready[h2], 16)
            tile_loop(sp, body)
            for b in range(2):
                sp.wait_ge(stored[b], 16 * ((TILES + 1 - b) // 2) + 16)

        @block.gpsimd
        def _(pool):
            def gather(t, n, b):
                hold(pool, idx_ready[b], n * 16 + 16, ph.passed)
                for k, dst in enumerate((y1[b], y2[b])):
                    pool.indirect_dma_start(dst[:], None, d["ypad"], bass.IndirectOffsetOnAxis(ap=gidx[b][:, k:k + 1], axis=0)).then_inc(y_ready[b], 16)

            tile_loop(pool, lambda t, n, b, first, last: gather(t, n, b))

        @block.tensor
        def _(pe):
            pe.wait_ge(s["const_ready"], 48)

            def prepare(t, n, b, first):
                pe.wait_ge(in_ready[b], n * 48 + 48)
                if not first:
                    pe.wait_ge(s["pn_ready"], t)
                for h2 in range(2):
                    for c in range(2):
                        mm = nc.tensor.matmul(p_p[h2][:], pT[b][:, c, :], wp[:, c, 512 * h2:512 * h2 + 512], start=(c == 0), stop=(c == 1))
                mm.then_inc(s["p_ready"], 1)
                pe.wait_ge(s["h_ready"], t + 1)
                if not first:
                    pe.wait_ge(s["h_copied"], t * 2)
                for c in range(KC):
                    mm = nc.tensor.transpose(p_t[c // 4][:, c % 4, :], h[b][:, c * P:c * P + P], ident[:])
                mm.then_inc(s["h_turned"], 1)

            def body(t, n, b, first, last):
                if last < 2:
                    prepare(*after_tile(t, n, b), False)
                pe.wait_ge(s["h_copied"], t * 2 + 2)
                if not first:
                    pe.wait_ge(s["e_ready"], t)
                for h2 in range(2):
                    if first:
                        pe.wait_ge(w_ready[h2], 16)
                    for c in range(KC):
                        mm = nc.tensor.matmul(p_g[h2][:], hT[b][:, c, :], wg[:, c, 512 * h2:512 * h2 + 512], start=(c == 0), stop=(c == KC - 1))
                mm.then_inc(s["g_ready"], 1)

            prepare(0, 0, 0, True)
            tile_loop(pe, body)

        @block.scalar
        def _(act):
            act.wait_ge(s["setup"], 1)

            def prepare(t, n, b):
                act.wait_ge(s["p_ready"], t + 1)
                for h2 in range(2):
                    ins = nc.scalar.activation(sq[:, 512 * h2:512 * h2 + 512], p_p[h2][:], ACT.Square, accum_out=ss[:, h2:h2 + 1])
                ins.then_inc(s["sq_ready"], 1)
                act.wait_ge(s["ss_ready"], t + 1)
                nc.scalar.activation(ss[:, 0:1], ss[:, 0:1], ACT.Ln, bias=eps[:], scale=1.0 / D_MODEL).then_inc(s["ln_ready"], 1)
                act.wait_ge(s["ln_ready"], t + 1)
                nc.scalar.activation(r[:], ss[:, 0:1], ACT.Exp, scale=-0.5).then_inc(s["r_ready"], 1)
                act.wait_ge(s["h_turned"], t + 1)
                nc.scalar.activation(hT[b][:, 4:8], p_t[1][:], ACT.Copy).then_inc(s["h_copied"], 1)

            def body(t, n, b, first, last):
                if last < 2:
                    prepare(*after_tile(t, n, b))
                act.wait_ge(s["g_ready"], t + 1)
                if not first:
                    act.wait_ge(s["out_ready"], t)
                for h2 in range(2):
                    ins = nc.scalar.activation(e[:, 512 * h2:512 * h2 + 512], p_g[h2][:], ACT.Sigmoid)
                ins.then_inc(s["e_ready"], 1)

            prepare(0, 0, 0)
            tile_loop(act, body)

        @block.vector
        def _(dve):
            nc.vector.memset(eps[:], EPS).then_inc(s["setup"], 1)
            for b in range(2):
                dve.sem_inc(stored[b], 16)
            dve.wait_ge(s["const_ready"], 48)

            def prepare(t, n, b):
                dve.wait_ge(in_ready[b], n * 48 + 48)
                dve.wait_ge(y_ready[b], n * 32 + 32)
                link = Chain(dve, s["dve_step"], 1, t)
                link(nc.vector.scalar_tensor_tensor(h[b][:], y1[b][:], wt[b][:, 0:1], h_in[b][:], ALU.mult, ALU.add))
                nc.vector.scalar_tensor_tensor(h[b][:], y2[b][:], wt[b][:, 1:2], h[b][:], ALU.mult, ALU.add).then_inc(s["h_ready"], 1)
                dve.wait_ge(s["sq_ready"], t + 1)
                dve.wait_ge(s["h_ready"], t + 1)
                dve.sem_inc(in_free[b], 1)
                nc.vector.tensor_tensor(ss[:, 0:1], ss[:, 0:1], ss[:, 1:2], ALU.add).then_inc(s["ss_ready"], 1)
                dve.wait_ge(s["h_turned"], t + 1)
                nc.vector.tensor_copy(hT[b][:, 0:4], p_t[0][:]).then_inc(s["h_copied"], 1)
                dve.wait_ge(s["r_ready"], t + 1)
                dve.wait_ge(stored[b], n * 16 + 16)
                for h2 in range(2):
                    c = slice(512 * h2, 512 * h2 + 512)
                    ins = nc.vector.scalar_tensor_tensor(pn[b][:, c], p_p[h2][:], r[:], gain[:, c], ALU.mult, ALU.mult)
                ins.then_inc(s["pn_ready"], 1)

            def body(t, n, b, first, last):
                if last < 2:
                    prepare(*after_tile(t, n, b))
                dve.wait_ge(s["e_ready"], t + 1)
                dve.wait_ge(s["pn_ready"], t + 1)
                mul = nc.vector.tensor_tensor(pn[b][:], pn[b][:], e[:], ALU.mult)
                mul.then_inc(s["gated"], 1)
                dve.wait_ge(s["gated"], t + 1)
                nc.vector.tensor_tensor(pn[b][:], pn[b][:], h[b][:], ALU.add).then_inc(s["out_ready"], 1)
                dve.wait_ge(s["out_ready"], t + 1)

            prepare(0, 0, 0)
            tile_loop(dve, body)



def _pool(cache):
    n = cache.shape[0]
    ops = cache[:, :, 0:2].reshape(n, 8, 8, 2, 2, KVH, HD)
    ops = ops.transpose(0, 3, 6, 4, 2, 5, 1).reshape(n, P, 256)
    keys = cache[:, :, 2].reshape(n, P, P).transpose(0, 2, 1)
    return np.concatenate([ops, keys, cache[:, :, 3].reshape(n, P, P)], 2)


def _layout(inputs):
    f = {k: np.asarray(v) for k, v in inputs.items()}
    pad = np.zeros((TOK - SEQ - N_SMP, D_MODEL), np.float32)
    x = np.concatenate([f["x_prompt"][0], f["x_sample"].reshape(N_SMP, D_MODEL), pad])
    pos = np.concatenate([np.arange(SEQ), PAST + np.arange(P) % DEC_SEQ]).astype(np.float32)
    half = HD // 2
    inv = np.float32(10000.0) ** (-np.arange(half, dtype=np.float32) / half)
    ang = (pos[:, None] * inv[None, :]).astype(np.float32)
    trig = np.stack([np.cos(ang), np.sin(ang)], 1).reshape(TILES, P, 2, half).astype(np.float32)
    w_in = f["w_in"][0].copy()
    w_in[:, :ATT_W] = w_in[:, :ATT_W].reshape(D_MODEL, KVH, HPG, HD).transpose(0, 2, 1, 3).reshape(D_MODEL, ATT_W)
    w_in[:, C_GL:C_Z] = w_in[:, C_GL:C_Z].reshape(D_MODEL, KVH, HPG, 3).transpose(0, 2, 1, 3).reshape(D_MODEL, 24)
    gains = np.concatenate([f["q_norm"][0][None], f["k_norm"][0]])
    tok = np.arange(P)
    seq = tok // DEC_SEQ
    same = np.stack([np.ones((P, P)), seq[:, None] == seq[None]], 1).astype(np.float32)
    tri = (same * (tok[:, None] <= tok[None])[:, None]).astype(np.float32)
    seqcol = (seq[:, None] == np.arange(DEC_BATCH)[None]).astype(np.float32)
    ends = np.arange(N_CMP_P) * S_CMP + L_CMP - 1
    w1 = f["cmp_w1"][0].reshape(2, 2, S_CMP, HD, HD)
    rg, rq = np.arange(64) // 32, np.arange(64) % DEC_SEQ
    gsum = ((rg[:, None] == rg[None]) & (rq[:, None] == rq[None])).astype(np.float32)
    nmask = np.where(np.arange(DEC_SEQ)[None] <= rq[:, None], 0, NEG).astype(np.float32)
    key = np.arange(WINDOW + DEC_SEQ)[None]
    wmask = np.where((key > rq[:, None]) & (key <= rq[:, None] + WINDOW), 0, NEG).astype(np.float32)
    c0, s0 = np.arange(2 * P)[:, None] * S_CMP, np.arange(N_SLC_S)[None] * L_SLC
    cover = np.maximum(np.minimum(c0 + L_CMP, s0 + L_SLC) - np.maximum(c0, s0), 0).astype(np.float32) / np.float32(L_CMP)
    cover = cover.reshape(2, P, N_SLC_S).transpose(1, 0, 2)
    cw = f["cache_win"][0].reshape(DEC_BATCH, WINDOW, 2, P)
    p_all = np.concatenate([f["p_prompt"][0, 0], f["p_sample"][0].reshape(N_SMP, PLE), np.zeros((TOK - SEQ - N_SMP, PLE), np.float32)])
    padoff = np.zeros((P, TILES, 2), np.float32)
    padoff[N_SMP:, NT, :] = DUMP + np.arange(2 * (P - N_SMP)).reshape(-1, 2)
    cm = {
        "xT": x.reshape(TILES, P, KC, P).transpose(0, 3, 2, 1),
        "trig": trig,
        "w_in": w_in.reshape(KC, P, C_END).transpose(1, 0, 2),
        "attn_norm": f["attn_norm"][0].reshape(KC, P).T,
        "head_gain": np.broadcast_to(gains, (P, 4, HD)),
        "ident": np.eye(P, dtype=np.float32),
        "cmp_pe": f["cmp_pe"][0].reshape(2, 2, 8, 2, HD).transpose(3, 4, 0, 2, 1).reshape(P, 2, 8, 2),
        "cmp_w2": f["cmp_w2"][0].transpose(1, 0, 2),
        "diag": np.where(tok[None] > tok[:, None], NEG, 0).astype(np.float32),
        "old": np.where(tok[None] <= tok[:, None], NEG, 0).astype(np.float32),
        "cmask": np.where(ends[None, None] <= (np.arange(NT)[None] * P + tok[:, None])[..., None], 0, NEG).astype(np.float32),
        "valid": (tok[:, None] >= L_CMP - 1).astype(np.float32),
        "cmp_w1_seg": w1.reshape(2, 2, 8, 2, HD, HD).transpose(3, 4, 0, 2, 1, 5).reshape(P, 2, 8, P),
        "cover": cover, "gsum": gsum, "nmask": nmask, "wmask": wmask,
        "page_table": f["page_table"],
        "pool": _pool(f["cache_kv"][0]),
        "win_pack": np.concatenate([cw[:, :, 0].transpose(0, 2, 1), cw[:, :, 1].reshape(DEC_BATCH, 4, P, P).transpose(0, 2, 1, 3).reshape(DEC_BATCH, P, 512)], 2),
        "cache_win": cw.reshape(DEC_BATCH, WINDOW, 256),
        "x": x,
        "w_out": np.concatenate([f["w_out"][0][:ATT_W].reshape(KVH, HPG, HD, D_MODEL).transpose(1, 0, 2, 3).reshape(ATT_W, D_MODEL), f["w_out"][0][ATT_W:]])
                   .reshape(KC, P, D_MODEL).transpose(1, 0, 2),
        "w_route": np.concatenate([f["w_rg"][0], f["w_re"][0]], 1).reshape(KC, P, 36).transpose(1, 0, 2),
        "b_route": np.broadcast_to(np.concatenate([f["b_rg"][0], f["b_re"][0]]), (P, 36)),
        "ffn_norm": np.broadcast_to(f["ffn_norm"][0], (P, D_MODEL)),
        "real": (tok < N_SMP).astype(np.float32)[:, None],
        "before": (tok[:, None] < tok[None]).astype(np.float32),
        "first": np.broadcast_to(np.arange(NE, dtype=np.float32) * P, (P, NE)),
        "padoff": padoff, "ids": np.arange(TOK, dtype=np.uint32).reshape(TILES, P).T,
        "blocks": np.broadcast_to(np.arange(OVER_BLOCKS, dtype=np.float32), (P, OVER_BLOCKS)),
        "w_gate": f["w_gate"][0], "w_up": f["w_up"][0], "w_down": f["w_down"][0],
        "w_ple_gate": f["w_ple_gate"][0].reshape(KC, P, D_MODEL).transpose(1, 0, 2),
        "w_ple_proj": f["w_ple_proj"][0].reshape(2, P, D_MODEL).transpose(1, 0, 2),
        "ple_norm": np.broadcast_to(f["ple_norm"][0], (P, D_MODEL)),
        "pT": p_all.reshape(TILES, P, 2, P).transpose(0, 3, 2, 1),
        "conv_w": f["conv_w"][0].T.reshape(6, P, CONV_W).transpose(1, 0, 2),
        "conv_b": f["conv_b"][0].reshape(6, P).T,
        "state_conv": f["state_conv"][0].transpose(2, 0, 1).reshape(6, P, DEC_BATCH, 3).transpose(1, 0, 2, 3),
        "tri": tri, "mask": np.where(tri > 0, 0, NEG).astype(np.float32), "same": same,
        "seqcol": seqcol, "seqrow": np.broadcast_to(seqcol.T, (P, DEC_BATCH, P)),
        "head_ssm": np.broadcast_to(np.stack([f["dt_bias"][0], f["a_log"][0], f["ssm_d"][0]]), (P, 3, SH)),
        "ssm_norm": np.broadcast_to(f["ssm_norm"][0], (P, D_INNER)),
        "state_ssm": f["state_ssm"][0].reshape(DEC_BATCH, 2, 4, HD, SN).transpose(1, 4, 0, 2, 3).reshape(P, DEC_BATCH, 256),
    }
    return {k: np.ascontiguousarray(v) for k, v in cm.items()}


_SCRATCH = {"z": (TOK, D_INNER), "gdt": (TOK, 32), "turned": (P, 12, TOK), "cv": (P, 6, TOK), "ssd": (TOK, 512), "pe_hid": (HD, 2), "kct": (P, N_CMP_P), "vc": (N_CMP_P, P), "attn": (TOK, 512),
            "h": (TOK, D_MODEL), "f": (TOK, D_MODEL), "route": (TOK, 66), "slot_tok": (SLOTS, 1, U32), "gidx": (TOK, 2, U32),
            "over": (1, OVER_BLOCKS + 1, I32), "ypad": (DUMP, D_MODEL)}
_OUTS = {"y": (TOK, D_MODEL), "win_new": (TOK, 256), "win_old": (DEC_BATCH, WINDOW - DEC_SEQ, 256), "kv_out": (TOK, 512), "conv_p": (P, 6, 3), "conv_s": (P, 6, DEC_BATCH, 3), "ssm_p": (P, 256), "ssm_s": (P, DEC_BATCH, 256)}


def build(nc, d):
    project_phase(nc, d)
    ssd_phase(nc, d)
    compress_prompt(nc, d)
    attend_prompt(nc, d)
    attend_samples(nc, d, d["pool"].shape[0])
    mix_phase(nc, d)
    dispatch_phase(nc, d)
    expert_phase(nc, d, False)
    expert_phase(nc, d, True)
    final_phase(nc, d)


def kernel(**inputs):
    import concourse.bacc as _bacc
    from concourse.bass_utils import run_bass_kernel_spmd as _run

    nc = _bacc.Bacc("TRN2", target_bir_lowering=False, num_devices=1)
    arrays, d = {}, {}
    for name, a in _layout(inputs).items():
        arrays[f"in_{name}"] = a
        d[name] = nc.dram_tensor(f"in_{name}", a.shape, mybir.dt.from_np(a.dtype), kind="ExternalInput").ap()
    for kind, tensors in (("Internal", _SCRATCH), ("ExternalOutput", _OUTS)):
        for name, shape in tensors.items():
            dt = F32 if isinstance(shape[-1], int) else shape[-1]
            shape = [n for n in shape if isinstance(n, int)]
            prefix = "scratch" if kind == "Internal" else "out"
            d[name] = nc.dram_tensor(f"{prefix}_{name}", shape, dt, kind=kind).ap()
    build(nc, d)
    r = _run(nc, [arrays], core_ids=[0])
    got = {k: np.asarray(r.results[0][f"out_{k}"]) for k in _OUTS}
    y, kv, win = got["y"], got["kv_out"], got["win_new"]
    smp = slice(SEQ, SEQ + N_SMP)
    win_s = np.concatenate([got["win_old"], win[smp].reshape(DEC_BATCH, DEC_SEQ, 256)], 1)
    ssm_p = got["ssm_p"].reshape(KVH, SN, HPG, HD).transpose(0, 2, 3, 1)
    ssm_s = got["ssm_s"].reshape(KVH, SN, DEC_BATCH, HPG, HD).transpose(2, 0, 3, 4, 1)
    return (y[:SEQ].reshape(1, SEQ, D_MODEL), y[smp].reshape(DEC_BATCH, DEC_SEQ, D_MODEL),
            kv[:SEQ].reshape(1, 1, SEQ, 4, KVH, HD), kv[smp].reshape(1, DEC_BATCH, DEC_SEQ, 4, KVH, HD),
            win[SEQ - WINDOW:SEQ].reshape(1, 1, WINDOW, 2, KVH, HD), win_s.reshape(1, DEC_BATCH, WINDOW, 2, KVH, HD),
            ssm_p.reshape(1, 1, SH, HD, SN), ssm_s.reshape(1, DEC_BATCH, SH, HD, SN),
            got["conv_p"].transpose(2, 1, 0).reshape(1, 1, CONV_W - 1, CONV_DIM), got["conv_s"].transpose(2, 3, 1, 0).reshape(1, DEC_BATCH, CONV_W - 1, CONV_DIM))
```
